# Optimizing a Trainium2 kernel written in Bass

```python
import math
import jax, jax.numpy as jnp
from jax import lax
import numpy as np

D_MODEL = 1024
BATCH = 1
SEQ = 256
DEPTH = 1

NSA_WIDTH = D_MODEL // 2
POOL_WIDTH = D_MODEL // 4
SGU_WIDTH = D_MODEL // 4
MIX_WIDTH = NSA_WIDTH + POOL_WIDTH + SGU_WIDTH

NSA_HEADS = 8
NSA_KV_GROUPS = 2
HEADS_PER_GROUP = NSA_HEADS // NSA_KV_GROUPS
HEAD_DIM = NSA_WIDTH // NSA_HEADS
KV_WIDTH = NSA_KV_GROUPS * HEAD_DIM
GATE_WIDTH = NSA_HEADS * 3
CMP_STRIDE = 16
CMP_LEN = 2 * CMP_STRIDE
CMP_HIDDEN = 2 * HEAD_DIM
SEL_BLOCK = 64
SEL_TOPK = 16
N_LOCAL_SEL = 2
SEL_RATIO = SEL_BLOCK // CMP_STRIDE
SEL_AGG = (1.0, 2.0, 2.0, 2.0, 1.0)
FORCE_SCORE = 1e9
WINDOW = 512
Q_BLOCK = 128

REL_BUCKETS = 32
REL_MAX_DIST = 1024

POOL_WINDOWS = (2, 4, 8, 16)
POOL_GROUPS = len(POOL_WINDOWS)
POOL_CH = POOL_WIDTH // POOL_GROUPS

SGU_GROUPS = 4
SGU_CH = SGU_WIDTH // SGU_GROUPS
SGU_CHUNK = 128

IN_WIDTHS = (NSA_WIDTH, KV_WIDTH, KV_WIDTH, KV_WIDTH, KV_WIDTH, KV_WIDTH, KV_WIDTH,
             GATE_WIDTH, POOL_WIDTH, SGU_WIDTH, SGU_WIDTH)
IN_WIDTH = sum(IN_WIDTHS)
IN_SPLITS = tuple(int(s) for s in np.cumsum(IN_WIDTHS)[:-1])

MEM_LEN = 256
MEM_HEADS = 4
MEM_HEAD_DIM = D_MODEL // MEM_HEADS

FFN_HIDDEN = ((11 * D_MODEL // 4) // 128) * 128
CONV_WIDTH = 3

EPS = 1e-6
F32 = jnp.float32


def rms_norm(x, g):
    xf = x.astype(F32)
    y = xf * lax.rsqrt(jnp.mean(xf * xf, axis=-1, keepdims=True) + EPS)
    return (y * g.astype(F32)).astype(x.dtype)

def layer_norm(x, g, b):
    xf = x.astype(F32)
    mu = jnp.mean(xf, axis=-1, keepdims=True)
    var = jnp.mean(jnp.square(xf - mu), axis=-1, keepdims=True)
    return ((xf - mu) * lax.rsqrt(var + EPS) * g.astype(F32) + b.astype(F32)).astype(x.dtype)

def t5_bucket(dist):
    n = jnp.maximum(dist, 0)
    max_exact = REL_BUCKETS // 2
    nf = jnp.maximum(n, 1).astype(F32)
    large = max_exact + (jnp.log(nf / max_exact) / math.log(REL_MAX_DIST / max_exact)
                         * (REL_BUCKETS - max_exact)).astype(jnp.int32)
    large = jnp.minimum(large, REL_BUCKETS - 1)
    return jnp.where(n < max_exact, n, large)

def masked_softmax(s, mask):
    s = jnp.where(mask, s.astype(F32), -jnp.inf)
    m = jnp.max(s, axis=-1, keepdims=True)
    m = jnp.where(jnp.isfinite(m), m, 0.0)
    e = jnp.where(mask, jnp.exp(s - m), 0.0)
    return e / jnp.maximum(jnp.sum(e, axis=-1, keepdims=True), 1.0)

def compress(kv, pos, w1, b1, w2, b2):
    B, S, G, dk = kv.shape
    r = kv.reshape(B, S // CMP_STRIDE, CMP_STRIDE, G, dk)
    blocks = jnp.concatenate([r[:, :-1], r[:, 1:]], axis=2) + pos[None, None, :, None, :]
    h = jax.nn.gelu(jnp.einsum('bclgd,ldh->bcgh', blocks, w1) + b1)
    return jnp.einsum('bcgh,hd->bcgd', h, w2) + b2

def nsa_mixer(q, k_cmp, v_cmp, k_sel, v_sel, k_win, v_win, gates, rel_bias,
              cmp_pos, cmp_w1, cmp_b1, cmp_w2, cmp_b2):
    B, S, G, Hg, dk = q.shape
    scale = dk ** -0.5
    kc = compress(k_cmp, cmp_pos[0], cmp_w1[0], cmp_b1[0], cmp_w2[0], cmp_b2[0])
    vc = compress(v_cmp, cmp_pos[1], cmp_w1[1], cmp_b1[1], cmp_w2[1], cmp_b2[1])
    NC = kc.shape[1]
    NS = S // SEL_BLOCK
    topk = min(SEL_TOPK, NS)
    ksb = jnp.transpose(k_sel.reshape(B, NS, SEL_BLOCK, G, dk), (0, 3, 1, 2, 4))
    vsb = jnp.transpose(v_sel.reshape(B, NS, SEL_BLOCK, G, dk), (0, 3, 1, 2, 4))
    kwp = jnp.pad(k_win, ((0, 0), (WINDOW, 0), (0, 0), (0, 0)))
    vwp = jnp.pad(v_win, ((0, 0), (WINDOW, 0), (0, 0), (0, 0)))
    cmp_end = jnp.arange(NC) * CMP_STRIDE + CMP_LEN - 1
    sel_start = jnp.arange(NS) * SEL_BLOCK
    jj = jnp.arange(NS)
    bias_g = jnp.transpose(rel_bias.reshape(REL_BUCKETS, G, Hg), (1, 0, 2))
    gidx = jnp.arange(G)
    bidx = jnp.arange(B)
    ti = jnp.arange(Q_BLOCK)
    wj = jnp.arange(Q_BLOCK + WINDOW)
    wdist = ti[:, None] + WINDOW - wj[None, :]
    win_band = (wdist >= 0) & (wdist < WINDOW)
    win_bias = jnp.transpose(rel_bias[t5_bucket(wdist)].reshape(Q_BLOCK, Q_BLOCK + WINDOW, G, Hg), (2, 3, 0, 1))
    nblk = S // Q_BLOCK
    qb = jnp.moveaxis(q.reshape(B, nblk, Q_BLOCK, G, Hg, dk), 1, 0)
    gb = jnp.moveaxis(gates.reshape(B, nblk, Q_BLOCK, G, Hg, 3), 1, 0)

    def block(args):
        qi, gi, i = args
        s0 = i * Q_BLOCK
        t = s0 + ti
        qs = qi * scale
        sc = jnp.einsum('btghd,bcgd->bghtc', qs, kc)
        cdist = t[:, None] - cmp_end[None, :]
        cbias = jnp.transpose(rel_bias[t5_bucket(cdist)].reshape(Q_BLOCK, NC, G, Hg), (2, 3, 0, 1))
        pc = masked_softmax(sc + cbias, cdist >= 0)
        o_cmp = jnp.einsum('bghtc,bcgd->btghd', pc.astype(vc.dtype), vc)
        imp = jnp.pad(jnp.sum(pc, axis=2), ((0, 0), (0, 0), (0, 0), (1, 1)))
        p_sel = sum(w * imp[..., m:m + SEL_RATIO * NS:SEL_RATIO] for m, w in enumerate(SEL_AGG))
        blk_q = t // SEL_BLOCK
        rel_blk = blk_q[:, None] - jj[None, :]
        svalid = sel_start[None, :] <= t[:, None]
        forced = (jj[None, :] == 0) | ((rel_blk >= 0) & (rel_blk < N_LOCAL_SEL))
        score = jnp.where(forced, FORCE_SCORE, jnp.where(svalid, p_sel, -1.0))
        _, sidx = lax.top_k(score, topk)
        ks = ksb[bidx[:, None, None, None], gidx[None, :, None, None], sidx]
        vs = vsb[bidx[:, None, None, None], gidx[None, :, None, None], sidx]
        spos = sidx[..., None] * SEL_BLOCK + jnp.arange(SEL_BLOCK)
        sdist = t[None, None, :, None, None] - spos
        sbias = bias_g[gidx[None, :, None, None, None], t5_bucket(sdist)]
        ss = jnp.einsum('btghd,bgtkld->bghtkl', qs, ks) + jnp.transpose(sbias, (0, 1, 5, 2, 3, 4))
        nsel = topk * SEL_BLOCK
        ps = masked_softmax(ss.reshape(B, G, Hg, Q_BLOCK, nsel), (sdist >= 0).reshape(B, G, 1, Q_BLOCK, nsel))
        o_sel = jnp.einsum('bghtn,bgtnd->btghd', ps.astype(vs.dtype), vs.reshape(B, G, Q_BLOCK, nsel, dk))
        kw = lax.dynamic_slice_in_dim(kwp, s0, Q_BLOCK + WINDOW, axis=1)
        vw = lax.dynamic_slice_in_dim(vwp, s0, Q_BLOCK + WINDOW, axis=1)
        wpos = s0 - WINDOW + wj
        sw = jnp.einsum('btghd,bsgd->bghts', qs, kw) + win_bias
        pw = masked_softmax(sw, win_band & (wpos >= 0)[None, :])
        o_win = jnp.einsum('bghts,bsgd->btghd', pw.astype(vw.dtype), vw)
        return gi[..., 0:1] * o_cmp + gi[..., 1:2] * o_sel + gi[..., 2:3] * o_win

    out = lax.map(block, (qb, gb, jnp.arange(nblk)))
    return jnp.moveaxis(out, 0, 1).reshape(B, S, G * Hg * dk)

def pool_mixer(p, w, scale):
    B, S, C = p.shape
    pf = p.astype(F32)
    cs = jnp.pad(jnp.cumsum(pf, axis=1), ((0, 0), (1, 0), (0, 0)))
    t = jnp.arange(S)
    outs = []
    for gi, win in enumerate(POOL_WINDOWS):
        seg = cs[:, :, gi * POOL_CH:(gi + 1) * POOL_CH]
        lo = jnp.maximum(t + 1 - win, 0)
        cnt = jnp.minimum(t + 1, win).astype(F32)
        outs.append((seg[:, 1:] - seg[:, lo]) / cnt[None, :, None] - pf[:, :, gi * POOL_CH:(gi + 1) * POOL_CH])
    d = jnp.stack(outs, axis=2).astype(p.dtype)
    return jnp.einsum('bsgc,gcd->bsgd', d, w).reshape(B, S, C) * scale

def sgu_mixer(u, v, norm_g, norm_b, w_s, b_s):
    B, S, C = u.shape
    u = jax.nn.gelu(u)
    v = layer_norm(jax.nn.gelu(v), norm_g, norm_b)
    vc = v.reshape(B, S // SGU_CHUNK, SGU_CHUNK, SGU_GROUPS, SGU_CH)
    causal = jnp.tril(jnp.ones((SGU_CHUNK, SGU_CHUNK), dtype=bool))
    ws = jnp.where(causal, w_s, 0.0)
    mixed = jnp.einsum('hts,bnshc->bnthc', ws, vc) + jnp.transpose(b_s)[:, :, None]
    return u * mixed.reshape(B, S, C)

def memory_attention(h, mem_n, wq, wk, wv, wo):
    B, S, D = h.shape
    M = mem_n.shape[1]
    q = (h @ wq).reshape(B, S, MEM_HEADS, MEM_HEAD_DIM)
    k = (mem_n @ wk).reshape(B, M, MEM_HEADS, MEM_HEAD_DIM)
    v = (mem_n @ wv).reshape(B, M, MEM_HEADS, MEM_HEAD_DIM)
    s = jnp.einsum('bshd,bmhd->bhsm', q, k).astype(F32) * (MEM_HEAD_DIM ** -0.5)
    p = jax.nn.softmax(s, axis=-1).astype(v.dtype)
    return jnp.einsum('bhsm,bmhd->bshd', p, v).reshape(B, S, D) @ wo

def conv_ffn(h, w_up, conv_w, conv_b, w_down):
    a = h @ w_up
    a = lax.conv_general_dilated(a, conv_w[:, None, :], window_strides=(1,),
                                 padding=[(CONV_WIDTH - 1, 0)],
                                 dimension_numbers=('NWC', 'WIO', 'NWC'),
                                 feature_group_count=a.shape[-1]) + conv_b
    gate, val = jnp.split(a, 2, axis=-1)
    return (jax.nn.gelu(gate) * val) @ w_down

def first_inputs(seed: int = 0) -> dict:
    key = jax.random.key(seed)
    ks = iter(jax.random.split(key, 40))

    def nrm(shape, scale):
        return jax.random.normal(next(ks), shape, F32) * scale

    def gain(shape):
        return 1.0 + 0.1 * jax.random.normal(next(ks), shape, F32)

    L, D, H2 = DEPTH, D_MODEL, 2 * FFN_HIDDEN
    return {
        'x': nrm((BATCH, SEQ, D), 1.0),
        'mem': nrm((BATCH, MEM_LEN, D), 1.0),
        'rel_bias': nrm((REL_BUCKETS, NSA_HEADS), 0.2),
        'mix_norm_pre': gain((L, D)),
        'mix_norm_post': gain((L, D)),
        'w_in': nrm((L, D, IN_WIDTH), D ** -0.5),
        'cmp_pos': nrm((L, 2, CMP_LEN, HEAD_DIM), 0.1),
        'cmp_w1': nrm((L, 2, CMP_LEN, HEAD_DIM, CMP_HIDDEN), (CMP_LEN * HEAD_DIM) ** -0.5),
        'cmp_b1': nrm((L, 2, CMP_HIDDEN), 0.01),
        'cmp_w2': nrm((L, 2, CMP_HIDDEN, HEAD_DIM), CMP_HIDDEN ** -0.5),
        'cmp_b2': nrm((L, 2, HEAD_DIM), 0.01),
        'pool_w': nrm((L, POOL_GROUPS, POOL_CH, POOL_CH), POOL_CH ** -0.5),
        'pool_scale': gain((L, POOL_WIDTH)),
        'sgu_norm_g': gain((L, SGU_WIDTH)),
        'sgu_norm_b': nrm((L, SGU_WIDTH), 0.01),
        'sgu_w': nrm((L, SGU_GROUPS, SGU_CHUNK, SGU_CHUNK), SGU_CHUNK ** -0.5),
        'sgu_b': gain((L, SGU_GROUPS, SGU_CHUNK)),
        'w_out': nrm((L, MIX_WIDTH, D), MIX_WIDTH ** -0.5),
        'mem_norm_pre': gain((L, D)),
        'mem_norm_kv': gain((L, D)),
        'mem_norm_post': gain((L, D)),
        'w_mq': nrm((L, D, D), D ** -0.5),
        'w_mk': nrm((L, D, D), D ** -0.5),
        'w_mv': nrm((L, D, D), D ** -0.5),
        'w_mo': nrm((L, D, D), D ** -0.5),
        'ffn_norm_pre': gain((L, D)),
        'ffn_norm_post': gain((L, D)),
        'w_up': nrm((L, D, H2), D ** -0.5),
        'conv_w': nrm((L, CONV_WIDTH, H2), CONV_WIDTH ** -0.5),
        'conv_b': nrm((L, H2), 0.01),
        'w_down': nrm((L, FFN_HIDDEN, D), FFN_HIDDEN ** -0.5),
    }

def first_block(x, mem, rel_bias, mix_norm_pre, mix_norm_post, w_in, cmp_pos, cmp_w1, cmp_b1,
              cmp_w2, cmp_b2, pool_w, pool_scale, sgu_norm_g, sgu_norm_b, sgu_w, sgu_b, w_out,
              mem_norm_pre, mem_norm_kv, mem_norm_post, w_mq, w_mk, w_mv, w_mo,
              ffn_norm_pre, ffn_norm_post, w_up, conv_w, conv_b, w_down):
    B, S, D = x.shape
    G, Hg, dk = NSA_KV_GROUPS, HEADS_PER_GROUP, HEAD_DIM
    for l in range(DEPTH):
        h = rms_norm(x, mix_norm_pre[l])
        proj = h @ w_in[l]
        q, kc, vc, ksl, vsl, kw, vw, gt, pin, u, v = jnp.split(proj, IN_SPLITS, axis=-1)
        gates = jax.nn.sigmoid(gt.astype(F32)).astype(x.dtype).reshape(B, S, G, Hg, 3)
        kv = lambda a: a.reshape(B, S, G, dk)
        out_a = nsa_mixer(q.reshape(B, S, G, Hg, dk), kv(kc), kv(vc), kv(ksl), kv(vsl), kv(kw), kv(vw),
                          gates, rel_bias, cmp_pos[l], cmp_w1[l], cmp_b1[l], cmp_w2[l], cmp_b2[l])
        out_b = pool_mixer(pin, pool_w[l], pool_scale[l])
        out_c = sgu_mixer(u, v, sgu_norm_g[l], sgu_norm_b[l], sgu_w[l], sgu_b[l])
        mix = jnp.concatenate([out_a, out_b, out_c], axis=-1) @ w_out[l]
        x = x + rms_norm(mix, mix_norm_post[l])
        h = rms_norm(x, mem_norm_pre[l])
        m = rms_norm(mem, mem_norm_kv[l])
        x = x + rms_norm(memory_attention(h, m, w_mq[l], w_mk[l], w_mv[l], w_mo[l]), mem_norm_post[l])
        h = rms_norm(x, ffn_norm_pre[l])
        x = x + rms_norm(conv_ffn(h, w_up[l], conv_w[l], conv_b[l], w_down[l]), ffn_norm_post[l])
    return x


D_MIX = 1024
GDN_HEADS = 4
GDN_HEAD_DIM = 128
GDN_WIDTH = 512
GDN_CONV = 4
GDN_CHUNK = 64
DSA_HEADS = 4
DSA_HEAD_DIM = 64
DSA_WIDTH = 256
DSA_Q_RANK = 256
DSA_KV_RANK = 128
IDX_HEADS = 4
IDX_DIM = 64
DSA_TOPK_MAX = 256
CONV_CH = 256
CONV_WIDTH_2 = 31
XA_HEADS = 4
XA_HEAD_DIM = 128
XA_WIDTH = 512
D_FF = 4 * D_MODEL

IN_SPLITS_2 = (3 * GDN_WIDTH, GDN_WIDTH, GDN_HEADS, GDN_HEADS,
             DSA_Q_RANK, DSA_KV_RANK, IDX_DIM, IDX_HEADS, 2 * CONV_CH)
N_IN = 3 * GDN_WIDTH + GDN_WIDTH + 2 * GDN_HEADS + DSA_Q_RANK + DSA_KV_RANK + IDX_DIM + IDX_HEADS + 2 * CONV_CH


def rms_norm_2(x, g):
    xf = x.astype(jnp.float32)
    y = xf * lax.rsqrt(jnp.mean(xf * xf, axis=-1, keepdims=True) + EPS)
    return (y * g.astype(jnp.float32)).astype(x.dtype)

def layer_norm_2(x, g, b):
    xf = x.astype(jnp.float32)
    mu = jnp.mean(xf, axis=-1, keepdims=True)
    xc = xf - mu
    var = jnp.mean(xc * xc, axis=-1, keepdims=True)
    y = xc * lax.rsqrt(var + EPS) * g.astype(jnp.float32) + b.astype(jnp.float32)
    return y.astype(x.dtype)

def l2_norm(x):
    return x * lax.rsqrt(jnp.sum(x * x, axis=-1, keepdims=True) + EPS)

def split_cols(t, sizes):
    out = []
    off = 0
    for n in sizes:
        out.append(t[..., off:off + n])
        off += n
    return out

def causal_depthwise_conv(x, w):
    k, c = w.shape
    return lax.conv_general_dilated(
        x, w[:, None, :].astype(x.dtype), window_strides=(1,), padding=((k - 1, 0),),
        dimension_numbers=("NWC", "WIO", "NWC"), feature_group_count=c)

def gated_delta_rule(q, k, v, g, beta):
    b, s, h, dk = q.shape
    dv = v.shape[-1]
    c = GDN_CHUNK
    n = s // c
    q = q * (dk ** -0.5)

    def chunk(t):
        return jnp.moveaxis(t.reshape((b, n, c) + t.shape[2:]), 3, 2)

    qc, kc, vc = chunk(q), chunk(k), chunk(v)
    gc, bc = chunk(g), chunk(beta)
    decay = jnp.cumsum(gc, axis=-1)
    tril = jnp.tril(jnp.ones((c, c), bool))
    strict = jnp.tril(jnp.ones((c, c), bool), -1)
    diff = decay[..., :, None] - decay[..., None, :]
    gamma = jnp.where(tril, jnp.exp(jnp.where(tril, diff, 0.0)), 0.0)
    kb = kc * bc[..., None]
    a_mat = jnp.where(strict, jnp.einsum("bnhid,bnhjd->bnhij", kb, kc) * gamma, 0.0)
    lhs = a_mat + jnp.eye(c, dtype=a_mat.dtype)
    rhs = jnp.concatenate([vc * bc[..., None], kb * jnp.exp(decay)[..., None]], axis=-1)
    sol = lax.linalg.triangular_solve(lhs, rhs, left_side=True, lower=True, unit_diagonal=True)
    u, w = sol[..., :dv], sol[..., dv:]
    qk = jnp.where(tril, jnp.einsum("bnhid,bnhjd->bnhij", qc, kc) * gamma, 0.0)

    def step(state, inp):
        q_i, k_i, u_i, w_i, qk_i, dec_i = inp
        v_new = u_i - jnp.einsum("bhcd,bhde->bhce", w_i, state)
        o = (jnp.einsum("bhcd,bhde->bhce", q_i * jnp.exp(dec_i)[..., None], state)
             + jnp.einsum("bhij,bhje->bhie", qk_i, v_new))
        last = dec_i[..., -1]
        k_dec = k_i * jnp.exp(last[..., None] - dec_i)[..., None]
        state = state * jnp.exp(last)[..., None, None] + jnp.einsum("bhcd,bhce->bhde", k_dec, v_new)
        return state, o

    xs = tuple(jnp.moveaxis(t, 1, 0) for t in (qc, kc, u, w, qk, decay))
    _, o = lax.scan(step, jnp.zeros((b, h, dk, dv), jnp.float32), xs)
    o = jnp.swapaxes(jnp.moveaxis(o, 0, 1), 2, 3)
    return o.reshape(b, s, h, dv)

def gdn_mixer(qkv, z, a_g, b_g, conv_w, a_log, dt_bias, norm_g):
    b, s, _ = qkv.shape
    dt = qkv.dtype
    qkv = jax.nn.silu(causal_depthwise_conv(qkv, conv_w)).astype(jnp.float32)
    q, k, v = jnp.split(qkv, 3, axis=-1)
    shp = (b, s, GDN_HEADS, GDN_HEAD_DIM)
    q = l2_norm(q.reshape(shp))
    k = l2_norm(k.reshape(shp))
    v = v.reshape(shp)
    g = -jnp.exp(a_log.astype(jnp.float32)) * jax.nn.softplus(a_g.astype(jnp.float32) + dt_bias.astype(jnp.float32))
    beta = jax.nn.sigmoid(b_g.astype(jnp.float32))
    o = gated_delta_rule(q, k, v, g, beta)
    o = rms_norm_2(o, norm_g) * jax.nn.silu(z.astype(jnp.float32).reshape(shp))
    return o.reshape(b, s, GDN_WIDTH).astype(dt)

def dsa_mixer(c_q, c_kv, k_idx, w_idx, w_qb, w_qi, w_kvb, q_norm_g, k_norm_g):
    b, s, _ = c_q.shape
    q = rms_norm_2((c_q @ w_qb).reshape(b, s, DSA_HEADS, DSA_HEAD_DIM), q_norm_g)
    kv = c_kv @ w_kvb
    k = rms_norm_2(kv[..., :DSA_HEAD_DIM], k_norm_g)
    v = kv[..., DSA_HEAD_DIM:]
    q_idx = (c_q @ w_qi).reshape(b, s, IDX_HEADS, IDX_DIM)
    w_idx = w_idx.astype(jnp.float32) * (IDX_HEADS ** -0.5 * IDX_DIM ** -0.5)
    k_idx = k_idx.astype(jnp.float32)
    topk = min(DSA_TOPK_MAX, s // 4)
    nb = s // Q_BLOCK
    pos = jnp.arange(s, dtype=jnp.int32)

    def blk(t):
        return jnp.moveaxis(t.reshape((b, nb, Q_BLOCK) + t.shape[2:]), 1, 0)

    def attend(inp):
        q_b, qi_b, w_b, t_b = inp
        causal = pos[None, :] <= t_b[:, None]
        idx_logits = jnp.einsum("bqhd,bsd->bqhs", qi_b.astype(jnp.float32), k_idx)
        score = jnp.einsum("bqh,bqhs->bqs", w_b, jax.nn.relu(idx_logits))
        score = jnp.where(causal[None], score, -jnp.inf)
        _, sel = lax.top_k(score, topk)
        k_sel = jax.vmap(lambda kk, ii: kk[ii])(k, sel)
        v_sel = jax.vmap(lambda vv, ii: vv[ii])(v, sel)
        valid = sel <= t_b[None, :, None]
        logits = jnp.einsum("bqhd,bqkd->bqhk", q_b.astype(jnp.float32), k_sel.astype(jnp.float32)) * (DSA_HEAD_DIM ** -0.5)
        logits = jnp.where(valid[:, :, None, :], logits, -jnp.inf)
        p = jax.nn.softmax(logits, axis=-1)
        return jnp.einsum("bqhk,bqkd->bqhd", p, v_sel.astype(jnp.float32)).astype(q_b.dtype)

    o = lax.map(attend, (blk(q), blk(q_idx), blk(w_idx), pos.reshape(nb, Q_BLOCK)))
    return jnp.moveaxis(o, 0, 1).reshape(b, s, DSA_WIDTH)

def conv_mixer(ug, dw, dw_b, ln_g, ln_b):
    u, gate = jnp.split(ug, 2, axis=-1)
    y = u * jax.nn.sigmoid(gate)
    y = causal_depthwise_conv(y, dw) + dw_b
    y = layer_norm_2(y, ln_g, ln_b)
    return jax.nn.silu(y)

def memory_cross_attention(h, mem_n, wq, wkv, q_g, k_g, wo):
    b, s, _ = h.shape
    m = mem_n.shape[1]
    q = rms_norm_2((h @ wq).reshape(b, s, XA_HEADS, XA_HEAD_DIM), q_g)
    kv = mem_n @ wkv
    k = rms_norm_2(kv[..., :XA_WIDTH].reshape(b, m, XA_HEADS, XA_HEAD_DIM), k_g)
    v = kv[..., XA_WIDTH:].reshape(b, m, XA_HEADS, XA_HEAD_DIM)
    logits = jnp.einsum("bshd,bmhd->bhsm", q.astype(jnp.float32), k.astype(jnp.float32)) * (XA_HEAD_DIM ** -0.5)
    p = jax.nn.softmax(logits, axis=-1)
    o = jnp.einsum("bhsm,bmhd->bshd", p, v.astype(jnp.float32)).astype(h.dtype)
    return o.reshape(b, s, XA_WIDTH) @ wo

def second_inputs(seed: int = 0) -> dict:
    key = jax.random.key(seed)
    ks = jax.random.split(key, 32)
    f32 = jnp.float32

    def nrm(k, shape, scale):
        return jax.random.normal(k, shape, f32) * scale

    def gain(k, shape):
        return 1.0 + 0.02 * jax.random.normal(k, shape, f32)

    dt = jnp.exp(jax.random.uniform(ks[5], (DEPTH, GDN_HEADS), f32, math.log(1e-3), math.log(1e-1)))
    dt_bias = dt + jnp.log(-jnp.expm1(-dt))
    return {
        "x": nrm(ks[0], (BATCH, SEQ, D_MODEL), 1.0),
        "mem": nrm(ks[1], (BATCH, MEM_LEN, D_MODEL), 1.0),
        "norm_mix": gain(ks[2], (DEPTH, D_MODEL)),
        "w_in": nrm(ks[3], (DEPTH, D_MODEL, N_IN), D_MODEL ** -0.5),
        "gdn_conv": nrm(ks[4], (DEPTH, GDN_CONV, 3 * GDN_WIDTH), GDN_CONV ** -0.5),
        "gdn_a_log": jnp.log(jax.random.uniform(ks[6], (DEPTH, GDN_HEADS), f32, 1.0, 16.0)),
        "gdn_dt_bias": dt_bias,
        "gdn_norm": gain(ks[7], (DEPTH, GDN_HEAD_DIM)),
        "dsa_w_qb": nrm(ks[8], (DEPTH, DSA_Q_RANK, DSA_WIDTH), DSA_Q_RANK ** -0.5),
        "dsa_w_qi": nrm(ks[9], (DEPTH, DSA_Q_RANK, IDX_HEADS * IDX_DIM), DSA_Q_RANK ** -0.5),
        "dsa_w_kvb": nrm(ks[10], (DEPTH, DSA_KV_RANK, 2 * DSA_HEAD_DIM), DSA_KV_RANK ** -0.5),
        "dsa_q_norm": gain(ks[11], (DEPTH, DSA_HEAD_DIM)),
        "dsa_k_norm": gain(ks[12], (DEPTH, DSA_HEAD_DIM)),
        "conv_dw": nrm(ks[13], (DEPTH, CONV_WIDTH_2, CONV_CH), CONV_WIDTH_2 ** -0.5),
        "conv_dw_b": nrm(ks[14], (DEPTH, CONV_CH), 0.02),
        "conv_ln_g": gain(ks[15], (DEPTH, CONV_CH)),
        "conv_ln_b": nrm(ks[16], (DEPTH, CONV_CH), 0.02),
        "w_out": nrm(ks[17], (DEPTH, D_MIX, D_MODEL), D_MIX ** -0.5),
        "norm_mem": gain(ks[18], (D_MODEL,)),
        "norm_cross": gain(ks[19], (DEPTH, D_MODEL)),
        "xa_wq": nrm(ks[20], (DEPTH, D_MODEL, XA_WIDTH), D_MODEL ** -0.5),
        "xa_wkv": nrm(ks[21], (DEPTH, D_MODEL, 2 * XA_WIDTH), D_MODEL ** -0.5),
        "xa_q_norm": gain(ks[22], (DEPTH, XA_HEAD_DIM)),
        "xa_k_norm": gain(ks[23], (DEPTH, XA_HEAD_DIM)),
        "xa_wo": nrm(ks[24], (DEPTH, XA_WIDTH, D_MODEL), XA_WIDTH ** -0.5),
        "norm_mlp": gain(ks[25], (DEPTH, D_MODEL)),
        "mlp_w1": nrm(ks[26], (DEPTH, D_MODEL, D_FF), D_MODEL ** -0.5),
        "mlp_w2": nrm(ks[27], (DEPTH, D_FF, D_MODEL), D_FF ** -0.5),
    }

def second_block(x, mem, norm_mix, w_in, gdn_conv, gdn_a_log, gdn_dt_bias, gdn_norm,
              dsa_w_qb, dsa_w_qi, dsa_w_kvb, dsa_q_norm, dsa_k_norm,
              conv_dw, conv_dw_b, conv_ln_g, conv_ln_b, w_out,
              norm_mem, norm_cross, xa_wq, xa_wkv, xa_q_norm, xa_k_norm, xa_wo,
              norm_mlp, mlp_w1, mlp_w2):
    mem_n = rms_norm_2(mem, norm_mem)
    for l in range(DEPTH):
        h = rms_norm_2(x, norm_mix[l])
        proj = h @ w_in[l]
        qkv, z, a_g, b_g, c_q, c_kv, k_idx, w_idx, ug = split_cols(proj, IN_SPLITS_2)
        y_a = gdn_mixer(qkv, z, a_g, b_g, gdn_conv[l], gdn_a_log[l], gdn_dt_bias[l], gdn_norm[l])
        y_b = dsa_mixer(c_q, c_kv, k_idx, w_idx, dsa_w_qb[l], dsa_w_qi[l], dsa_w_kvb[l],
                        dsa_q_norm[l], dsa_k_norm[l])
        y_c = conv_mixer(ug, conv_dw[l], conv_dw_b[l], conv_ln_g[l], conv_ln_b[l])
        x = x + jnp.concatenate([y_a, y_b, y_c], axis=-1) @ w_out[l]
        x = x + memory_cross_attention(rms_norm_2(x, norm_cross[l]), mem_n, xa_wq[l], xa_wkv[l],
                                       xa_q_norm[l], xa_k_norm[l], xa_wo[l])
        hm = rms_norm_2(x, norm_mlp[l]) @ mlp_w1[l]
        x = x + jnp.square(jax.nn.relu(hm)) @ mlp_w2[l]
    return x


def setup_inputs(seed=0):
    out = dict(first_inputs(seed))
    for name, value in second_inputs(seed + 1).items():
        if name != "x":
            out[name + "_2"] = value
    return out


def reference(
    x, mem, rel_bias, mix_norm_pre, mix_norm_post, w_in, cmp_pos, cmp_w1, cmp_b1, cmp_w2,
    cmp_b2, pool_w, pool_scale, sgu_norm_g, sgu_norm_b, sgu_w, sgu_b, w_out, mem_norm_pre,
    mem_norm_kv, mem_norm_post, w_mq, w_mk, w_mv, w_mo, ffn_norm_pre, ffn_norm_post, w_up,
    conv_w, conv_b, w_down, mem_2, norm_mix_2, w_in_2, gdn_conv_2, gdn_a_log_2, gdn_dt_bias_2,
    gdn_norm_2, dsa_w_qb_2, dsa_w_qi_2, dsa_w_kvb_2, dsa_q_norm_2, dsa_k_norm_2, conv_dw_2,
    conv_dw_b_2, conv_ln_g_2, conv_ln_b_2, w_out_2, norm_mem_2, norm_cross_2, xa_wq_2, xa_wkv_2,
    xa_q_norm_2, xa_k_norm_2, xa_wo_2, norm_mlp_2, mlp_w1_2, mlp_w2_2,
):
    x = first_block(
        x, mem, rel_bias, mix_norm_pre, mix_norm_post, w_in, cmp_pos, cmp_w1, cmp_b1, cmp_w2,
        cmp_b2, pool_w, pool_scale, sgu_norm_g, sgu_norm_b, sgu_w, sgu_b, w_out, mem_norm_pre,
        mem_norm_kv, mem_norm_post, w_mq, w_mk, w_mv, w_mo, ffn_norm_pre, ffn_norm_post, w_up,
        conv_w, conv_b, w_down,
    )
    return second_block(
        x, mem_2, norm_mix_2, w_in_2, gdn_conv_2, gdn_a_log_2, gdn_dt_bias_2, gdn_norm_2,
        dsa_w_qb_2, dsa_w_qi_2, dsa_w_kvb_2, dsa_q_norm_2, dsa_k_norm_2, conv_dw_2, conv_dw_b_2,
        conv_ln_g_2, conv_ln_b_2, w_out_2, norm_mem_2, norm_cross_2, xa_wq_2, xa_wkv_2,
        xa_q_norm_2, xa_k_norm_2, xa_wo_2, norm_mlp_2, mlp_w1_2, mlp_w2_2,
    )


_drawn_inputs = setup_inputs


def setup_inputs(seed=0):
    import zlib

    import numpy as np

    out = dict(_drawn_inputs(seed))
    spreads = {}
    factors = {'cmp_b1': 8.0,
     'cmp_b2': 8.0,
     'sgu_norm_b': 8.0,
     'conv_b': 6.794,
     'norm_mix_2': 5.807,
     'gdn_norm_2': 8.0,
     'dsa_q_norm_2': 8.0,
     'dsa_k_norm_2': 8.0,
     'conv_dw_b_2': 8.0,
     'conv_ln_g_2': 64.0,
     'conv_ln_b_2': 43.938,
     'norm_mem_2': 8.0,
     'norm_cross_2': 8.0,
     'xa_q_norm_2': 8.0,
     'xa_k_norm_2': 8.0,
     'norm_mlp_2': 15.185}
    for name, (base, spread) in spreads.items():
        noise = np.random.default_rng([zlib.crc32(name.encode()), seed]).standard_normal(out[name].shape)
        drawn = base * np.exp(spread * noise) if base else spread * noise
        out[name] = __import__('jax').numpy.asarray(drawn.astype(out[name].dtype))
    for name, factor in factors.items():
        out[name] = (out[name] * factor).astype(out[name].dtype)
    return out
```

```python
from contextlib import ExitStack

import numpy as np

import concourse.bass as bass
from concourse import mybir

F32 = mybir.dt.float32
F32R = mybir.dt.float32r
ALU = mybir.AluOpType
ACT = mybir.ActivationFunctionType
AX = mybir.AxisListType.X

P = 128
SEQ = 256
TT = SEQ // P
D = 1024
KD = D // P
EPS = 1e-6
MASKED = -1e30

HEADS = 8
GROUPS = 2
HG = HEADS // GROUPS
DK = 64
CMP_STRIDE = 16
CMP_LEN = 32
NCMP = SEQ // CMP_STRIDE - 1
CMP_PAIRS = CMP_LEN // 2
MEM_HEADS = 4
FFN = ((11 * D // 4) // 128) * 128
FFN_PAIRS = FFN // P
POOL_WINDOWS = (2, 4, 8, 16)
REL_BUCKETS = 32
REL_MAX_DIST = 1024
DIST_COLS = 2 * SEQ

GDN_HEADS = 4
CHUNK = 64
NCHUNK = SEQ // CHUNK
LEVELS = 6
DSA_HEADS = 4
DSA_TOPK = 64
CONV_TAPS = 31
XA_HEADS = 4
MLP_UNITS = 4 * D // 256
PICKED = -3.3e38
FUTURE = -3.0e38


def t5_bucket(dist):
    n = np.maximum(dist, 0)
    exact = REL_BUCKETS // 2
    nf = np.maximum(n, 1).astype(np.float32)
    scale = np.float32(np.log(REL_MAX_DIST / exact))
    large = exact + (np.log(nf / np.float32(exact)) / scale * np.float32(REL_BUCKETS - exact)).astype(np.int32)
    return np.where(n < exact, n, np.minimum(large, REL_BUCKETS - 1))


def columns(spec):
    at, out = 0, {}
    for name, width in spec:
        out[name] = (at, at + width)
        at += width
    return out, at


PAR, NPAR = columns([
    ("gains", 8 * KD), ("cmp_pos", 2 * CMP_PAIRS), ("cmp_b1", 2), ("cmp_w2", 128), ("cmp_b2k", 1),
    ("cmp_b2v", 128), ("relb", HEADS), ("pool_w", 128), ("pool_scale", 2), ("sgu_g", 256), ("sgu_b", 256),
    ("sgu_wT", 512), ("sgu_bias", 256),
    ("conv_w", FFN_PAIRS * 6), ("conv_b", FFN_PAIRS * 2), ("gdn_conv", 48), ("a_log", 1), ("dt_bias", 1),
    ("gdn_norm", 1), ("w_qb", 512), ("w_qi", 512), ("w_kvb", 128), ("dq_norm", 1), ("dk_norm", 1),
    ("conv_dw", 2 * CONV_TAPS), ("dw_b", 2), ("ln_g", 2), ("ln_b", 2), ("xq_norm", 1), ("xk_norm", 1),
])
CON, NCON = columns([
    ("ident", 128), ("neg_half", 8), ("eps", 8), ("tri_incl", 128), ("tri_strict", 128), ("levels", LEVELS * 128), ("block_ones", 128),
    ("ones", 128), ("inv_count", 512), ("pick_row", 4 * 128), ("chunk_keep", SEQ),
])
EPS_VALUES = [EPS, 64 * EPS, P * EPS, 0, 0, 0, 0, 0]
GAIN = {n: i for i, n in enumerate(["mix", "memkv", "mem", "ffn", "mix2", "mem2", "cross", "mlp"])}


def shape_constants():
    c = np.zeros((P, NCON), np.float32)

    def put(name, a):
        lo, hi = CON[name]
        c[:a.shape[0], lo:hi] = a.reshape(a.shape[0], hi - lo)

    i = np.arange(P)
    row, col = i[:, None], i[None, :]
    same = row // CHUNK == col // CHUNK
    put("ident", np.eye(P))
    put("neg_half", np.full((P, 8), -0.5))
    put("eps", np.tile(np.array(EPS_VALUES, np.float32), (P, 1)))
    put("tri_incl", (same & (col >= row)).astype(np.float32))
    put("tri_strict", (same & (col > row)).astype(np.float32))
    put("levels", np.stack([
        (row // (2 * s) == col // (2 * s)) & (row % (2 * s) >= s) & (col % (2 * s) < s)
        for s in (2 ** n for n in range(LEVELS))], 1).astype(np.float32))
    put("block_ones", same.astype(np.float32))
    put("ones", np.ones((P, P)))
    t = np.arange(SEQ)
    counts = np.zeros((P, 2, SEQ), np.float32)
    for g, w in enumerate(POOL_WINDOWS):
        counts[64 * (g % 2):64 * (g % 2) + 64, g // 2] = np.float32(1) / np.minimum(t + 1, w).astype(np.float32)
    put("inv_count", counts)
    put("pick_row", np.repeat(np.eye(4, dtype=np.float32), P, 1))
    put("chunk_keep", np.tile((t % CHUNK != 0).astype(np.float32), (4, 1)))
    return c


def bucket_one_hots():
    dist = np.arange(DIST_COLS) - (SEQ - 1)
    h = np.zeros((REL_BUCKETS + 1, DIST_COLS), np.float32)
    h[np.where(dist < 0, REL_BUCKETS, t5_bucket(dist)), np.arange(DIST_COLS)] = 1
    return h


RING = 5
DOWN_LAG = 2
NB = 4
ARENA = 24576
SPLIT_PRODUCTS = ("up", "down", "m1", "m2")
SPLIT_STAGES = ("ffn", "mlp")
SPLIT_RING = 3
TOPK_ROUNDS = DSA_TOPK // 8
MLP_LAG = 2
MEM_DIM = D // MEM_HEADS
STATS = [(n, t) for n in ("mix", "memkv", "out_post", "mem", "wo_post", "ffn", "down_post", "mix2", "mem2", "cross", "mlp") for t in range(TT)] + [
    ("sgu", t) for t in range(TT)]
NSTAT = len(STATS)


def plan():
    tiles = [("bias_row",), ("bias_cmp",)]

    def norm(stage):
        tiles.extend(("normT", stage, t, half) for t in range(TT) for half in range(2))

    norm("mix")
    tiles.extend((n,) for n in ("q0", "q1", "kcvc", "ksvs", "kwvw", "gates", "pool", "u", "v", "cmp_h", "cmp_kv"))
    for t in range(TT):
        tiles.extend(("cmp_s", t, g) for g in range(GROUPS))
        tiles.extend(("s", t, h) for h in range(HEADS))
    tiles.extend((("pool_out",), ("sgu_out",)))
    norm("memkv")
    tiles.extend(("mk", c) for c in range(4))
    tiles.extend(("cmp_pT", t) for t in range(TT))
    tiles.extend(("pT", t, h) for h in range(HEADS) for t in range(TT))
    norm("mem")
    tiles.extend(("mq", c) for c in range(4))
    tiles.extend(("ms", t, hp) for t in range(TT) for hp in range(2))
    tiles.extend(("mpT", t, hp) for t in range(TT) for hp in range(2))
    tiles.extend(("mo", c) for c in range(4))
    norm("ffn")
    tiles.extend(("up", j) for j in range(FFN_PAIRS))
    norm("mix2")
    tiles.extend((n,) for n in ("cq", "ck", "ab", "widx", "ug0", "ug1", "dq", "dqi", "dk"))
    tiles.append(("qkv", 0))
    tiles.extend((("across", "dq"), ("across", "dk")))
    tiles.extend(("il", t, par) for t in range(TT) for par in range(2))
    tiles.extend(("qkv", i) for i in range(1, 6))
    tiles.extend((("z", 0), ("z", 1)))
    norm("mem2")
    tiles.extend((("xk", 0), ("xk", 1), ("across", "xk0"), ("across", "xk1")))
    tiles.extend(("dl", t, par) for t in range(TT) for par in range(2))
    tiles.extend(("dpT", t, par) for t in range(TT) for par in range(2))
    tiles.append(("do",))
    tiles.extend(("across", f"l{i}") for i in range(4))
    tiles.extend((("cols",), ("dr", 0), ("dr", 1), ("br", 0), ("br", 1)))
    tiles.extend((n, t) for n in ("kA", "vA", "kk", "qk") for t in range(TT))
    for level in range(LEVELS):
        for kind in ("y", "d", "dT"):
            if (kind, level) != ("d", LEVELS - 1):
                tiles.extend((kind, level, t) for t in range(TT))
    tiles.extend((n, t) for n in ("gu", "gw") for t in range(TT))
    tiles.extend((("ln_mean",), ("ln_var",)))
    for n in range(NCHUNK):
        if n:
            tiles.append(("ws", n))
        tiles.append(("go", n))
        if n < NCHUNK - 1:
            tiles.append(("kv", n))
    tiles.extend((("across", "o0"), ("across", "o1")))
    norm("cross")
    tiles.extend((("xq", 0), ("xq", 1), ("across", "xq0"), ("across", "xq1")))
    tiles.extend(("xs", t, hp) for t in range(TT) for hp in range(2))
    tiles.extend(("xpT", t, hp) for t in range(TT) for hp in range(2))
    tiles.extend(("xo", c) for c in range(2))
    norm("mlp")
    tiles.extend(("m1", j) for j in range(MLP_UNITS))

    units = ["q0", "q1", "kcvc", "ksvs", "kwvw", "gates", "pool", "u", "v", "cmp_w1k", "cmp_w1v"]
    for product in ("mk", "mv", "out", "mq", "wo"):
        units += [(product, c) for c in range(4)]
    for j in range(FFN_PAIRS + DOWN_LAG):
        if j < FFN_PAIRS:
            units.append(("up", j))
        if j >= DOWN_LAG and j % 2 == 1:
            units.append(("down", (j - DOWN_LAG) // 2))
    units += ["cq", "ck", "ab", "ug0", "ug1"] + [("qkv", i) for i in range(6)] + [("z", 0), ("z", 1)]
    units += [("xk", 0), ("xk", 1), ("xv", 0), ("xv", 1)] + [("out2", i) for i in range(4)]
    units += [("xq", 0), ("xq", 1), ("xwo", 0), ("xwo", 1)]
    for j in range(MLP_UNITS + MLP_LAG):
        if j < MLP_UNITS:
            units.append(("m1", j))
        if j >= MLP_LAG:
            units.append(("m2", j - MLP_LAG))

    fills = []
    for product in ("mv", "o", "out", "wo", "down", "xv", "out2", "xwo", "m2"):
        fills += [(product, i) for i in range(2 if product in ("o", "xv") else 4)]
    return tiles, units, fills


def block_kernel(nc, a, out):
    ctx = ExitStack()
    with ctx:
        def sb(name, shape):
            return ctx.enter_context(nc.sbuf_tensor(name, shape, F32))

        def sem(name):
            return ctx.enter_context(nc.semaphore(name))

        ring = sb("weight_ring", [P, RING, 2048])
        x = sb("x_res", [P, TT, D])
        xn = sb("x_normed", [P, TT, D])
        hT = sb("hT", [P, KD, SEQ])
        mixT = sb("mixT", [P, KD, SEQ])
        par = sb("par", [P, NPAR])
        con = sb("con", [P, NCON])
        post_gain = sb("post_gain", [P, D])
        junk = sb("act_junk", [P, D])
        stats = sb("stats", [P, 2 * NSTAT])
        with nc.sbuf_tensor("arena", [P, ARENA], F32) as arena:
            pass
        SPLIT_AT = 4096
        sb("arena_below_split", [P, SPLIT_AT])
        split = ctx.enter_context(nc.sbuf_tensor("split_operands", [P, ARENA - SPLIT_AT], F32R))
        banks = [ctx.enter_context(nc.psum_tensor(f"work{b}", [P, 512], F32)) for b in range(NB)]
        accs = [ctx.enter_context(nc.psum_tensor(f"acc{b}", [P, 512], F32)) for b in range(4)]
        bias_rows_dram = nc.dram_tensor("bias_rows_scratch", [HEADS, DIST_COLS], F32, kind="Internal").ap()

        def parc(name):
            return par[:, PAR[name][0]:PAR[name][1]]

        def conc(name):
            return con[:, CON[name][0]:CON[name][1]]

        def cut(at, *shape):
            n = int(np.prod(shape))
            assert at + n <= ARENA
            v = arena[:, at:at + n]
            if len(shape) == 1:
                return v
            names = "abcd"[:len(shape)]
            return v.rearrange(f"p ({' '.join(names)}) -> p {' '.join(names)}", **dict(zip(names, shape)))

        def cut_split(at, *shape):
            n = int(np.prod(shape))
            assert at >= SPLIT_AT and at + n <= ARENA
            names = "abcd"[:len(shape)]
            return split[:, at - SPLIT_AT:at - SPLIT_AT + n].rearrange(
                f"p ({' '.join(names)}) -> p {' '.join(names)}", **dict(zip(names, shape)))

        def eps_col(v):
            k = CON["eps"][0] + EPS_VALUES.index(v)
            return con[:, k:k + 1]

        ident = conc("ident")
        gains = parc("gains").rearrange("p (s k) -> p s k", k=KD)

        tiles, units, fills = plan()
        TILE = {n: i for i, n in enumerate(tiles)}
        UNIT = {n: i for i, n in enumerate(units)}
        FILL = {n: i for i, n in enumerate(fills)}
        tile_full = sem("tile_full")
        tile_read = [sem(f"tile_read{b}") for b in range(NB)]
        acc_full = sem("acc_full")
        acc_read = sem("acc_read")
        unit_loaded = [sem(f"unit_loaded{s}") for s in range(RING)]
        unit_spent = sem("unit_spent")

        def bank(name):
            return banks[TILE[name] % NB]

        def full(name):
            return tile_full, TILE[name] + 1

        def drained(name):
            return tile_read[TILE[name] % NB], TILE[name] // NB + 1

        def reader(name):
            return tile_read[TILE[name] % NB]

        def acc(name):
            return accs[FILL[name] % 4]

        def acc_filled(name):
            return acc_full, FILL[name] + 1

        def acc_drained(name):
            return acc_read, FILL[name] + 1

        def weights(name, *shape):
            v = ring[:, UNIT[name] % RING, :]
            n = int(np.prod(shape))
            names = "abcd"[:len(shape)]
            return v[:, 0:n].rearrange(f"p ({' '.join(names)}) -> p {' '.join(names)}", **dict(zip(names, shape)))

        split_units = [u for u in units if u[0] in SPLIT_PRODUCTS]
        SPLIT = {u: i for i, u in enumerate(split_units)}
        high_ready = sem("weights_high_ready")
        low_ready = sem("weights_low_ready")
        h_high = sem("h_high_ready")
        h_low = sem("h_low_ready")

        def split_before(name):
            return SPLIT[name] - 1 if name in SPLIT else -1

        def split_weights(name, *shape):
            names = "abcd"[:len(shape)]
            return split_ring[SPLIT[name] % SPLIT_RING].rearrange(
                f"p s ({' '.join(names)}) -> p s {' '.join(names)}", **dict(zip(names, shape)))

        def loaded(name):
            return unit_loaded[UNIT[name] % RING], 16 * (UNIT[name] // RING + 1)

        params_in = sem("params_in")
        consts_in = sem("consts_in")
        x_in = [sem(f"x_in{t}") for t in range(TT)]
        mem_in = sem("mem_in")
        hots_in = sem("hots_in")
        bias_rows_out = sem("bias_rows_out")
        bias_tile_in = sem("bias_tile_in")
        gain_in = sem("post_gain_in")
        shifted_in = sem("kv_shifted_in")
        squares = sem("squares_summed")
        rstd_ready = sem("rstd_ready")
        normed = sem("x_normed_ready")
        x_done = sem("x_updated")
        blocks_ready = sem("cmp_blocks_ready")
        scored = sem("scores_biased")
        neg_max = sem("neg_max_ready")
        exped = sem("exp_done")
        weighed = sem("probs_weighed")
        sgu_stat = sem("sgu_stats_ready")
        sgu_rstd = sem("sgu_rstd_ready")
        sgu_normed = sem("sgu_normed_ready")
        masked_ws = sem("sgu_weights_masked")
        pooled = sem("pool_diff_ready")
        dve_chain = sem("dve_chain")
        act_chain = sem("act_chain")
        pool_chain = sem("pool_chain")
        gated = sem("ffn_gated")
        gate_act = sem("ffn_gate_act")
        tap2 = sem("ffn_tap2")
        out_done = sem("out_done")
        heads_done = sem("heads_attended")
        across_sq = sem("across_squares_ready")
        across_done = sem("across_normed")
        bands_y = sem("conv_input_ready")
        tap3 = sem("gdn_last_tap")
        silu_done = sem("gdn_silu_done")
        idx_relu = sem("index_relu_ready")
        idx_sum = sem("index_scores_summed")
        idx_causal = sem("index_scores_causal")
        picked = sem("topk_picked")
        dmask_ready = sem("dsa_mask_ready")
        d_max = sem("dsa_neg_max")
        d_exp = sem("dsa_exp_done")
        d_weighed = sem("dsa_probs_weighed")
        softplus_ln = sem("softplus_ln_ready")
        decay_sum = sem("decay_summed")
        decay_exp = sem("decay_exps_ready")
        rows_ready = sem("gate_rows_ready")
        exp_rows = sem("exp_decay_ready")
        gamma_diff = sem("gamma_exponents")
        gamma_exp = sem("gamma_exp_done")
        gamma_ready = sem("gammas_masked")
        kb_ready = sem("kb_ready")
        qe_ready = sem("qe_ready")
        v_news = sem("v_new_ready")
        states = sem("state_updated")
        o_read = sem("o_collected")
        conv_out = sem("conv31_done")
        conv_sq_ready = sem("ln_squares_ready")
        conv_norm = sem("ln_normed")
        conv_mix = sem("conv_mix_ready")
        o_mix = sem("gdn_mix_ready")
        x_max = sem("cross_neg_max")
        x_weighed = sem("cross_probs_weighed")
        relu_sq = sem("mlp_squared")
        relu_high = sem("mlp_square_high")
        mix_tail = sem("mix_tail_ready")

        qT = cut(0, 4, SEQ)
        toeplitz = cut(1024, HEADS, SEQ)
        pairs = cut(3072, 2, GROUPS, SEQ)
        blocks = cut(4096, 2, CMP_PAIRS, GROUPS, NCMP)
        kcvcT = cut(5056, 2, SEQ)
        probsT = [cut(3072 + 1024 * i, 2, TT, SEQ) for i in range(2)]
        keysT = cut(5568, 2, SEQ)
        values = cut(6080, 2, TT, P)
        cmp_hT = cut(6592, 2, 32)
        cmp_kT = cut(6656, NCMP)
        cmp_v = cut(6672, P)
        gates = cut(6800, TT, HEADS, 3)
        cmp_bias = cut(6848, TT, HEADS, NCMP)
        cmp_p = cut(7088, TT, HEADS, 32)
        cmp_pT = cut(7600, GROUPS, SEQ)
        soft = cut(8112, TT, 3, HEADS, 4)
        bias_rows = cut(8304, 384)
        probs = [[cut(8704 + (2048 if t else 0) + h * (512 if t else 256), 2, P * (t + 1)) for h in range(HEADS)]
                 for t in range(TT)]
        uT = cut(14848, 2, SEQ)
        v_n = cut(15360, TT, SEQ)
        v_g = cut(15872, TT, SEQ)
        kmT = cut(16384, KD, SEQ)
        vm = cut(18432, TT, D)
        hots = cut(16384, DIST_COLS)
        pool_a = cut(17408, 2, 272)
        pool_b = cut(17952, 2, 272)
        pool_c = cut(18496, 2, 272)
        pool_s = cut(19040, 2, SEQ)
        pool_d = cut(19552, 2, SEQ)
        qmT = cut(0, KD, SEQ)
        mprobs = [cut(2048 + 1024 * t, MEM_HEADS, SEQ) for t in range(TT)]
        mprobsT = cut(4096, MEM_HEADS, TT, SEQ)
        msoft = cut(6144, TT, 3, MEM_HEADS)
        conv = [cut(0 + 512 * i, 2, SEQ) for i in range(3)]
        act_g = [cut(1536 + 256 * i, SEQ) for i in range(2)]
        prod = [cut(2048 + 256 * i, SEQ) for i in range(2)]
        prod_s = [cut_split(4096 + 512 * i, 2, SEQ) for i in range(4)]
        hT_s = cut_split(16384, 2, KD, SEQ)
        split_ring = [cut_split(at, 2, 2048) for at in (12288, 20480, 8192)]

        cqT = cut(0, 2, SEQ)
        ckvT = cut(512, SEQ)
        kidxT = cut(768, SEQ)
        dqT = cut(1024, 2, SEQ)
        dqiT = cut(1536, 2, SEQ)
        dkT = cut(2048, SEQ)
        dv = cut(2304, TT, DK)
        dsq = cut(2432, 2, SEQ)
        dsk = cut(2944, SEQ)
        w_idx = cut(3968, TT, 4)
        top8 = cut(3976, TT, 8)
        dsoft = cut(3992, TT, 2, DSA_HEADS)
        idx_score = [cut(4096 + 256 * t, P * (t + 1)) for t in range(TT)]
        dmask = [cut(4608 + 256 * t, P * (t + 1)) for t in range(TT)]
        relu_l = [[cut(5120 + 1024 * t + 512 * par, 2, P * (t + 1)) for par in range(2)] for t in range(TT)]
        dprobs = [cut(7168 + 512 * t, DSA_HEADS, P * (t + 1)) for t in range(TT)]
        dprobsT = [cut(8704, 2, TT, SEQ), cut(4096, 2, TT, SEQ)]
        gate_s = cut(10240, 2, SEQ)
        y_pad = cut(10752, 2, CONV_TAPS - 1 + SEQ)
        conv_y = cut(11328, 2, SEQ)
        conv_sq = cut(11840, 2, SEQ)
        qkv = cut(12352, 12, SEQ)
        zT = cut(15424, GDN_HEADS, SEQ)
        gate_rows = cut(16448, 4, SEQ)
        row_tmp = cut(17472, 2, SEQ)
        gate_cols = cut(18496, TT, 4, GDN_HEADS)
        state = cut(18528, GDN_HEADS, P)
        v_new = cut(19040, GDN_HEADS, P)
        a_rate = cut(19552, 1)
        kbT = cut(20480, GDN_HEADS, SEQ)
        qeT = cut(21504, GDN_HEADS, SEQ)
        exp_decay = cut(22528, GDN_HEADS, SEQ)
        xkT = cut(23552, XA_HEADS, SEQ)
        xv = post_gain[:, :].rearrange("p (s n) -> p s n", s=TT)
        AT, qkT, inv, invT, Y, bke, kdec, bv, u_n, wT = [
            [cut(1024 * i + 512 * t, GDN_HEADS, P) for t in range(TT)] for i in range(10)]
        l2_sq = cut(5120, 8, SEQ)
        oT = cut(2048, GDN_HEADS, SEQ)
        o_sq = cut(0, GDN_HEADS, SEQ)
        xqT = cut(4096, XA_HEADS, SEQ)
        xq_sq = cut(5120, XA_HEADS, SEQ)
        xsoft = cut(6144, TT, 2, XA_HEADS)
        xprobs = [cut(6656 + 1024 * t, XA_HEADS, SEQ) for t in range(TT)]
        xprobsT = cut(8704, XA_HEADS, TT, SEQ)
        relu_h = [cut(0 + 512 * i, 2, SEQ) for i in range(2)]
        relu2 = [cut(1024 + 512 * i, 2, SEQ) for i in range(2)]
        relu2_s = [cut_split(4096 + 1024 * i, 2, 2, SEQ) for i in range(3)]

        chunk2 = {"dq": (dqT, dsq, 1.0, 64 * EPS, "dq_norm"),
                  "dk": (dkT, dsk, 1.0 / 64, EPS, "dk_norm")}
        for i in range(2):
            chunk2[f"xk{i}"] = (xkT[:, 2 * i:2 * i + 2, :], mixT[:, 2 * i:2 * i + 2, :], 1.0 / P, EPS, "xk_norm")
        for i in range(4):
            scale = P if i < 2 else 1
            chunk2[f"l{i}"] = (qkv[:, 2 * i:2 * i + 2, :], l2_sq[:, 2 * i:2 * i + 2, :], float(scale), scale * EPS, None)
        for i in range(2):
            chunk2[f"o{i}"] = (oT[:, 2 * i:2 * i + 2, :], o_sq[:, 2 * i:2 * i + 2, :], 1.0 / P, EPS, "gdn_norm")
        for i in range(2):
            chunk2[f"xq{i}"] = (xqT[:, 2 * i:2 * i + 2, :], xq_sq[:, 2 * i:2 * i + 2, :], 1.0, P * EPS, "xq_norm")
        ACROSS = {n: i for i, n in enumerate(chunk2)}

        STATI = {n: i for i, n in enumerate(STATS)}

        def stat(name, j=0):
            c = 2 * STATI[name] + j
            return stats[:, c:c + 1]

        hT_free = {"mix": None, "memkv": full(("v",)), "mem": acc_filled(("mv", 3)), "ffn": full(("mq", 3))}
        hT_free.update({"mix2": full(("up", FFN_PAIRS - 1)), "mem2": full(("z", 1)), "cross": acc_filled(("xv", 1)),
                        "mlp": full(("xq", 1))})
        LAST_OF_UNIT = {u: full((u,)) for u in ("q0", "q1", "kcvc", "ksvs", "kwvw", "gates", "pool", "u", "v")}
        LAST_OF_UNIT.update({"cmp_w1k": full(("cmp_h",)), "cmp_w1v": full(("cmp_h",))})
        LAST_OF_UNIT.update({u: full(u) for u in units if u in TILE})
        LAST_OF_UNIT.update({u: full((u,)) for u in ("cq", "ck", "ug0", "ug1")})
        LAST_OF_UNIT["ab"] = full(("widx",))
        spent = 0
        last_unit = {}
        for u in units:
            if isinstance(u, tuple) and u not in TILE:
                last_unit[u[0]] = u
        SPENT = {}
        for u in units:
            if u in LAST_OF_UNIT:
                continue
            product = u[0]
            if last_unit[product] == u:
                LAST_OF_UNIT[u] = acc_filled((product, 1 if product == "xv" else 3))
            else:
                spent += 1
                SPENT[u] = spent
                LAST_OF_UNIT[u] = (unit_spent, spent)

        w_in = a["w_in"].rearrange("(k p) c -> p k c", p=P)
        w_up = a["w_up"].rearrange("(k p) c -> p k c", p=P)

        w_in2 = a["w_in2"].rearrange("(k p) c -> p k c", p=P)
        xa_wkv = a["xa_wkv"].rearrange("(k p) c -> p k c", p=P)

        def cols(w, lo, n):
            return w[:, :, lo:lo + n]

        def rows(w, i, n=2):
            return w.rearrange("(k p) c -> p k c", p=P)[:, n * i:n * i + n, :]

        def source(u):
            at = {"q0": 0, "q1": 256, "kcvc": 512, "ksvs": 768, "kwvw": 1024, "gates": 1280, "pool": 1304,
                  "u": 1560, "v": 1816}
            if u in at:
                n = 24 if u == "gates" else 256
                return (KD, n), cols(w_in, at[u], n)
            if u in ("cmp_w1k", "cmp_w1v"):
                return (CMP_PAIRS, P), a["cmp_w1"][int(u == "cmp_w1v")].rearrange("(j p) c -> p j c", p=P)
            at2 = {"cq": (2048, 256), "ck": (2304, 192), "ab": (2496, 12), "ug0": (2508, 256), "ug1": (2764, 256)}
            if u in at2:
                lo, n = at2[u]
                return (KD, n), cols(w_in2, lo, n)
            kind, i = u
            wide = {"mk": "w_mk", "mq": "w_mq"}
            tall = {"mv": "w_mv", "out": "w_out", "wo": "w_mo", "down": "w_down"}
            if kind in wide:
                return (KD, 256), cols(a[wide[kind]].rearrange("(k p) c -> p k c", p=P), 256 * i, 256)
            if kind in tall:
                return (2, D), rows(a[tall[kind]], i)
            if kind == "up":
                return (KD, 256), cols(w_up, 256 * i, 256)
            if kind == "qkv":
                return (KD, 256), cols(w_in2, 256 * i, 256)
            if kind == "z":
                return (KD, 256), cols(w_in2, 1536 + 256 * i, 256)
            if kind == "xk":
                return (KD, 256), cols(xa_wkv, 256 * i, 256)
            if kind == "xv":
                return (4, 512), xa_wkv[:, 4 * i:4 * i + 4, 512:1024]
            if kind == "xq":
                return (KD, 256), cols(a["xa_wq"].rearrange("(k p) c -> p k c", p=P), 256 * i, 256)
            if kind == "m1":
                return (KD, 256), cols(a["mlp_w1"].rearrange("(k p) c -> p k c", p=P), 256 * i, 256)
            return (2, D), rows(a[{"out2": "w_out2", "xwo": "xa_wo", "m2": "mlp_w2"}[kind]], i)

        block = ctx.enter_context(nc.Block())

        @block.sync
        def _(sp):
            def load(u):
                i = UNIT[u]
                if i >= RING:
                    held = units[i - RING]
                    sp.wait_ge(*((low_ready, SPLIT[held] + 1) if held in SPLIT else LAST_OF_UNIT[held]))
                shape, src = source(u)
                sp.dma_start(weights(u, *shape), src).then_inc(unit_loaded[i % RING], 16)

            sp.dma_start(x[:, 0, :], a["x"][0:P, :]).then_inc(x_in[0], 16)
            sp.dma_start(x[:, 1, :], a["x"][P:2 * P, :]).then_inc(x_in[1], 16)
            for u in units:
                load(u)
            for t in range(TT):
                sp.wait_ge(*acc_drained(("m2", 2 * t + 1)))
                sp.dma_start(out[P * t:P * t + P, :], x[:, t, :]).then_inc(out_done, 16)
            sp.wait_ge(out_done, 16 * TT)

        @block.gpsimd
        def _(pool):
            chain = [0]

            def link(ins):
                chain[0] += 1
                ins.then_inc(pool_chain, 1)
                pool.wait_ge(pool_chain, chain[0])

            pool.dma_start(con[:, :], a["consts"]).then_inc(consts_in, 16)
            pool.dma_start(hots[0:REL_BUCKETS + 1, :], a["hots"]).then_inc(hots_in, 16)
            pool.dma_start(par[:, :], a["params"]).then_inc(params_in, 16)

            def rstd(name, halves, n=D):
                pool.wait_ge(squares, STATI[name] + 1)
                if halves:
                    link(pool.tensor_tensor(stat(name), stat(name), stat(name, 1), ALU.add))
                link(pool.tensor_scalar(stat(name), stat(name), 1.0 / n, EPS, ALU.mult, ALU.add))
                pool.tensor_tensor(stat(name), stat(name), conc("neg_half")[:, 0:1], ALU.pow).then_inc(rstd_ready, 1)

            def load_post_gain(n):
                if n:
                    pool.wait_ge(x_done, 2 * n)
                g = a[("mix_norm_post", "mem_norm_post", "ffn_norm_post")[n]]
                pool.dma_start(post_gain[:, :], bass.AP(tensor=g.tensor, offset=g.offset, ap=[[0, P], [1, D]])).then_inc(gain_in, 16)

            pool.wait_ge(consts_in, 16)
            for t in range(TT):
                rstd(("mix", t), False)
            pool.wait_ge(*drained(("bias_row",)))
            pool.dma_start(bias_rows_dram[:, 0:384], bias_rows[0:HEADS, :]).then_inc(bias_rows_out, 16)
            pool.wait_ge(bias_rows_out, 16)
            pool.dma_start(toeplitz, bass.AP(tensor=bias_rows_dram.tensor, offset=bias_rows_dram.offset,
                                             ap=[[1, P], [DIST_COLS, HEADS], [1, SEQ]])).then_inc(bias_tile_in, 16)
            pool.wait_ge(params_in, 16)
            wsT = parc("sgu_wT").rearrange("p (h t) -> p h t", h=4)
            pool.affine_select(out=wsT, in_=wsT, compare_op=ALU.is_ge, fill=0.0, base=0,
                               pattern=[[0, 4], [1, P]], channel_multiplier=-1).then_inc(masked_ws, 1)
            link(pool.memset(pool_b[:, :, 0:16], 0.0))
            link(pool.memset(pool_c[:, :, 0:16], 0.0))
            link(pool.memset(pool_a[:, :, 0:16], 0.0))
            pool.wait_ge(*drained(("pool",)))
            src, spare = pool_a, [pool_b, pool_c, pool_b, pool_c]
            for g, w in enumerate(POOL_WINDOWS):
                dst = spare[g]
                link(pool.tensor_tensor(dst[:, :, 16:272], src[:, :, 16:272], src[:, :, 16 - w // 2:272 - w // 2], ALU.add))
                half = slice(64 * (g % 2), 64 * (g % 2) + 64)
                link(pool.tensor_copy(pool_s[half, g // 2, :], dst[half, g // 2, 16:272]))
                src = dst
            link(pool.tensor_tensor(pool_s, pool_s, conc("inv_count").rearrange("p (c t) -> p c t", c=2), ALU.mult))
            pool.tensor_tensor(pool_d, pool_s, pool_a[:, :, 16:272], ALU.subtract).then_inc(pooled, 1)
            for t in range(TT):
                pool.wait_ge(sgu_stat, t + 1)
                link(pool.tensor_scalar(stat(("sgu", t), 1), stat(("sgu", t), 1), EPS, None, ALU.add))
                pool.tensor_tensor(stat(("sgu", t), 1), stat(("sgu", t), 1), conc("neg_half")[:, 0:1],
                                   ALU.pow).then_inc(sgu_rstd, 1)
            load_post_gain(0)
            for name in STATS:
                if name[0] in ("mem2", "cross", "mlp"):
                    continue
                if name[0] not in ("mix", "sgu"):
                    rstd(name, name[0].endswith("_post"))
                if name in (("mem", 1), ("ffn", 1)):
                    load_post_gain(1 if name[0] == "mem" else 2)
            for t in range(TT):
                pool.wait_ge(idx_sum, t + 1)
                pool.affine_select(out=idx_score[t], in_=idx_score[t], compare_op=ALU.is_ge, fill=FUTURE, base=P * t,
                                   pattern=[[-1, P * (t + 1)]], channel_multiplier=1).then_inc(idx_causal, 1)
            for t in range(TT):
                pool.wait_ge(picked, t + 1)
                link(pool.tensor_scalar(dmask[t], idx_score[t], -3.2e38, 1.0, ALU.is_le, ALU.subtract))
                link(pool.tensor_scalar(dmask[t], dmask[t], -MASKED, None, ALU.mult))
                pool.affine_select(out=dmask[t], in_=dmask[t], compare_op=ALU.is_ge, fill=MASKED, base=P * t,
                                   pattern=[[-1, P * (t + 1)]], channel_multiplier=1).then_inc(dmask_ready, 1)
            for t in range(TT):
                rstd(("mem2", t), False)
            for t in range(TT):
                pool.wait_ge(gamma_exp, t + 1)
                for h in range(GDN_HEADS):
                    pool.tensor_tensor(inv[t][:, h, :], Y[t][:, h, :], conc("tri_strict"), ALU.mult)
                for h in range(GDN_HEADS):
                    ins = pool.tensor_tensor(Y[t][:, h, :], Y[t][:, h, :], conc("tri_incl"), ALU.mult)
                ins.then_inc(gamma_ready, 1)
            for stage in ("cross", "mlp"):
                for t in range(TT):
                    rstd((stage, t), False)

        @block.scalar
        def _(act):
            chain = [0]

            def link(ins):
                chain[0] += 1
                ins.then_inc(act_chain, 1)
                act.wait_ge(act_chain, chain[0])

            def square(name, views):
                if STATI[name]:
                    act.wait_ge(squares, STATI[name])
                for j, v in enumerate(views):
                    ins = act.activation(junk[:, 0:v.shape[-1]], v, ACT.Square, accum_out=stat(name, j))
                    if j < len(views) - 1:
                        link(ins)
                ins.then_inc(squares, 1)

            def drain(name, dst, src, func=ACT.Copy, **kw):
                act.wait_ge(*full(name))
                return act.activation(dst, src, func, **kw)

            for t in range(TT):
                act.wait_ge(x_in[t], 16)
                square(("mix", t), [x[:, t, :]])

            def halves(name):
                return bank(name)[:, :].rearrange("p (c t) -> p c t", c=2)

            for i in range(2):
                name = (f"q{i}",)
                drain(name, qT[:, 2 * i:2 * i + 2, :], halves(name), scale=DK ** -0.5).then_inc(reader(name), 1)
            drain(("kcvc",), kcvcT, halves(("kcvc",))).then_inc(reader(("kcvc",)), 1)
            act.wait_ge(*full(("normT", "mix", 1, 1)))
            act.dma_start(xn[:, :, :], a["mem"].rearrange("(t p) d -> p t d", p=P)).then_inc(mem_in, 16)
            act.wait_ge(*drained(("kcvc",)))
            for g in range(GROUPS):
                src = kcvcT[DK * g:DK * g + DK]
                act.dma_start(pairs[0:DK, :, g, :], src).then_inc(shifted_in, 16)
                act.dma_start(pairs[DK:P, :, g, 0:SEQ - 1], src[:, :, 1:SEQ]).then_inc(shifted_in, 16)
            for j, u in enumerate(("ksvs", "kwvw")):
                name = (u,)
                drain(name, keysT[:, j, :], bank(name)[:, 0:SEQ])
                act.activation(values[:, j, :, :], bank(name)[:, SEQ:512].rearrange("p (t d) -> p t d", t=TT),
                               ACT.Copy).then_inc(reader(name), 1)
            drain(("gates",), gates.rearrange("p t h b -> p t (h b)"),
                  bank(("gates",))[:, 0:48].rearrange("p (t n) -> p t n", t=TT), ACT.Sigmoid).then_inc(reader(("gates",)), 1)
            drain(("pool",), pool_a[:, :, 16:272], halves(("pool",))).then_inc(reader(("pool",)), 1)
            drain(("u",), uT, halves(("u",)), ACT.Gelu_apprx_tanh).then_inc(reader(("u",)), 1)
            drain(("v",), v_g, halves(("v",)), ACT.Gelu_apprx_tanh).then_inc(reader(("v",)), 1)
            act.wait_ge(*full(("cmp_h",)))
            b1 = parc("cmp_b1")
            for kv in range(2):
                ins = act.activation(cmp_hT[:, kv, 0:30], bank(("cmp_h",))[:, 32 * kv:32 * kv + 30],
                                     ACT.Gelu_apprx_tanh, bias=b1[:, kv:kv + 1])
            ins.then_inc(reader(("cmp_h",)), 1)

            act.wait_ge(mem_in, 16)
            for t in range(TT):
                square(("memkv", t), [xn[:, t, :]])

            n = 0
            for t in range(TT):
                for h in range(HEADS):
                    n += 1
                    act.wait_ge(neg_max, n + t + 1)
                    if h == 0:
                        for hh in range(HEADS):
                            ins = act.activation(cmp_p[:, t, hh, 0:NCMP], cmp_p[:, t, hh, 0:NCMP], ACT.Exp,
                                                 bias=soft[:, t, 0, hh, 0:1], accum_out=soft[:, t, 1, hh, 0:1])
                        ins.then_inc(exped, 1)
                    for j in range(2):
                        ins = act.activation(probs[t][h][:, j, :], probs[t][h][:, j, :], ACT.Exp,
                                             bias=soft[:, t, 0, h, j + 1:j + 2], accum_out=soft[:, t, 1, h, j + 1:j + 2])
                    ins.then_inc(exped, 1)
            for c in range(4):
                drain(("mk", c), kmT[:, 2 * c:2 * c + 2, :], halves(("mk", c))).then_inc(reader(("mk", c)), 1)
            for t in range(TT):
                for half in range(2):
                    f = ("mv", 2 * t + half)
                    act.wait_ge(*acc_filled(f))
                    act.activation(vm[:, t, 512 * half:512 * half + 512], acc(f)[:, :], ACT.Copy).then_inc(acc_read, 1)
            for i in range(2):
                f = ("o", i)
                act.wait_ge(*acc_filled(f))
                act.activation(mixT[:, 2 * i:2 * i + 2, :], acc(f)[:, :].rearrange("p (c t) -> p c t", c=2),
                               ACT.Copy).then_inc(acc_read, 1)

            def post_squares(product, stage):
                for t in range(TT):
                    act.wait_ge(*acc_filled((product, 2 * t + 1)))
                    square((stage, t), [acc((product, 2 * t + half))[:, :] for half in range(2)])

            def next_squares(stage, n_updates):
                for t in range(TT):
                    act.wait_ge(x_done, n_updates + t + 1)
                    square((stage, t), [x[:, t, :]])

            post_squares("out", "out_post")
            next_squares("mem", 0)
            for c in range(4):
                drain(("mq", c), qmT[:, 2 * c:2 * c + 2, :], halves(("mq", c)), scale=MEM_DIM ** -0.5).then_inc(reader(("mq", c)), 1)
            m = HEADS * TT + TT
            for t in range(TT):
                for hp in range(2):
                    m += 1
                    act.wait_ge(neg_max, m)
                    for j in range(2):
                        h = 2 * hp + j
                        ins = act.activation(mprobs[t][:, h, :], bank(("ms", t, hp))[:, SEQ * j:SEQ * j + SEQ], ACT.Exp,
                                             bias=msoft[:, t, 0, h:h + 1], accum_out=msoft[:, t, 1, h:h + 1])
                    ins.then_inc(reader(("ms", t, hp)), 1)
            for c in range(4):
                drain(("mo", c), mixT[:, 2 * c:2 * c + 2, :], halves(("mo", c))).then_inc(reader(("mo", c)), 1)
            split_done = [0]

            def high_parts(upto):
                while split_done[0] < min(upto + 1, len(split_units)):
                    i = split_done[0]
                    u = split_units[i]
                    act.wait_ge(*loaded(u))
                    if i >= SPLIT_RING:
                        act.wait_ge(*LAST_OF_UNIT[split_units[i - SPLIT_RING]])
                    act.activation(split_ring[i % SPLIT_RING][:, 0, :], weights(u, 2048), ACT.Copy).then_inc(high_ready, 1)
                    split_done[0] += 1

            def high_rows(stage):
                for t in range(TT):
                    for half in range(2):
                        act.wait_ge(*drained(("normT", stage, t, half)))
                        act.activation(hT_s[:, 0, 4 * half:4 * half + 4, P * t:P * t + P],
                                       hT[:, 4 * half:4 * half + 4, P * t:P * t + P], ACT.Copy).then_inc(h_high, 1)

            high_parts(2)
            post_squares("wo", "wo_post")
            next_squares("ffn", 2)
            high_rows("ffn")
            cw = parc("conv_w").rearrange("p (j g w) -> p j g w", g=2, w=3)
            cb = parc("conv_b").rearrange("p (j g) -> p j g", g=2)

            def last_tap(j):
                name = ("up", j)
                act.wait_ge(*full(name))
                if j >= 3:
                    act.wait_ge(gated, j - 2)
                for g in range(2):
                    ins = act.activation(conv[j % 3][:, g, :], bank(name)[:, SEQ * g:SEQ * g + SEQ], ACT.Identity,
                                         scale=cw[:, j, g, 2:3], bias=cb[:, j, g:g + 1])
                ins.then_inc(tap2, 1)

            def gate_gelu(j):
                act.wait_ge(*drained(("up", j)))
                if j >= 2:
                    act.wait_ge(gated, j - 1)
                act.activation(act_g[j % 2], conv[j % 3][:, 0, :], ACT.Gelu_apprx_tanh).then_inc(gate_act, 1)

            for j in range(FFN_PAIRS + 1):
                if j < FFN_PAIRS:
                    high_parts(SPLIT[("up", j)] + 2)
                    last_tap(j)
                    high_parts(split_before(("up", j + 1)) + 2)
                if j >= 1:
                    gate_gelu(j - 1)
            post_squares("down", "down_post")
            next_squares("mix2", 4)

            def across_squares(tag):
                raw, sq = chunk2[tag][:2]
                act.activation(sq, raw, ACT.Square).then_inc(across_sq, 1)

            def across_root(tag):
                raw, sq, scale, bias, _ = chunk2[tag]
                name = ("across", tag)
                act.wait_ge(*full(name))
                src = bank(name)[:, 0:SEQ] if tag == "dk" else halves(name)
                act.activation(sq, src, ACT.Sqrt, scale=scale, bias=eps_col(bias)).then_inc(reader(name), 1)

            drain(("cq",), cqT, halves(("cq",))).then_inc(reader(("cq",)), 1)
            drain(("ck",), ckvT, bank(("ck",))[:, 0:SEQ])
            act.activation(kidxT, bank(("ck",))[:, SEQ:512], ACT.Copy).then_inc(reader(("ck",)), 1)
            drain(("ab",), row_tmp[0:4, 0, :], bank(("ab",))[0:4, 0:SEQ], ACT.Identity, bias=parc("dt_bias")[0:4, :])
            act.activation(gate_rows[0:4, 0, :], bank(("ab",))[0:4, SEQ:512], ACT.Sigmoid).then_inc(reader(("ab",)), 1)
            drain(("widx",), w_idx, bank(("widx",))[:, 0:8].rearrange("p (t h) -> p t h", t=TT), scale=1.0 / 16
                  ).then_inc(reader(("widx",)), 1)
            drain(("ug1",), gate_s, halves(("ug1",)), ACT.Sigmoid).then_inc(reader(("ug1",)), 1)
            drain(("dq",), dqT, halves(("dq",))).then_inc(reader(("dq",)), 1)
            drain(("dqi",), dqiT, halves(("dqi",))).then_inc(reader(("dqi",)), 1)
            drain(("dk",), dkT, bank(("dk",))[:, 0:SEQ])
            act.activation(dv, bank(("dk",))[:, SEQ:SEQ + P].rearrange("p (t d) -> p t d", t=TT), ACT.Copy
                           ).then_inc(reader(("dk",)), 1)
            act.wait_ge(*drained(("dk",)))
            across_squares("dq")
            across_squares("dk")
            gconv = parc("gdn_conv").rearrange("p (c w) -> p c w", w=4)

            def gdn_last_tap(i):
                name = ("qkv", i)
                act.wait_ge(*full(name))
                for c in range(2):
                    ins = act.activation(qkv[:, 2 * i + c, :], bank(name)[:, SEQ * c:SEQ * c + SEQ], ACT.Copy,
                                         scale=gconv[:, 2 * i + c, 3:4])
                ins.then_inc(tap3, 1)

            def gdn_silu(i):
                act.wait_ge(*drained(("qkv", i)))
                act.activation(qkv[:, 2 * i:2 * i + 2, :], qkv[:, 2 * i:2 * i + 2, :], ACT.Silu).then_inc(silu_done, 1)

            gdn_last_tap(0)
            across_root("dq")
            across_root("dk")
            for t in range(TT):
                for par in range(2):
                    name = ("il", t, par)
                    n = P * (t + 1)
                    drain(name, relu_l[t][par], bank(name)[:, 0:2 * n].rearrange("p (j s) -> p j s", j=2), ACT.Relu
                          ).then_inc(reader(name), 1)
            for i in range(1, 6):
                gdn_last_tap(i)
                gdn_silu(i - 1)
            gdn_silu(5)
            for i in range(2):
                drain(("z", i), zT[:, 2 * i:2 * i + 2, :], halves(("z", i)), ACT.Silu).then_inc(reader(("z", i)), 1)
            act.wait_ge(*drained(("ab",)))
            link(act.activation(row_tmp[0:4, 1, :], row_tmp[0:4, 0, :], ACT.Abs))
            link(act.activation(row_tmp[0:4, 1, :], row_tmp[0:4, 1, :], ACT.Exp, scale=-1.0))
            act.activation(a_rate[0:4, :], parc("a_log")[0:4, :], ACT.Exp)
            act.activation(row_tmp[0:4, 1, :], row_tmp[0:4, 1, :], ACT.Ln, bias=1.0).then_inc(softplus_ln, 1)
            act.wait_ge(*full(("normT", "mix2", 1, 1)))
            act.dma_start(xn[:, :, :], a["mem2"].rearrange("(t p) d -> p t d", p=P)).then_inc(mem_in, 16)
            act.wait_ge(mem_in, 32)
            for t in range(TT):
                square(("mem2", t), [xn[:, t, :]])
            act.wait_ge(decay_sum, 1)
            link(act.activation(row_tmp[0:4, 0, :], gate_rows[0:4, 3, :], ACT.Exp))
            act.activation(gate_rows[0:4, 2, :], gate_rows[0:4, 2, :], ACT.Exp).then_inc(decay_exp, 1)
            for i in range(2):
                drain(("xk", i), xkT[:, 2 * i:2 * i + 2, :], halves(("xk", i))).then_inc(reader(("xk", i)), 1)
            act.wait_ge(*drained(("xk", 1)))
            for i in range(2):
                across_squares(f"xk{i}")
            for t in range(TT):
                act.wait_ge(*acc_filled(("xv", t)))
                act.activation(xv[:, t, :], acc(("xv", t))[:, :], ACT.Copy).then_inc(acc_read, 1)
            for i in range(2):
                across_root(f"xk{i}")
            n = 0
            for t in range(TT):
                for par in range(2):
                    n += 1
                    act.wait_ge(d_max, n)
                    for j in range(2):
                        h = 2 * j + par
                        ins = act.activation(dprobs[t][:, h, :], dprobs[t][:, h, :], ACT.Exp, bias=dsoft[:, t, 0, h:h + 1],
                                             accum_out=dsoft[:, t, 1, h:h + 1])
                    ins.then_inc(d_exp, 1)
            drain(("do",), mixT[:, 4:6, :], halves(("do",))).then_inc(reader(("do",)), 1)
            act.wait_ge(silu_done, 6)
            for i in range(4):
                across_squares(f"l{i}")
            for i in range(4):
                across_root(f"l{i}")
            for i in range(2):
                act.wait_ge(gamma_diff, i + 1)
                drain(("dr", i), exp_decay[:, 2 * i:2 * i + 2, :], halves(("dr", i)), ACT.Exp
                      ).then_inc(reader(("dr", i)), 1)
            act.wait_ge(gamma_diff, 2)
            for t in range(TT):
                act.activation(Y[t], Y[t], ACT.Exp).then_inc(gamma_exp, 1)
            for t in range(TT):
                drain(("gu", t), u_n[t], bank(("gu", t))[:, :].rearrange("p (h d) -> p h d", h=GDN_HEADS)
                      ).then_inc(reader(("gu", t)), 1)
            for t in range(TT):
                drain(("gw", t), wT[t], bank(("gw", t))[:, :].rearrange("p (h d) -> p h d", h=GDN_HEADS)
                      ).then_inc(reader(("gw", t)), 1)
            act.wait_ge(*drained(("ln_mean",)))
            act.activation(conv_sq, conv_y, ACT.Square).then_inc(conv_sq_ready, 1)
            name = ("ln_var",)
            drain(name, conv_sq[:, 0, :], bank(name)[:, 0:SEQ], ACT.Sqrt, scale=1.0 / SEQ, bias=eps_col(EPS)
                  ).then_inc(reader(name), 1)
            for n in range(NCHUNK):
                name = ("go", n)
                drain(name, oT[:, :, CHUNK * n:CHUNK * n + CHUNK],
                      bank(name)[:, 0:4 * CHUNK].rearrange("p (h i) -> p h i", h=GDN_HEADS)).then_inc(reader(name), 1)
            act.wait_ge(*drained(("go", NCHUNK - 1)))
            for i in range(2):
                across_squares(f"o{i}")
            for i in range(2):
                across_root(f"o{i}")
            act.wait_ge(conv_norm, 1)
            for c in range(2):
                ins = act.activation(mixT[:, 6 + c, :], conv_y[:, c, :], ACT.Silu, scale=parc("ln_g")[:, c:c + 1],
                                     bias=parc("ln_b")[:, c:c + 1])
            ins.then_inc(conv_mix, 1)

            def squares_of_sum(product, stage):
                for t in range(TT):
                    act.wait_ge(*acc_drained((product, 2 * t + 1)))
                    square((stage, t), [x[:, t, :]])

            squares_of_sum("out2", "cross")
            for i in range(2):
                drain(("xq", i), xqT[:, 2 * i:2 * i + 2, :], halves(("xq", i))).then_inc(reader(("xq", i)), 1)
            act.wait_ge(*drained(("xq", 1)))
            for i in range(2):
                across_squares(f"xq{i}")
            for i in range(2):
                across_root(f"xq{i}")
            n = 0
            for t in range(TT):
                for hp in range(2):
                    n += 1
                    act.wait_ge(x_max, n)
                    for j in range(2):
                        h = 2 * hp + j
                        ins = act.activation(xprobs[t][:, h, :], bank(("xs", t, hp))[:, SEQ * j:SEQ * j + SEQ], ACT.Exp,
                                             bias=xsoft[:, t, 0, h:h + 1], accum_out=xsoft[:, t, 1, h:h + 1])
                    ins.then_inc(reader(("xs", t, hp)), 1)
            for c in range(2):
                drain(("xo", c), mixT[:, 2 * c:2 * c + 2, :], halves(("xo", c))).then_inc(reader(("xo", c)), 1)
            high_parts(SPLIT[("m1", 0)] + 2)
            squares_of_sum("xwo", "mlp")
            high_rows("mlp")
            for j in range(MLP_UNITS):
                high_parts(SPLIT[("m1", j)] + 2)
                if j >= 2:
                    act.wait_ge(relu_sq, j - 1)
                drain(("m1", j), relu_h[j % 2], halves(("m1", j)), ACT.Relu).then_inc(reader(("m1", j)), 1)
                act.wait_ge(*drained(("m1", j)))
                if j >= 3:
                    act.wait_ge(unit_spent, SPENT[("m2", j - 3)])
                act.activation(relu2_s[j % 3][:, 0], relu_h[j % 2], ACT.Square).then_inc(relu_high, 1)
                high_parts(split_before(("m1", j + 1)) + 2)
            high_parts(len(split_units) - 1)

        @block.vector
        def _(dve):
            chain = [0]

            def link(ins):
                chain[0] += 1
                ins.then_inc(dve_chain, 1)
                dve.wait_ge(dve_chain, chain[0])

            def scale_rows(stage, src):
                for t in range(TT):
                    dve.wait_ge(rstd_ready, STATI[(stage, t)] + 1 - 0)
                    dve.tensor_scalar(xn[:, t, :], src(t), stat((stage, t)), None, ALU.mult).then_inc(normed, 1)

            n_parts = [0]

            def drain_norm(stage):
                free = hT_free[stage]
                if free is not None:
                    dve.wait_ge(*free)
                for t in range(TT):
                    for half in range(2):
                        name = ("normT", stage, t, half)
                        dve.wait_ge(*full(name))
                        g = gains[:, GAIN[stage], 4 * half:4 * half + 4].unsqueeze(2).broadcast_to([P, 4, P])
                        dve.tensor_tensor(hT[:, 4 * half:4 * half + 4, P * t:P * t + P],
                                          bank(name)[:, :].rearrange("p (k t) -> p k t", k=4), g,
                                          ALU.mult).then_inc(reader(name), 1)
                if stage in SPLIT_STAGES:
                    for t in range(TT):
                        for half in range(2):
                            n_parts[0] += 1
                            dve.wait_ge(h_high, n_parts[0])
                            at = slice(4 * half, 4 * half + 4), slice(P * t, P * t + P)
                            dve.tensor_tensor(hT_s[:, 1, *at], hT[:, *at], hT_s[:, 0, *at], ALU.subtract).then_inc(h_low, 1)

            dve.wait_ge(*full(("bias_row",)))
            dve.tensor_copy(bias_rows[0:HEADS, :], bank(("bias_row",))[0:HEADS, 0:384]).then_inc(reader(("bias_row",)), 1)
            dve.wait_ge(*full(("bias_cmp",)))
            dve.tensor_copy(cmp_bias, bank(("bias_cmp",))[:, 0:240].rearrange("p (t c h) -> p t h c", t=TT, c=NCMP)
                            ).then_inc(reader(("bias_cmp",)), 1)
            scale_rows("mix", lambda t: x[:, t, :])
            dve.wait_ge(params_in, 16)
            drain_norm("mix")
            dve.wait_ge(shifted_in, 64)
            pos = parc("cmp_pos").rearrange("p (v j) -> p v j", v=2)
            for kv in range(2):
                for g in range(GROUPS):
                    v = pairs[:, kv, g, :].rearrange("p (c j e) -> p j c e", j=8, e=2)
                    for hi in range(2):
                        ins = dve.tensor_tensor(blocks[:, kv, 8 * hi:8 * hi + 8, g, :], v[:, :, hi:hi + NCMP, 0],
                                                pos[:, kv, 8 * hi:8 * hi + 8].unsqueeze(2).broadcast_to([P, 8, NCMP]), ALU.add)
            ins.then_inc(blocks_ready, 1)
            for t in range(TT):
                dve.wait_ge(*drained(("v",)))
                link(dve.bn_stats(soft.rearrange("p t a h b -> p (t a h b)")[:, 6 * t:6 * t + 6], v_g[:, t, :]))
                dve.bn_aggr(stats[:, 2 * STATI[("sgu", t)]:2 * STATI[("sgu", t)] + 2],
                            soft.rearrange("p t a h b -> p (t a h b)")[:, 6 * t:6 * t + 6]).then_inc(sgu_stat, 1)
            for t in range(TT):
                dve.wait_ge(sgu_rstd, t + 1)
                link(dve.tensor_scalar(v_n[:, t, :], v_g[:, t, :], stat(("sgu", t)), stat(("sgu", t), 1),
                                       ALU.subtract, ALU.mult))
                link(dve.tensor_tensor(v_n[:, t, :], v_n[:, t, :], parc("sgu_g"), ALU.mult))
                dve.tensor_tensor(v_n[:, t, :], v_n[:, t, :], parc("sgu_b"), ALU.add).then_inc(sgu_normed, 1)
            name = ("cmp_kv",)
            dve.wait_ge(*full(name))
            dve.tensor_scalar(cmp_kT, bank(name)[:, 0:NCMP], parc("cmp_b2k"), None, ALU.add)
            for j in range(4):
                rows_j = slice(32 * j, 32 * j + NCMP)
                ins = dve.tensor_tensor(cmp_v[rows_j, :], bank(name)[rows_j, 64:64 + P], parc("cmp_b2v")[rows_j, :], ALU.add)
            ins.then_inc(reader(name), 1)

            scale_rows("memkv", lambda t: xn[:, t, :])
            for t in range(TT):
                if t == 0:
                    dve.memset(cmp_p.rearrange("p t h c -> p (t h c)"), 0.0).then_inc(scored, 1)
                    dve.wait_ge(scored, 1)
                for g in range(GROUPS):
                    name = ("cmp_s", t, g)
                    hs = slice(HG * g, HG * g + HG)
                    dve.wait_ge(*full(name))
                    dve.tensor_tensor(cmp_p[:, t, hs, 0:NCMP],
                                      bank(name)[:, 0:HG * NCMP].rearrange("p (h c) -> p h c", h=HG),
                                      cmp_bias[:, t, hs, :], ALU.add).then_inc(reader(name), 1)
                dve.wait_ge(*drained(name))
                link(dve.tensor_reduce(soft[:, t, 0, :, 0], cmp_p[:, t, :, 0:NCMP], AX, ALU.max))
                dve.tensor_scalar(soft[:, t, 0, :, 0], soft[:, t, 0, :, 0], MASKED / 2, -1.0, ALU.max, ALU.mult
                                  ).then_inc(neg_max, 1)
                if t == 0:
                    dve.wait_ge(bias_tile_in, 16)
                for h in range(HEADS):
                    name = ("s", t, h)
                    n = P * (t + 1)
                    dve.wait_ge(*full(name))
                    dve.tensor_tensor(probs[t][h], bank(name)[:, 0:2 * n].rearrange("p (j s) -> p j s", j=2),
                                      toeplitz[:, h, 0:n][:, ::-1].unsqueeze(1).broadcast_to([P, 2, n]), ALU.add
                                      ).then_inc(reader(name), 1)
                    dve.wait_ge(*drained(name))
                    dve.tensor_reduce(soft[:, t, 0, h, 1:3], probs[t][h], AX, ALU.max, negate=True).then_inc(neg_max, 1)
            name = ("pool_out",)
            dve.wait_ge(*full(name))
            dve.tensor_tensor(mixT[:, 4:6, :], bank(name)[:, :].rearrange("p (c t) -> p c t", c=2),
                              parc("pool_scale").unsqueeze(2).broadcast_to([P, 2, SEQ]), ALU.mult).then_inc(reader(name), 1)
            name = ("sgu_out",)
            dve.wait_ge(*full(name))
            for c in range(2):
                ins = dve.tensor_tensor(mixT[:, 6 + c, :].rearrange("p (t i) -> p t i", t=TT),
                                        bank(name)[:, SEQ * c:SEQ * c + SEQ].rearrange("p (t i) -> p t i", t=TT),
                                        parc("sgu_bias")[:, P * c:P * c + P].unsqueeze(1).broadcast_to([P, TT, P]), ALU.add)
            ins.then_inc(reader(name), 1)
            dve.wait_ge(*drained(name))
            dve.wait_ge(*drained(("u",)))
            dve.tensor_tensor(mixT[:, 6:8, :], mixT[:, 6:8, :], uT, ALU.mult).then_inc(mix_tail, 1)
            drain_norm("memkv")
            for t in range(TT):
                dve.wait_ge(exped, (HEADS + 1) * (t + 1))
                den = soft[:, t, 1, :, 0:3]
                link(dve.tensor_scalar(den, den, 1.0, None, ALU.max))
                link(dve.reciprocal(den, den))
                link(dve.tensor_tensor(den, den, gates[:, t, :, :], ALU.mult))
                dve.tensor_tensor(cmp_p[:, t, :, 0:NCMP], cmp_p[:, t, :, 0:NCMP],
                                  den[:, :, 0:1].broadcast_to([P, HEADS, NCMP]), ALU.mult).then_inc(weighed, 1)
                for h in range(HEADS):
                    dve.tensor_tensor(probs[t][h], probs[t][h],
                                      den[:, h, 1:3].unsqueeze(2).broadcast_to([P, 2, P * (t + 1)]), ALU.mult
                                      ).then_inc(weighed, 1)
            for t in range(TT):
                name = ("cmp_pT", t)
                dve.wait_ge(*full(name))
                dve.tensor_copy(cmp_pT[:, :, P * t:P * t + P], bank(name)[:, 0:SEQ].rearrange("p (g t) -> p g t", g=GROUPS)
                                ).then_inc(reader(name), 1)
            for h in range(HEADS):
                if h >= 2:
                    k = h - 2
                    dve.wait_ge(*(acc_filled(("o", k // 4)) if k % 4 == 3 else (heads_done, k - k // 4 + 1)))
                for t in range(TT):
                    name = ("pT", t, h)
                    n = t + 1
                    dve.wait_ge(*full(name))
                    dve.tensor_copy(probsT[h % 2][:, :, 0:n, P * t:P * t + P],
                                    bank(name)[:, 0:SEQ * n].rearrange("p (j s t) -> p j s t", j=2, s=n)
                                    ).then_inc(reader(name), 1)

            def post_norm(product, stage, n_gain):
                dve.wait_ge(gain_in, 16 * n_gain)
                for t in range(TT):
                    dve.wait_ge(rstd_ready, STATI[(stage, t)] + 1)
                    for half in range(2):
                        c = slice(512 * half, 512 * half + 512)
                        dve.scalar_tensor_tensor(out=xn[:, t, c], in0=acc((product, 2 * t + half))[:, :],
                                                 scalar=stat((stage, t)), in1=post_gain[:, c], op0=ALU.mult,
                                                 op1=ALU.mult).then_inc(acc_read, 1)
                    dve.wait_ge(*acc_drained((product, 2 * t + 1)))
                    dve.tensor_tensor(x[:, t, :], x[:, t, :], xn[:, t, :], ALU.add).then_inc(x_done, 1)
                    dve.wait_ge(x_done, 2 * (n_gain - 1) + t + 1)

            post_norm("out", "out_post", 1)
            scale_rows("mem", lambda t: x[:, t, :])
            drain_norm("mem")
            for t in range(TT):
                for hp in range(2):
                    dve.wait_ge(*full(("ms", t, hp)))
                    dve.tensor_reduce(msoft[:, t, 0, 2 * hp:2 * hp + 2],
                                      bank(("ms", t, hp))[:, :].rearrange("p (h s) -> p h s", h=2), AX, ALU.max,
                                      negate=True).then_inc(neg_max, 1)
            for t in range(TT):
                for hp in range(2):
                    dve.wait_ge(*drained(("ms", t, hp)))
                    den = msoft[:, t, 1, 2 * hp:2 * hp + 2]
                    link(dve.reciprocal(den, den))
                    dve.tensor_tensor(mprobs[t][:, 2 * hp:2 * hp + 2, :], mprobs[t][:, 2 * hp:2 * hp + 2, :],
                                      den.unsqueeze(2).broadcast_to([P, 2, SEQ]), ALU.mult).then_inc(weighed, 1)
            for t in range(TT):
                for hp in range(2):
                    name = ("mpT", t, hp)
                    dve.wait_ge(*full(name))
                    dve.tensor_copy(mprobsT[:, 2 * hp:2 * hp + 2, :, P * t:P * t + P],
                                    bank(name)[:, :].rearrange("p (h s t) -> p h s t", h=2, s=TT)
                                    ).then_inc(reader(name), 1)
            split_done = [0]

            def low_parts(upto):
                while split_done[0] < min(upto + 1, len(split_units)):
                    i = split_done[0]
                    dve.wait_ge(high_ready, i + 1)
                    dve.tensor_tensor(split_ring[i % SPLIT_RING][:, 1, :], weights(split_units[i], 2048),
                                      split_ring[i % SPLIT_RING][:, 0, :], ALU.subtract).then_inc(low_ready, 1)
                    split_done[0] += 1

            low_parts(2)
            post_norm("wo", "wo_post", 2)
            scale_rows("ffn", lambda t: x[:, t, :])
            drain_norm("ffn")
            cw = parc("conv_w").rearrange("p (j g w) -> p j g w", g=2, w=3)

            def taps(j):
                name = ("up", j)
                dve.wait_ge(tap2, j + 1)
                for s in (1, 2):
                    for g in range(2):
                        c = conv[j % 3][:, g, s:SEQ]
                        ins = dve.scalar_tensor_tensor(out=c, in0=bank(name)[:, SEQ * g:SEQ * g + SEQ - s],
                                                       scalar=cw[:, j, g, 2 - s:3 - s], in1=c, op0=ALU.mult, op1=ALU.add)
                    if s == 1:
                        link(ins)
                ins.then_inc(reader(name), 1)

            def gate_times_value(j):
                dve.wait_ge(gate_act, j + 1)
                if j >= 4:
                    dve.wait_ge(unit_spent, SPENT[("down", (j - 4) // 2)])
                dve.tensor_tensor(prod_s[j % 4][:, 0, :], act_g[j % 2], conv[j % 3][:, 1, :], ALU.mult)
                link(dve.tensor_tensor(prod[j % 2], act_g[j % 2], conv[j % 3][:, 1, :], ALU.mult))
                dve.tensor_tensor(prod_s[j % 4][:, 1, :], prod[j % 2], prod_s[j % 4][:, 0, :], ALU.subtract
                                  ).then_inc(gated, 1)

            for j in range(FFN_PAIRS + 1):
                if j < FFN_PAIRS:
                    low_parts(SPLIT[("up", j)] + 2)
                    taps(j)
                    low_parts(split_before(("up", j + 1)) + 2)
                if j >= 1:
                    gate_times_value(j - 1)
            post_norm("down", "down_post", 3)
            scale_rows("mix2", lambda t: x[:, t, :])
            drain_norm("mix2")
            link(dve.memset(y_pad[:, :, 0:CONV_TAPS - 1], 0.0))
            name = ("ug0",)
            dve.wait_ge(*full(name))
            dve.wait_ge(*drained(("ug1",)))
            dve.tensor_tensor(y_pad[:, :, CONV_TAPS - 1:CONV_TAPS - 1 + SEQ], bank(name)[:, :].rearrange("p (c t) -> p c t", c=2),
                              gate_s, ALU.mult).then_inc(reader(name), 1)
            gconv = parc("gdn_conv").rearrange("p (c w) -> p c w", w=4)

            def gdn_taps(i):
                name = ("qkv", i)
                dve.wait_ge(tap3, i + 1)
                for s in (1, 2, 3):
                    for c in range(2):
                        o = qkv[:, 2 * i + c, s:SEQ]
                        ins = dve.scalar_tensor_tensor(out=o, in0=bank(name)[:, SEQ * c:SEQ * c + SEQ - s],
                                                       scalar=gconv[:, 2 * i + c, 3 - s:4 - s], in1=o, op0=ALU.mult,
                                                       op1=ALU.add)
                    if s < 3:
                        link(ins)
                ins.then_inc(reader(name), 1)

            def across_norm(tag):
                raw, sq, _, _, gain = chunk2[tag]
                dve.wait_ge(*drained(("across", tag)))
                link(dve.reciprocal(sq, sq))
                if gain is None:
                    ins = dve.tensor_tensor(raw, raw, sq, ALU.mult)
                else:
                    ins = dve.scalar_tensor_tensor(out=raw, in0=raw, scalar=parc(gain), in1=sq, op0=ALU.mult, op1=ALU.mult)
                ins.then_inc(across_done, 1)

            gdn_taps(0)
            across_norm("dq")
            across_norm("dk")
            dve.wait_ge(*drained(("widx",)))
            for t in range(TT):
                for par in range(2):
                    dve.wait_ge(*drained(("il", t, par)))
                s = idx_score[t]
                link(dve.tensor_scalar(s, relu_l[t][0][:, 0, :], w_idx[:, t, 0:1], None, ALU.mult))
                for h in range(1, 4):
                    ins = dve.scalar_tensor_tensor(out=s, in0=relu_l[t][h % 2][:, h // 2, :], scalar=w_idx[:, t, h:h + 1],
                                                   in1=s, op0=ALU.mult, op1=ALU.add)
                    if h < 3:
                        link(ins)
                ins.then_inc(idx_sum, 1)

            def topk_round(t, last):
                link(dve.max(top8[:, t, :], idx_score[t]))
                ins = dve.match_replace(out=idx_score[t], in_to_replace=top8[:, t, :], in_values=idx_score[t],
                                        imm_value=PICKED)
                if last:
                    ins.then_inc(picked, 1)
                else:
                    link(ins)

            taps_left = list(range(1, 6))
            for t in range(TT):
                dve.wait_ge(idx_causal, t + 1)
                for r in range(TOPK_ROUNDS):
                    topk_round(t, r == TOPK_ROUNDS - 1)
                    if r % 3 == 2 and taps_left:
                        gdn_taps(taps_left.pop(0))
            while taps_left:
                gdn_taps(taps_left.pop(0))
            u_row, ln_row = row_tmp[0:4, 0, :], row_tmp[0:4, 1, :]
            dec, last_less = gate_rows[0:4, 3, :], gate_rows[0:4, 2, :]
            dve.wait_ge(softplus_ln, 1)
            link(dve.scalar_tensor_tensor(out=ln_row, in0=u_row, scalar=0.0, in1=ln_row, op0=ALU.max, op1=ALU.add))
            link(dve.tensor_scalar(ln_row, ln_row, a_rate[0:4, :], -1.0, ALU.mult, ALU.mult))
            link(dve.tensor_tensor_scan(dec, conc("chunk_keep")[0:4, :], ln_row, 0.0, ALU.mult, ALU.add))

            def by_chunk(v):
                return v.rearrange("p (n i) -> p n i", n=NCHUNK)

            dve.tensor_tensor(by_chunk(last_less), by_chunk(dec)[:, :, CHUNK - 1:CHUNK].broadcast_to([4, NCHUNK, CHUNK]),
                              by_chunk(dec), ALU.subtract).then_inc(decay_sum, 1)
            dve.wait_ge(decay_exp, 1)
            dve.tensor_tensor(gate_rows[0:4, 1, :], gate_rows[0:4, 0, :], u_row, ALU.mult).then_inc(rows_ready, 1)
            scale_rows("mem2", lambda t: xn[:, t, :])
            drain_norm("mem2")
            for i in range(2):
                across_norm(f"xk{i}")
            for t in range(TT):
                dve.wait_ge(dmask_ready, t + 1)
                for par in range(2):
                    name = ("dl", t, par)
                    n = P * (t + 1)
                    v = dprobs[t][:, par::2, :]
                    dve.wait_ge(*full(name))
                    dve.tensor_tensor(v, bank(name)[:, 0:2 * n].rearrange("p (j s) -> p j s", j=2),
                                      dmask[t].unsqueeze(1).broadcast_to([P, 2, n]), ALU.add).then_inc(reader(name), 1)
                    dve.wait_ge(*drained(name))
                    dve.tensor_reduce(dsoft[:, t, 0, par::2], v, AX, ALU.max, negate=True).then_inc(d_max, 1)
            for t in range(TT):
                dve.wait_ge(d_exp, 2 * t + 2)
                den = dsoft[:, t, 1, :]
                link(dve.reciprocal(den, den))
                dve.tensor_tensor(dprobs[t], dprobs[t], den.unsqueeze(2).broadcast_to([P, DSA_HEADS, P * (t + 1)]),
                                  ALU.mult).then_inc(d_weighed, 1)
            for t in range(TT):
                for par in range(2):
                    name = ("dpT", t, par)
                    n = t + 1
                    dve.wait_ge(*full(name))
                    dve.tensor_copy(dprobsT[par][:, :, 0:n, P * t:P * t + P],
                                    bank(name)[:, 0:SEQ * n].rearrange("p (j s t) -> p j s t", j=2, s=n)
                                    ).then_inc(reader(name), 1)
            for i in range(4):
                across_norm(f"l{i}")
            dve.wait_ge(*full(("cols",)))
            dve.tensor_copy(gate_cols, bank(("cols",))[:, 0:32].rearrange("p (t k h) -> p t k h", t=TT, k=4)
                            ).then_inc(reader(("cols",)), 1)
            dve.wait_ge(*drained(("cols",)))
            for i in range(2):
                name = ("dr", i)
                dve.wait_ge(*full(name))
                for t in range(TT):
                    for j in range(2):
                        h = 2 * i + j
                        ins = dve.tensor_scalar(Y[t][:, h, :], bank(name)[:, SEQ * j + P * t:SEQ * j + P * t + P],
                                                gate_cols[:, t, 3, h:h + 1], 0.0, ALU.subtract, ALU.min)
                ins.then_inc(gamma_diff, 1)
            qT2, kT2, vT2 = qkv[:, 0:4, :], qkv[:, 4:8, :], qkv[:, 8:12, :]
            dve.wait_ge(across_done, ACROSS["l3"] + 1)
            for i in range(2):
                name = ("br", i)
                dve.wait_ge(*full(name))
                dve.tensor_tensor(kbT[:, 2 * i:2 * i + 2, :], bank(name)[:, :].rearrange("p (c t) -> p c t", c=2),
                                  kT2[:, 2 * i:2 * i + 2, :], ALU.mult).then_inc(reader(name), 1)
            dve.wait_ge(*drained(("dr", 1)))
            dve.tensor_tensor(qeT, qT2, exp_decay, ALU.mult).then_inc(qe_ready, 1)

            def heads(name):
                return bank(name)[:, :].rearrange("p (h d) -> p h d", h=GDN_HEADS)

            def col(t, kind):
                return gate_cols[:, t, kind, :].unsqueeze(2).broadcast_to([P, GDN_HEADS, P])

            for t in range(TT):
                name = ("kA", t)
                dve.wait_ge(*full(name))
                dve.tensor_tensor(bke[t], heads(name), col(t, 1), ALU.mult)
                dve.tensor_tensor(kdec[t], heads(name), col(t, 2), ALU.mult).then_inc(reader(name), 1)
            for t in range(TT):
                name = ("vA", t)
                dve.wait_ge(*full(name))
                dve.tensor_tensor(bv[t], heads(name), col(t, 0), ALU.mult).then_inc(reader(name), 1)
            for kind, dst, decay in (("kk", AT, inv), ("qk", qkT, Y)):
                for t in range(TT):
                    name = (kind, t)
                    dve.wait_ge(*full(name))
                    dve.wait_ge(gamma_ready, t + 1)
                    dve.tensor_tensor(dst[t], heads(name), decay[t], ALU.mult).then_inc(reader(name), 1)

            dw = parc("conv_dw").rearrange("p (c w) -> p c w", c=2)
            taps31 = [0]

            def conv_tap():
                w = taps31[0]
                if w == CONV_TAPS:
                    return
                taps31[0] += 1
                for c in range(2):
                    src = y_pad[:, c, w:w + SEQ]
                    if w == 0:
                        ins = dve.tensor_scalar(conv_y[:, c, :], src, dw[:, c, 0:1], parc("dw_b")[:, c:c + 1], ALU.mult, ALU.add)
                    else:
                        ins = dve.scalar_tensor_tensor(out=conv_y[:, c, :], in0=src, scalar=dw[:, c, w:w + 1],
                                                       in1=conv_y[:, c, :], op0=ALU.mult, op1=ALU.add)
                if w == CONV_TAPS - 1:
                    ins.then_inc(conv_out, 1)
                    dve.wait_ge(conv_out, 1)
                else:
                    link(ins)

            masks = conc("levels").rearrange("p (l j) -> p l j", l=LEVELS)
            eye = ident.unsqueeze(1).broadcast_to([P, GDN_HEADS, P])
            for level in range(LEVELS):
                for t in range(TT):
                    name = ("y", level, t)
                    dve.wait_ge(*full(name))
                    dve.tensor_tensor(Y[t], heads(name), masks[:, level, :].unsqueeze(1).broadcast_to([P, GDN_HEADS, P]),
                                      ALU.mult).then_inc(reader(name), 1)
                    conv_tap()
                for kind, dst in (("d", inv), ("dT", invT)):
                    if (kind, level) == ("d", LEVELS - 1):
                        continue
                    for t in range(TT):
                        name = (kind, level, t)
                        dve.wait_ge(*full(name))
                        dve.scalar_tensor_tensor(out=dst[t], in0=heads(name), scalar=-1.0, in1=(dst[t] if level else eye),
                                                 op0=ALU.mult, op1=ALU.add).then_inc(reader(name), 1)
                        conv_tap()
            while taps31[0] < CONV_TAPS:
                conv_tap()
            name = ("ln_mean",)
            dve.wait_ge(*full(name))
            dve.scalar_tensor_tensor(out=conv_y[:, 0, :], in0=bank(name)[:, 0:SEQ], scalar=-1.0 / SEQ, in1=conv_y[:, 0, :],
                                     op0=ALU.mult, op1=ALU.add)
            dve.scalar_tensor_tensor(out=conv_y[:, 1, :], in0=bank(name)[:, 0:SEQ], scalar=-1.0 / SEQ, in1=conv_y[:, 1, :],
                                     op0=ALU.mult, op1=ALU.add).then_inc(reader(name), 1)
            dve.wait_ge(*drained(("ln_var",)))
            link(dve.reciprocal(conv_sq[:, 0, :], conv_sq[:, 0, :]))
            dve.tensor_tensor(conv_y, conv_y, conv_sq[:, 0:1, :].broadcast_to([P, 2, SEQ]), ALU.mult).then_inc(conv_norm, 1)
            for n in range(NCHUNK):
                t, r = n // 2, slice(CHUNK * (n % 2), CHUNK * (n % 2) + CHUNK)
                if n == 0:
                    dve.wait_ge(*drained(("gu", 0)))
                    dve.tensor_copy(v_new[r, :, :], u_n[t][r, :, :]).then_inc(v_news, 1)
                else:
                    name = ("ws", n)
                    dve.wait_ge(*full(name))
                    dve.wait_ge(*drained(("gu", t)))
                    dve.scalar_tensor_tensor(out=v_new[r, :, :], in0=heads(name)[r, :, :], scalar=-1.0, in1=u_n[t][r, :, :],
                                             op0=ALU.mult, op1=ALU.add).then_inc(reader(name), 1)
                if n < NCHUNK - 1:
                    name = ("kv", n)
                    dve.wait_ge(*full(name))
                    if n == 0:
                        dve.tensor_copy(state, heads(name)).then_inc(reader(name), 1)
                    else:
                        for h in range(GDN_HEADS):
                            at = CHUNK * n + CHUNK - 1
                            ins = dve.scalar_tensor_tensor(out=state[:, h, :], in0=state[:, h, :],
                                                           scalar=exp_decay[:, h, at:at + 1], in1=heads(name)[:, h, :],
                                                           op0=ALU.mult, op1=ALU.add)
                        ins.then_inc(reader(name), 1)
            for i in range(2):
                across_norm(f"o{i}")
            dve.wait_ge(across_done, ACROSS["o1"] + 1)
            dve.wait_ge(*drained(("z", 1)))
            dve.tensor_tensor(mixT[:, 0:4, :], oT, zT, ALU.mult).then_inc(o_mix, 1)

            def add_product(product):
                for t in range(TT):
                    for half in range(2):
                        f = (product, 2 * t + half)
                        c = slice(512 * half, 512 * half + 512)
                        dve.wait_ge(*acc_filled(f))
                        dve.tensor_tensor(x[:, t, c], acc(f)[:, :], x[:, t, c], ALU.add).then_inc(acc_read, 1)

            add_product("out2")
            scale_rows("cross", lambda t: x[:, t, :])
            drain_norm("cross")
            for i in range(2):
                across_norm(f"xq{i}")
            for t in range(TT):
                for hp in range(2):
                    name = ("xs", t, hp)
                    dve.wait_ge(*full(name))
                    dve.tensor_reduce(xsoft[:, t, 0, 2 * hp:2 * hp + 2], bank(name)[:, :].rearrange("p (h s) -> p h s", h=2),
                                      AX, ALU.max, negate=True).then_inc(x_max, 1)
            for t in range(TT):
                for hp in range(2):
                    dve.wait_ge(*drained(("xs", t, hp)))
                    den = xsoft[:, t, 1, 2 * hp:2 * hp + 2]
                    link(dve.reciprocal(den, den))
                    dve.tensor_tensor(xprobs[t][:, 2 * hp:2 * hp + 2, :], xprobs[t][:, 2 * hp:2 * hp + 2, :],
                                      den.unsqueeze(2).broadcast_to([P, 2, SEQ]), ALU.mult).then_inc(x_weighed, 1)
            for t in range(TT):
                for hp in range(2):
                    name = ("xpT", t, hp)
                    dve.wait_ge(*full(name))
                    dve.tensor_copy(xprobsT[:, 2 * hp:2 * hp + 2, :, P * t:P * t + P],
                                    bank(name)[:, :].rearrange("p (h s t) -> p h s t", h=2, s=TT)).then_inc(reader(name), 1)
            low_parts(SPLIT[("m1", 0)] + 2)
            add_product("xwo")
            scale_rows("mlp", lambda t: x[:, t, :])
            drain_norm("mlp")
            for j in range(MLP_UNITS):
                low_parts(SPLIT[("m1", j)] + 2)
                dve.wait_ge(*drained(("m1", j)))
                link(dve.tensor_tensor(relu2[j % 2], relu_h[j % 2], relu_h[j % 2], ALU.mult))
                dve.wait_ge(relu_high, j + 1)
                dve.tensor_tensor(relu2_s[j % 3][:, 1], relu2[j % 2], relu2_s[j % 3][:, 0], ALU.subtract).then_inc(relu_sq, 1)
                low_parts(split_before(("m1", j + 1)) + 2)
            low_parts(len(split_units) - 1)
            add_product("m2")

        @block.tensor
        def _(pe):
            def open_tile(name):
                i = TILE[name]
                if i >= NB:
                    pe.wait_ge(tile_read[i % NB], i // NB)
                return banks[i % NB]

            def norm_T(stage, first):
                for t in range(TT):
                    pe.wait_ge(normed, first + t + 1)
                    for half in range(2):
                        ps = open_tile(("normT", stage, t, half))
                        for k in range(4):
                            c = P * (4 * half + k)
                            ins = pe.transpose(ps[:, P * k:P * k + P], xn[:, t, c:c + P], ident)
                        ins.then_inc(tile_full, 1)

            def wide(out, w, lo, n=P, src=None):
                for k in range(KD):
                    ins = pe.matmul(out, w[:, k, lo:lo + n], (hT if src is None else src)[:, k, :], start=(k == 0), stop=(k == KD - 1))
                return ins

            def tall(out, w, lo, n, t):
                for k in range(KD):
                    ins = pe.matmul(out, hT[:, k, P * t:P * t + P], w[:, k, lo:lo + n], start=(k == 0), stop=(k == KD - 1))
                return ins

            def pair_of_chunks(name, unit):
                ps = open_tile(name)
                pe.wait_ge(*loaded(unit))
                w = weights(unit, KD, 256)
                wide(ps[:, 0:SEQ], w, 0)
                wide(ps[:, SEQ:512], w, P).then_inc(tile_full, 1)

            def split_matmul(out, lhs, rhs, start, stop):
                for n, (p, q) in enumerate(((0, 0), (0, 1), (1, 0))):
                    ins = pe.matmul(out, lhs(p), rhs(q), start=(start and n == 0), stop=(stop and n == 2))
                return ins

            def split_pair(name):
                ps = open_tile(name)
                pe.wait_ge(low_ready, SPLIT[name] + 1)
                w = split_weights(name, KD, 256)
                for c in range(2):
                    for k in range(KD):
                        ins = split_matmul(ps[:, SEQ * c:SEQ * c + SEQ], lambda p: w[:, p, k, P * c:P * c + P],
                                           lambda p: hT_s[:, p, k, :], k == 0, k == KD - 1)
                ins.then_inc(tile_full, 1)

            def split_product_unit(unit, first, last, lhs):
                pe.wait_ge(low_ready, SPLIT[unit] + 1)
                w = split_weights(unit, 2, D)
                for kk in range(2):
                    for t in range(TT):
                        for half in range(2):
                            ins = split_matmul(acc((unit[0], 2 * t + half))[:, :], lambda p: lhs(p, kk, t),
                                               lambda p: w[:, p, kk, 512 * half:512 * half + 512], first and kk == 0,
                                               last and kk == 1)
                            if last and kk == 1:
                                ins.then_inc(acc_full, 1)
                if not last:
                    ins.then_inc(unit_spent, 1)

            def product_unit(product, unit, first, last, lhs, nk=2):
                pe.wait_ge(*loaded(unit))
                w = weights(unit, nk, 2048 // nk)
                for kk in range(nk):
                    for t in range(TT):
                        for half in range(2):
                            ins = pe.matmul(acc((product, 2 * t + half))[:, :], lhs(kk, t),
                                            w[:, kk, 512 * half:512 * half + 512], start=(first and kk == 0),
                                            stop=(last and kk == nk - 1))
                            if last and kk == nk - 1:
                                ins.then_inc(acc_full, 1)
                if not last:
                    ins.then_inc(unit_spent, 1)

            def open_product(product):
                if FILL[(product, 0)]:
                    pe.wait_ge(acc_read, FILL[(product, 0)])

            def product(name, unit, src):
                open_product(name)
                for i in range(4):
                    product_unit(name, (unit, i), i == 0, i == 3, lambda kk, t: src[:, 2 * i + kk, P * t:P * t + P])

            pe.wait_ge(params_in, 16)
            pe.wait_ge(consts_in, 16)
            pe.wait_ge(hots_in, 16)
            relb = parc("relb")[0:REL_BUCKETS + 1, :]
            ps = open_tile(("bias_row",))
            pe.matmul(ps[0:HEADS, 0:384], relb, hots[0:REL_BUCKETS + 1, P:DIST_COLS], start=True, stop=True).then_inc(tile_full, 1)
            ps = open_tile(("bias_cmp",))
            for t in range(TT):
                for c in range(NCMP):
                    lo = SEQ - 1 + P * t - (CMP_STRIDE * c + CMP_LEN - 1)
                    at = (t * NCMP + c) * HEADS
                    ins = pe.matmul(ps[:, at:at + HEADS], hots[0:REL_BUCKETS + 1, lo:lo + P], relb, start=True, stop=True)
            ins.then_inc(tile_full, 1)

            norm_T("mix", 0)
            for stage_tile in (("normT", "mix", t, half) for t in range(TT) for half in range(2)):
                pe.wait_ge(*drained(stage_tile))
            pair_of_chunks(("q0",), "q0")
            pair_of_chunks(("q1",), "q1")
            pair_of_chunks(("kcvc",), "kcvc")
            for u in ("ksvs", "kwvw"):
                ps = open_tile((u,))
                pe.wait_ge(*loaded(u))
                w = weights(u, KD, 256)
                wide(ps[:, 0:SEQ], w, 0)
                for t in range(TT):
                    ins = tall(ps[:, SEQ + P * t:SEQ + P * t + P], w, P, P, t)
                ins.then_inc(tile_full, 1)
            ps = open_tile(("gates",))
            pe.wait_ge(*loaded("gates"))
            for t in range(TT):
                ins = tall(ps[:, 24 * t:24 * t + 24], weights("gates", KD, 24), 0, 24, t)
            ins.then_inc(tile_full, 1)
            pair_of_chunks(("pool",), "pool")
            pair_of_chunks(("u",), "u")
            ps = open_tile(("v",))
            pe.wait_ge(*loaded("v"))
            for t in range(TT):
                ins = tall(ps[:, SEQ * t:SEQ * t + SEQ], weights("v", KD, 256), 0, 256, t)
            ins.then_inc(tile_full, 1)

            ps = open_tile(("cmp_h",))
            pe.wait_ge(blocks_ready, 1)
            for kv, u in enumerate(("cmp_w1k", "cmp_w1v")):
                pe.wait_ge(*loaded(u))
                w = weights(u, CMP_PAIRS, P)
                for j in range(CMP_PAIRS):
                    ins = pe.matmul(ps[:, 32 * kv:32 * kv + 30], w[:, j, :],
                                    blocks[:, kv, j, :, :].rearrange("p g c -> p (g c)"),
                                    start=(j == 0), stop=(j == CMP_PAIRS - 1))
            ins.then_inc(tile_full, 1)
            ps = open_tile(("cmp_kv",))
            pe.wait_ge(*drained(("cmp_h",)))
            w2 = parc("cmp_w2").rearrange("p (v d) -> p v d", v=2)
            for g in range(GROUPS):
                pe.matmul(ps[DK * g:DK * g + DK, 0:NCMP], w2[:, 0, :], cmp_hT[:, 0, NCMP * g:NCMP * g + NCMP],
                          start=True, stop=True)
            for j in range(4):
                for g in range(GROUPS):
                    ins = pe.matmul(ps[32 * j:32 * j + NCMP, 64 + DK * g:64 + DK * g + DK],
                                    cmp_hT[:, 1, NCMP * g:NCMP * g + NCMP], w2[:, 1, :], start=True, stop=True)
            ins.then_inc(tile_full, 1)

            def head_rows(h):
                return slice(DK * (h // HG), DK * (h // HG) + DK)

            for u in ("q0", "q1", "ksvs", "kwvw", "cmp_kv"):
                pe.wait_ge(*drained((u,)))
            for t in range(TT):
                for g in range(GROUPS):
                    ps = open_tile(("cmp_s", t, g))
                    for i in range(HG):
                        ins = pe.matmul(ps[:, NCMP * i:NCMP * i + NCMP], qT[head_rows(HG * g), i, P * t:P * t + P],
                                        cmp_kT[head_rows(HG * g), :], start=True, stop=True)
                    ins.then_inc(tile_full, 1)
                for h in range(HEADS):
                    ps = open_tile(("s", t, h))
                    n = P * (t + 1)
                    pe.matmul(ps[:, 0:2 * n].rearrange("p (j s) -> p j s", j=2), qT[head_rows(h), h % HG, P * t:P * t + P],
                              keysT[head_rows(h), :, 0:n], start=True, stop=True).then_inc(tile_full, 1)
            ps = open_tile(("pool_out",))
            pe.wait_ge(pooled, 1)
            pw = parc("pool_w").rearrange("p (c d) -> p c d", c=2)
            for g in range(4):
                r = slice(64 * (g % 2), 64 * (g % 2) + 64)
                ins = pe.matmul(ps[r, SEQ * (g // 2):SEQ * (g // 2) + SEQ], pw[r, g // 2, :], pool_d[r, g // 2, :],
                                start=True, stop=True)
            ins.then_inc(tile_full, 1)
            ps = open_tile(("sgu_out",))
            pe.wait_ge(sgu_normed, TT)
            pe.wait_ge(masked_ws, 1)
            wsT = parc("sgu_wT").rearrange("p (h t) -> p h t", h=4)
            for h in range(4):
                for t in range(TT):
                    at = SEQ * (h // 2) + P * t
                    ins = pe.matmul(ps[64 * (h % 2):64 * (h % 2) + 64, at:at + P], v_n[:, t, 64 * h:64 * h + 64],
                                    wsT[:, h, :], start=True, stop=True)
            ins.then_inc(tile_full, 1)

            norm_T("memkv", 2)
            for t in range(TT):
                for half in range(2):
                    pe.wait_ge(*drained(("normT", "memkv", t, half)))
            for c in range(4):
                pair_of_chunks(("mk", c), ("mk", c))
            product("mv", "mv", hT)

            for t in range(TT):
                pe.wait_ge(weighed, 1 + t * (HEADS + 1))
                ps = open_tile(("cmp_pT", t))
                for g in range(GROUPS):
                    ins = pe.transpose(ps[:, P * g:P * g + P],
                                       cmp_p[:, t, HG * g:HG * g + HG, :].rearrange("p h c -> p (h c)"), ident)
                ins.then_inc(tile_full, 1)

            def probs_T(h):
                for t in range(TT):
                    pe.wait_ge(weighed, 1 + t * (HEADS + 1) + h + 1)
                    ps = open_tile(("pT", t, h))
                    for j in range(2):
                        for s in range(t + 1):
                            at = P * (j * (t + 1) + s)
                            ins = pe.transpose(ps[:, at:at + P], probs[t][h][:, j, P * s:P * s + P], ident)
                    ins.then_inc(tile_full, 1)

            def attend(h):
                g, c = h // HG, h // 2
                f = ("o", c // 2)
                if h % 4 == 0 and FILL[f] >= 4:
                    pe.wait_ge(acc_read, FILL[f] - 3)
                if h == 0:
                    for t in range(TT):
                        pe.wait_ge(*drained(("cmp_pT", t)))
                for t in range(TT):
                    pe.wait_ge(*drained(("pT", t, h)))
                o = acc(f)[DK * (h % 2):DK * (h % 2) + DK, SEQ * (c % 2):SEQ * (c % 2) + SEQ]
                pT = probsT[h % 2]
                for j in range(2):
                    pe.matmul(o, values[:, j, 0, DK * g:DK * g + DK], pT[:, j, 0, :], start=(j == 0), stop=False)
                    pe.matmul(o[:, P:SEQ], values[:, j, 1, DK * g:DK * g + DK], pT[:, j, 1, P:SEQ], start=False, stop=False)
                r = slice(32 * (h % HG), 32 * (h % HG) + NCMP)
                return pe.matmul(o, cmp_v[r, DK * g:DK * g + DK], cmp_pT[r, g, :], start=False, stop=True)

            for h in range(HEADS + 1):
                if h < HEADS:
                    probs_T(h)
                if h >= 1:
                    attend(h - 1).then_inc(acc_full if (h - 1) % 4 == 3 else heads_done, 1)
            pe.wait_ge(*drained(("pool_out",)))
            pe.wait_ge(mix_tail, 1)
            for i in range(2):
                pe.wait_ge(*acc_drained(("o", i)))
            product("out", "out", mixT)

            norm_T("mem", 4)
            for t in range(TT):
                for half in range(2):
                    pe.wait_ge(*drained(("normT", "mem", t, half)))
            for c in range(4):
                pair_of_chunks(("mq", c), ("mq", c))
            for c in range(4):
                pe.wait_ge(*drained(("mk", c)))
                pe.wait_ge(*drained(("mq", c)))
            for t in range(TT):
                for hp in range(2):
                    ps = open_tile(("ms", t, hp))
                    for j in range(2):
                        h = 2 * hp + j
                        for dd in range(2):
                            ins = pe.matmul(ps[:, SEQ * j:SEQ * j + SEQ], qmT[:, 2 * h + dd, P * t:P * t + P],
                                            kmT[:, 2 * h + dd, :], start=(dd == 0), stop=(dd == 1))
                    ins.then_inc(tile_full, 1)
            for t in range(TT):
                for hp in range(2):
                    pe.wait_ge(weighed, TT * (HEADS + 1) + 2 * t + hp + 1)
                    ps = open_tile(("mpT", t, hp))
                    for j in range(2):
                        for s in range(TT):
                            at = P * (2 * j + s)
                            ins = pe.transpose(ps[:, at:at + P], mprobs[t][:, 2 * hp + j, P * s:P * s + P], ident)
                    ins.then_inc(tile_full, 1)
            pe.wait_ge(*acc_drained(("mv", 3)))
            for c in range(4):
                if c % 2 == 0:
                    for t in range(TT):
                        pe.wait_ge(*drained(("mpT", t, c // 2)))
                ps = open_tile(("mo", c))
                for dd in range(2):
                    for s in range(TT):
                        ins = pe.matmul(ps[:, SEQ * dd:SEQ * dd + SEQ], vm[:, s, SEQ * c + P * dd:SEQ * c + P * dd + P],
                                        mprobsT[:, c, s, :], start=(s == 0), stop=(s == TT - 1))
                ins.then_inc(tile_full, 1)
            for c in range(4):
                pe.wait_ge(*drained(("mo", c)))
            product("wo", "wo", mixT)

            norm_T("ffn", 6)
            pe.wait_ge(h_low, 4)
            open_product("down")
            for j in range(FFN_PAIRS + DOWN_LAG):
                if j < FFN_PAIRS:
                    split_pair(("up", j))
                if j >= DOWN_LAG and j % 2 == 1:
                    i = (j - DOWN_LAG) // 2
                    pe.wait_ge(gated, 2 * i + 2)
                    split_product_unit(("down", i), i == 0, i == FFN_PAIRS // 2 - 1,
                                       lambda p, kk, t: prod_s[(2 * i + kk) % 4][:, p, P * t:P * t + P])

            def drained_norm(stage):
                for t in range(TT):
                    for half in range(2):
                        pe.wait_ge(*drained(("normT", stage, t, half)))

            def across_sum(tag):
                pe.wait_ge(across_sq, ACROSS[tag] + 1)
                ps = open_tile(("across", tag))
                sq = chunk2[tag][1]
                if tag == "dk":
                    ins = pe.matmul(ps[:, 0:SEQ], conc("block_ones"), sq, start=True, stop=True)
                else:
                    ones = conc("block_ones") if tag == "dq" else conc("ones")
                    ins = pe.matmul(ps[:, :], ones, sq.rearrange("p c t -> p (c t)"), start=True, stop=True)
                ins.then_inc(tile_full, 1)

            norm_T("mix2", 8)
            drained_norm("mix2")
            pair_of_chunks(("cq",), "cq")
            ps = open_tile(("ck",))
            pe.wait_ge(*loaded("ck"))
            w = weights("ck", KD, 192)
            wide(ps[:, 0:SEQ], w, 0)
            wide(ps[0:DK, SEQ:512], w, P, DK)
            wide(ps[DK:P, SEQ:512], w, P, DK).then_inc(tile_full, 1)
            ps = open_tile(("ab",))
            pe.wait_ge(*loaded("ab"))
            w = weights("ab", KD, 12)
            wide(ps[0:4, 0:SEQ], w, 0, 4)
            wide(ps[0:4, SEQ:512], w, 4, 4).then_inc(tile_full, 1)
            ps = open_tile(("widx",))
            for t in range(TT):
                ins = tall(ps[:, 4 * t:4 * t + 4], w, 8, 4, t)
            ins.then_inc(tile_full, 1)
            pair_of_chunks(("ug0",), "ug0")
            pair_of_chunks(("ug1",), "ug1")
            w_qb = parc("w_qb").rearrange("p (k c) -> p k c", k=2)
            w_qi = parc("w_qi").rearrange("p (k c) -> p k c", k=2)
            pe.wait_ge(*drained(("cq",)))
            for name, w in ((("dq",), w_qb), (("dqi",), w_qi)):
                ps = open_tile(name)
                for c in range(2):
                    for k in range(2):
                        ins = pe.matmul(ps[:, SEQ * c:SEQ * c + SEQ], w[:, k, P * c:P * c + P], cqT[:, k, :],
                                        start=(k == 0), stop=(k == 1))
                ins.then_inc(tile_full, 1)
            ps = open_tile(("dk",))
            pe.wait_ge(*drained(("ck",)))
            w_kvb = parc("w_kvb")
            pe.matmul(ps[0:DK, 0:SEQ], w_kvb[:, 0:DK], ckvT, start=True, stop=True)
            pe.matmul(ps[DK:P, 0:SEQ], w_kvb[:, 0:DK], ckvT, start=True, stop=True)
            for t in range(TT):
                ins = pe.matmul(ps[:, SEQ + DK * t:SEQ + DK * t + DK], ckvT[:, P * t:P * t + P], w_kvb[:, DK:P],
                                start=True, stop=True)
            ins.then_inc(tile_full, 1)
            pair_of_chunks(("qkv", 0), ("qkv", 0))
            across_sum("dq")
            across_sum("dk")
            for t in range(TT):
                for par in range(2):
                    ps = open_tile(("il", t, par))
                    pe.wait_ge(*drained(("dqi",)))
                    n = P * (t + 1)
                    r = slice(DK * par, DK * par + DK)
                    for j in range(2):
                        ins = pe.matmul(ps[:, n * j:n * j + n], dqiT[r, j, P * t:P * t + P], kidxT[r, 0:n],
                                        start=True, stop=True)
                    ins.then_inc(tile_full, 1)
            for i in range(1, 6):
                pair_of_chunks(("qkv", i), ("qkv", i))
            for i in range(2):
                pair_of_chunks(("z", i), ("z", i))
            norm_T("mem2", 10)
            drained_norm("mem2")
            for i in range(2):
                pair_of_chunks(("xk", i), ("xk", i))
            pe.wait_ge(acc_read, FILL[("xv", 0)])
            for i in range(2):
                pe.wait_ge(*loaded(("xv", i)))
                w = weights(("xv", i), 4, 512)
                for kk in range(4):
                    for t in range(TT):
                        ins = pe.matmul(acc(("xv", t))[:, :], hT[:, 4 * i + kk, P * t:P * t + P], w[:, kk, :],
                                        start=(i == 0 and kk == 0), stop=(i == 1 and kk == 3))
                        if i == 1 and kk == 3:
                            ins.then_inc(acc_full, 1)
                if i == 0:
                    ins.then_inc(unit_spent, 1)
            for i in range(2):
                across_sum(f"xk{i}")
            pe.wait_ge(across_done, ACROSS["dk"] + 1)
            for t in range(TT):
                for par in range(2):
                    ps = open_tile(("dl", t, par))
                    n = P * (t + 1)
                    r = slice(DK * par, DK * par + DK)
                    for j in range(2):
                        ins = pe.matmul(ps[:, n * j:n * j + n], dqT[r, j, P * t:P * t + P], dkT[r, 0:n],
                                        start=True, stop=True)
                    ins.then_inc(tile_full, 1)
            for t in range(TT):
                pe.wait_ge(d_weighed, t + 1)
                for par in range(2):
                    ps = open_tile(("dpT", t, par))
                    for j in range(2):
                        for s in range(t + 1):
                            at = P * (j * (t + 1) + s)
                            ins = pe.transpose(ps[:, at:at + P], dprobs[t][:, 2 * j + par, P * s:P * s + P], ident)
                    ins.then_inc(tile_full, 1)
            ps = open_tile(("do",))
            for t in range(TT):
                for par in range(2):
                    pe.wait_ge(*drained(("dpT", t, par)))
            for j in range(2):
                for par in range(2):
                    o = ps[DK * par:DK * par + DK, SEQ * j:SEQ * j + SEQ]
                    pe.matmul(o, dv[:, 0, :], dprobsT[par][:, j, 0, :], start=True, stop=False)
                    ins = pe.matmul(o[:, P:SEQ], dv[:, 1, :], dprobsT[par][:, j, 1, P:SEQ], start=False, stop=True)
            ins.then_inc(tile_full, 1)
            for i in range(4):
                across_sum(f"l{i}")
            pe.wait_ge(rows_ready, 1)
            ps = open_tile(("cols",))
            for t in range(TT):
                for kind in range(4):
                    at = 16 * t + 4 * kind
                    ins = pe.transpose(ps[:, at:at + 4], gate_rows[0:4, kind, P * t:P * t + P], ident[0:4, 0:4])
            ins.then_inc(tile_full, 1)
            pick = conc("pick_row").rearrange("p (h m) -> p h m", h=4)
            for tag, kind in (("dr", 3), ("br", 0)):
                for i in range(2):
                    ps = open_tile((tag, i))
                    for j in range(2):
                        ins = pe.matmul(ps[:, SEQ * j:SEQ * j + SEQ], pick[0:4, 2 * i + j, :], gate_rows[0:4, kind, :],
                                        start=True, stop=True)
                    ins.then_inc(tile_full, 1)
            qT2, kT2, vT2 = qkv[:, 0:4, :], qkv[:, 4:8, :], qkv[:, 8:12, :]
            pe.wait_ge(across_done, ACROSS["l3"] + 1)
            for tag, src in (("kA", kT2), ("vA", vT2)):
                for t in range(TT):
                    ps = open_tile((tag, t))
                    for h in range(GDN_HEADS):
                        ins = pe.transpose(ps[:, P * h:P * h + P], src[:, h, P * t:P * t + P], ident)
                    ins.then_inc(tile_full, 1)
            pe.wait_ge(*drained(("br", 1)))
            for tag, moving in (("kk", kbT), ("qk", qT2)):
                for t in range(TT):
                    ps = open_tile((tag, t))
                    for h in range(GDN_HEADS):
                        ins = pe.matmul(ps[:, P * h:P * h + P], kT2[:, h, P * t:P * t + P], moving[:, h, P * t:P * t + P],
                                        start=True, stop=True)
                    ins.then_inc(tile_full, 1)

            def four(name, lhs, rhs):
                ps = open_tile(name)
                for h in range(GDN_HEADS):
                    ins = pe.matmul(ps[:, P * h:P * h + P], lhs(h), rhs(h), start=True, stop=True)
                ins.then_inc(tile_full, 1)

            for level in range(LEVELS):
                for t in range(TT):
                    pe.wait_ge(*drained(("qk", t) if level == 0 else ("d", level - 1, t)))
                    four(("y", level, t), lambda h: AT[t][:, h, :], lambda h: inv[t][:, h, :] if level else ident)
                if level < LEVELS - 1:
                    for t in range(TT):
                        pe.wait_ge(*drained(("y", level, t)))
                        if level:
                            pe.wait_ge(*drained(("dT", level - 1, t)))
                        four(("d", level, t), lambda h: invT[t][:, h, :] if level else ident, lambda h: Y[t][:, h, :])
                for t in range(TT):
                    pe.wait_ge(*drained(("y", level, t)))
                    pe.wait_ge(*drained(("dT", level - 1, t))) if level else None
                    four(("dT", level, t), lambda h: Y[t][:, h, :], lambda h: invT[t][:, h, :] if level else ident)
            for t in range(TT):
                pe.wait_ge(*drained(("dT", LEVELS - 1, t)))
                four(("gu", t), lambda h: invT[t][:, h, :], lambda h: bv[t][:, h, :])
            for t in range(TT):
                four(("gw", t), lambda h: bke[t][:, h, :], lambda h: invT[t][:, h, :])
            pe.wait_ge(conv_out, 1)
            ps = open_tile(("ln_mean",))
            for c in range(2):
                ins = pe.matmul(ps[:, 0:SEQ], conc("ones"), conv_y[:, c, :], start=(c == 0), stop=(c == 1))
            ins.then_inc(tile_full, 1)
            pe.wait_ge(conv_sq_ready, 1)
            ps = open_tile(("ln_var",))
            for c in range(2):
                ins = pe.matmul(ps[:, 0:SEQ], conc("ones"), conv_sq[:, c, :], start=(c == 0), stop=(c == 1))
            ins.then_inc(tile_full, 1)
            pe.wait_ge(qe_ready, 1)
            for t in range(TT):
                pe.wait_ge(*drained(("gw", t)))
                pe.wait_ge(*drained(("qk", t)))
            for n in range(NCHUNK):
                t, lo = n // 2, CHUNK * (n % 2)
                r = slice(lo, lo + CHUNK)
                if n:
                    pe.wait_ge(*drained(("kv", n - 1)))
                    ps = open_tile(("ws", n))
                    for h in range(GDN_HEADS):
                        ins = pe.matmul(ps[r, P * h:P * h + P], wT[t][:, h, r], state[:, h, :], start=True, stop=True)
                    ins.then_inc(tile_full, 1)
                    pe.wait_ge(*drained(("ws", n)))
                else:
                    pe.wait_ge(v_news, 1)
                ps = open_tile(("go", n))
                for h in range(GDN_HEADS):
                    o = ps[:, CHUNK * h:CHUNK * h + CHUNK]
                    if n:
                        pe.matmul(o, state[:, h, :], qeT[:, h, CHUNK * n:CHUNK * n + CHUNK], start=True, stop=False)
                    ins = pe.matmul(o, v_new[r, h, :], qkT[t][r, h, r], start=(n == 0), stop=True)
                ins.then_inc(tile_full, 1)
                if n < NCHUNK - 1:
                    ps = open_tile(("kv", n))
                    for h in range(GDN_HEADS):
                        ins = pe.matmul(ps[:, P * h:P * h + P], kdec[t][r, h, :], v_new[r, h, :], start=True, stop=True)
                    ins.then_inc(tile_full, 1)
            for i in range(2):
                across_sum(f"o{i}")
            pe.wait_ge(o_mix, 1)
            pe.wait_ge(conv_mix, 1)
            pe.wait_ge(*drained(("do",)))
            product("out2", "out2", mixT)

            norm_T("cross", 12)
            drained_norm("cross")
            for i in range(2):
                pair_of_chunks(("xq", i), ("xq", i))
            for i in range(2):
                across_sum(f"xq{i}")
            pe.wait_ge(across_done, ACROSS["xq1"] + 1)
            for t in range(TT):
                for hp in range(2):
                    ps = open_tile(("xs", t, hp))
                    for j in range(2):
                        h = 2 * hp + j
                        ins = pe.matmul(ps[:, SEQ * j:SEQ * j + SEQ], xqT[:, h, P * t:P * t + P], xkT[:, h, :],
                                        start=True, stop=True)
                    ins.then_inc(tile_full, 1)
            for t in range(TT):
                for hp in range(2):
                    pe.wait_ge(x_weighed, 2 * t + hp + 1)
                    ps = open_tile(("xpT", t, hp))
                    for j in range(2):
                        for s in range(TT):
                            at = P * (2 * j + s)
                            ins = pe.transpose(ps[:, at:at + P], xprobs[t][:, 2 * hp + j, P * s:P * s + P], ident)
                    ins.then_inc(tile_full, 1)
            pe.wait_ge(*acc_drained(("xv", 1)))
            for c in range(2):
                for t in range(TT):
                    pe.wait_ge(*drained(("xpT", t, c)))
                ps = open_tile(("xo", c))
                for j in range(2):
                    h = 2 * c + j
                    for s in range(TT):
                        ins = pe.matmul(ps[:, SEQ * j:SEQ * j + SEQ], xv[:, s, P * h:P * h + P], xprobsT[:, h, s, :],
                                        start=(s == 0), stop=(s == TT - 1))
                ins.then_inc(tile_full, 1)
            for c in range(2):
                pe.wait_ge(*drained(("xo", c)))
            open_product("xwo")
            for i in range(2):
                product_unit("xwo", ("xwo", i), i == 0, i == 1, lambda kk, t: mixT[:, 2 * i + kk, P * t:P * t + P])

            norm_T("mlp", 14)
            pe.wait_ge(h_low, 8)
            open_product("m2")
            for j in range(MLP_UNITS + MLP_LAG):
                if j < MLP_UNITS:
                    split_pair(("m1", j))
                if j >= MLP_LAG:
                    i = j - MLP_LAG
                    pe.wait_ge(relu_sq, i + 1)
                    split_product_unit(("m2", i), i == 0, i == MLP_UNITS - 1,
                                       lambda p, kk, t: relu2_s[i % 3][:, p, kk, P * t:P * t + P])


def pack(n, spec, parts):
    c = np.zeros((P, n), np.float32)
    for name, v in parts.items():
        lo, hi = spec[name]
        v = np.asarray(v)
        c[:v.shape[0], lo:hi] = v.reshape(v.shape[0], hi - lo)
    return c


def by_partition(v, k):
    return np.asarray(v).reshape(k, P).T


def twice(v):
    v = np.asarray(v).reshape(64, -1)
    return np.concatenate([v, v], 0)


def small_parameters(i):
    def a(name):
        return np.asarray(i[name])

    both = {}
    both["gains"] = np.stack([by_partition(a(n), KD) for n in (
        "mix_norm_pre", "mem_norm_kv", "mem_norm_pre", "ffn_norm_pre", "norm_mix_2", "norm_mem_2", "norm_cross_2",
        "norm_mlp_2")], 1)
    both["cmp_pos"] = a("cmp_pos")[0].reshape(2, CMP_PAIRS, P).transpose(2, 0, 1)
    both["cmp_b1"] = a("cmp_b1")[0].T
    both["cmp_w2"] = a("cmp_w2")[0].transpose(1, 0, 2)
    both["cmp_b2k"] = twice(a("cmp_b2")[0, 0])
    both["cmp_b2v"] = np.broadcast_to(np.tile(a("cmp_b2")[0, 1], GROUPS), (P, P))
    both["relb"] = np.concatenate([a("rel_bias"), np.full((1, HEADS), MASKED, np.float32)], 0)
    pw = a("pool_w")[0]
    both["pool_w"] = np.concatenate([pw[0::2].transpose(1, 0, 2), pw[1::2].transpose(1, 0, 2)], 0)
    both["pool_scale"] = by_partition(a("pool_scale")[0], 2)
    both["sgu_g"] = np.broadcast_to(a("sgu_norm_g")[0], (P, 256))
    both["sgu_b"] = np.broadcast_to(a("sgu_norm_b")[0], (P, 256))
    both["sgu_wT"] = a("sgu_w")[0].transpose(2, 0, 1)
    both["sgu_bias"] = np.repeat(a("sgu_b")[0].reshape(2, 2, P).transpose(1, 0, 2), 64, 0)
    both["conv_w"] = a("conv_w")[0].reshape(3, 2, FFN_PAIRS, P).transpose(3, 2, 1, 0)
    both["conv_b"] = a("conv_b")[0].reshape(2, FFN_PAIRS, P).transpose(2, 1, 0)
    both["gdn_conv"] = a("gdn_conv_2")[0].reshape(4, 12, P).transpose(2, 1, 0)
    both["a_log"] = a("gdn_a_log_2")[0].reshape(4, 1)
    both["dt_bias"] = a("gdn_dt_bias_2")[0].reshape(4, 1)
    both["gdn_norm"] = a("gdn_norm_2")[0].reshape(P, 1)
    both["w_qb"] = a("dsa_w_qb_2")[0].reshape(2, P, 256).transpose(1, 0, 2)
    both["w_qi"] = a("dsa_w_qi_2")[0].reshape(2, P, 256).transpose(1, 0, 2)
    both["w_kvb"] = a("dsa_w_kvb_2")[0]
    both["dq_norm"] = twice(a("dsa_q_norm_2")[0])
    both["dk_norm"] = twice(a("dsa_k_norm_2")[0])
    both["conv_dw"] = a("conv_dw_2")[0].reshape(CONV_TAPS, 2, P).transpose(2, 1, 0)
    both["dw_b"] = by_partition(a("conv_dw_b_2")[0], 2)
    both["ln_g"] = by_partition(a("conv_ln_g_2")[0], 2)
    both["ln_b"] = by_partition(a("conv_ln_b_2")[0], 2)
    both["xq_norm"] = a("xa_q_norm_2")[0].reshape(P, 1)
    both["xk_norm"] = a("xa_k_norm_2")[0].reshape(P, 1)
    return pack(NPAR, PAR, both)


def kernel(**inputs):
    import concourse.bacc as bacc
    from concourse.bass_utils import run_bass_kernel_spmd

    i = {n: np.ascontiguousarray(v) for n, v in inputs.items()}
    w_in = i["w_in"][0]
    q = w_in[:, :512].reshape(D, GROUPS, HG, DK).transpose(0, 2, 1, 3).reshape(D, 512)
    w_up = i["w_up"][0].reshape(D, 2, FFN_PAIRS, P).transpose(0, 2, 1, 3).reshape(D, 2 * FFN)
    w2 = i["w_in_2"][0]
    w_in2 = np.concatenate([w2[:, :2048], w2[:, 2056:2504], w2[:, 2048:2056], w2[:, 2504:]], 1)
    arrays = {
        "x": i["x"][0], "mem": i["mem"][0], "params": small_parameters(i), "consts": shape_constants(),
        "hots": bucket_one_hots(), "w_in": np.concatenate([q, w_in[:, 512:]], 1), "cmp_w1": i["cmp_w1"][0].reshape(2, CMP_LEN * DK, P),
        "w_out": i["w_out"][0], "w_mk": i["w_mk"][0], "w_mv": i["w_mv"][0], "w_mq": i["w_mq"][0], "w_mo": i["w_mo"][0],
        "w_up": w_up, "w_down": i["w_down"][0], "mix_norm_post": i["mix_norm_post"], "mem_norm_post": i["mem_norm_post"],
        "ffn_norm_post": i["ffn_norm_post"],
        "mem2": i["mem_2"][0], "w_in2": w_in2, "w_out2": i["w_out_2"][0], "xa_wkv": i["xa_wkv_2"][0],
        "xa_wq": i["xa_wq_2"][0], "xa_wo": i["xa_wo_2"][0], "mlp_w1": i["mlp_w1_2"][0], "mlp_w2": i["mlp_w2_2"][0],
    }
    nc = bacc.Bacc("TRN2", target_bir_lowering=False, num_devices=1)
    feed, args = {}, {}
    for n, v in arrays.items():
        v = np.ascontiguousarray(v)
        feed[f"in_{n}"] = v
        args[n] = nc.dram_tensor(f"in_{n}", v.shape, mybir.dt.from_np(v.dtype), kind="ExternalInput").ap()
    out = nc.dram_tensor("out_x", (SEQ, D), F32, kind="ExternalOutput").ap()
    block_kernel(nc, args, out)
    r = run_bass_kernel_spmd(nc, [feed], core_ids=[0])
    return r.results[0]["out_x"].reshape(1, SEQ, D)
```

```python
from contextlib import ExitStack

import numpy as np

import concourse.bass as bass
from concourse import mybir

F32 = mybir.dt.float32
F32R = mybir.dt.float32r
ALU = mybir.AluOpType
ACT = mybir.ActivationFunctionType
AX = mybir.AxisListType.X

P = 128
SEQ = 256
TT = SEQ // P
D = 1024
KD = D // P
EPS = 1e-6
MASKED = -1e30

HEADS = 8
GROUPS = 2
HG = HEADS // GROUPS
DK = 64
CMP_STRIDE = 16
CMP_LEN = 32
NCMP = SEQ // CMP_STRIDE - 1
CMP_PAIRS = CMP_LEN // 2
MEM_HEADS = 4
FFN = ((11 * D // 4) // 128) * 128
FFN_PAIRS = FFN // P
POOL_WINDOWS = (2, 4, 8, 16)
REL_BUCKETS = 32
REL_MAX_DIST = 1024
DIST_COLS = 2 * SEQ

GDN_HEADS = 4
CHUNK = 64
NCHUNK = SEQ // CHUNK
LEVELS = 6
DSA_HEADS = 4
DSA_TOPK = 64
CONV_TAPS = 31
XA_HEADS = 4
MLP_UNITS = 4 * D // 256
PICKED = -3.3e38
FUTURE = -3.0e38


def t5_bucket(dist):
    n = np.maximum(dist, 0)
    exact = REL_BUCKETS // 2
    nf = np.maximum(n, 1).astype(np.float32)
    scale = np.float32(np.log(REL_MAX_DIST / exact))
    large = exact + (np.log(nf / np.float32(exact)) / scale * np.float32(REL_BUCKETS - exact)).astype(np.int32)
    return np.where(n < exact, n, np.minimum(large, REL_BUCKETS - 1))


def columns(spec):
    at, out = 0, {}
    for name, width in spec:
        out[name] = (at, at + width)
        at += width
    return out, at


PAR, NPAR = columns([
    ("gains", 8 * KD), ("cmp_pos", 2 * CMP_PAIRS), ("cmp_b1", 2), ("cmp_w2", 128), ("cmp_b2k", 1),
    ("cmp_b2v", 128), ("relb", HEADS), ("pool_w", 128), ("pool_scale", 2), ("sgu_g", 256), ("sgu_b", 256),
    ("sgu_wT", 512), ("sgu_bias", 256),
    ("conv_w", FFN_PAIRS * 6), ("conv_b", FFN_PAIRS * 2), ("gdn_conv", 48), ("a_log", 1), ("dt_bias", 1),
    ("gdn_norm", 1), ("w_qb", 512), ("w_qi", 512), ("w_kvb", 128), ("dq_norm", 1), ("dk_norm", 1),
    ("conv_dw", 2 * CONV_TAPS), ("dw_b", 2), ("ln_g", 2), ("ln_b", 2), ("xq_norm", 1), ("xk_norm", 1),
])
CON, NCON = columns([
    ("ident", 128), ("neg_half", 8), ("eps", 8), ("root_scale", 1), ("root_bias", 1), ("pick_col", 16),
    ("tri_incl", 128), ("tri_strict", 128), ("levels", LEVELS * 128), ("block_ones", 128),
    ("ones", 128), ("inv_count", 512), ("chunk_keep", SEQ),
])
CON_FIRST = CON["pick_col"][1]
PAR_FIRST = PAR["gains"][1]
EPS_VALUES = [EPS, 64 * EPS, P * EPS, 0, 0, 0, 0, 0]
GAIN = {n: i for i, n in enumerate(["mix", "memkv", "mem", "ffn", "mix2", "mem2", "cross", "mlp"])}


def shape_constants():
    c = np.zeros((P, NCON), np.float32)

    def put(name, a):
        lo, hi = CON[name]
        c[:a.shape[0], lo:hi] = a.reshape(a.shape[0], hi - lo)

    i = np.arange(P)
    row, col = i[:, None], i[None, :]
    same = row // CHUNK == col // CHUNK
    put("ident", np.eye(P))
    put("neg_half", np.full((P, 8), -0.5))
    put("eps", np.tile(np.array(EPS_VALUES, np.float32), (P, 1)))
    put("tri_incl", (same & (col >= row)).astype(np.float32))
    put("tri_strict", (same & (col > row)).astype(np.float32))
    c[:, CON["pick_col"][0] + 8] = 1
    put("root_scale", np.array([P] * 4 + [1] * 4, np.float32)[:, None])
    put("root_bias", np.array([P * EPS] * 4 + [EPS] * 4, np.float32)[:, None])
    put("levels", np.stack([
        (row // (2 * s) == col // (2 * s)) & (col % (2 * s) >= s) & (row % (2 * s) < s)
        for s in (2 ** n for n in range(LEVELS))], 1).astype(np.float32))
    put("block_ones", same.astype(np.float32))
    put("ones", np.ones((P, P)))
    t = np.arange(SEQ)
    counts = np.zeros((P, 2, SEQ), np.float32)
    for g, w in enumerate(POOL_WINDOWS):
        counts[64 * (g % 2):64 * (g % 2) + 64, g // 2] = np.float32(1) / np.minimum(t + 1, w).astype(np.float32)
    put("inv_count", counts)
    put("chunk_keep", np.tile((t % CHUNK != 0).astype(np.float32), (4, 1)))
    return c


def bucket_one_hots():
    dist = np.arange(DIST_COLS) - (SEQ - 1)
    h = np.zeros((REL_BUCKETS + 1, DIST_COLS), np.float32)
    h[np.where(dist < 0, REL_BUCKETS, t5_bucket(dist)), np.arange(DIST_COLS)] = 1
    return h


RING = 5
DOWN_LAG = 2
NB = 4
ARENA = 26624
SPLIT_PRODUCTS = ("out", "mq", "wo", "up", "down", "out2", "xq", "xwo", "m1", "m2")
SPLIT_STAGES = ("mem", "ffn", "cross", "mlp")
MIX_ORDER = (2, 3, 0, 1)
SPLIT_RING = 3
TOPK_ROUNDS = DSA_TOPK // 8
TAPS_EARLY = 16
MLP_LAG = 2
MEM_DIM = D // MEM_HEADS
STATS = [(n, t) for n in ("mix", "memkv", "out_post", "mem", "wo_post", "ffn", "down_post", "mix2", "mem2", "cross", "mlp") for t in range(TT)] + [
    ("sgu", t) for t in range(TT)]
NSTAT = len(STATS)


def plan():
    tiles = []

    def norm(stage):
        tiles.extend(("normT", stage, t, half) for t in range(TT) for half in range(2))

    norm("mix")
    tiles.extend((n,) for n in ("q0", "q1", "bias_row", "bias_cmp", "kcvc", "ksvs", "kwvw", "gates", "pool", "u", "v", "cmp_h", "cmp_kv"))
    for t in range(TT):
        tiles.extend(("cmp_s", t, g) for g in range(GROUPS))
        tiles.extend(("s", t, h) for h in range(HEADS))
    tiles.extend((("pool_out",), ("sgu_out",)))
    norm("memkv")
    tiles.extend(("mk", c) for c in range(4))
    tiles.extend(("cmp_pT", t) for t in range(TT))
    tiles.extend(("pT", t, h) for h in range(HEADS) for t in range(TT))
    norm("mem")
    tiles.extend(("mq", c) for c in range(4))
    tiles.extend(("ms", t, hp) for t in range(TT) for hp in range(2))
    tiles.extend(("mpT", t, hp) for t in range(TT) for hp in range(2))
    tiles.extend(("mo", c) for c in range(4))
    norm("ffn")
    tiles.extend(("up", j) for j in range(FFN_PAIRS))
    norm("mix2")
    tiles.extend((n,) for n in ("cq", "ck", "ab", "widx", "ug0", "ug1", "dq", "dqi", "dk"))
    tiles.append(("qkv", 0))
    tiles.extend((("across", "dq"), ("across", "dk")))
    tiles.extend(("il", t, par) for t in range(TT) for par in range(2))
    tiles.extend(("qkv", i) for i in range(1, 6))
    tiles.extend((("z", 0), ("z", 1)))
    norm("mem2")
    tiles.extend((("xk", 0), ("row_sum", "l")))
    tiles.extend(("dl", t, par) for t in range(TT) for par in range(2))
    tiles.append(("xk", 1))
    tiles.extend(("row_all", "l", i) for i in range(4))
    tiles.extend((("cols",), ("dr", 0), ("dr", 1), ("br", 0), ("br", 1), ("row_sum", "xk")))
    tiles.extend((n, t) for n in ("kA", "vA", "kk", "qk") for t in range(TT))
    tiles.extend(("dpT", t, par) for t in range(TT) for par in range(2))
    tiles.append(("do",))
    tiles.extend(("row_all", "xk", i) for i in range(2))
    for level in range(LEVELS):
        for kind in ("y", "d", "dT"):
            if kind == "y" or level and (kind, level) != ("d", LEVELS - 1):
                tiles.extend((kind, level, t) for t in range(TT))
    tiles.extend((n, t) for n in ("gu", "gw") for t in range(TT))
    tiles.extend((("ln_mean",), ("ln_var",)))
    for n in range(NCHUNK):
        if n:
            tiles.append(("ws", n))
        tiles.append(("go", n))
        if n < NCHUNK - 1:
            tiles.append(("kv", n))
    tiles.extend((("row_sum", "o"), ("row_all", "o", 0), ("row_all", "o", 1)))
    norm("cross")
    tiles.extend((("xq", 0), ("xq", 1), ("xq_sums",)))
    tiles.extend(("xs", t, hp) for t in range(TT) for hp in range(2))
    tiles.extend(("xpT", t, hp) for t in range(TT) for hp in range(2))
    tiles.extend(("xo", c) for c in range(2))
    norm("mlp")
    tiles.extend(("m1", j) for j in range(MLP_UNITS))

    units = ["q0", "q1", "kcvc", "ksvs", "kwvw", "gates", "pool", "u", "v", "cmp_w1k", "cmp_w1v"]
    for product in ("mk", "mv", "out", "mq", "wo"):
        units += [(product, c) for c in (MIX_ORDER if product == "out" else range(4))]
    for j in range(FFN_PAIRS + DOWN_LAG):
        if j < FFN_PAIRS:
            units.append(("up", j))
        if j >= DOWN_LAG and j % 2 == 1:
            units.append(("down", (j - DOWN_LAG) // 2))
    units += ["cq", "ck", "ab", "ug0", "ug1"] + [("qkv", i) for i in range(6)] + [("z", 0), ("z", 1)]
    units += [("xk", 0), ("xk", 1), ("xv", 0), ("xv", 1)] + [("out2", i) for i in MIX_ORDER]
    units += [("xq", 0), ("xq", 1), ("xwo", 0), ("xwo", 1)]
    for j in range(MLP_UNITS + MLP_LAG):
        if j < MLP_UNITS:
            units.append(("m1", j))
        if j >= MLP_LAG:
            units.append(("m2", j - MLP_LAG))

    fills = []
    for product in ("mv", "o", "out", "wo", "down", "xv", "out2", "xwo", "m2"):
        fills += [(product, i) for i in range(2 if product in ("o", "xv") else 4)]
    return tiles, units, fills


def block_kernel(nc, a, out):
    ctx = ExitStack()
    with ctx:
        def sb(name, shape):
            return ctx.enter_context(nc.sbuf_tensor(name, shape, F32))

        def sem(name):
            return ctx.enter_context(nc.semaphore(name))

        ring = sb("weight_ring", [P, RING, 2048])
        x = sb("x_res", [P, TT, D])
        xn = sb("x_normed", [P, TT, D])
        hT = sb("hT", [P, KD, SEQ])
        mixT = sb("mixT", [P, KD, SEQ])
        par = sb("par", [P, NPAR])
        con = sb("con", [P, NCON])
        post_gain = sb("post_gain", [P, D])
        junk = sb("act_junk", [P, D])
        stats = sb("stats", [P, 2 * NSTAT])
        small = sb("small_sums", [P, 32])
        with nc.sbuf_tensor("arena", [P, ARENA], F32) as arena:
            pass
        SPLIT_AT = 4096
        sb("arena_below_split", [P, SPLIT_AT])
        split = ctx.enter_context(nc.sbuf_tensor("split_operands", [P, ARENA - SPLIT_AT], F32R))
        banks = [ctx.enter_context(nc.psum_tensor(f"work{b}", [P, 512], F32)) for b in range(NB)]
        accs = [ctx.enter_context(nc.psum_tensor(f"acc{b}", [P, 512], F32)) for b in range(4)]
        bias_rows_dram = nc.dram_tensor("bias_rows_scratch", [HEADS, DIST_COLS], F32, kind="Internal").ap()

        def parc(name):
            return par[:, PAR[name][0]:PAR[name][1]]

        def conc(name):
            return con[:, CON[name][0]:CON[name][1]]

        def cut(at, *shape):
            n = int(np.prod(shape))
            assert at + n <= ARENA
            v = arena[:, at:at + n]
            if len(shape) == 1:
                return v
            names = "abcd"[:len(shape)]
            return v.rearrange(f"p ({' '.join(names)}) -> p {' '.join(names)}", **dict(zip(names, shape)))

        def cut_split(at, *shape):
            n = int(np.prod(shape))
            assert at >= SPLIT_AT and at + n <= ARENA
            names = "abcd"[:len(shape)]
            return split[:, at - SPLIT_AT:at - SPLIT_AT + n].rearrange(
                f"p ({' '.join(names)}) -> p {' '.join(names)}", **dict(zip(names, shape)))

        def eps_col(v):
            k = CON["eps"][0] + EPS_VALUES.index(v)
            return con[:, k:k + 1]

        ident = conc("ident")
        gains = parc("gains").rearrange("p (s k) -> p s k", k=KD)

        tiles, units, fills = plan()
        TILE = {n: i for i, n in enumerate(tiles)}
        UNIT = {n: i for i, n in enumerate(units)}
        FILL = {n: i for i, n in enumerate(fills)}
        tile_full = sem("tile_full")
        tile_read = [sem(f"tile_read{b}") for b in range(NB)]
        acc_full = sem("acc_full")
        acc_read = sem("acc_read")
        unit_loaded = [sem(f"unit_loaded{s}") for s in range(RING)]
        unit_spent = sem("unit_spent")

        def bank(name):
            return banks[TILE[name] % NB]

        def full(name):
            return tile_full, TILE[name] + 1

        def drained(name):
            return tile_read[TILE[name] % NB], TILE[name] // NB + 1

        def reader(name):
            return tile_read[TILE[name] % NB]

        def acc(name):
            return accs[FILL[name] % 4]

        def acc_filled(name):
            return acc_full, FILL[name] + 1

        def acc_drained(name):
            return acc_read, FILL[name] + 1

        def weights(name, *shape):
            v = ring[:, UNIT[name] % RING, :]
            n = int(np.prod(shape))
            names = "abcd"[:len(shape)]
            return v[:, 0:n].rearrange(f"p ({' '.join(names)}) -> p {' '.join(names)}", **dict(zip(names, shape)))

        def split_slot(i):
            return split_slots[int(i >= SPLIT[("out2", MIX_ORDER[0])])][i % SPLIT_RING]

        split_units = [u for u in units if u[0] in SPLIT_PRODUCTS]
        SPLIT = {u: i for i, u in enumerate(split_units)}
        high_ready = sem("weights_high_ready")
        low_ready = sem("weights_low_ready")
        acts_high = sem("acts_high_ready")
        acts_low = sem("acts_low_ready")
        act_parts = [("mix", "out", c) for c in MIX_ORDER] + [("rows", "mem", t, half) for t in range(TT) for half in range(2)]
        act_parts += [("mix", "wo", c) for c in range(4)] + [("rows", "ffn", t, half) for t in range(TT) for half in range(2)]
        act_parts += [("mix", "out2", c) for c in MIX_ORDER] + [("rows", "cross", t, half) for t in range(TT) for half in range(2)]
        act_parts += [("mix", "xwo", c) for c in range(2)] + [("rows", "mlp", t, half) for t in range(TT) for half in range(2)]
        ACTS = {n: i for i, n in enumerate(act_parts)}

        def high_there(name):
            return acts_high, ACTS[name] + 1

        low_drains = {("mix", "out", c): lambda c=c: acc_drained(("o", c)) for c in range(2)}
        low_drains.update({("mix", "wo", c): lambda c=c: drained(("mo", c)) for c in range(4)})
        low_drains.update({("mix", "xwo", c): lambda c=c: drained(("xo", c)) for c in range(2)})
        LOWS = {n: i for i, n in enumerate(n for n in act_parts if n not in low_drains)}

        def low_there(name):
            return low_drains[name]() if name in low_drains else (acts_low, LOWS[name] + 1)

        def split_before(name):
            return SPLIT[name] - 1 if name in SPLIT else -1

        def split_weights(name, *shape):
            names = "abcd"[:len(shape)]
            return split_slot(SPLIT[name]).rearrange(
                f"p s ({' '.join(names)}) -> p s {' '.join(names)}", **dict(zip(names, shape)))

        def loaded(name):
            return unit_loaded[UNIT[name] % RING], 16 * (UNIT[name] // RING + 1)

        params_in = sem("params_in")
        consts_in = sem("consts_in")
        first_params_in = sem("first_params_in")
        first_consts_in = sem("first_consts_in")
        x_in = [sem(f"x_in{t}") for t in range(TT)]
        mem_in = sem("mem_in")
        hots_in = sem("hots_in")
        bias_rows_out = sem("bias_rows_out")
        bias_tile_in = sem("bias_tile_in")
        gain_in = sem("post_gain_in")
        shifted_in = sem("kv_shifted_in")
        squares = sem("squares_summed")
        rstd_ready = sem("rstd_ready")
        normed = sem("x_normed_ready")
        x_done = sem("x_updated")
        blocks_ready = sem("cmp_blocks_ready")
        scored = sem("scores_biased")
        neg_max = sem("neg_max_ready")
        exped = sem("exp_done")
        weighed = sem("probs_weighed")
        sgu_stat = sem("sgu_stats_ready")
        sgu_rstd = sem("sgu_rstd_ready")
        sgu_normed = sem("sgu_normed_ready")
        masked_ws = sem("sgu_weights_masked")
        pooled = sem("pool_diff_ready")
        dve_chain = sem("dve_chain")
        act_chain = sem("act_chain")
        pool_chain = sem("pool_chain")
        gated = sem("ffn_gated")
        gate_act = sem("ffn_gate_act")
        tap2 = sem("ffn_tap2")
        out_done = sem("out_done")
        heads_done = sem("heads_attended")
        across_sq = sem("across_squares_ready")
        across_done = sem("across_normed")
        row_squares = sem("row_squares_ready")
        row_roots = {tag: sem(f"row_roots_{tag}") for tag in ("l", "xk", "o")}
        scaled_o = sem("gdn_o_scaled")
        level_masked = sem("level_masked")
        first_invT = sem("first_invT_ready")
        xq_squares = sem("xq_squares_ready")
        xq_rstd = sem("xq_rstd_ready")
        mem2_in = sem("mem2_in")
        bands_y = sem("conv_input_ready")
        tap3 = sem("gdn_last_tap")
        silu_done = sem("gdn_silu_done")
        idx_relu = sem("index_relu_ready")
        idx_sum = sem("index_scores_summed")
        idx_causal = sem("index_scores_causal")
        picked = sem("topk_picked")
        dmask_ready = sem("dsa_mask_ready")
        d_max = sem("dsa_neg_max")
        d_exp = sem("dsa_exp_done")
        d_weighed = sem("dsa_probs_weighed")
        softplus_ln = sem("softplus_ln_ready")
        decay_sum = sem("decay_summed")
        decay_exp = sem("decay_exps_ready")
        rows_ready = sem("gate_rows_ready")
        exp_rows = sem("exp_decay_ready")
        gamma_diff = sem("gamma_exponents")
        gamma_exp = sem("gamma_exp_done")
        gamma_ready = sem("gammas_masked")
        kb_ready = sem("kb_ready")
        qe_ready = sem("qe_ready")
        v_news = sem("v_new_ready")
        states = sem("state_updated")
        o_read = sem("o_collected")
        conv_out = sem("conv31_done")
        conv_sq_ready = sem("ln_squares_ready")
        conv_norm = sem("ln_normed")
        conv_mix = sem("conv_mix_ready")
        o_mix = sem("gdn_mix_ready")
        x_max = sem("cross_neg_max")
        x_weighed = sem("cross_probs_weighed")
        relu_sq = sem("mlp_squared")
        relu_high = sem("mlp_square_high")
        mix_tail = sem("mix_tail_ready")

        qT = cut(0, 4, SEQ)
        toeplitz = cut(1024, HEADS, SEQ)
        pairs = cut(3072, 2, GROUPS, SEQ)
        blocks = cut(4096, 2, CMP_PAIRS, GROUPS, NCMP)
        kcvcT = cut(5056, 2, SEQ)
        probsT = [cut(3072 + 1024 * i, 2, TT, SEQ) for i in range(2)]
        keysT = cut(5568, 2, SEQ)
        values = cut(6080, 2, TT, P)
        cmp_hT = cut(6592, 2, 32)
        cmp_kT = cut(6656, NCMP)
        cmp_v = cut(6672, P)
        gates = cut(6800, TT, HEADS, 3)
        cmp_bias = cut(6848, TT, HEADS, NCMP)
        cmp_p = cut(7088, TT, HEADS, 32)
        cmp_pT = cut(7600, GROUPS, SEQ)
        soft = cut(8112, TT, 3, HEADS, 4)
        bias_rows = cut(8304, 384)
        probs = [[cut(8704 + (2048 if t else 0) + h * (512 if t else 256), 2, P * (t + 1)) for h in range(HEADS)]
                 for t in range(TT)]
        uT = cut(14848, 2, SEQ)
        v_n = cut(15360, TT, SEQ)
        v_g = cut(15872, TT, SEQ)
        kmT = cut(16384, KD, SEQ)
        vm = cut(18432, TT, D)
        hots = cut(16384, DIST_COLS)
        pool_a = cut(17408, 2, 272)
        pool_b = cut(17952, 2, 272)
        pool_c = cut(18496, 2, 272)
        pool_s = cut(19040, 2, SEQ)
        pool_d = cut(19552, 2, SEQ)
        qmT = cut(0, KD, SEQ)
        mprobs = [cut(2048 + 1024 * t, MEM_HEADS, SEQ) for t in range(TT)]
        mprobsT = cut(24576, MEM_HEADS, TT, SEQ)
        msoft = small[:, 0:TT * 3 * MEM_HEADS].rearrange("p (t k h) -> p t k h", t=TT, k=3)
        conv = [cut(0 + 512 * i, 2, SEQ) for i in range(3)]
        act_g = [cut(1536 + 256 * i, SEQ) for i in range(2)]
        prod = [cut(2048 + 256 * i, SEQ) for i in range(2)]
        prod_s = [cut_split(16384 + 512 * i, 2, SEQ) for i in range(4)]
        act_s = cut_split(4096, 2, KD, SEQ)
        split_slots = [[cut_split(at, 2, 2048) for at in (20480, 12288, 8192)],
                       [cut_split(at, 2, 2048) for at in (12352, 20480, 8192)]]

        cqT = cut(0, 2, SEQ)
        ckvT = cut(512, SEQ)
        kidxT = cut(768, SEQ)
        dqT = cut(1024, 2, SEQ)
        dqiT = cut(1536, 2, SEQ)
        dkT = cut(2048, SEQ)
        dv = cut(19576, TT, DK)
        dsq = cut(2432, 2, SEQ)
        dsk = cut(2944, SEQ)
        w_idx = cut(3968, TT, 4)
        top8 = cut(3976, TT, 8)
        dsoft = cut(19704, TT, 2, DSA_HEADS)
        idx_score = [cut(4096 + 256 * t, P * (t + 1)) for t in range(TT)]
        dmask = [cut(4608 + 256 * t, P * (t + 1)) for t in range(TT)]
        relu_l = [[cut(5120 + 1024 * t + 512 * par, 2, P * (t + 1)) for par in range(2)] for t in range(TT)]
        dprobs = [cut(at, DSA_HEADS, P * (t + 1)) for t, at in enumerate((19720, 25600))]
        dprobsT = [cut(4096, 2, TT, SEQ), cut(20480, 2, TT, SEQ)]
        gate_s = cut(10240, 2, SEQ)
        y_pad = cut(10752, 2, CONV_TAPS - 1 + SEQ)
        conv_y = cut(11328, 2, SEQ)
        conv_sq = cut(11840, 2, SEQ)
        qkv = cut(12352, 12, SEQ)
        zT = cut(16448, GDN_HEADS, SEQ)
        gate_rows = cut(15424, 4, SEQ)
        row_tmp = cut(17472, 2, SEQ)
        gate_cols = cut(18496, TT, 4, GDN_HEADS)
        state = cut(18528, GDN_HEADS, P)
        v_new = cut(19040, GDN_HEADS, P)
        a_rate = cut(19552, 1)
        kbT = cut(20480, GDN_HEADS, SEQ)
        qeT = cut(21504, GDN_HEADS, SEQ)
        exp_decay = cut(22528, GDN_HEADS, SEQ)
        xkT = cut(24576, XA_HEADS, SEQ)
        xv = post_gain[:, :].rearrange("p (s n) -> p s n", s=TT)
        AT, qkT, inv, invT, Y, bke, kdec, bv, u_n, wT = [
            [cut(1024 * i + 512 * t, GDN_HEADS, P) for t in range(TT)] for i in range(10)]
        l2_sq = cut(20480, 8, SEQ)
        AT_level = [[cut(at + 512 * t, GDN_HEADS, P) for t in range(TT)] for at in (9216, 8192)]
        oT = cut(2048, GDN_HEADS, SEQ)
        o_sq = cut(0, GDN_HEADS, SEQ)
        xqT = cut(0, XA_HEADS, SEQ)
        xq_sq = cut(1024, XA_HEADS, SEQ)
        xprobs = [cut(2048 + 1024 * t, XA_HEADS, SEQ) for t in range(TT)]
        xprobsT = cut(16448, XA_HEADS, TT, SEQ)
        xsoft = cut(18496, TT, 2, XA_HEADS)
        xq_root = cut(18512, TT, XA_HEADS)
        relu_h = [cut(0 + 512 * i, 2, SEQ) for i in range(2)]
        relu2 = [cut(1024 + 512 * i, 2, SEQ) for i in range(2)]
        relu2_s = [cut_split(16448 + 1024 * i, 2, 2, SEQ) for i in range(3)]

        chunk2 = {"dq": (dqT, dsq, 1.0, 64 * EPS, "dq_norm"),
                  "dk": (dkT, dsk, 1.0 / 64, EPS, "dk_norm")}
        ACROSS = {n: i for i, n in enumerate(chunk2)}

        root_rows = cut(17984, 2, SEQ)
        ROWS = {"l": (qkv[:, 0:8, :], l2_sq, 8, conc("root_scale")[0:8, :], conc("root_bias")[0:8, :], root_rows[0:8, 0, :]),
                "xk": (xkT, mixT[:, 0:4, :], 4, 1.0 / P, eps_col(EPS)[0:4, :], root_rows[0:4, 1, :]),
                "o": (oT, o_sq, 4, 1.0 / P, eps_col(EPS)[0:4, :], root_rows[0:4, 0, :])}

        STATI = {n: i for i, n in enumerate(STATS)}

        def stat(name, j=0):
            c = 2 * STATI[name] + j
            return stats[:, c:c + 1]

        hT_free = {"mix": None, "memkv": full(("v",)), "mem": acc_filled(("mv", 3)), "ffn": full(("mq", 3))}
        hT_free.update({"mix2": full(("up", FFN_PAIRS - 1)), "mem2": full(("z", 1)), "cross": acc_filled(("xv", 1)),
                        "mlp": full(("xq", 1))})
        LAST_OF_UNIT = {u: full((u,)) for u in ("q0", "q1", "kcvc", "ksvs", "kwvw", "gates", "pool", "u", "v")}
        LAST_OF_UNIT.update({"cmp_w1k": full(("cmp_h",)), "cmp_w1v": full(("cmp_h",))})
        LAST_OF_UNIT.update({u: full(u) for u in units if u in TILE})
        LAST_OF_UNIT.update({u: full((u,)) for u in ("cq", "ck", "ug0", "ug1")})
        LAST_OF_UNIT["ab"] = full(("widx",))
        spent = 0
        last_unit = {}
        for u in units:
            if isinstance(u, tuple) and u not in TILE:
                last_unit[u[0]] = u
        SPENT = {}
        for u in units:
            if u in LAST_OF_UNIT:
                continue
            product = u[0]
            if last_unit[product] == u:
                LAST_OF_UNIT[u] = acc_filled((product, 1 if product == "xv" else 3))
            else:
                spent += 1
                SPENT[u] = spent
                LAST_OF_UNIT[u] = (unit_spent, spent)

        w_in = a["w_in"].rearrange("(k p) c -> p k c", p=P)
        w_up = a["w_up"].rearrange("(k p) c -> p k c", p=P)

        w_in2 = a["w_in2"].rearrange("(k p) c -> p k c", p=P)
        xa_wkv = a["xa_wkv"].rearrange("(k p) c -> p k c", p=P)

        def cols(w, lo, n):
            return w[:, :, lo:lo + n]

        def rows(w, i, n=2):
            return w.rearrange("(k p) c -> p k c", p=P)[:, n * i:n * i + n, :]

        def source(u):
            at = {"q0": 0, "q1": 256, "kcvc": 512, "ksvs": 768, "kwvw": 1024, "gates": 1280, "pool": 1304,
                  "u": 1560, "v": 1816}
            if u in at:
                n = 24 if u == "gates" else 256
                return (KD, n), cols(w_in, at[u], n)
            if u in ("cmp_w1k", "cmp_w1v"):
                return (CMP_PAIRS, P), a["cmp_w1"][int(u == "cmp_w1v")].rearrange("(j p) c -> p j c", p=P)
            at2 = {"cq": (2048, 256), "ck": (2304, 192), "ab": (2496, 12), "ug0": (2508, 256), "ug1": (2764, 256)}
            if u in at2:
                lo, n = at2[u]
                return (KD, n), cols(w_in2, lo, n)
            kind, i = u
            wide = {"mk": "w_mk", "mq": "w_mq"}
            tall = {"mv": "w_mv", "out": "w_out", "wo": "w_mo", "down": "w_down"}
            if kind in wide:
                return (KD, 256), cols(a[wide[kind]].rearrange("(k p) c -> p k c", p=P), 256 * i, 256)
            if kind in tall:
                return (2, D), rows(a[tall[kind]], i)
            if kind == "up":
                return (KD, 256), cols(w_up, 256 * i, 256)
            if kind == "qkv":
                return (KD, 256), cols(w_in2, 256 * i, 256)
            if kind == "z":
                return (KD, 256), cols(w_in2, 1536 + 256 * i, 256)
            if kind == "xk":
                return (KD, 256), cols(xa_wkv, 256 * i, 256)
            if kind == "xv":
                return (4, 512), xa_wkv[:, 4 * i:4 * i + 4, 512:1024]
            if kind == "xq":
                return (KD, 256), cols(a["xa_wq"].rearrange("(k p) c -> p k c", p=P), 256 * i, 256)
            if kind == "m1":
                return (KD, 256), cols(a["mlp_w1"].rearrange("(k p) c -> p k c", p=P), 256 * i, 256)
            return (2, D), rows(a[{"out2": "w_out2", "xwo": "xa_wo", "m2": "mlp_w2"}[kind]], i)

        block = ctx.enter_context(nc.Block())

        @block.sync
        def _(sp):
            def load(u):
                i = UNIT[u]
                if i >= RING:
                    held = units[i - RING]
                    sp.wait_ge(*((low_ready, SPLIT[held] + 1) if held in SPLIT else LAST_OF_UNIT[held]))
                shape, src = source(u)
                sp.dma_start(weights(u, *shape), src).then_inc(unit_loaded[i % RING], 16)

            sp.dma_start(x[:, 0, :], a["x"][0:P, :]).then_inc(x_in[0], 16)
            sp.dma_start(x[:, 1, :], a["x"][P:2 * P, :]).then_inc(x_in[1], 16)
            sp.dma_start(con[:, 0:CON_FIRST], a["consts"][:, 0:CON_FIRST]).then_inc(first_consts_in, 16)
            sp.dma_start(par[:, 0:PAR_FIRST], a["params"][:, 0:PAR_FIRST]).then_inc(first_params_in, 16)
            for u in units[:2]:
                load(u)
            sp.dma_start(hots[0:REL_BUCKETS + 1, :], a["hots"]).then_inc(hots_in, 16)
            sp.dma_start(par[:, PAR_FIRST:], a["params"][:, PAR_FIRST:]).then_inc(params_in, 16)
            for u in units[2:4]:
                load(u)
            sp.dma_start(con[:, CON_FIRST:], a["consts"][:, CON_FIRST:]).then_inc(consts_in, 16)
            for u in units[4:]:
                load(u)
            for t in range(TT):
                sp.wait_ge(*acc_drained(("m2", 2 * t + 1)))
                sp.dma_start(out[P * t:P * t + P, :], x[:, t, :]).then_inc(out_done, 16)
            sp.wait_ge(out_done, 16 * TT)

        @block.gpsimd
        def _(pool):
            chain = [0]

            def link(ins):
                chain[0] += 1
                ins.then_inc(pool_chain, 1)
                pool.wait_ge(pool_chain, chain[0])


            def rstd(name, halves, n=D):
                pool.wait_ge(squares, STATI[name] + 1)
                if halves:
                    link(pool.tensor_tensor(stat(name), stat(name), stat(name, 1), ALU.add))
                link(pool.tensor_scalar(stat(name), stat(name), 1.0 / n, EPS, ALU.mult, ALU.add))
                pool.tensor_tensor(stat(name), stat(name), conc("neg_half")[:, 0:1], ALU.pow).then_inc(rstd_ready, 1)

            def load_post_gain(n):
                if n:
                    pool.wait_ge(x_done, 2 * n)
                g = a[("mix_norm_post", "mem_norm_post", "ffn_norm_post")[n]]
                pool.dma_start(post_gain[:, :], bass.AP(tensor=g.tensor, offset=g.offset, ap=[[0, P], [1, D]])).then_inc(gain_in, 16)

            pool.wait_ge(first_consts_in, 16)
            for t in range(TT):
                rstd(("mix", t), False)
            pool.wait_ge(*drained(("bias_row",)))
            pool.dma_start(bias_rows_dram[:, 0:384], bias_rows[0:HEADS, :]).then_inc(bias_rows_out, 16)
            pool.wait_ge(bias_rows_out, 16)
            pool.dma_start(toeplitz, bass.AP(tensor=bias_rows_dram.tensor, offset=bias_rows_dram.offset,
                                             ap=[[1, P], [DIST_COLS, HEADS], [1, SEQ]])).then_inc(bias_tile_in, 16)
            pool.wait_ge(params_in, 16)
            wsT = parc("sgu_wT").rearrange("p (h t) -> p h t", h=4)
            pool.affine_select(out=wsT, in_=wsT, compare_op=ALU.is_ge, fill=0.0, base=0,
                               pattern=[[0, 4], [1, P]], channel_multiplier=-1).then_inc(masked_ws, 1)
            link(pool.memset(pool_b[:, :, 0:16], 0.0))
            link(pool.memset(pool_c[:, :, 0:16], 0.0))
            link(pool.memset(pool_a[:, :, 0:16], 0.0))
            pool.wait_ge(*drained(("pool",)))
            src, spare = pool_a, [pool_b, pool_c, pool_b, pool_c]
            for g, w in enumerate(POOL_WINDOWS):
                dst = spare[g]
                link(pool.tensor_tensor(dst[:, :, 16:272], src[:, :, 16:272], src[:, :, 16 - w // 2:272 - w // 2], ALU.add))
                half = slice(64 * (g % 2), 64 * (g % 2) + 64)
                link(pool.tensor_copy(pool_s[half, g // 2, :], dst[half, g // 2, 16:272]))
                src = dst
            pool.wait_ge(consts_in, 16)
            link(pool.tensor_tensor(pool_s, pool_s, conc("inv_count").rearrange("p (c t) -> p c t", c=2), ALU.mult))
            pool.tensor_tensor(pool_d, pool_s, pool_a[:, :, 16:272], ALU.subtract).then_inc(pooled, 1)
            for t in range(TT):
                pool.wait_ge(sgu_stat, t + 1)
                link(pool.tensor_scalar(stat(("sgu", t), 1), stat(("sgu", t), 1), EPS, None, ALU.add))
                pool.tensor_tensor(stat(("sgu", t), 1), stat(("sgu", t), 1), conc("neg_half")[:, 0:1],
                                   ALU.pow).then_inc(sgu_rstd, 1)
            load_post_gain(0)
            for name in STATS:
                if name[0] in ("mem2", "cross", "mlp"):
                    continue
                if name[0] not in ("mix", "sgu"):
                    rstd(name, name[0].endswith("_post"))
                if name in (("mem", 1), ("ffn", 1)):
                    load_post_gain(1 if name[0] == "mem" else 2)
            for t in range(TT):
                pool.wait_ge(idx_sum, t + 1)
                pool.affine_select(out=idx_score[t], in_=idx_score[t], compare_op=ALU.is_ge, fill=FUTURE, base=P * t,
                                   pattern=[[-1, P * (t + 1)]], channel_multiplier=1).then_inc(idx_causal, 1)
            for t in range(TT):
                rstd(("mem2", t), False)
            for t in range(TT):
                pool.wait_ge(picked, t + 1)
                link(pool.tensor_scalar(dmask[t], idx_score[t], -3.2e38, 1.0, ALU.is_le, ALU.subtract))
                link(pool.tensor_scalar(dmask[t], dmask[t], -MASKED, None, ALU.mult))
                pool.affine_select(out=dmask[t], in_=dmask[t], compare_op=ALU.is_ge, fill=MASKED, base=P * t,
                                   pattern=[[-1, P * (t + 1)]], channel_multiplier=1).then_inc(dmask_ready, 1)
            for t in range(TT):
                pool.wait_ge(gamma_exp, t + 1)
                for h in range(GDN_HEADS):
                    pool.tensor_tensor(inv[t][:, h, :], Y[t][:, h, :], conc("tri_strict"), ALU.mult)
                for h in range(GDN_HEADS):
                    ins = pool.tensor_tensor(Y[t][:, h, :], Y[t][:, h, :], conc("tri_incl"), ALU.mult)
                ins.then_inc(gamma_ready, 1)
            masks = conc("levels").rearrange("p (l j) -> p l j", l=LEVELS)
            for level in range(LEVELS):
                if level == 1:
                    pool.wait_ge(*full(("do",)))
                elif level == 2:
                    pool.wait_ge(first_invT, TT)
                for t in range(TT):
                    pool.wait_ge(*(full(("y", level - 2, t)) if level >= 2 else drained(("kk", t))))
                    pool.tensor_tensor(AT_level[level % 2][t], AT[t], masks[:, level, :].unsqueeze(1).broadcast_to(
                        [P, GDN_HEADS, P]), ALU.mult).then_inc(level_masked, 1)
            for stage in ("cross", "mlp"):
                for t in range(TT):
                    rstd((stage, t), False)

        @block.scalar
        def _(act):
            chain = [0]

            def link(ins):
                chain[0] += 1
                ins.then_inc(act_chain, 1)
                act.wait_ge(act_chain, chain[0])

            def square(name, views):
                if STATI[name]:
                    act.wait_ge(squares, STATI[name])
                for j, v in enumerate(views):
                    ins = act.activation(junk[:, 0:v.shape[-1]], v, ACT.Square, accum_out=stat(name, j))
                    if j < len(views) - 1:
                        link(ins)
                ins.then_inc(squares, 1)

            def drain(name, dst, src, func=ACT.Copy, **kw):
                act.wait_ge(*full(name))
                return act.activation(dst, src, func, **kw)

            for t in range(TT):
                act.wait_ge(x_in[t], 16)
                square(("mix", t), [x[:, t, :]])

            def halves(name):
                return bank(name)[:, :].rearrange("p (c t) -> p c t", c=2)

            for i in range(2):
                name = (f"q{i}",)
                drain(name, qT[:, 2 * i:2 * i + 2, :], halves(name), scale=DK ** -0.5).then_inc(reader(name), 1)
            drain(("kcvc",), kcvcT, halves(("kcvc",))).then_inc(reader(("kcvc",)), 1)
            act.wait_ge(*full(("normT", "mix", 1, 1)))
            act.dma_start(xn[:, :, :], a["mem"].rearrange("(t p) d -> p t d", p=P)).then_inc(mem_in, 16)
            act.wait_ge(*drained(("kcvc",)))
            for g in range(GROUPS):
                src = kcvcT[DK * g:DK * g + DK]
                act.dma_start(pairs[0:DK, :, g, :], src).then_inc(shifted_in, 16)
                act.dma_start(pairs[DK:P, :, g, 0:SEQ - 1], src[:, :, 1:SEQ]).then_inc(shifted_in, 16)
            for j, u in enumerate(("ksvs", "kwvw")):
                name = (u,)
                drain(name, keysT[:, j, :], bank(name)[:, 0:SEQ])
                act.activation(values[:, j, :, :], bank(name)[:, SEQ:512].rearrange("p (t d) -> p t d", t=TT),
                               ACT.Copy).then_inc(reader(name), 1)
            drain(("gates",), gates.rearrange("p t h b -> p t (h b)"),
                  bank(("gates",))[:, 0:48].rearrange("p (t n) -> p t n", t=TT), ACT.Sigmoid).then_inc(reader(("gates",)), 1)
            drain(("pool",), pool_a[:, :, 16:272], halves(("pool",))).then_inc(reader(("pool",)), 1)
            drain(("u",), uT, halves(("u",)), ACT.Gelu_apprx_tanh).then_inc(reader(("u",)), 1)
            drain(("v",), v_g, halves(("v",)), ACT.Gelu_apprx_tanh).then_inc(reader(("v",)), 1)
            act.wait_ge(*full(("cmp_h",)))
            b1 = parc("cmp_b1")
            for kv in range(2):
                ins = act.activation(cmp_hT[:, kv, 0:30], bank(("cmp_h",))[:, 32 * kv:32 * kv + 30],
                                     ACT.Gelu_apprx_tanh, bias=b1[:, kv:kv + 1])
            ins.then_inc(reader(("cmp_h",)), 1)

            act.wait_ge(mem_in, 16)
            for t in range(TT):
                square(("memkv", t), [xn[:, t, :]])

            n = 0
            for t in range(TT):
                for h in range(HEADS):
                    n += 1
                    act.wait_ge(neg_max, n + t + 1)
                    if h == 0:
                        for hh in range(HEADS):
                            ins = act.activation(cmp_p[:, t, hh, 0:NCMP], cmp_p[:, t, hh, 0:NCMP], ACT.Exp,
                                                 bias=soft[:, t, 0, hh, 0:1], accum_out=soft[:, t, 1, hh, 0:1])
                        ins.then_inc(exped, 1)
                    for j in range(2):
                        ins = act.activation(probs[t][h][:, j, :], probs[t][h][:, j, :], ACT.Exp,
                                             bias=soft[:, t, 0, h, j + 1:j + 2], accum_out=soft[:, t, 1, h, j + 1:j + 2])
                    ins.then_inc(exped, 1)
            for c in range(4):
                drain(("mk", c), kmT[:, 2 * c:2 * c + 2, :], halves(("mk", c))).then_inc(reader(("mk", c)), 1)
            for t in range(TT):
                for half in range(2):
                    f = ("mv", 2 * t + half)
                    act.wait_ge(*acc_filled(f))
                    act.activation(vm[:, t, 512 * half:512 * half + 512], acc(f)[:, :], ACT.Copy).then_inc(acc_read, 1)
            split_done = [0]

            def high_parts(upto):
                while split_done[0] < min(upto + 1, len(split_units)):
                    i = split_done[0]
                    u = split_units[i]
                    act.wait_ge(*loaded(u))
                    if i >= SPLIT_RING:
                        act.wait_ge(*LAST_OF_UNIT[split_units[i - SPLIT_RING]])
                    act.activation(split_slot(i)[:, 0, :], weights(u, 2048), ACT.Copy).then_inc(high_ready, 1)
                    split_done[0] += 1

            def high_rows(stage):
                for t in range(TT):
                    for half in range(2):
                        act.wait_ge(*drained(("normT", stage, t, half)))
                        act.activation(act_s[:, 0, 4 * half:4 * half + 4, P * t:P * t + P],
                                       hT[:, 4 * half:4 * half + 4, P * t:P * t + P], ACT.Copy).then_inc(acts_high, 1)

            def high_mix(product, c, src, ready=None):
                if ready is not None:
                    act.wait_ge(*ready)
                act.activation(act_s[:, 0, 2 * c:2 * c + 2, :], src, ACT.Copy).then_inc(acts_high, 1)

            high_parts(SPLIT[("out", MIX_ORDER[0])])
            for i in range(2):
                act.wait_ge(*acc_filled(("o", i)))
            act.wait_ge(mix_tail, 1)
            act.wait_ge(*drained(("pool_out",)))
            for c in MIX_ORDER:
                high_mix("out", c, mixT[:, 2 * c:2 * c + 2, :] if c >= 2 else
                         acc(("o", c))[:, :].rearrange("p (c t) -> p c t", c=2))
            high_parts(SPLIT[("mq", 1)])

            def post_squares(product, stage):
                for t in range(TT):
                    act.wait_ge(*acc_filled((product, 2 * t + 1)))
                    square((stage, t), [acc((product, 2 * t + half))[:, :] for half in range(2)])

            def next_squares(stage, n_updates):
                for t in range(TT):
                    act.wait_ge(x_done, n_updates + t + 1)
                    square((stage, t), [x[:, t, :]])

            post_squares("out", "out_post")
            high_parts(SPLIT[("mq", 2)])
            next_squares("mem", 0)
            high_rows("mem")
            for c in range(4):
                drain(("mq", c), qmT[:, 2 * c:2 * c + 2, :], halves(("mq", c)), scale=MEM_DIM ** -0.5).then_inc(reader(("mq", c)), 1)
                if c < 2:
                    high_parts(SPLIT[("mq", 3)] + c)
            m = HEADS * TT + TT
            for t in range(TT):
                for hp in range(2):
                    m += 1
                    act.wait_ge(neg_max, m)
                    for j in range(2):
                        h = 2 * hp + j
                        ins = act.activation(mprobs[t][:, h, :], bank(("ms", t, hp))[:, SEQ * j:SEQ * j + SEQ], ACT.Exp,
                                             bias=msoft[:, t, 0, h:h + 1], accum_out=msoft[:, t, 1, h:h + 1])
                    ins.then_inc(reader(("ms", t, hp)), 1)
            high_parts(SPLIT[("wo", 2)])
            for c in range(4):
                high_mix("wo", c, halves(("mo", c)), full(("mo", c)))
            high_parts(SPLIT[("up", 1)])
            post_squares("wo", "wo_post")
            high_parts(SPLIT[("up", 2)])
            next_squares("ffn", 2)
            high_rows("ffn")
            cw = parc("conv_w").rearrange("p (j g w) -> p j g w", g=2, w=3)
            cb = parc("conv_b").rearrange("p (j g) -> p j g", g=2)

            def last_tap(j):
                name = ("up", j)
                act.wait_ge(*full(name))
                if j >= 3:
                    act.wait_ge(gated, j - 2)
                for g in range(2):
                    ins = act.activation(conv[j % 3][:, g, :], bank(name)[:, SEQ * g:SEQ * g + SEQ], ACT.Identity,
                                         scale=cw[:, j, g, 2:3], bias=cb[:, j, g:g + 1])
                ins.then_inc(tap2, 1)

            def gate_gelu(j):
                act.wait_ge(*drained(("up", j)))
                if j >= 2:
                    act.wait_ge(gated, j - 1)
                act.activation(act_g[j % 2], conv[j % 3][:, 0, :], ACT.Gelu_apprx_tanh).then_inc(gate_act, 1)

            for j in range(FFN_PAIRS + 1):
                if j < FFN_PAIRS:
                    high_parts(SPLIT[("up", j)] + 2)
                    last_tap(j)
                    high_parts(split_before(("up", j + 1)) + 2)
                if j >= 1:
                    gate_gelu(j - 1)
            post_squares("down", "down_post")
            next_squares("mix2", 4)

            def across_squares(tag):
                raw, sq = chunk2[tag][:2]
                act.activation(sq, raw, ACT.Square).then_inc(across_sq, 1)

            def across_root(tag):
                raw, sq, scale, bias, _ = chunk2[tag]
                name = ("across", tag)
                act.wait_ge(*full(name))
                src = bank(name)[:, 0:SEQ] if tag == "dk" else halves(name)
                act.activation(sq, src, ACT.Sqrt, scale=scale, bias=eps_col(bias)).then_inc(reader(name), 1)

            act.wait_ge(*full(("normT", "mix2", 1, 1)))
            act.dma_start(xn[:, :, :], a["mem2"].rearrange("(t p) d -> p t d", p=P)).then_inc(mem2_in, 16)
            drain(("cq",), cqT, halves(("cq",))).then_inc(reader(("cq",)), 1)
            drain(("ck",), ckvT, bank(("ck",))[:, 0:SEQ])
            act.activation(kidxT, bank(("ck",))[:, SEQ:512], ACT.Copy).then_inc(reader(("ck",)), 1)
            drain(("ab",), row_tmp[0:4, 0, :], bank(("ab",))[0:4, 0:SEQ], ACT.Identity, bias=parc("dt_bias")[0:4, :])
            act.activation(gate_rows[0:4, 0, :], bank(("ab",))[0:4, SEQ:512], ACT.Sigmoid).then_inc(reader(("ab",)), 1)
            drain(("widx",), w_idx, bank(("widx",))[:, 0:8].rearrange("p (t h) -> p t h", t=TT), scale=1.0 / 16
                  ).then_inc(reader(("widx",)), 1)
            act.wait_ge(*drained(("ab",)))
            link(act.activation(row_tmp[0:4, 1, :], row_tmp[0:4, 0, :], ACT.Abs))
            link(act.activation(row_tmp[0:4, 1, :], row_tmp[0:4, 1, :], ACT.Exp, scale=-1.0))
            act.activation(a_rate[0:4, :], parc("a_log")[0:4, :], ACT.Exp)
            act.activation(row_tmp[0:4, 1, :], row_tmp[0:4, 1, :], ACT.Ln, bias=1.0).then_inc(softplus_ln, 1)
            drain(("ug1",), gate_s, halves(("ug1",)), ACT.Sigmoid).then_inc(reader(("ug1",)), 1)
            act.wait_ge(mem2_in, 16)
            for t in range(TT):
                square(("mem2", t), [xn[:, t, :]])
            drain(("dq",), dqT, halves(("dq",))).then_inc(reader(("dq",)), 1)
            drain(("dqi",), dqiT, halves(("dqi",))).then_inc(reader(("dqi",)), 1)
            drain(("dk",), dkT, bank(("dk",))[:, 0:SEQ])
            act.activation(dv, bank(("dk",))[:, SEQ:SEQ + P].rearrange("p (t d) -> p t d", t=TT), ACT.Copy
                           ).then_inc(reader(("dk",)), 1)
            act.wait_ge(*drained(("dk",)))
            across_squares("dq")
            across_squares("dk")
            gconv = parc("gdn_conv").rearrange("p (c w) -> p c w", w=4)

            def gdn_last_tap(i):
                name = ("qkv", i)
                act.wait_ge(*full(name))
                for c in range(2):
                    ins = act.activation(qkv[:, 2 * i + c, :], bank(name)[:, SEQ * c:SEQ * c + SEQ], ACT.Copy,
                                         scale=gconv[:, 2 * i + c, 3:4])
                ins.then_inc(tap3, 1)

            def gdn_silu(i):
                act.wait_ge(*drained(("qkv", i)))
                act.activation(qkv[:, 2 * i:2 * i + 2, :], qkv[:, 2 * i:2 * i + 2, :], ACT.Silu).then_inc(silu_done, 1)

            gdn_last_tap(0)
            across_root("dq")
            across_root("dk")
            for t in range(TT):
                for par in range(2):
                    name = ("il", t, par)
                    n = P * (t + 1)
                    drain(name, relu_l[t][par], bank(name)[:, 0:2 * n].rearrange("p (j s) -> p j s", j=2), ACT.Relu
                          ).then_inc(reader(name), 1)
            act.wait_ge(decay_sum, 1)
            link(act.activation(row_tmp[0:4, 0, :], gate_rows[0:4, 3, :], ACT.Exp))
            act.activation(gate_rows[0:4, 2, :], gate_rows[0:4, 2, :], ACT.Exp).then_inc(decay_exp, 1)
            for i in range(1, 6):
                gdn_last_tap(i)
                gdn_silu(i - 1)
            gdn_silu(5)
            for t in range(TT):
                act.wait_ge(rstd_ready, STATI[("mem2", t)] + 1)
                act.activation(xn[:, t, :], xn[:, t, :], ACT.Copy, scale=stat(("mem2", t))).then_inc(normed, 1)
            for i in range(2):
                drain(("z", i), zT[:, 2 * i:2 * i + 2, :], halves(("z", i)), ACT.Silu).then_inc(reader(("z", i)), 1)
            def row_square(tag):
                raw, sq, n = ROWS[tag][:3]
                for i in range(0, n, 2):
                    ins = act.activation(sq[:, i:i + 2, :], raw[:, i:i + 2, :], ACT.Square)
                ins.then_inc(row_squares, 1)

            def row_root(tag):
                _, _, n, scale, bias, roots = ROWS[tag]
                name = ("row_sum", tag)
                drain(name, roots, bank(name)[0:n, 0:SEQ], ACT.Sqrt, scale=scale, bias=bias).then_inc(reader(name), 1)

            act.wait_ge(silu_done, 6)
            row_square("l")
            drain(("xk", 0), xkT[:, 0:2, :], halves(("xk", 0))).then_inc(reader(("xk", 0)), 1)
            row_root("l")
            n = 0
            for t in range(TT):
                for par in range(2):
                    n += 1
                    act.wait_ge(d_max, n)
                    for j in range(2):
                        h = 2 * j + par
                        ins = act.activation(dprobs[t][:, h, :], dprobs[t][:, h, :], ACT.Exp, bias=dsoft[:, t, 0, h:h + 1],
                                             accum_out=dsoft[:, t, 1, h:h + 1])
                    ins.then_inc(d_exp, 1)
            drain(("xk", 1), xkT[:, 2:4, :], halves(("xk", 1))).then_inc(reader(("xk", 1)), 1)
            act.wait_ge(*drained(("xk", 1)))
            row_square("xk")
            for i in range(2):
                act.wait_ge(gamma_diff, i + 1)
                drain(("dr", i), exp_decay[:, 2 * i:2 * i + 2, :], halves(("dr", i)), ACT.Exp
                      ).then_inc(reader(("dr", i)), 1)
            act.wait_ge(gamma_diff, 2)
            for t in range(TT):
                act.activation(Y[t], Y[t], ACT.Exp).then_inc(gamma_exp, 1)
            row_root("xk")
            drain(("do",), mixT[:, 4:6, :], halves(("do",))).then_inc(reader(("do",)), 1)
            for level in range(1, LEVELS):
                for t in range(TT):
                    name = ("y", level, t)
                    drain(name, Y[t], bank(name)[:, :].rearrange("p (h d) -> p h d", h=GDN_HEADS)).then_inc(reader(name), 1)
            for t in range(TT):
                drain(("gu", t), u_n[t], bank(("gu", t))[:, :].rearrange("p (h d) -> p h d", h=GDN_HEADS)
                      ).then_inc(reader(("gu", t)), 1)
            for t in range(TT):
                drain(("gw", t), wT[t], bank(("gw", t))[:, :].rearrange("p (h d) -> p h d", h=GDN_HEADS)
                      ).then_inc(reader(("gw", t)), 1)
            act.wait_ge(*drained(("ln_mean",)))
            act.activation(conv_sq, conv_y, ACT.Square).then_inc(conv_sq_ready, 1)
            name = ("ln_var",)
            drain(name, conv_sq[:, 0, :], bank(name)[:, 0:SEQ], ACT.Sqrt, scale=1.0 / SEQ, bias=eps_col(EPS)
                  ).then_inc(reader(name), 1)
            high_parts(SPLIT[("out2", MIX_ORDER[0])])
            for n in range(NCHUNK):
                name = ("go", n)
                drain(name, oT[:, :, CHUNK * n:CHUNK * n + CHUNK],
                      bank(name)[:, 0:4 * CHUNK].rearrange("p (h i) -> p h i", h=GDN_HEADS)).then_inc(reader(name), 1)
            act.wait_ge(*drained(("go", NCHUNK - 1)))
            row_square("o")
            row_root("o")
            high_parts(SPLIT[("out2", MIX_ORDER[1])])
            for t in range(TT):
                act.wait_ge(*acc_filled(("xv", t)))
                act.activation(xv[:, t, :], acc(("xv", t))[:, :], ACT.Copy).then_inc(acc_read, 1)
            act.wait_ge(conv_norm, 1)
            for c in range(2):
                ins = act.activation(mixT[:, 6 + c, :], conv_y[:, c, :], ACT.Silu, scale=parc("ln_g")[:, c:c + 1],
                                     bias=parc("ln_b")[:, c:c + 1])
            ins.then_inc(conv_mix, 1)
            act.wait_ge(conv_mix, 1)
            act.wait_ge(*drained(("do",)))
            for c in MIX_ORDER:
                high_mix("out2", c, mixT[:, 2 * c:2 * c + 2, :], None if c >= 2 else drained(("row_all", "o", c)))
            high_parts(SPLIT[("xq", 1)])

            def squares_of_sum(product, stage):
                for t in range(TT):
                    act.wait_ge(*acc_drained((product, 2 * t + 1)))
                    square((stage, t), [x[:, t, :]])

            squares_of_sum("out2", "cross")
            high_rows("cross")
            high_parts(SPLIT[("xwo", 0)])
            for i in range(2):
                name = ("xq", i)
                drain(name, xq_sq[:, 2 * i:2 * i + 2, :], halves(name), ACT.Square).then_inc(xq_squares, 1)
                act.activation(xqT[:, 2 * i:2 * i + 2, :], halves(name), ACT.Copy, scale=parc("xq_norm")
                               ).then_inc(reader(name), 1)
            drain(("xq_sums",), xq_root, bank(("xq_sums",))[:, 0:8].rearrange("p (t h) -> p t h", t=TT), ACT.Sqrt,
                  bias=eps_col(P * EPS)).then_inc(reader(("xq_sums",)), 1)
            n = 0
            for t in range(TT):
                for hp in range(2):
                    n += 1
                    act.wait_ge(x_max, n)
                    for j in range(2):
                        h = 2 * hp + j
                        ins = act.activation(xprobs[t][:, h, :], bank(("xs", t, hp))[:, SEQ * j:SEQ * j + SEQ], ACT.Exp,
                                             scale=xq_root[:, t, h:h + 1], bias=xsoft[:, t, 0, h:h + 1],
                                             accum_out=xsoft[:, t, 1, h:h + 1])
                    ins.then_inc(reader(("xs", t, hp)), 1)
            high_parts(SPLIT[("m1", 0)])
            for c in range(2):
                high_mix("xwo", c, halves(("xo", c)), full(("xo", c)))
            high_parts(SPLIT[("m1", 1)])
            squares_of_sum("xwo", "mlp")
            high_rows("mlp")
            high_parts(SPLIT[("m1", 2)])
            for j in range(MLP_UNITS):
                high_parts(SPLIT[("m1", j)] + 2)
                if j >= 2:
                    act.wait_ge(relu_sq, j - 1)
                drain(("m1", j), relu_h[j % 2], halves(("m1", j)), ACT.Relu).then_inc(reader(("m1", j)), 1)
                act.wait_ge(*drained(("m1", j)))
                if j >= 3:
                    act.wait_ge(unit_spent, SPENT[("m2", j - 3)])
                act.activation(relu2_s[j % 3][:, 0], relu_h[j % 2], ACT.Square).then_inc(relu_high, 1)
                high_parts(split_before(("m1", j + 1)) + 2)
            high_parts(len(split_units) - 1)

        @block.vector
        def _(dve):
            chain = [0]

            def link(ins):
                chain[0] += 1
                ins.then_inc(dve_chain, 1)
                dve.wait_ge(dve_chain, chain[0])

            def scale_rows(stage, src):
                for t in range(TT):
                    dve.wait_ge(rstd_ready, STATI[(stage, t)] + 1 - 0)
                    dve.tensor_scalar(xn[:, t, :], src(t), stat((stage, t)), None, ALU.mult).then_inc(normed, 1)

            def drain_norm(stage):
                free = hT_free[stage]
                if free is not None:
                    dve.wait_ge(*free)
                for t in range(TT):
                    for half in range(2):
                        name = ("normT", stage, t, half)
                        dve.wait_ge(*full(name))
                        g = gains[:, GAIN[stage], 4 * half:4 * half + 4].unsqueeze(2).broadcast_to([P, 4, P])
                        dve.tensor_tensor(hT[:, 4 * half:4 * half + 4, P * t:P * t + P],
                                          bank(name)[:, :].rearrange("p (k t) -> p k t", k=4), g,
                                          ALU.mult).then_inc(reader(name), 1)
                if stage in SPLIT_STAGES:
                    for t in range(TT):
                        for half in range(2):
                            dve.wait_ge(*high_there(("rows", stage, t, half)))
                            at = slice(4 * half, 4 * half + 4), slice(P * t, P * t + P)
                            dve.tensor_tensor(act_s[:, 1, *at], hT[:, *at], act_s[:, 0, *at], ALU.subtract).then_inc(acts_low, 1)

            scale_rows("mix", lambda t: x[:, t, :])
            dve.wait_ge(first_params_in, 16)
            drain_norm("mix")
            dve.wait_ge(*full(("bias_row",)))
            dve.tensor_copy(bias_rows[0:HEADS, :], bank(("bias_row",))[0:HEADS, 0:384]).then_inc(reader(("bias_row",)), 1)
            dve.wait_ge(*full(("bias_cmp",)))
            dve.tensor_copy(cmp_bias, bank(("bias_cmp",))[:, 0:240].rearrange("p (t c h) -> p t h c", t=TT, c=NCMP)
                            ).then_inc(reader(("bias_cmp",)), 1)
            dve.wait_ge(shifted_in, 64)
            pos = parc("cmp_pos").rearrange("p (v j) -> p v j", v=2)
            for kv in range(2):
                for g in range(GROUPS):
                    v = pairs[:, kv, g, :].rearrange("p (c j e) -> p j c e", j=8, e=2)
                    for hi in range(2):
                        ins = dve.tensor_tensor(blocks[:, kv, 8 * hi:8 * hi + 8, g, :], v[:, :, hi:hi + NCMP, 0],
                                                pos[:, kv, 8 * hi:8 * hi + 8].unsqueeze(2).broadcast_to([P, 8, NCMP]), ALU.add)
            ins.then_inc(blocks_ready, 1)
            for t in range(TT):
                dve.wait_ge(*drained(("v",)))
                link(dve.bn_stats(soft.rearrange("p t a h b -> p (t a h b)")[:, 6 * t:6 * t + 6], v_g[:, t, :]))
                dve.bn_aggr(stats[:, 2 * STATI[("sgu", t)]:2 * STATI[("sgu", t)] + 2],
                            soft.rearrange("p t a h b -> p (t a h b)")[:, 6 * t:6 * t + 6]).then_inc(sgu_stat, 1)
            for t in range(TT):
                dve.wait_ge(sgu_rstd, t + 1)
                link(dve.tensor_scalar(v_n[:, t, :], v_g[:, t, :], stat(("sgu", t)), stat(("sgu", t), 1),
                                       ALU.subtract, ALU.mult))
                link(dve.tensor_tensor(v_n[:, t, :], v_n[:, t, :], parc("sgu_g"), ALU.mult))
                dve.tensor_tensor(v_n[:, t, :], v_n[:, t, :], parc("sgu_b"), ALU.add).then_inc(sgu_normed, 1)
            name = ("cmp_kv",)
            dve.wait_ge(*full(name))
            dve.tensor_scalar(cmp_kT, bank(name)[:, 0:NCMP], parc("cmp_b2k"), None, ALU.add)
            for j in range(4):
                rows_j = slice(32 * j, 32 * j + NCMP)
                ins = dve.tensor_tensor(cmp_v[rows_j, :], bank(name)[rows_j, 64:64 + P], parc("cmp_b2v")[rows_j, :], ALU.add)
            ins.then_inc(reader(name), 1)

            scale_rows("memkv", lambda t: xn[:, t, :])
            for t in range(TT):
                if t == 0:
                    dve.memset(cmp_p.rearrange("p t h c -> p (t h c)"), 0.0).then_inc(scored, 1)
                    dve.wait_ge(scored, 1)
                for g in range(GROUPS):
                    name = ("cmp_s", t, g)
                    hs = slice(HG * g, HG * g + HG)
                    dve.wait_ge(*full(name))
                    dve.tensor_tensor(cmp_p[:, t, hs, 0:NCMP],
                                      bank(name)[:, 0:HG * NCMP].rearrange("p (h c) -> p h c", h=HG),
                                      cmp_bias[:, t, hs, :], ALU.add).then_inc(reader(name), 1)
                dve.wait_ge(*drained(name))
                link(dve.tensor_reduce(soft[:, t, 0, :, 0], cmp_p[:, t, :, 0:NCMP], AX, ALU.max))
                dve.tensor_scalar(soft[:, t, 0, :, 0], soft[:, t, 0, :, 0], MASKED / 2, -1.0, ALU.max, ALU.mult
                                  ).then_inc(neg_max, 1)
                if t == 0:
                    dve.wait_ge(bias_tile_in, 16)
                for h in range(HEADS):
                    name = ("s", t, h)
                    n = P * (t + 1)
                    dve.wait_ge(*full(name))
                    dve.tensor_tensor(probs[t][h], bank(name)[:, 0:2 * n].rearrange("p (j s) -> p j s", j=2),
                                      toeplitz[:, h, 0:n][:, ::-1].unsqueeze(1).broadcast_to([P, 2, n]), ALU.add
                                      ).then_inc(reader(name), 1)
                    dve.wait_ge(*drained(name))
                    dve.tensor_reduce(soft[:, t, 0, h, 1:3], probs[t][h], AX, ALU.max, negate=True).then_inc(neg_max, 1)
            name = ("pool_out",)
            dve.wait_ge(*full(name))
            dve.tensor_tensor(mixT[:, 4:6, :], bank(name)[:, :].rearrange("p (c t) -> p c t", c=2),
                              parc("pool_scale").unsqueeze(2).broadcast_to([P, 2, SEQ]), ALU.mult).then_inc(reader(name), 1)
            name = ("sgu_out",)
            dve.wait_ge(*full(name))
            for c in range(2):
                ins = dve.tensor_tensor(mixT[:, 6 + c, :].rearrange("p (t i) -> p t i", t=TT),
                                        bank(name)[:, SEQ * c:SEQ * c + SEQ].rearrange("p (t i) -> p t i", t=TT),
                                        parc("sgu_bias")[:, P * c:P * c + P].unsqueeze(1).broadcast_to([P, TT, P]), ALU.add)
            ins.then_inc(reader(name), 1)
            dve.wait_ge(*drained(name))
            dve.wait_ge(*drained(("u",)))
            dve.tensor_tensor(mixT[:, 6:8, :], mixT[:, 6:8, :], uT, ALU.mult).then_inc(mix_tail, 1)
            drain_norm("memkv")
            for t in range(TT):
                dve.wait_ge(exped, (HEADS + 1) * (t + 1))
                den = soft[:, t, 1, :, 0:3]
                link(dve.tensor_scalar(den, den, 1.0, None, ALU.max))
                link(dve.reciprocal(den, den))
                link(dve.tensor_tensor(den, den, gates[:, t, :, :], ALU.mult))
                dve.tensor_tensor(cmp_p[:, t, :, 0:NCMP], cmp_p[:, t, :, 0:NCMP],
                                  den[:, :, 0:1].broadcast_to([P, HEADS, NCMP]), ALU.mult).then_inc(weighed, 1)
                for h in range(HEADS):
                    dve.tensor_tensor(probs[t][h], probs[t][h],
                                      den[:, h, 1:3].unsqueeze(2).broadcast_to([P, 2, P * (t + 1)]), ALU.mult
                                      ).then_inc(weighed, 1)
            for t in range(TT):
                name = ("cmp_pT", t)
                dve.wait_ge(*full(name))
                dve.tensor_copy(cmp_pT[:, :, P * t:P * t + P], bank(name)[:, 0:SEQ].rearrange("p (g t) -> p g t", g=GROUPS)
                                ).then_inc(reader(name), 1)
            for h in range(HEADS):
                if h >= 2:
                    k = h - 2
                    dve.wait_ge(*(acc_filled(("o", k // 4)) if k % 4 == 3 else (heads_done, k - k // 4 + 1)))
                for t in range(TT):
                    name = ("pT", t, h)
                    n = t + 1
                    dve.wait_ge(*full(name))
                    dve.tensor_copy(probsT[h % 2][:, :, 0:n, P * t:P * t + P],
                                    bank(name)[:, 0:SEQ * n].rearrange("p (j s t) -> p j s t", j=2, s=n)
                                    ).then_inc(reader(name), 1)

            def post_norm(product, stage, n_gain):
                dve.wait_ge(gain_in, 16 * n_gain)
                for t in range(TT):
                    dve.wait_ge(rstd_ready, STATI[(stage, t)] + 1)
                    for half in range(2):
                        c = slice(512 * half, 512 * half + 512)
                        dve.scalar_tensor_tensor(out=xn[:, t, c], in0=acc((product, 2 * t + half))[:, :],
                                                 scalar=stat((stage, t)), in1=post_gain[:, c], op0=ALU.mult,
                                                 op1=ALU.mult).then_inc(acc_read, 1)
                    dve.wait_ge(*acc_drained((product, 2 * t + 1)))
                    dve.tensor_tensor(x[:, t, :], x[:, t, :], xn[:, t, :], ALU.add).then_inc(x_done, 1)
                    dve.wait_ge(x_done, 2 * (n_gain - 1) + t + 1)

            split_done = [0]

            def low_parts(upto):
                while split_done[0] < min(upto + 1, len(split_units)):
                    i = split_done[0]
                    dve.wait_ge(high_ready, i + 1)
                    dve.tensor_tensor(split_slot(i)[:, 1, :], weights(split_units[i], 2048),
                                      split_slot(i)[:, 0, :], ALU.subtract).then_inc(low_ready, 1)
                    split_done[0] += 1

            def low_mix(product, c, src):
                dve.wait_ge(*high_there(("mix", product, c)))
                return dve.tensor_tensor(act_s[:, 1, 2 * c:2 * c + 2, :], src, act_s[:, 0, 2 * c:2 * c + 2, :], ALU.subtract)

            low_parts(SPLIT[("out", MIX_ORDER[0])])
            for c in MIX_ORDER:
                low_mix("out", c, mixT[:, 2 * c:2 * c + 2, :] if c >= 2 else
                        acc(("o", c))[:, :].rearrange("p (c t) -> p c t", c=2)
                        ).then_inc(acts_low if c >= 2 else acc_read, 1)
            low_parts(SPLIT[("mq", 1)])
            post_norm("out", "out_post", 1)
            scale_rows("mem", lambda t: x[:, t, :])
            low_parts(SPLIT[("mq", 2)])
            drain_norm("mem")
            low_parts(SPLIT[("wo", 0)])
            for t in range(TT):
                for hp in range(2):
                    dve.wait_ge(*full(("ms", t, hp)))
                    dve.tensor_reduce(msoft[:, t, 0, 2 * hp:2 * hp + 2],
                                      bank(("ms", t, hp))[:, :].rearrange("p (h s) -> p h s", h=2), AX, ALU.max,
                                      negate=True).then_inc(neg_max, 1)
            for t in range(TT):
                for hp in range(2):
                    dve.wait_ge(*drained(("ms", t, hp)))
                    den = msoft[:, t, 1, 2 * hp:2 * hp + 2]
                    link(dve.reciprocal(den, den))
                    dve.tensor_tensor(mprobs[t][:, 2 * hp:2 * hp + 2, :], mprobs[t][:, 2 * hp:2 * hp + 2, :],
                                      den.unsqueeze(2).broadcast_to([P, 2, SEQ]), ALU.mult).then_inc(weighed, 1)
            low_parts(SPLIT[("wo", 2)])
            for t in range(TT):
                for hp in range(2):
                    name = ("mpT", t, hp)
                    dve.wait_ge(*full(name))
                    dve.tensor_copy(mprobsT[:, 2 * hp:2 * hp + 2, :, P * t:P * t + P],
                                    bank(name)[:, :].rearrange("p (h s t) -> p h s t", h=2, s=TT)
                                    ).then_inc(reader(name), 1)
            for c in range(4):
                low_mix("wo", c, bank(("mo", c))[:, :].rearrange("p (c t) -> p c t", c=2)).then_inc(reader(("mo", c)), 1)
            low_parts(SPLIT[("up", 1)])
            post_norm("wo", "wo_post", 2)
            scale_rows("ffn", lambda t: x[:, t, :])
            low_parts(SPLIT[("up", 2)])
            drain_norm("ffn")
            cw = parc("conv_w").rearrange("p (j g w) -> p j g w", g=2, w=3)

            def taps(j):
                name = ("up", j)
                dve.wait_ge(tap2, j + 1)
                for s in (1, 2):
                    for g in range(2):
                        c = conv[j % 3][:, g, s:SEQ]
                        ins = dve.scalar_tensor_tensor(out=c, in0=bank(name)[:, SEQ * g:SEQ * g + SEQ - s],
                                                       scalar=cw[:, j, g, 2 - s:3 - s], in1=c, op0=ALU.mult, op1=ALU.add)
                    if s == 1:
                        link(ins)
                ins.then_inc(reader(name), 1)

            def gate_times_value(j):
                dve.wait_ge(gate_act, j + 1)
                if j >= 4:
                    dve.wait_ge(unit_spent, SPENT[("down", (j - 4) // 2)])
                dve.tensor_tensor(prod_s[j % 4][:, 0, :], act_g[j % 2], conv[j % 3][:, 1, :], ALU.mult)
                link(dve.tensor_tensor(prod[j % 2], act_g[j % 2], conv[j % 3][:, 1, :], ALU.mult))
                dve.tensor_tensor(prod_s[j % 4][:, 1, :], prod[j % 2], prod_s[j % 4][:, 0, :], ALU.subtract
                                  ).then_inc(gated, 1)

            for j in range(FFN_PAIRS + 1):
                if j < FFN_PAIRS:
                    low_parts(SPLIT[("up", j)] + 2)
                    taps(j)
                    low_parts(split_before(("up", j + 1)) + 2)
                if j >= 1:
                    gate_times_value(j - 1)
            post_norm("down", "down_post", 3)
            scale_rows("mix2", lambda t: x[:, t, :])
            drain_norm("mix2")
            link(dve.memset(y_pad[:, :, 0:CONV_TAPS - 1], 0.0))
            name = ("ug0",)
            dve.wait_ge(*full(name))
            dve.wait_ge(*drained(("ug1",)))
            dve.tensor_tensor(y_pad[:, :, CONV_TAPS - 1:CONV_TAPS - 1 + SEQ], bank(name)[:, :].rearrange("p (c t) -> p c t", c=2),
                              gate_s, ALU.mult).then_inc(reader(name), 1)
            gconv = parc("gdn_conv").rearrange("p (c w) -> p c w", w=4)

            def gdn_taps(i):
                name = ("qkv", i)
                dve.wait_ge(tap3, i + 1)
                for s in (1, 2, 3):
                    for c in range(2):
                        o = qkv[:, 2 * i + c, s:SEQ]
                        ins = dve.scalar_tensor_tensor(out=o, in0=bank(name)[:, SEQ * c:SEQ * c + SEQ - s],
                                                       scalar=gconv[:, 2 * i + c, 3 - s:4 - s], in1=o, op0=ALU.mult,
                                                       op1=ALU.add)
                    if s < 3:
                        link(ins)
                ins.then_inc(reader(name), 1)

            def across_norm(tag):
                raw, sq, _, _, gain = chunk2[tag]
                dve.wait_ge(*drained(("across", tag)))
                link(dve.reciprocal(sq, sq))
                if gain is None:
                    ins = dve.tensor_tensor(raw, raw, sq, ALU.mult)
                else:
                    ins = dve.scalar_tensor_tensor(out=raw, in0=raw, scalar=parc(gain), in1=sq, op0=ALU.mult, op1=ALU.mult)
                ins.then_inc(across_done, 1)

            gdn_taps(0)
            u_row, ln_row = row_tmp[0:4, 0, :], row_tmp[0:4, 1, :]
            dec, last_less = gate_rows[0:4, 3, :], gate_rows[0:4, 2, :]
            dve.wait_ge(softplus_ln, 1)
            link(dve.scalar_tensor_tensor(out=ln_row, in0=u_row, scalar=0.0, in1=ln_row, op0=ALU.max, op1=ALU.add))
            link(dve.tensor_scalar(ln_row, ln_row, a_rate[0:4, :], -1.0, ALU.mult, ALU.mult))
            link(dve.tensor_tensor_scan(dec, conc("chunk_keep")[0:4, :], ln_row, 0.0, ALU.mult, ALU.add))

            def by_chunk(v):
                return v.rearrange("p (n i) -> p n i", n=NCHUNK)

            dve.tensor_tensor(by_chunk(last_less), by_chunk(dec)[:, :, CHUNK - 1:CHUNK].broadcast_to([4, NCHUNK, CHUNK]),
                              by_chunk(dec), ALU.subtract).then_inc(decay_sum, 1)
            across_norm("dq")
            across_norm("dk")
            dve.wait_ge(*drained(("widx",)))
            for t in range(TT):
                for par in range(2):
                    dve.wait_ge(*drained(("il", t, par)))
                s = idx_score[t]
                link(dve.tensor_scalar(s, relu_l[t][0][:, 0, :], w_idx[:, t, 0:1], None, ALU.mult))
                for h in range(1, 4):
                    ins = dve.scalar_tensor_tensor(out=s, in0=relu_l[t][h % 2][:, h // 2, :], scalar=w_idx[:, t, h:h + 1],
                                                   in1=s, op0=ALU.mult, op1=ALU.add)
                    if h < 3:
                        link(ins)
                ins.then_inc(idx_sum, 1)

            def topk_round(t, last):
                link(dve.max(top8[:, t, :], idx_score[t]))
                ins = dve.match_replace(out=idx_score[t], in_to_replace=top8[:, t, :], in_values=idx_score[t],
                                        imm_value=PICKED)
                if last:
                    ins.then_inc(picked, 1)
                else:
                    link(ins)

            taps_left = list(range(1, 6))
            for t in range(TT):
                dve.wait_ge(idx_causal, t + 1)
                for r in range(TOPK_ROUNDS):
                    topk_round(t, r == TOPK_ROUNDS - 1)
                    if r % 3 == 2 and taps_left:
                        gdn_taps(taps_left.pop(0))
            while taps_left:
                gdn_taps(taps_left.pop(0))
            dve.wait_ge(decay_exp, 1)
            dve.tensor_tensor(gate_rows[0:4, 1, :], gate_rows[0:4, 0, :], u_row, ALU.mult).then_inc(rows_ready, 1)
            dw = parc("conv_dw").rearrange("p (c w) -> p c w", c=2)
            taps31 = [0]

            def conv_tap():
                w = taps31[0]
                if w == CONV_TAPS:
                    return
                taps31[0] += 1
                for c in range(2):
                    src = y_pad[:, c, w:w + SEQ]
                    if w == 0:
                        ins = dve.tensor_scalar(conv_y[:, c, :], src, dw[:, c, 0:1], parc("dw_b")[:, c:c + 1], ALU.mult, ALU.add)
                    else:
                        ins = dve.scalar_tensor_tensor(out=conv_y[:, c, :], in0=src, scalar=dw[:, c, w:w + 1],
                                                       in1=conv_y[:, c, :], op0=ALU.mult, op1=ALU.add)
                if w == CONV_TAPS - 1:
                    ins.then_inc(conv_out, 1)
                    dve.wait_ge(conv_out, 1)
                else:
                    link(ins)

            for _ in range(TAPS_EARLY):
                conv_tap()
            drain_norm("mem2")
            for _ in range(CONV_TAPS - TAPS_EARLY):
                conv_tap()

            def row_inverse(tag):
                roots = ROWS[tag][5]
                dve.wait_ge(*drained(("row_sum", tag)))
                dve.reciprocal(roots, roots).then_inc(row_roots[tag], 1)

            row_inverse("l")
            for t in range(TT):
                dve.wait_ge(dmask_ready, t + 1)
                for par in range(2):
                    name = ("dl", t, par)
                    n = P * (t + 1)
                    v = dprobs[t][:, par::2, :]
                    dve.wait_ge(*full(name))
                    dve.tensor_tensor(v, bank(name)[:, 0:2 * n].rearrange("p (j s) -> p j s", j=2),
                                      dmask[t].unsqueeze(1).broadcast_to([P, 2, n]), ALU.add).then_inc(reader(name), 1)
                    dve.wait_ge(*drained(name))
                    dve.tensor_reduce(dsoft[:, t, 0, par::2], v, AX, ALU.max, negate=True).then_inc(d_max, 1)
            for t in range(TT):
                dve.wait_ge(d_exp, 2 * t + 2)
                den = dsoft[:, t, 1, :]
                link(dve.reciprocal(den, den))
                dve.tensor_tensor(dprobs[t], dprobs[t], den.unsqueeze(2).broadcast_to([P, DSA_HEADS, P * (t + 1)]),
                                  ALU.mult).then_inc(d_weighed, 1)
            for i in range(4):
                name = ("row_all", "l", i)
                dve.wait_ge(*full(name))
                dve.tensor_tensor(qkv[:, 2 * i:2 * i + 2, :], qkv[:, 2 * i:2 * i + 2, :],
                                  bank(name)[:, :].rearrange("p (c t) -> p c t", c=2), ALU.mult).then_inc(reader(name), 1)
            dve.wait_ge(*full(("cols",)))
            dve.tensor_copy(gate_cols, bank(("cols",))[:, 0:32].rearrange("p (t k h) -> p t k h", t=TT, k=4)
                            ).then_inc(reader(("cols",)), 1)
            dve.wait_ge(*drained(("cols",)))
            for i in range(2):
                name = ("dr", i)
                dve.wait_ge(*full(name))
                for t in range(TT):
                    for j in range(2):
                        h = 2 * i + j
                        ins = dve.tensor_scalar(Y[t][:, h, :], bank(name)[:, SEQ * j + P * t:SEQ * j + P * t + P],
                                                gate_cols[:, t, 3, h:h + 1], 0.0, ALU.subtract, ALU.min)
                ins.then_inc(gamma_diff, 1)
            qT2, kT2, vT2 = qkv[:, 0:4, :], qkv[:, 4:8, :], qkv[:, 8:12, :]
            dve.wait_ge(*drained(("row_all", "l", 3)))
            dve.wait_ge(*drained(("row_all", "l", 2)))
            for i in range(2):
                name = ("br", i)
                dve.wait_ge(*full(name))
                dve.tensor_tensor(kbT[:, 2 * i:2 * i + 2, :], bank(name)[:, :].rearrange("p (c t) -> p c t", c=2),
                                  kT2[:, 2 * i:2 * i + 2, :], ALU.mult).then_inc(reader(name), 1)
            dve.wait_ge(*drained(("dr", 1)))
            dve.tensor_tensor(qeT, qT2, exp_decay, ALU.mult).then_inc(qe_ready, 1)
            row_inverse("xk")

            def heads(name):
                return bank(name)[:, :].rearrange("p (h d) -> p h d", h=GDN_HEADS)

            def col(t, kind):
                return gate_cols[:, t, kind, :].unsqueeze(2).broadcast_to([P, GDN_HEADS, P])

            for t in range(TT):
                name = ("kA", t)
                dve.wait_ge(*full(name))
                dve.tensor_tensor(bke[t], heads(name), col(t, 1), ALU.mult)
                dve.tensor_tensor(kdec[t], heads(name), col(t, 2), ALU.mult).then_inc(reader(name), 1)
            for t in range(TT):
                name = ("vA", t)
                dve.wait_ge(*full(name))
                dve.tensor_tensor(bv[t], heads(name), col(t, 0), ALU.mult).then_inc(reader(name), 1)
            for kind, dst, decay in (("kk", AT, inv), ("qk", qkT, Y)):
                for t in range(TT):
                    name = (kind, t)
                    dve.wait_ge(*full(name))
                    dve.wait_ge(gamma_ready, t + 1)
                    dve.tensor_tensor(dst[t], heads(name), decay[t], ALU.mult).then_inc(reader(name), 1)

            for t in range(TT):
                dve.wait_ge(*drained(("qk", t)))
            for t in range(TT):
                for par in range(2):
                    name = ("dpT", t, par)
                    n = t + 1
                    dve.wait_ge(*full(name))
                    dve.tensor_copy(dprobsT[par][:, :, 0:n, P * t:P * t + P],
                                    bank(name)[:, 0:SEQ * n].rearrange("p (j s t) -> p j s t", j=2, s=n)
                                    ).then_inc(reader(name), 1)
            for i in range(2):
                name = ("row_all", "xk", i)
                dve.wait_ge(*full(name))
                dve.scalar_tensor_tensor(out=xkT[:, 2 * i:2 * i + 2, :], in0=xkT[:, 2 * i:2 * i + 2, :],
                                         scalar=parc("xk_norm"), in1=bank(name)[:, :].rearrange("p (c t) -> p c t", c=2),
                                         op0=ALU.mult, op1=ALU.mult).then_inc(reader(name), 1)
            eye = ident.unsqueeze(1).broadcast_to([P, GDN_HEADS, P])
            for t in range(TT):
                dve.wait_ge(level_masked, t + 1)
                dve.scalar_tensor_tensor(out=invT[t], in0=AT_level[0][t], scalar=-1.0, in1=eye, op0=ALU.mult,
                                         op1=ALU.add).then_inc(first_invT, 1)
                name = ("y", 0, t)
                dve.wait_ge(*full(name))
                dve.scalar_tensor_tensor(out=inv[t], in0=heads(name), scalar=-1.0, in1=eye, op0=ALU.mult,
                                         op1=ALU.add).then_inc(reader(name), 1)
            for level in range(1, LEVELS):
                for kind, dst in (("d", inv), ("dT", invT)):
                    if (kind, level) == ("d", LEVELS - 1):
                        continue
                    for t in range(TT):
                        name = (kind, level, t)
                        dve.wait_ge(*full(name))
                        dve.scalar_tensor_tensor(out=dst[t], in0=heads(name), scalar=-1.0, in1=dst[t],
                                                 op0=ALU.mult, op1=ALU.add).then_inc(reader(name), 1)
            name = ("ln_mean",)
            dve.wait_ge(*full(name))
            dve.scalar_tensor_tensor(out=conv_y[:, 0, :], in0=bank(name)[:, 0:SEQ], scalar=-1.0 / SEQ, in1=conv_y[:, 0, :],
                                     op0=ALU.mult, op1=ALU.add)
            dve.scalar_tensor_tensor(out=conv_y[:, 1, :], in0=bank(name)[:, 0:SEQ], scalar=-1.0 / SEQ, in1=conv_y[:, 1, :],
                                     op0=ALU.mult, op1=ALU.add).then_inc(reader(name), 1)
            dve.wait_ge(*drained(("ln_var",)))
            link(dve.reciprocal(conv_sq[:, 0, :], conv_sq[:, 0, :]))
            dve.tensor_tensor(conv_y, conv_y, conv_sq[:, 0:1, :].broadcast_to([P, 2, SEQ]), ALU.mult).then_inc(conv_norm, 1)
            for n in range(NCHUNK):
                t, r = n // 2, slice(CHUNK * (n % 2), CHUNK * (n % 2) + CHUNK)
                if n == 0:
                    dve.wait_ge(*drained(("gu", 0)))
                    dve.tensor_copy(v_new[r, :, :], u_n[t][r, :, :]).then_inc(v_news, 1)
                else:
                    name = ("ws", n)
                    dve.wait_ge(*full(name))
                    dve.wait_ge(*drained(("gu", t)))
                    dve.scalar_tensor_tensor(out=v_new[r, :, :], in0=heads(name)[r, :, :], scalar=-1.0, in1=u_n[t][r, :, :],
                                             op0=ALU.mult, op1=ALU.add).then_inc(reader(name), 1)
                if n < NCHUNK - 1:
                    name = ("kv", n)
                    dve.wait_ge(*full(name))
                    if n == 0:
                        dve.tensor_copy(state, heads(name)).then_inc(reader(name), 1)
                    else:
                        for h in range(GDN_HEADS):
                            at = CHUNK * n + CHUNK - 1
                            ins = dve.scalar_tensor_tensor(out=state[:, h, :], in0=state[:, h, :],
                                                           scalar=exp_decay[:, h, at:at + 1], in1=heads(name)[:, h, :],
                                                           op0=ALU.mult, op1=ALU.add)
                        ins.then_inc(reader(name), 1)
            low_parts(SPLIT[("out2", MIX_ORDER[0])])
            dve.wait_ge(row_squares, 3)
            dve.wait_ge(*drained(("go", NCHUNK - 1)))
            dve.scalar_tensor_tensor(out=zT, in0=oT, scalar=parc("gdn_norm"), in1=zT, op0=ALU.mult, op1=ALU.mult
                                     ).then_inc(scaled_o, 1)
            row_inverse("o")
            low_parts(SPLIT[("out2", MIX_ORDER[1])])
            for c in MIX_ORDER[:2]:
                low_mix("out2", c, mixT[:, 2 * c:2 * c + 2, :]).then_inc(acts_low, 1)
            dve.wait_ge(scaled_o, 1)
            for i in range(2):
                name = ("row_all", "o", i)
                dve.wait_ge(*full(name))
                dve.tensor_tensor(mixT[:, 2 * i:2 * i + 2, :], zT[:, 2 * i:2 * i + 2, :],
                                  bank(name)[:, :].rearrange("p (c t) -> p c t", c=2), ALU.mult).then_inc(reader(name), 1)
            for c in MIX_ORDER[2:]:
                low_mix("out2", c, mixT[:, 2 * c:2 * c + 2, :]).then_inc(acts_low, 1)
            low_parts(SPLIT[("xq", 1)])

            def add_product(product):
                for t in range(TT):
                    for half in range(2):
                        f = (product, 2 * t + half)
                        c = slice(512 * half, 512 * half + 512)
                        dve.wait_ge(*acc_filled(f))
                        dve.tensor_tensor(x[:, t, c], acc(f)[:, :], x[:, t, c], ALU.add).then_inc(acc_read, 1)

            add_product("out2")
            scale_rows("cross", lambda t: x[:, t, :])
            drain_norm("cross")
            low_parts(SPLIT[("xwo", 0)])
            dve.wait_ge(*drained(("xq_sums",)))
            link(dve.reciprocal(xq_root, xq_root))
            for t in range(TT):
                for hp in range(2):
                    name = ("xs", t, hp)
                    dve.wait_ge(*full(name))
                    high = xsoft[:, t, 0, 2 * hp:2 * hp + 2]
                    link(dve.tensor_reduce(high, bank(name)[:, :].rearrange("p (h s) -> p h s", h=2),
                                           AX, ALU.max, negate=True))
                    dve.tensor_tensor(high, high, xq_root[:, t, 2 * hp:2 * hp + 2], ALU.mult).then_inc(x_max, 1)
            for t in range(TT):
                for hp in range(2):
                    dve.wait_ge(*drained(("xs", t, hp)))
                    den = xsoft[:, t, 1, 2 * hp:2 * hp + 2]
                    link(dve.reciprocal(den, den))
                    dve.tensor_tensor(xprobs[t][:, 2 * hp:2 * hp + 2, :], xprobs[t][:, 2 * hp:2 * hp + 2, :],
                                      den.unsqueeze(2).broadcast_to([P, 2, SEQ]), ALU.mult).then_inc(x_weighed, 1)
            for t in range(TT):
                for hp in range(2):
                    name = ("xpT", t, hp)
                    dve.wait_ge(*full(name))
                    dve.tensor_copy(xprobsT[:, 2 * hp:2 * hp + 2, :, P * t:P * t + P],
                                    bank(name)[:, :].rearrange("p (h s t) -> p h s t", h=2, s=TT)).then_inc(reader(name), 1)
            low_parts(SPLIT[("m1", 0)])
            for c in range(2):
                low_mix("xwo", c, bank(("xo", c))[:, :].rearrange("p (c t) -> p c t", c=2)).then_inc(reader(("xo", c)), 1)
            low_parts(SPLIT[("m1", 1)])
            add_product("xwo")
            scale_rows("mlp", lambda t: x[:, t, :])
            drain_norm("mlp")
            low_parts(SPLIT[("m1", 2)])
            for j in range(MLP_UNITS):
                low_parts(SPLIT[("m1", j)] + 2)
                dve.wait_ge(*drained(("m1", j)))
                link(dve.tensor_tensor(relu2[j % 2], relu_h[j % 2], relu_h[j % 2], ALU.mult))
                dve.wait_ge(relu_high, j + 1)
                dve.tensor_tensor(relu2_s[j % 3][:, 1], relu2[j % 2], relu2_s[j % 3][:, 0], ALU.subtract).then_inc(relu_sq, 1)
                low_parts(split_before(("m1", j + 1)) + 2)
            low_parts(len(split_units) - 1)
            add_product("m2")

        @block.tensor
        def _(pe):
            def open_tile(name):
                i = TILE[name]
                if i >= NB:
                    pe.wait_ge(tile_read[i % NB], i // NB)
                return banks[i % NB]

            def norm_T(stage, first):
                for t in range(TT):
                    pe.wait_ge(normed, first + t + 1)
                    for half in range(2):
                        ps = open_tile(("normT", stage, t, half))
                        for k in range(4):
                            c = P * (4 * half + k)
                            ins = pe.transpose(ps[:, P * k:P * k + P], xn[:, t, c:c + P], ident)
                        ins.then_inc(tile_full, 1)

            def wide(out, w, lo, n=P, src=None):
                for k in range(KD):
                    ins = pe.matmul(out, w[:, k, lo:lo + n], (hT if src is None else src)[:, k, :], start=(k == 0), stop=(k == KD - 1))
                return ins

            def tall(out, w, lo, n, t):
                for k in range(KD):
                    ins = pe.matmul(out, hT[:, k, P * t:P * t + P], w[:, k, lo:lo + n], start=(k == 0), stop=(k == KD - 1))
                return ins

            def pair_of_chunks(name, unit):
                ps = open_tile(name)
                pe.wait_ge(*loaded(unit))
                w = weights(unit, KD, 256)
                wide(ps[:, 0:SEQ], w, 0)
                wide(ps[:, SEQ:512], w, P).then_inc(tile_full, 1)

            def split_matmul(out, lhs, rhs, start, stop):
                for n, (p, q) in enumerate(((0, 0), (0, 1), (1, 0))):
                    ins = pe.matmul(out, lhs(p), rhs(q), start=(start and n == 0), stop=(stop and n == 2))
                return ins

            def split_pair(name):
                ps = open_tile(name)
                pe.wait_ge(low_ready, SPLIT[name] + 1)
                w = split_weights(name, KD, 256)
                for c in range(2):
                    for k in range(KD):
                        ins = split_matmul(ps[:, SEQ * c:SEQ * c + SEQ], lambda p: w[:, p, k, P * c:P * c + P],
                                           lambda p: act_s[:, p, k, :], k == 0, k == KD - 1)
                ins.then_inc(tile_full, 1)

            def split_product_unit(unit, first, last, lhs):
                pe.wait_ge(low_ready, SPLIT[unit] + 1)
                w = split_weights(unit, 2, D)
                for kk in range(2):
                    for t in range(TT):
                        for half in range(2):
                            ins = split_matmul(acc((unit[0], 2 * t + half))[:, :], lambda p: lhs(p, kk, t),
                                               lambda p: w[:, p, kk, 512 * half:512 * half + 512], first and kk == 0,
                                               last and kk == 1)
                            if last and kk == 1:
                                ins.then_inc(acc_full, 1)
                if not last:
                    ins.then_inc(unit_spent, 1)

            def product_unit(product, unit, first, last, lhs, nk=2):
                pe.wait_ge(*loaded(unit))
                w = weights(unit, nk, 2048 // nk)
                for kk in range(nk):
                    for t in range(TT):
                        for half in range(2):
                            ins = pe.matmul(acc((product, 2 * t + half))[:, :], lhs(kk, t),
                                            w[:, kk, 512 * half:512 * half + 512], start=(first and kk == 0),
                                            stop=(last and kk == nk - 1))
                            if last and kk == nk - 1:
                                ins.then_inc(acc_full, 1)
                if not last:
                    ins.then_inc(unit_spent, 1)

            def split_product(name, order):
                open_product(name)
                for n, c in enumerate(order):
                    pe.wait_ge(*low_there(("mix", name, c)))
                    split_product_unit((name, c), n == 0, n == len(order) - 1,
                                       lambda p, kk, t: act_s[:, p, 2 * c + kk, P * t:P * t + P])

            def rows_split(stage):
                pe.wait_ge(*low_there(("rows", stage, TT - 1, 1)))

            def open_product(product):
                if FILL[(product, 0)]:
                    pe.wait_ge(acc_read, FILL[(product, 0)])

            def product(name, unit, src):
                open_product(name)
                for i in range(4):
                    product_unit(name, (unit, i), i == 0, i == 3, lambda kk, t: src[:, 2 * i + kk, P * t:P * t + P])

            pe.wait_ge(first_consts_in, 16)
            norm_T("mix", 0)
            for stage_tile in (("normT", "mix", t, half) for t in range(TT) for half in range(2)):
                pe.wait_ge(*drained(stage_tile))
            pair_of_chunks(("q0",), "q0")
            pair_of_chunks(("q1",), "q1")
            pe.wait_ge(params_in, 16)
            pe.wait_ge(hots_in, 16)
            relb = parc("relb")[0:REL_BUCKETS + 1, :]
            ps = open_tile(("bias_row",))
            pe.matmul(ps[0:HEADS, 0:384], relb, hots[0:REL_BUCKETS + 1, P:DIST_COLS], start=True, stop=True).then_inc(tile_full, 1)
            ps = open_tile(("bias_cmp",))
            for t in range(TT):
                for c in range(NCMP):
                    lo = SEQ - 1 + P * t - (CMP_STRIDE * c + CMP_LEN - 1)
                    at = (t * NCMP + c) * HEADS
                    ins = pe.matmul(ps[:, at:at + HEADS], hots[0:REL_BUCKETS + 1, lo:lo + P], relb, start=True, stop=True)
            ins.then_inc(tile_full, 1)
            pair_of_chunks(("kcvc",), "kcvc")
            for u in ("ksvs", "kwvw"):
                ps = open_tile((u,))
                pe.wait_ge(*loaded(u))
                w = weights(u, KD, 256)
                wide(ps[:, 0:SEQ], w, 0)
                for t in range(TT):
                    ins = tall(ps[:, SEQ + P * t:SEQ + P * t + P], w, P, P, t)
                ins.then_inc(tile_full, 1)
            ps = open_tile(("gates",))
            pe.wait_ge(*loaded("gates"))
            for t in range(TT):
                ins = tall(ps[:, 24 * t:24 * t + 24], weights("gates", KD, 24), 0, 24, t)
            ins.then_inc(tile_full, 1)
            pair_of_chunks(("pool",), "pool")
            pair_of_chunks(("u",), "u")
            ps = open_tile(("v",))
            pe.wait_ge(*loaded("v"))
            for t in range(TT):
                ins = tall(ps[:, SEQ * t:SEQ * t + SEQ], weights("v", KD, 256), 0, 256, t)
            ins.then_inc(tile_full, 1)

            ps = open_tile(("cmp_h",))
            pe.wait_ge(blocks_ready, 1)
            for kv, u in enumerate(("cmp_w1k", "cmp_w1v")):
                pe.wait_ge(*loaded(u))
                w = weights(u, CMP_PAIRS, P)
                for j in range(CMP_PAIRS):
                    ins = pe.matmul(ps[:, 32 * kv:32 * kv + 30], w[:, j, :],
                                    blocks[:, kv, j, :, :].rearrange("p g c -> p (g c)"),
                                    start=(j == 0), stop=(j == CMP_PAIRS - 1))
            ins.then_inc(tile_full, 1)
            ps = open_tile(("cmp_kv",))
            pe.wait_ge(*drained(("cmp_h",)))
            w2 = parc("cmp_w2").rearrange("p (v d) -> p v d", v=2)
            for g in range(GROUPS):
                pe.matmul(ps[DK * g:DK * g + DK, 0:NCMP], w2[:, 0, :], cmp_hT[:, 0, NCMP * g:NCMP * g + NCMP],
                          start=True, stop=True)
            for j in range(4):
                for g in range(GROUPS):
                    ins = pe.matmul(ps[32 * j:32 * j + NCMP, 64 + DK * g:64 + DK * g + DK],
                                    cmp_hT[:, 1, NCMP * g:NCMP * g + NCMP], w2[:, 1, :], start=True, stop=True)
            ins.then_inc(tile_full, 1)

            def head_rows(h):
                return slice(DK * (h // HG), DK * (h // HG) + DK)

            for u in ("q0", "q1", "ksvs", "kwvw", "cmp_kv"):
                pe.wait_ge(*drained((u,)))
            for t in range(TT):
                for g in range(GROUPS):
                    ps = open_tile(("cmp_s", t, g))
                    for i in range(HG):
                        ins = pe.matmul(ps[:, NCMP * i:NCMP * i + NCMP], qT[head_rows(HG * g), i, P * t:P * t + P],
                                        cmp_kT[head_rows(HG * g), :], start=True, stop=True)
                    ins.then_inc(tile_full, 1)
                for h in range(HEADS):
                    ps = open_tile(("s", t, h))
                    n = P * (t + 1)
                    pe.matmul(ps[:, 0:2 * n].rearrange("p (j s) -> p j s", j=2), qT[head_rows(h), h % HG, P * t:P * t + P],
                              keysT[head_rows(h), :, 0:n], start=True, stop=True).then_inc(tile_full, 1)
            ps = open_tile(("pool_out",))
            pe.wait_ge(pooled, 1)
            pw = parc("pool_w").rearrange("p (c d) -> p c d", c=2)
            for g in range(4):
                r = slice(64 * (g % 2), 64 * (g % 2) + 64)
                ins = pe.matmul(ps[r, SEQ * (g // 2):SEQ * (g // 2) + SEQ], pw[r, g // 2, :], pool_d[r, g // 2, :],
                                start=True, stop=True)
            ins.then_inc(tile_full, 1)
            ps = open_tile(("sgu_out",))
            pe.wait_ge(sgu_normed, TT)
            pe.wait_ge(masked_ws, 1)
            wsT = parc("sgu_wT").rearrange("p (h t) -> p h t", h=4)
            for h in range(4):
                for t in range(TT):
                    at = SEQ * (h // 2) + P * t
                    ins = pe.matmul(ps[64 * (h % 2):64 * (h % 2) + 64, at:at + P], v_n[:, t, 64 * h:64 * h + 64],
                                    wsT[:, h, :], start=True, stop=True)
            ins.then_inc(tile_full, 1)

            norm_T("memkv", 2)
            for t in range(TT):
                for half in range(2):
                    pe.wait_ge(*drained(("normT", "memkv", t, half)))
            for c in range(4):
                pair_of_chunks(("mk", c), ("mk", c))
            product("mv", "mv", hT)

            for t in range(TT):
                pe.wait_ge(weighed, 1 + t * (HEADS + 1))
                ps = open_tile(("cmp_pT", t))
                for g in range(GROUPS):
                    ins = pe.transpose(ps[:, P * g:P * g + P],
                                       cmp_p[:, t, HG * g:HG * g + HG, :].rearrange("p h c -> p (h c)"), ident)
                ins.then_inc(tile_full, 1)

            def probs_T(h):
                for t in range(TT):
                    pe.wait_ge(weighed, 1 + t * (HEADS + 1) + h + 1)
                    ps = open_tile(("pT", t, h))
                    for j in range(2):
                        for s in range(t + 1):
                            at = P * (j * (t + 1) + s)
                            ins = pe.transpose(ps[:, at:at + P], probs[t][h][:, j, P * s:P * s + P], ident)
                    ins.then_inc(tile_full, 1)

            def attend(h):
                g, c = h // HG, h // 2
                f = ("o", c // 2)
                if h % 4 == 0 and FILL[f] >= 4:
                    pe.wait_ge(acc_read, FILL[f] - 3)
                if h == 0:
                    for t in range(TT):
                        pe.wait_ge(*drained(("cmp_pT", t)))
                for t in range(TT):
                    pe.wait_ge(*drained(("pT", t, h)))
                o = acc(f)[DK * (h % 2):DK * (h % 2) + DK, SEQ * (c % 2):SEQ * (c % 2) + SEQ]
                pT = probsT[h % 2]
                for j in range(2):
                    pe.matmul(o, values[:, j, 0, DK * g:DK * g + DK], pT[:, j, 0, :], start=(j == 0), stop=False)
                    pe.matmul(o[:, P:SEQ], values[:, j, 1, DK * g:DK * g + DK], pT[:, j, 1, P:SEQ], start=False, stop=False)
                r = slice(32 * (h % HG), 32 * (h % HG) + NCMP)
                return pe.matmul(o, cmp_v[r, DK * g:DK * g + DK], cmp_pT[r, g, :], start=False, stop=True)

            for h in range(HEADS + 1):
                if h < HEADS:
                    probs_T(h)
                if h >= 1:
                    attend(h - 1).then_inc(acc_full if (h - 1) % 4 == 3 else heads_done, 1)
            split_product("out", MIX_ORDER)

            norm_T("mem", 4)
            rows_split("mem")
            for c in range(4):
                split_pair(("mq", c))
            for c in range(4):
                pe.wait_ge(*drained(("mk", c)))
                pe.wait_ge(*drained(("mq", c)))
            for t in range(TT):
                for hp in range(2):
                    ps = open_tile(("ms", t, hp))
                    for j in range(2):
                        h = 2 * hp + j
                        for dd in range(2):
                            ins = pe.matmul(ps[:, SEQ * j:SEQ * j + SEQ], qmT[:, 2 * h + dd, P * t:P * t + P],
                                            kmT[:, 2 * h + dd, :], start=(dd == 0), stop=(dd == 1))
                    ins.then_inc(tile_full, 1)
            for t in range(TT):
                for hp in range(2):
                    pe.wait_ge(weighed, TT * (HEADS + 1) + 2 * t + hp + 1)
                    ps = open_tile(("mpT", t, hp))
                    for j in range(2):
                        for s in range(TT):
                            at = P * (2 * j + s)
                            ins = pe.transpose(ps[:, at:at + P], mprobs[t][:, 2 * hp + j, P * s:P * s + P], ident)
                    ins.then_inc(tile_full, 1)
            pe.wait_ge(*acc_drained(("mv", 3)))
            for c in range(4):
                if c % 2 == 0:
                    for t in range(TT):
                        pe.wait_ge(*drained(("mpT", t, c // 2)))
                ps = open_tile(("mo", c))
                for dd in range(2):
                    for s in range(TT):
                        ins = pe.matmul(ps[:, SEQ * dd:SEQ * dd + SEQ], vm[:, s, SEQ * c + P * dd:SEQ * c + P * dd + P],
                                        mprobsT[:, c, s, :], start=(s == 0), stop=(s == TT - 1))
                ins.then_inc(tile_full, 1)
            split_product("wo", range(4))

            norm_T("ffn", 6)
            rows_split("ffn")
            open_product("down")
            for j in range(FFN_PAIRS + DOWN_LAG):
                if j < FFN_PAIRS:
                    split_pair(("up", j))
                if j >= DOWN_LAG and j % 2 == 1:
                    i = (j - DOWN_LAG) // 2
                    pe.wait_ge(gated, 2 * i + 2)
                    split_product_unit(("down", i), i == 0, i == FFN_PAIRS // 2 - 1,
                                       lambda p, kk, t: prod_s[(2 * i + kk) % 4][:, p, P * t:P * t + P])

            def drained_norm(stage):
                for t in range(TT):
                    for half in range(2):
                        pe.wait_ge(*drained(("normT", stage, t, half)))

            def across_sum(tag):
                pe.wait_ge(across_sq, ACROSS[tag] + 1)
                ps = open_tile(("across", tag))
                sq = chunk2[tag][1]
                if tag == "dk":
                    ins = pe.matmul(ps[:, 0:SEQ], conc("block_ones"), sq, start=True, stop=True)
                else:
                    ones = conc("block_ones") if tag == "dq" else conc("ones")
                    ins = pe.matmul(ps[:, :], ones, sq.rearrange("p c t -> p (c t)"), start=True, stop=True)
                ins.then_inc(tile_full, 1)

            norm_T("mix2", 8)
            drained_norm("mix2")
            pair_of_chunks(("cq",), "cq")
            ps = open_tile(("ck",))
            pe.wait_ge(*loaded("ck"))
            w = weights("ck", KD, 192)
            wide(ps[:, 0:SEQ], w, 0)
            wide(ps[0:DK, SEQ:512], w, P, DK)
            wide(ps[DK:P, SEQ:512], w, P, DK).then_inc(tile_full, 1)
            ps = open_tile(("ab",))
            pe.wait_ge(*loaded("ab"))
            w = weights("ab", KD, 12)
            wide(ps[0:4, 0:SEQ], w, 0, 4)
            wide(ps[0:4, SEQ:512], w, 4, 4).then_inc(tile_full, 1)
            ps = open_tile(("widx",))
            for t in range(TT):
                ins = tall(ps[:, 4 * t:4 * t + 4], w, 8, 4, t)
            ins.then_inc(tile_full, 1)
            pair_of_chunks(("ug0",), "ug0")
            pair_of_chunks(("ug1",), "ug1")
            w_qb = parc("w_qb").rearrange("p (k c) -> p k c", k=2)
            w_qi = parc("w_qi").rearrange("p (k c) -> p k c", k=2)
            pe.wait_ge(*drained(("cq",)))
            for name, w in ((("dq",), w_qb), (("dqi",), w_qi)):
                ps = open_tile(name)
                for c in range(2):
                    for k in range(2):
                        ins = pe.matmul(ps[:, SEQ * c:SEQ * c + SEQ], w[:, k, P * c:P * c + P], cqT[:, k, :],
                                        start=(k == 0), stop=(k == 1))
                ins.then_inc(tile_full, 1)
            ps = open_tile(("dk",))
            pe.wait_ge(*drained(("ck",)))
            w_kvb = parc("w_kvb")
            pe.matmul(ps[0:DK, 0:SEQ], w_kvb[:, 0:DK], ckvT, start=True, stop=True)
            pe.matmul(ps[DK:P, 0:SEQ], w_kvb[:, 0:DK], ckvT, start=True, stop=True)
            for t in range(TT):
                ins = pe.matmul(ps[:, SEQ + DK * t:SEQ + DK * t + DK], ckvT[:, P * t:P * t + P], w_kvb[:, DK:P],
                                start=True, stop=True)
            ins.then_inc(tile_full, 1)
            pair_of_chunks(("qkv", 0), ("qkv", 0))
            across_sum("dq")
            across_sum("dk")
            for t in range(TT):
                for par in range(2):
                    ps = open_tile(("il", t, par))
                    pe.wait_ge(*drained(("dqi",)))
                    n = P * (t + 1)
                    r = slice(DK * par, DK * par + DK)
                    for j in range(2):
                        ins = pe.matmul(ps[:, n * j:n * j + n], dqiT[r, j, P * t:P * t + P], kidxT[r, 0:n],
                                        start=True, stop=True)
                    ins.then_inc(tile_full, 1)
            for i in range(1, 6):
                pair_of_chunks(("qkv", i), ("qkv", i))
            for i in range(2):
                pair_of_chunks(("z", i), ("z", i))
            def pick_row(n, h):
                return ident[0:n, h:h + 1].broadcast_to([n, P])

            def row_sum(tag):
                sq, n = ROWS[tag][1:3]
                pe.wait_ge(row_squares, ("l", "xk", "o").index(tag) + 1)
                ps = open_tile(("row_sum", tag))
                for h in range(n):
                    lo = 8 - h
                    ins = pe.matmul(ps[0:n, 0:SEQ], conc("pick_col")[:, lo:lo + n], sq[:, h, :], start=(h == 0), stop=(h == n - 1))
                ins.then_inc(tile_full, 1)

            def row_all(tag, i):
                n, roots = ROWS[tag][2], ROWS[tag][5]
                pe.wait_ge(row_roots[tag], 1)
                ps = open_tile(("row_all", tag, i))
                for j in range(2):
                    ins = pe.matmul(ps[:, SEQ * j:SEQ * j + SEQ], pick_row(n, 2 * i + j), roots, start=True, stop=True)
                ins.then_inc(tile_full, 1)

            norm_T("mem2", 10)
            drained_norm("mem2")
            pair_of_chunks(("xk", 0), ("xk", 0))
            row_sum("l")
            pe.wait_ge(across_done, ACROSS["dk"] + 1)
            for t in range(TT):
                for par in range(2):
                    ps = open_tile(("dl", t, par))
                    n = P * (t + 1)
                    r = slice(DK * par, DK * par + DK)
                    for j in range(2):
                        ins = pe.matmul(ps[:, n * j:n * j + n], dqT[r, j, P * t:P * t + P], dkT[r, 0:n],
                                        start=True, stop=True)
                    ins.then_inc(tile_full, 1)
            pair_of_chunks(("xk", 1), ("xk", 1))
            for i in range(4):
                row_all("l", i)
            pe.wait_ge(rows_ready, 1)
            ps = open_tile(("cols",))
            for t in range(TT):
                for kind in range(4):
                    at = 16 * t + 4 * kind
                    ins = pe.transpose(ps[:, at:at + 4], gate_rows[0:4, kind, P * t:P * t + P], ident[0:4, 0:4])
            ins.then_inc(tile_full, 1)
            for tag, kind in (("dr", 3), ("br", 0)):
                for i in range(2):
                    ps = open_tile((tag, i))
                    for j in range(2):
                        ins = pe.matmul(ps[:, SEQ * j:SEQ * j + SEQ], pick_row(4, 2 * i + j), gate_rows[0:4, kind, :],
                                        start=True, stop=True)
                    ins.then_inc(tile_full, 1)
            row_sum("xk")
            qT2, kT2, vT2 = qkv[:, 0:4, :], qkv[:, 4:8, :], qkv[:, 8:12, :]
            for i in range(4):
                pe.wait_ge(*drained(("row_all", "l", i)))
            for tag, src in (("kA", kT2), ("vA", vT2)):
                for t in range(TT):
                    ps = open_tile((tag, t))
                    for h in range(GDN_HEADS):
                        ins = pe.transpose(ps[:, P * h:P * h + P], src[:, h, P * t:P * t + P], ident)
                    ins.then_inc(tile_full, 1)
            pe.wait_ge(*drained(("br", 1)))
            for tag, moving in (("kk", kbT), ("qk", qT2)):
                for t in range(TT):
                    ps = open_tile((tag, t))
                    for h in range(GDN_HEADS):
                        ins = pe.matmul(ps[:, P * h:P * h + P], kT2[:, h, P * t:P * t + P], moving[:, h, P * t:P * t + P],
                                        start=True, stop=True)
                    ins.then_inc(tile_full, 1)

            def four(name, lhs, rhs):
                ps = open_tile(name)
                for h in range(GDN_HEADS):
                    ins = pe.matmul(ps[:, P * h:P * h + P], lhs(h), rhs(h), start=True, stop=True)
                ins.then_inc(tile_full, 1)

            for t in range(TT):
                pe.wait_ge(d_weighed, t + 1)
                for par in range(2):
                    ps = open_tile(("dpT", t, par))
                    for j in range(2):
                        for s in range(t + 1):
                            at = P * (j * (t + 1) + s)
                            ins = pe.transpose(ps[:, at:at + P], dprobs[t][:, 2 * j + par, P * s:P * s + P], ident)
                    ins.then_inc(tile_full, 1)
            ps = open_tile(("do",))
            for t in range(TT):
                for par in range(2):
                    pe.wait_ge(*drained(("dpT", t, par)))
            for j in range(2):
                for par in range(2):
                    o = ps[DK * par:DK * par + DK, SEQ * j:SEQ * j + SEQ]
                    pe.matmul(o, dv[:, 0, :], dprobsT[par][:, j, 0, :], start=True, stop=False)
                    ins = pe.matmul(o[:, P:SEQ], dv[:, 1, :], dprobsT[par][:, j, 1, P:SEQ], start=False, stop=True)
            ins.then_inc(tile_full, 1)
            for i in range(2):
                row_all("xk", i)

            pe.wait_ge(acc_read, FILL[("xv", 0)])
            value_steps = [(i, kk, t) for i in range(2) for kk in range(4) for t in range(TT)]

            def cross_values(n):
                for i, kk, t in value_steps[:n]:
                    if kk == 0 and t == 0:
                        pe.wait_ge(*loaded(("xv", i)))
                    ins = pe.matmul(acc(("xv", t))[:, :], hT[:, 4 * i + kk, P * t:P * t + P],
                                    weights(("xv", i), 4, 512)[:, kk, :], start=(i == 0 and kk == 0),
                                    stop=(i == 1 and kk == 3))
                    if i == 1 and kk == 3:
                        ins.then_inc(acc_full, 1)
                    elif kk == 3 and t == 1:
                        ins.then_inc(unit_spent, 1)
                del value_steps[:n]

            for level in range(LEVELS):
                for t in range(TT):
                    pe.wait_ge(level_masked, 2 * level + t + 1)
                    if level:
                        pe.wait_ge(*drained(("d", level - 1, t) if level > 1 else ("y", 0, t)))
                    four(("y", level, t), lambda h: AT_level[level % 2][t][:, h, :],
                         lambda h: inv[t][:, h, :] if level else ident)
                cross_values(1)
                if level == 0:
                    pe.wait_ge(first_invT, 2)
                    continue
                for t in range(TT):
                    pe.wait_ge(*drained(("y", level, t)))
                    if level > 1:
                        pe.wait_ge(*drained(("dT", level - 1, t)))
                if level < LEVELS - 1:
                    for t in range(TT):
                        four(("d", level, t), lambda h: invT[t][:, h, :], lambda h: Y[t][:, h, :])
                for t in range(TT):
                    four(("dT", level, t), lambda h: Y[t][:, h, :], lambda h: invT[t][:, h, :])
            cross_values(1)
            for t in range(TT):
                pe.wait_ge(*drained(("dT", LEVELS - 1, t)))
                four(("gu", t), lambda h: invT[t][:, h, :], lambda h: bv[t][:, h, :])
            for t in range(TT):
                four(("gw", t), lambda h: bke[t][:, h, :], lambda h: invT[t][:, h, :])
            pe.wait_ge(conv_out, 1)
            ps = open_tile(("ln_mean",))
            for c in range(2):
                ins = pe.matmul(ps[:, 0:SEQ], conc("ones"), conv_y[:, c, :], start=(c == 0), stop=(c == 1))
            ins.then_inc(tile_full, 1)
            pe.wait_ge(conv_sq_ready, 1)
            ps = open_tile(("ln_var",))
            for c in range(2):
                ins = pe.matmul(ps[:, 0:SEQ], conc("ones"), conv_sq[:, c, :], start=(c == 0), stop=(c == 1))
            ins.then_inc(tile_full, 1)
            pe.wait_ge(qe_ready, 1)
            for t in range(TT):
                pe.wait_ge(*drained(("gw", t)))
                pe.wait_ge(*drained(("qk", t)))
            for n in range(NCHUNK):
                t, lo = n // 2, CHUNK * (n % 2)
                r = slice(lo, lo + CHUNK)
                if n:
                    cross_values(1)
                    pe.wait_ge(*drained(("kv", n - 1)))
                    ps = open_tile(("ws", n))
                    for h in range(GDN_HEADS):
                        ins = pe.matmul(ps[r, P * h:P * h + P], wT[t][:, h, r], state[:, h, :], start=True, stop=True)
                    ins.then_inc(tile_full, 1)
                    cross_values(1)
                    pe.wait_ge(*drained(("ws", n)))
                else:
                    pe.wait_ge(v_news, 1)
                ps = open_tile(("go", n))
                for h in range(GDN_HEADS):
                    o = ps[:, CHUNK * h:CHUNK * h + CHUNK]
                    if n:
                        pe.matmul(o, state[:, h, :], qeT[:, h, CHUNK * n:CHUNK * n + CHUNK], start=True, stop=False)
                    ins = pe.matmul(o, v_new[r, h, :], qkT[t][r, h, r], start=(n == 0), stop=True)
                ins.then_inc(tile_full, 1)
                if n < NCHUNK - 1:
                    ps = open_tile(("kv", n))
                    for h in range(GDN_HEADS):
                        ins = pe.matmul(ps[:, P * h:P * h + P], kdec[t][r, h, :], v_new[r, h, :], start=True, stop=True)
                    ins.then_inc(tile_full, 1)
            cross_values(1)
            row_sum("o")
            cross_values(2)
            for i in range(2):
                row_all("o", i)
            split_product("out2", MIX_ORDER)

            norm_T("cross", 12)
            rows_split("cross")
            for i in range(2):
                split_pair(("xq", i))
            ps = open_tile(("xq_sums",))
            pe.wait_ge(xq_squares, 2)
            for t in range(TT):
                for h in range(XA_HEADS):
                    at = XA_HEADS * t + h
                    ins = pe.matmul(ps[:, at:at + 1], xq_sq[:, h, P * t:P * t + P], conc("ones")[:, 0:1], start=True, stop=True)
            ins.then_inc(tile_full, 1)
            for i in range(2):
                pe.wait_ge(*drained(("xq", i)))
            for i in range(2):
                pe.wait_ge(*drained(("row_all", "xk", i)))
            for t in range(TT):
                for hp in range(2):
                    ps = open_tile(("xs", t, hp))
                    for j in range(2):
                        h = 2 * hp + j
                        ins = pe.matmul(ps[:, SEQ * j:SEQ * j + SEQ], xqT[:, h, P * t:P * t + P], xkT[:, h, :],
                                        start=True, stop=True)
                    ins.then_inc(tile_full, 1)
            for t in range(TT):
                for hp in range(2):
                    pe.wait_ge(x_weighed, 2 * t + hp + 1)
                    ps = open_tile(("xpT", t, hp))
                    for j in range(2):
                        for s in range(TT):
                            at = P * (2 * j + s)
                            ins = pe.transpose(ps[:, at:at + P], xprobs[t][:, 2 * hp + j, P * s:P * s + P], ident)
                    ins.then_inc(tile_full, 1)
            pe.wait_ge(*acc_drained(("xv", 1)))
            for c in range(2):
                for t in range(TT):
                    pe.wait_ge(*drained(("xpT", t, c)))
                ps = open_tile(("xo", c))
                for j in range(2):
                    h = 2 * c + j
                    for s in range(TT):
                        ins = pe.matmul(ps[:, SEQ * j:SEQ * j + SEQ], xv[:, s, P * h:P * h + P], xprobsT[:, h, s, :],
                                        start=(s == 0), stop=(s == TT - 1))
                ins.then_inc(tile_full, 1)
            split_product("xwo", range(2))

            norm_T("mlp", 14)
            rows_split("mlp")
            open_product("m2")
            for j in range(MLP_UNITS + MLP_LAG):
                if j < MLP_UNITS:
                    split_pair(("m1", j))
                if j >= MLP_LAG:
                    i = j - MLP_LAG
                    pe.wait_ge(relu_sq, i + 1)
                    split_product_unit(("m2", i), i == 0, i == MLP_UNITS - 1,
                                       lambda p, kk, t: relu2_s[i % 3][:, p, kk, P * t:P * t + P])


def pack(n, spec, parts):
    c = np.zeros((P, n), np.float32)
    for name, v in parts.items():
        lo, hi = spec[name]
        v = np.asarray(v)
        c[:v.shape[0], lo:hi] = v.reshape(v.shape[0], hi - lo)
    return c


def by_partition(v, k):
    return np.asarray(v).reshape(k, P).T


def twice(v):
    v = np.asarray(v).reshape(64, -1)
    return np.concatenate([v, v], 0)


def small_parameters(i):
    def a(name):
        return np.asarray(i[name])

    both = {}
    both["gains"] = np.stack([by_partition(a(n), KD) for n in (
        "mix_norm_pre", "mem_norm_kv", "mem_norm_pre", "ffn_norm_pre", "norm_mix_2", "norm_mem_2", "norm_cross_2",
        "norm_mlp_2")], 1)
    both["cmp_pos"] = a("cmp_pos")[0].reshape(2, CMP_PAIRS, P).transpose(2, 0, 1)
    both["cmp_b1"] = a("cmp_b1")[0].T
    both["cmp_w2"] = a("cmp_w2")[0].transpose(1, 0, 2)
    both["cmp_b2k"] = twice(a("cmp_b2")[0, 0])
    both["cmp_b2v"] = np.broadcast_to(np.tile(a("cmp_b2")[0, 1], GROUPS), (P, P))
    both["relb"] = np.concatenate([a("rel_bias"), np.full((1, HEADS), MASKED, np.float32)], 0)
    pw = a("pool_w")[0]
    both["pool_w"] = np.concatenate([pw[0::2].transpose(1, 0, 2), pw[1::2].transpose(1, 0, 2)], 0)
    both["pool_scale"] = by_partition(a("pool_scale")[0], 2)
    both["sgu_g"] = np.broadcast_to(a("sgu_norm_g")[0], (P, 256))
    both["sgu_b"] = np.broadcast_to(a("sgu_norm_b")[0], (P, 256))
    both["sgu_wT"] = a("sgu_w")[0].transpose(2, 0, 1)
    both["sgu_bias"] = np.repeat(a("sgu_b")[0].reshape(2, 2, P).transpose(1, 0, 2), 64, 0)
    both["conv_w"] = a("conv_w")[0].reshape(3, 2, FFN_PAIRS, P).transpose(3, 2, 1, 0)
    both["conv_b"] = a("conv_b")[0].reshape(2, FFN_PAIRS, P).transpose(2, 1, 0)
    both["gdn_conv"] = a("gdn_conv_2")[0].reshape(4, 12, P).transpose(2, 1, 0)
    both["a_log"] = a("gdn_a_log_2")[0].reshape(4, 1)
    both["dt_bias"] = a("gdn_dt_bias_2")[0].reshape(4, 1)
    both["gdn_norm"] = a("gdn_norm_2")[0].reshape(P, 1)
    both["w_qb"] = a("dsa_w_qb_2")[0].reshape(2, P, 256).transpose(1, 0, 2)
    both["w_qi"] = a("dsa_w_qi_2")[0].reshape(2, P, 256).transpose(1, 0, 2)
    both["w_kvb"] = a("dsa_w_kvb_2")[0]
    both["dq_norm"] = twice(a("dsa_q_norm_2")[0])
    both["dk_norm"] = twice(a("dsa_k_norm_2")[0])
    both["conv_dw"] = a("conv_dw_2")[0].reshape(CONV_TAPS, 2, P).transpose(2, 1, 0)
    both["dw_b"] = by_partition(a("conv_dw_b_2")[0], 2)
    both["ln_g"] = by_partition(a("conv_ln_g_2")[0], 2)
    both["ln_b"] = by_partition(a("conv_ln_b_2")[0], 2)
    both["xq_norm"] = a("xa_q_norm_2")[0].reshape(P, 1)
    both["xk_norm"] = a("xa_k_norm_2")[0].reshape(P, 1)
    return pack(NPAR, PAR, both)


def kernel(**inputs):
    import concourse.bacc as bacc
    from concourse.bass_utils import run_bass_kernel_spmd

    i = {n: np.ascontiguousarray(v) for n, v in inputs.items()}
    w_in = i["w_in"][0]
    q = w_in[:, :512].reshape(D, GROUPS, HG, DK).transpose(0, 2, 1, 3).reshape(D, 512)
    w_up = i["w_up"][0].reshape(D, 2, FFN_PAIRS, P).transpose(0, 2, 1, 3).reshape(D, 2 * FFN)
    w2 = i["w_in_2"][0]
    w_in2 = np.concatenate([w2[:, :2048], w2[:, 2056:2504], w2[:, 2048:2056], w2[:, 2504:]], 1)
    arrays = {
        "x": i["x"][0], "mem": i["mem"][0], "params": small_parameters(i), "consts": shape_constants(),
        "hots": bucket_one_hots(), "w_in": np.concatenate([q, w_in[:, 512:]], 1), "cmp_w1": i["cmp_w1"][0].reshape(2, CMP_LEN * DK, P),
        "w_out": i["w_out"][0], "w_mk": i["w_mk"][0], "w_mv": i["w_mv"][0], "w_mq": i["w_mq"][0], "w_mo": i["w_mo"][0],
        "w_up": w_up, "w_down": i["w_down"][0], "mix_norm_post": i["mix_norm_post"], "mem_norm_post": i["mem_norm_post"],
        "ffn_norm_post": i["ffn_norm_post"],
        "mem2": i["mem_2"][0], "w_in2": w_in2, "w_out2": i["w_out_2"][0], "xa_wkv": i["xa_wkv_2"][0],
        "xa_wq": i["xa_wq_2"][0], "xa_wo": i["xa_wo_2"][0], "mlp_w1": i["mlp_w1_2"][0], "mlp_w2": i["mlp_w2_2"][0],
    }
    nc = bacc.Bacc("TRN2", target_bir_lowering=False, num_devices=1)
    feed, args = {}, {}
    for n, v in arrays.items():
        v = np.ascontiguousarray(v)
        feed[f"in_{n}"] = v
        args[n] = nc.dram_tensor(f"in_{n}", v.shape, mybir.dt.from_np(v.dtype), kind="ExternalInput").ap()
    out = nc.dram_tensor("out_x", (SEQ, D), F32, kind="ExternalOutput").ap()
    block_kernel(nc, args, out)
    r = run_bass_kernel_spmd(nc, [feed], core_ids=[0])
    return r.results[0]["out_x"].reshape(1, SEQ, D)
```

```python
from contextlib import ExitStack

import numpy as np

import concourse.bass as bass
from concourse import mybir

F32 = mybir.dt.float32
F32R = mybir.dt.float32r
ALU = mybir.AluOpType
ACT = mybir.ActivationFunctionType
AX = mybir.AxisListType.X

P = 128
SEQ = 256
TT = SEQ // P
D = 1024
KD = D // P
EPS = 1e-6
MASKED = -1e30

HEADS = 8
GROUPS = 2
HG = HEADS // GROUPS
HEAD_ORDER = tuple(g * HG + i for i in range(HG) for g in range(GROUPS))
DK = 64
CMP_STRIDE = 16
CMP_LEN = 32
NCMP = SEQ // CMP_STRIDE - 1
CMP_PAIRS = CMP_LEN // 2
MEM_HEADS = 4
FFN = ((11 * D // 4) // 128) * 128
FFN_PAIRS = FFN // P
POOL_WINDOWS = (2, 4, 8, 16)
REL_BUCKETS = 32
REL_MAX_DIST = 1024
DIST_COLS = 2 * SEQ

GDN_HEADS = 4
CHUNK = 64
NCHUNK = SEQ // CHUNK
LEVELS = 6
DSA_HEADS = 4
DSA_TOPK = 64
CONV_TAPS = 31
XA_HEADS = 4
MLP_UNITS = 4 * D // 256
PICKED = -3.3e38
FUTURE = -3.0e38


def t5_bucket(dist):
    n = np.maximum(dist, 0)
    exact = REL_BUCKETS // 2
    nf = np.maximum(n, 1).astype(np.float32)
    scale = np.float32(np.log(REL_MAX_DIST / exact))
    large = exact + (np.log(nf / np.float32(exact)) / scale * np.float32(REL_BUCKETS - exact)).astype(np.int32)
    return np.where(n < exact, n, np.minimum(large, REL_BUCKETS - 1))


def columns(spec):
    at, out = 0, {}
    for name, width in spec:
        out[name] = (at, at + width)
        at += width
    return out, at


PAR, NPAR = columns([
    ("gains", 8 * KD), ("cmp_pos", 2 * CMP_PAIRS), ("cmp_b1", 2), ("cmp_w2", 128), ("cmp_b2k", 1),
    ("cmp_b2v", 128), ("relb", HEADS), ("pool_w", 128), ("pool_scale", 2), ("sgu_g", 256), ("sgu_b", 256),
    ("sgu_wT", 512), ("sgu_bias", 256),
    ("conv_w", FFN_PAIRS * 6), ("conv_b", FFN_PAIRS * 2), ("gdn_conv", 48), ("a_log", 1), ("dt_bias", 1),
    ("gdn_norm", 1), ("w_qb", 512), ("w_qi", 512), ("w_kvb", 128), ("dq_norm", 1), ("dk_norm", 1),
    ("conv_dw", 2 * CONV_TAPS), ("dw_b", 2), ("ln_g", 2), ("ln_b", 2), ("xq_norm", 1), ("xk_norm", 1),
])
CON, NCON = columns([
    ("ident", 128), ("neg_half", 8), ("eps", 8), ("root_scale", 1), ("root_bias", 1), ("pick_col", 16),
    ("tri_incl", 128), ("tri_strict", 128), ("levels", LEVELS * 128), ("block_ones", 128),
    ("ones", 128), ("inv_count", 512), ("chunk_keep", SEQ),
])
CON_FIRST = CON["pick_col"][1]
PAR_FIRST = PAR["gains"][1]
EPS_VALUES = [EPS, 64 * EPS, P * EPS, 0, 0, 0, 0, 0]
GAIN = {n: i for i, n in enumerate(["mix", "memkv", "mem", "ffn", "mix2", "mem2", "cross", "mlp"])}


def shape_constants():
    c = np.zeros((P, NCON), np.float32)

    def put(name, a):
        lo, hi = CON[name]
        c[:a.shape[0], lo:hi] = a.reshape(a.shape[0], hi - lo)

    i = np.arange(P)
    row, col = i[:, None], i[None, :]
    same = row // CHUNK == col // CHUNK
    put("ident", np.eye(P))
    put("neg_half", np.full((P, 8), -0.5))
    put("eps", np.tile(np.array(EPS_VALUES, np.float32), (P, 1)))
    put("tri_incl", (same & (col >= row)).astype(np.float32))
    put("tri_strict", (same & (col > row)).astype(np.float32))
    c[:, CON["pick_col"][0] + 8] = 1
    put("root_scale", np.array([P] * 4 + [1] * 4, np.float32)[:, None])
    put("root_bias", np.array([P * EPS] * 4 + [EPS] * 4, np.float32)[:, None])
    put("levels", np.stack([
        (row // (2 * s) == col // (2 * s)) & (col % (2 * s) >= s) & (row % (2 * s) < s)
        for s in (2 ** n for n in range(LEVELS))], 1).astype(np.float32))
    put("block_ones", same.astype(np.float32))
    put("ones", np.ones((P, P)))
    t = np.arange(SEQ)
    counts = np.zeros((P, 2, SEQ), np.float32)
    for g, w in enumerate(POOL_WINDOWS):
        counts[64 * (g % 2):64 * (g % 2) + 64, g // 2] = np.float32(1) / np.minimum(t + 1, w).astype(np.float32)
    put("inv_count", counts)
    put("chunk_keep", np.tile((t % CHUNK != 0).astype(np.float32), (4, 1)))
    return c


def bucket_one_hots():
    dist = np.arange(DIST_COLS) - (SEQ - 1)
    h = np.zeros((REL_BUCKETS + 1, DIST_COLS), np.float32)
    h[np.where(dist < 0, REL_BUCKETS, t5_bucket(dist)), np.arange(DIST_COLS)] = 1
    return h


RING = 3
DOWN_LAG = 2
NB = 4
ARENA = 26624
WHOLE = ("q0", ("mk", 0), ("mq", 0), ("up", 0), "ug0", ("xq", 0), ("m1", 0))
SPLIT_INPUTS_2 = ("ug0", "ug1", "cq", "ck")
SPLIT_INPUTS = ("q0", "q1", "kcvc", "kskw", "vsvw", "pool", "u", "v")
SPLIT_PRODUCTS = ("mk", "mv", "out", "mq", "wo", "up", "down", "qkv", "z", "out2", "xq", "xwo", "m1", "m2")
SPLIT_STAGES = ("mix", "memkv", "mem", "ffn", "mix2", "cross", "mlp")
MIX_ORDER = (2, 3, 0, 1)
TOPK_ROUNDS = DSA_TOPK // 8
WARM_BEFORE = {"mem": 8, "ffn": 8, "mix2": 8, "cross": 2, "mlp": 2}
MLP_LAG = 2
MEM_DIM = D // MEM_HEADS
STATS = [(n, t) for n in ("mix", "memkv", "out_post", "mem", "wo_post", "ffn", "down_post", "mix2", "mem2", "cross", "mlp") for t in range(TT)] + [
    ("sgu", t) for t in range(TT)]
NSTAT = len(STATS)


def plan():
    tiles = []

    def norm(stage):
        tiles.extend(("normT", stage, t, half) for t in range(TT) for half in range(2))

    norm("mix")
    tiles.extend((n,) for n in ("q0", "q1", "bias_row", "kcvc", "kskw", "vsvw", "gates", "pool", "u", "v", "cmp_h", "cmp_kv"))
    for t in range(TT):
        tiles.extend(("cmp_s", t, g) for g in range(GROUPS))
        tiles.extend(("s", t, h) for h in HEAD_ORDER)
    tiles.extend((("pool_out",), ("sgu_out",)))
    norm("memkv")
    tiles.extend(("mk", c) for c in range(4))
    tiles.extend(("cmp_pT", t) for t in range(TT))
    tiles.extend(("pT", t, h) for h in range(HEADS) for t in range(TT))
    norm("mem")
    tiles.extend(("mq", c) for c in range(4))
    tiles.extend(("ms", t, hp) for t in range(TT) for hp in range(2))
    tiles.extend(("mpT", t, hp) for t in range(TT) for hp in range(2))
    tiles.extend(("mo", c) for c in range(4))
    norm("ffn")
    tiles.extend(("up", j) for j in range(FFN_PAIRS))
    norm("mix2")
    tiles.extend((n,) for n in ("ug0", "ug1", "cq", "ck", "abw", "ab", "dq", "dqi", "dk"))
    tiles.append(("qkv", 0))
    tiles.extend((("across", "dq"), ("across", "dk")))
    tiles.extend(("il", t, par) for t in range(TT) for par in range(2))
    tiles.extend(("qkv", i) for i in range(1, 6))
    tiles.extend((("z", 0), ("ln_mean",), ("z", 1)))
    norm("mem2")
    tiles.extend((("xk", 0), ("row_sum", "l")))
    tiles.extend(("dl", t, par) for t in range(TT) for par in range(2))
    tiles.extend((("ln_var",), ("xk", 1)))
    tiles.extend(("row_all", "l", i) for i in range(4))
    tiles.extend((("cols",), ("dr", 0), ("dr", 1), ("br", 0), ("br", 1), ("row_sum", "xk")))
    tiles.extend((n, t) for n in ("kA", "vA", "kk", "qk") for t in range(TT))
    tiles.extend(("dpT", t, par) for t in range(TT) for par in range(2))
    tiles.append(("do",))
    tiles.extend(("row_all", "xk", i) for i in range(2))
    for level in range(LEVELS):
        for kind in ("y", "d", "dT"):
            if kind == "y" or level and (kind, level) != ("d", LEVELS - 1):
                tiles.extend((kind, level, t) for t in range(TT))
    tiles.extend((n, t) for n in ("gu", "gw") for t in range(TT))
    for n in range(NCHUNK):
        if n:
            tiles.append(("ws", n))
        tiles.append(("go", n))
        if n < NCHUNK - 1:
            tiles.append(("kv", n))
    tiles.extend((("row_sum", "o"), ("row_all", "o", 0), ("row_all", "o", 1)))
    norm("cross")
    tiles.extend((("xq", 0), ("xq", 1), ("xq_sums",)))
    tiles.extend(("xs", t, hp) for t in range(TT) for hp in range(2))
    tiles.extend(("xpT", t, hp) for t in range(TT) for hp in range(2))
    tiles.extend(("xo", c) for c in range(2))
    norm("mlp")
    tiles.extend(("m1", j) for j in range(MLP_UNITS))

    units = ["q0", "q1", "kcvc", "kskw", "vsvw", "gates", "pool", "u", "v", "cmp_w1k", "cmp_w1v"]
    for product in ("mk", "mv", "out", "mq", "wo"):
        units += [(product, c) for c in (MIX_ORDER if product == "out" else range(4))]
    for j in range(FFN_PAIRS + DOWN_LAG):
        if j < FFN_PAIRS:
            units.append(("up", j))
        if j >= DOWN_LAG and j % 2 == 1:
            units.append(("down", (j - DOWN_LAG) // 2))
    units += ["ug0", "ug1", "cq", "ck", "ab"] + [("qkv", i) for i in range(6)] + [("z", 0), ("z", 1)]
    units += [("xk", 0), ("xk", 1), ("xv", 0), ("xv", 1)] + [("out2", i) for i in MIX_ORDER]
    units += [("xq", 0), ("xq", 1), ("xwo", 0), ("xwo", 1)]
    for j in range(MLP_UNITS + MLP_LAG):
        if j < MLP_UNITS:
            units.append(("m1", j))
        if j >= MLP_LAG:
            units.append(("m2", j - MLP_LAG))

    fills = []
    for product in ("mv", "o", "out", "wo", "down", "xv", "out2", "xwo", "m2"):
        fills += [(product, i) for i in range(2 if product in ("o", "xv") else 4)]
    return tiles, units, fills


def block_kernel(nc, a, out):
    ctx = ExitStack()
    with ctx:
        def sb(name, shape):
            return ctx.enter_context(nc.sbuf_tensor(name, shape, F32))

        def sem(name):
            return ctx.enter_context(nc.semaphore(name))

        ring = sb("weight_ring", [P, RING, 2048])
        x = sb("x_res", [P, TT, D])
        xn = sb("x_normed", [P, TT, D])
        hT = sb("hT", [P, KD, SEQ])
        mixT = sb("mixT", [P, KD, SEQ])
        par = sb("par", [P, NPAR])
        con = sb("con", [P, NCON])
        post_gain = sb("post_gain", [P, D])
        junk = sb("act_junk", [P, D])
        stats = sb("stats", [P, 2 * NSTAT])
        small = sb("small_sums", [P, 32])
        with nc.sbuf_tensor("arena", [P, ARENA], F32) as arena:
            pass
        SPLIT_AT = 3072
        sb("arena_below_split", [P, SPLIT_AT])
        split = ctx.enter_context(nc.sbuf_tensor("split_operands", [P, ARENA - SPLIT_AT], F32R))
        extra_slot = ctx.enter_context(nc.sbuf_tensor("split_extra_slot", [P, 4096], F32R))[:, :]
        banks = [ctx.enter_context(nc.psum_tensor(f"work{b}", [P, 512], F32)) for b in range(NB)]
        accs = [ctx.enter_context(nc.psum_tensor(f"acc{b}", [P, 512], F32)) for b in range(4)]
        bias_rows_dram = nc.dram_tensor("bias_rows_scratch", [HEADS, DIST_COLS], F32, kind="Internal").ap()

        def parc(name):
            return par[:, PAR[name][0]:PAR[name][1]]

        def conc(name):
            return con[:, CON[name][0]:CON[name][1]]

        def cut(at, *shape):
            n = int(np.prod(shape))
            assert at + n <= ARENA
            v = arena[:, at:at + n]
            if len(shape) == 1:
                return v
            names = "abcd"[:len(shape)]
            return v.rearrange(f"p ({' '.join(names)}) -> p {' '.join(names)}", **dict(zip(names, shape)))

        def cut_split(at, *shape):
            n = int(np.prod(shape))
            assert at >= SPLIT_AT and at + n <= ARENA
            names = "abcd"[:len(shape)]
            return split[:, at - SPLIT_AT:at - SPLIT_AT + n].rearrange(
                f"p ({' '.join(names)}) -> p {' '.join(names)}", **dict(zip(names, shape)))

        def eps_col(v):
            k = CON["eps"][0] + EPS_VALUES.index(v)
            return con[:, k:k + 1]

        ident = conc("ident")
        gains = parc("gains").rearrange("p (s k) -> p s k", k=KD)

        tiles, units, fills = plan()
        TILE = {n: i for i, n in enumerate(tiles)}
        UNIT = {n: i for i, n in enumerate(units)}
        FILL = {n: i for i, n in enumerate(fills)}
        tile_full = sem("tile_full")
        tile_read = [sem(f"tile_read{b}") for b in range(NB)]
        acc_full = sem("acc_full")
        acc_read = sem("acc_read")
        unit_loaded = [sem(f"unit_loaded{s}") for s in range(RING)]
        unit_spent = sem("unit_spent")

        def bank(name):
            return banks[TILE[name] % NB]

        def full(name):
            return tile_full, TILE[name] + 1

        def drained(name):
            return tile_read[TILE[name] % NB], TILE[name] // NB + 1

        def reader(name):
            return tile_read[TILE[name] % NB]

        def acc(name):
            return accs[FILL[name] % 4]

        def acc_filled(name):
            return acc_full, FILL[name] + 1

        def acc_drained(name):
            return acc_read, FILL[name] + 1

        def weights(name, *shape):
            v = ring[:, UNIT[name] % RING, :]
            n = int(np.prod(shape))
            names = "abcd"[:len(shape)]
            return v[:, 0:n].rearrange(f"p ({' '.join(names)}) -> p {' '.join(names)}", **dict(zip(names, shape)))

        split_units = [u for u in units if u not in WHOLE and
                       (u in SPLIT_INPUTS + SPLIT_INPUTS_2 or isinstance(u, tuple) and u[0] in SPLIT_PRODUCTS)]
        SPLIT = {u: i for i, u in enumerate(split_units)}
        high_ready = sem("weights_high_ready")
        low_ready = sem("weights_low_ready")
        acts_high = sem("acts_high_ready")
        acts_low = sem("acts_low_ready")
        act_parts = [("rows", stage, t, half) for stage in ("mix", "memkv") for t in range(TT) for half in range(2)]
        act_parts += [("mix", "out", c) for c in MIX_ORDER] + [("rows", "mem", t, half) for t in range(TT) for half in range(2)]
        act_parts += [("mix", "wo", c) for c in range(4)] + [("rows", "ffn", t, half) for t in range(TT) for half in range(2)]
        act_parts += [("rows", "mix2", t, half) for t in range(TT) for half in range(2)]
        act_parts += [("mix", "out2", c) for c in MIX_ORDER] + [("rows", "cross", t, half) for t in range(TT) for half in range(2)]
        act_parts += [("mix", "xwo", c) for c in range(2)] + [("rows", "mlp", t, half) for t in range(TT) for half in range(2)]
        ACTS = {n: i for i, n in enumerate(act_parts)}

        def high_there(name):
            return acts_high, ACTS[name] + 1

        low_drains = {("mix", "out", c): lambda c=c: acc_drained(("o", c)) for c in range(2)}
        low_drains.update({("mix", "wo", c): lambda c=c: drained(("mo", c)) for c in range(4)})
        low_drains.update({("mix", "xwo", c): lambda c=c: drained(("xo", c)) for c in range(2)})
        LOWS = {n: i for i, n in enumerate(n for n in act_parts if n not in low_drains)}

        def low_there(name):
            return low_drains[name]() if name in low_drains else (acts_low, LOWS[name] + 1)

        last_down = SPLIT[("down", FFN_PAIRS // 2 - 1)]

        def upto(name):
            return sum(u in SPLIT for u in units[:UNIT[name] + 1]) - 1

        def ffn_ahead(j):
            return 2 if j < 4 else 3

        def before(name):
            return upto(name) - 1 if name in UNIT else -1

        def split_weights(name, *shape):
            names = "abcd"[:len(shape)]
            return slot_of(name).rearrange(
                f"p s ({' '.join(names)}) -> p s {' '.join(names)}", **dict(zip(names, shape)))

        def loaded(name):
            return unit_loaded[UNIT[name] % RING], 16 * (UNIT[name] // RING + 1)

        params_in = sem("params_in")
        consts_in = sem("consts_in")
        first_params_in = sem("first_params_in")
        first_consts_in = sem("first_consts_in")
        x_in = [sem(f"x_in{t}") for t in range(TT)]
        mem_in = sem("mem_in")
        hots_in = sem("hots_in")
        bias_rows_out = sem("bias_rows_out")
        bias_tile_in = sem("bias_tile_in")
        gain_in = sem("post_gain_in")
        shifted_in = sem("kv_shifted_in")
        squares = sem("squares_summed")
        rstd_ready = sem("rstd_ready")
        normed = sem("x_normed_ready")
        x_done = sem("x_updated")
        blocks_ready = sem("cmp_blocks_ready")
        scored = sem("scores_biased")
        neg_max = sem("neg_max_ready")
        exped = sem("exp_done")
        weighed = sem("probs_weighed")
        sgu_stat = sem("sgu_stats_ready")
        sgu_rstd = sem("sgu_rstd_ready")
        sgu_normed = sem("sgu_normed_ready")
        masked_ws = sem("sgu_weights_masked")
        pooled = sem("pool_diff_ready")
        cmp_biases = sem("cmp_bias_ready")
        dve_chain = sem("dve_chain")
        act_chain = sem("act_chain")
        pool_chain = sem("pool_chain")
        gated = sem("ffn_gated")
        gate_act = sem("ffn_gate_act")
        tap2 = sem("ffn_tap2")
        out_done = sem("out_done")
        heads_done = sem("heads_attended")
        across_sq = sem("across_squares_ready")
        across_done = sem("across_normed")
        row_squares = sem("row_squares_ready")
        row_roots = {tag: sem(f"row_roots_{tag}") for tag in ("l", "xk", "o")}
        scaled_o = sem("gdn_o_scaled")
        level_masked = sem("level_masked")
        first_invT = sem("first_invT_ready")
        xq_squares = sem("xq_squares_ready")
        mem2_in = sem("mem2_in")
        tap3 = sem("gdn_last_tap")
        silu_done = sem("gdn_silu_done")
        idx_sum = sem("index_scores_summed")
        idx_causal = sem("index_scores_causal")
        picked = sem("topk_picked")
        dmask_ready = sem("dsa_mask_ready")
        d_max = sem("dsa_neg_max")
        d_exp = sem("dsa_exp_done")
        d_weighed = sem("dsa_probs_weighed")
        softplus_ln = sem("softplus_ln_ready")
        decay_sum = sem("decay_summed")
        decay_exp = sem("decay_exps_ready")
        rows_ready = sem("gate_rows_ready")
        gamma_diff = sem("gamma_exponents")
        gamma_exp = sem("gamma_exp_done")
        gamma_ready = sem("gammas_masked")
        kb_ready = sem("kb_ready")
        qe_ready = sem("qe_ready")
        v_news = sem("v_new_ready")
        conv_out = sem("conv31_done")
        conv_out_low = sem("conv31_first_half_done")
        conv_sq_ready = sem("ln_squares_ready")
        conv_norm = sem("ln_normed")
        conv_mix = sem("conv_mix_ready")
        x_max = sem("cross_neg_max")
        x_weighed = sem("cross_probs_weighed")
        relu_sq = sem("mlp_squared")
        relu_high = sem("mlp_square_high")
        mix_tail = sem("mix_tail_ready")

        qT = cut(0, 4, SEQ)
        toeplitz = cut(1024, HEADS, SEQ)
        pairs = cut(3072, 2, GROUPS, SEQ)
        blocks = cut(4096, 2, CMP_PAIRS, GROUPS, NCMP)
        kcvcT = cut(5056, 2, SEQ)
        probsT = [cut(3072 + 1024 * i, 2, TT, SEQ) for i in range(2)]
        keysT = cut(5568, 2, SEQ)
        values = cut(6080, 2, TT, P)
        cmp_hT = cut(6592, 2, 32)
        cmp_kT = cut(6656, NCMP)
        cmp_v = cut(6672, P)
        gates = cut(6800, TT, HEADS, 3)
        cmp_bias = cut(6848, TT, HEADS, NCMP)
        cmp_p = cut(7088, TT, HEADS, 32)
        cmp_pT = cut(7600, GROUPS, SEQ)
        soft = cut(8112, TT, 3, HEADS, 4)
        bias_rows = cut(8304, 384)
        probs = [[cut(8704 + (2048 if t else 0) + h * (512 if t else 256), 2, P * (t + 1)) for h in range(HEADS)]
                 for t in range(TT)]
        uT = cut(14848, 2, SEQ)
        v_n = cut(15360, TT, SEQ)
        v_g = cut(15872, TT, SEQ)
        kmT = cut(16384, KD, SEQ)
        vm = cut(18432, TT, D)
        hots = cut(16384, DIST_COLS)
        pool_a = cut(17408, 2, 272)
        pool_b = cut(17952, 2, 272)
        pool_c = cut(18496, 2, 272)
        pool_s = cut(19040, 2, SEQ)
        pool_d = cut(19552, 2, SEQ)
        qmT = cut(0, KD, SEQ)
        mprobs = [cut(2048 + 1024 * t, MEM_HEADS, SEQ) for t in range(TT)]
        mprobsT = cut(24576, MEM_HEADS, TT, SEQ)
        msoft = small[:, 0:TT * 3 * MEM_HEADS].rearrange("p (t k h) -> p t k h", t=TT, k=3)
        conv = [cut(512 * i, 2, SEQ) for i in range(3)]
        act_g = [cut(1536 + 256 * i, SEQ) for i in range(2)]
        prod = [cut(2048 + 256 * i, SEQ) for i in range(2)]
        prod_s = [cut_split(16384 + 512 * i, 2, SEQ) for i in range(4)]
        at_rest = cut_split(4096, 2, KD, SEQ)
        act_s = {"mix": (cut_split(12800, KD, SEQ), cut_split(24576, KD, SEQ)),
                 "memkv": (cut_split(24576, KD, SEQ), cut_split(3072, KD, SEQ)),
                 "mix2": (cut_split(24576, KD, SEQ), cut_split(7168, KD, SEQ))}
        act_s.update({stage: (at_rest[:, 0], at_rest[:, 1]) for stage in
                      ("out", "mem", "wo", "ffn", "out2", "cross", "xwo", "mlp")})
        slot_of_unit, held_before, in_slot = {}, {}, {}
        phases = ((SPLIT_INPUTS, (None, 20480, 8704)), (("mk", "mv"), (None, 20480)),
                  (("out", "mq", "wo", "up", "down"), (None, 20480, 12288, 8192)),
                  (SPLIT_INPUTS_2 + ("qkv", "z"), (None, 20480)),
                  (("out2", "xq", "xwo", "m1", "m2"), (None, 12352, 20480, 8192)))
        for kinds, slots in phases:
            phase_units = [u for u in split_units if (u if isinstance(u, str) else u[0]) in kinds]
            for i, u in enumerate(phase_units):
                at = slots[i % len(slots)]
                slot_of_unit[u] = extra_slot.rearrange("p (s n) -> p s n", s=2) if at is None else cut_split(at, 2, 2048)
                overlapping = [v for v, where in in_slot.items() if where == at or None not in (where, at)
                               and abs(where - at) < 4096]
                held_before[u] = max(overlapping, key=split_units.index) if overlapping else None
                in_slot[u] = at

        def slot_of(name):
            return slot_of_unit[name]

        cqT = cut(0, 2, SEQ)
        ckvT = cut(512, SEQ)
        kidxT = cut(768, SEQ)
        dqT = cut(1024, 2, SEQ)
        dqiT = cut(1536, 2, SEQ)
        dkT = cut(2048, SEQ)
        dv = cut(19576, TT, DK)
        dsq = cut(2432, 2, SEQ)
        dsk = cut(2944, SEQ)
        w_idx = cut(3968, TT, 4)
        ab_cols = small[:, 0:TT * 8].rearrange("p (t n) -> p t n", t=TT)
        top8 = cut(3976, TT, 8)
        dsoft = cut(19704, TT, 2, DSA_HEADS)
        idx_score = [cut(4096 + 256 * t, P * (t + 1)) for t in range(TT)]
        dmask = [cut(4608 + 256 * t, P * (t + 1)) for t in range(TT)]
        relu_l = [[cut(5120 + 1024 * t + 512 * par, 2, P * (t + 1)) for par in range(2)] for t in range(TT)]
        dprobs = [cut(at, DSA_HEADS, P * (t + 1)) for t, at in enumerate((19720, 25600))]
        dprobsT = [cut(4096, 2, TT, SEQ), cut(20480, 2, TT, SEQ)]
        gate_s = cut(10240, 2, SEQ)
        y_pad = cut(10752, 2, CONV_TAPS - 1 + SEQ)
        conv_y = cut(11328, 2, SEQ)
        conv_sq = cut(11840, 2, SEQ)
        conv_term = [cut(9216 + SEQ * i, SEQ) for i in range(2)]
        qkv = cut(12352, 12, SEQ)
        zT = cut(16448, GDN_HEADS, SEQ)
        gate_rows = cut(15424, 4, SEQ)
        row_tmp = cut(17472, 2, SEQ)
        gate_cols = cut(18496, TT, 4, GDN_HEADS)
        state = cut(18528, GDN_HEADS, P)
        v_new = cut(19040, GDN_HEADS, P)
        a_rate = cut(19552, 1)
        kbT = cut(20480, GDN_HEADS, SEQ)
        qeT = cut(21504, GDN_HEADS, SEQ)
        exp_decay = cut(22528, GDN_HEADS, SEQ)
        xkT = cut(24576, XA_HEADS, SEQ)
        xv = post_gain[:, :].rearrange("p (s n) -> p s n", s=TT)
        AT, qkT, inv, invT, Y, bke, kdec, bv, u_n, wT = [
            [cut(1024 * i + 512 * t, GDN_HEADS, P) for t in range(TT)] for i in range(10)]
        l2_sq = cut(20480, 8, SEQ)
        AT_level = [[cut(at + 512 * t, GDN_HEADS, P) for t in range(TT)] for at in (9216, 8192)]
        oT = cut(2048, GDN_HEADS, SEQ)
        o_sq = cut(0, GDN_HEADS, SEQ)
        xqT = cut(0, XA_HEADS, SEQ)
        xq_sq = cut(1024, XA_HEADS, SEQ)
        xprobs = [cut(2048 + 1024 * t, XA_HEADS, SEQ) for t in range(TT)]
        xprobsT = cut(16448, XA_HEADS, TT, SEQ)
        xsoft = cut(18496, TT, 2, XA_HEADS)
        xq_root = cut(18512, TT, XA_HEADS)
        relu_h = [cut(512 * i, 2, SEQ) for i in range(2)]
        relu2 = [cut(1024 + 512 * i, 2, SEQ) for i in range(2)]
        relu2_s = [cut_split(16448 + 1024 * i, 2, 2, SEQ) for i in range(3)]

        chunk2 = {"dq": (dqT, dsq, 1.0, 64 * EPS, "dq_norm"),
                  "dk": (dkT, dsk, 1.0 / 64, EPS, "dk_norm")}
        ACROSS = {n: i for i, n in enumerate(chunk2)}

        root_rows = cut(17984, 2, SEQ)
        ROWS = {"l": (qkv[:, 0:8, :], l2_sq, 8, conc("root_scale")[0:8, :], conc("root_bias")[0:8, :], root_rows[0:8, 0, :]),
                "xk": (xkT, mixT[:, 0:4, :], 4, 1.0 / P, eps_col(EPS)[0:4, :], root_rows[0:4, 1, :]),
                "o": (oT, o_sq, 4, 1.0 / P, eps_col(EPS)[0:4, :], root_rows[0:4, 0, :])}

        STATI = {n: i for i, n in enumerate(STATS)}

        def stat(name, j=0):
            c = 2 * STATI[name] + j
            return stats[:, c:c + 1]

        hT_free = {"mix": None, "memkv": full(("v",)), "mem": acc_filled(("mv", 3)), "ffn": full(("mq", 3))}
        hT_free.update({"mix2": full(("up", FFN_PAIRS - 1)), "mem2": full(("z", 1)), "cross": acc_filled(("xv", 1)),
                        "mlp": full(("xq", 1))})
        LAST_OF_UNIT = {u: full((u,)) for u in ("q0", "q1", "kcvc", "kskw", "vsvw", "gates", "pool", "u", "v")}
        LAST_OF_UNIT.update({"cmp_w1k": full(("cmp_h",)), "cmp_w1v": full(("cmp_h",))})
        LAST_OF_UNIT.update({u: full(u) for u in units if u in TILE})
        LAST_OF_UNIT.update({u: full((u,)) for u in ("cq", "ck", "ug0", "ug1")})
        LAST_OF_UNIT["ab"] = full(("abw",))
        spent = 0
        last_unit = {}
        for u in units:
            if isinstance(u, tuple) and u not in TILE:
                last_unit[u[0]] = u
        SPENT = {}
        for u in units:
            if u in LAST_OF_UNIT:
                continue
            product = u[0]
            if last_unit[product] == u:
                LAST_OF_UNIT[u] = acc_filled((product, 1 if product == "xv" else 3))
            else:
                spent += 1
                SPENT[u] = spent
                LAST_OF_UNIT[u] = (unit_spent, spent)

        w_in = a["w_in"].rearrange("(k p) c -> p k c", p=P)
        w_up = a["w_up"].rearrange("(k p) c -> p k c", p=P)

        w_in2 = a["w_in2"].rearrange("(k p) c -> p k c", p=P)
        xa_wkv = a["xa_wkv"].rearrange("(k p) c -> p k c", p=P)

        def cols(w, lo, n):
            return w[:, :, lo:lo + n]

        def rows(w, i, n=2):
            return w.rearrange("(k p) c -> p k c", p=P)[:, n * i:n * i + n, :]

        def source(u):
            at = {"q0": 0, "q1": 256, "kcvc": 512, "kskw": 768, "vsvw": 1024, "gates": 1280, "pool": 1304,
                  "u": 1560, "v": 1816}
            if u in at:
                n = 24 if u == "gates" else 256
                return (KD, n), cols(w_in, at[u], n)
            if u in ("cmp_w1k", "cmp_w1v"):
                return (CMP_PAIRS, P), a["cmp_w1"][int(u == "cmp_w1v")].rearrange("(j p) c -> p j c", p=P)
            at2 = {"cq": (2048, 256), "ck": (2304, 256), "ab": (2560, 12), "ug0": (2572, 256), "ug1": (2828, 256)}
            if u in at2:
                lo, n = at2[u]
                return (KD, n), cols(w_in2, lo, n)
            kind, i = u
            wide = {"mk": "w_mk", "mq": "w_mq"}
            tall = {"mv": "w_mv", "out": "w_out", "wo": "w_mo", "down": "w_down"}
            if kind in wide:
                return (KD, 256), cols(a[wide[kind]].rearrange("(k p) c -> p k c", p=P), 256 * i, 256)
            if kind in tall:
                return (2, D), rows(a[tall[kind]], i)
            if kind == "up":
                return (KD, 256), cols(w_up, 256 * i, 256)
            if kind == "qkv":
                return (KD, 256), cols(w_in2, 256 * i, 256)
            if kind == "z":
                return (KD, 256), cols(w_in2, 1536 + 256 * i, 256)
            if kind == "xk":
                return (KD, 256), cols(xa_wkv, 256 * i, 256)
            if kind == "xv":
                return (4, 512), xa_wkv[:, 4 * i:4 * i + 4, 512:1024]
            if kind == "xq":
                return (KD, 256), cols(a["xa_wq"].rearrange("(k p) c -> p k c", p=P), 256 * i, 256)
            if kind == "m1":
                return (KD, 256), cols(a["mlp_w1"].rearrange("(k p) c -> p k c", p=P), 256 * i, 256)
            return (2, D), rows(a[{"out2": "w_out2", "xwo": "xa_wo", "m2": "mlp_w2"}[kind]], i)

        block = ctx.enter_context(nc.Block())

        @block.sync
        def _(sp):
            def load(u):
                i = UNIT[u]
                if i >= RING:
                    held = units[i - RING]
                    sp.wait_ge(*((low_ready, SPLIT[held] + 1) if held in SPLIT else LAST_OF_UNIT[held]))
                shape, src = source(u)
                sp.dma_start(weights(u, *shape), src).then_inc(unit_loaded[i % RING], 16)

            sp.dma_start(x[:, 0, :], a["x"][0:P, :]).then_inc(x_in[0], 16)
            sp.dma_start(x[:, 1, :], a["x"][P:2 * P, :]).then_inc(x_in[1], 16)
            sp.dma_start(con[:, 0:CON_FIRST], a["consts"][:, 0:CON_FIRST]).then_inc(first_consts_in, 16)
            sp.dma_start(par[:, 0:PAR_FIRST], a["params"][:, 0:PAR_FIRST]).then_inc(first_params_in, 16)
            for u in units[:2]:
                load(u)
            sp.dma_start(hots[0:REL_BUCKETS + 1, :], a["hots"]).then_inc(hots_in, 16)
            sp.dma_start(par[:, PAR_FIRST:], a["params"][:, PAR_FIRST:]).then_inc(params_in, 16)
            for u in units[2:4]:
                load(u)
            sp.dma_start(con[:, CON_FIRST:], a["consts"][:, CON_FIRST:]).then_inc(consts_in, 16)
            for u in units[4:]:
                load(u)
            for t in range(TT):
                sp.wait_ge(*acc_drained(("m2", 2 * t + 1)))
                sp.dma_start(out[P * t:P * t + P, :], x[:, t, :]).then_inc(out_done, 16)
            sp.wait_ge(out_done, 16 * TT)

        @block.gpsimd
        def _(pool):
            chain = [0]

            def link(ins):
                chain[0] += 1
                ins.then_inc(pool_chain, 1)
                pool.wait_ge(pool_chain, chain[0])


            def rstd(name, halves, n=D):
                pool.wait_ge(squares, STATI[name] + 1)
                if halves:
                    link(pool.tensor_tensor(stat(name), stat(name), stat(name, 1), ALU.add))
                link(pool.tensor_scalar(stat(name), stat(name), 1.0 / n, EPS, ALU.mult, ALU.add))
                pool.tensor_tensor(stat(name), stat(name), conc("neg_half")[:, 0:1], ALU.pow).then_inc(rstd_ready, 1)

            def load_post_gain(n):
                if n:
                    pool.wait_ge(x_done, 2 * n)
                g = a[("mix_norm_post", "mem_norm_post", "ffn_norm_post")[n]]
                pool.dma_start(post_gain[:, :], bass.AP(tensor=g.tensor, offset=g.offset, ap=[[0, P], [1, D]])).then_inc(gain_in, 16)

            pool.wait_ge(first_consts_in, 16)
            for t in range(TT):
                rstd(("mix", t), False)
            pool.wait_ge(*drained(("bias_row",)))
            pool.dma_start(bias_rows_dram[:, 0:384], bias_rows[0:HEADS, :]).then_inc(bias_rows_out, 16)
            pool.wait_ge(bias_rows_out, 16)
            pool.dma_start(toeplitz, bass.AP(tensor=bias_rows_dram.tensor, offset=bias_rows_dram.offset,
                                             ap=[[1, P], [DIST_COLS, HEADS], [1, SEQ]])).then_inc(bias_tile_in, 16)
            pool.wait_ge(params_in, 16)
            wsT = parc("sgu_wT").rearrange("p (h t) -> p h t", h=4)
            pool.affine_select(out=wsT, in_=wsT, compare_op=ALU.is_ge, fill=0.0, base=0,
                               pattern=[[0, 4], [1, P]], channel_multiplier=-1).then_inc(masked_ws, 1)
            link(pool.memset(pool_b[:, :, 0:16], 0.0))
            link(pool.memset(pool_c[:, :, 0:16], 0.0))
            link(pool.memset(pool_a[:, :, 0:16], 0.0))
            pool.wait_ge(*drained(("pool",)))
            src, spare = pool_a, [pool_b, pool_c, pool_b, pool_c]
            for g, w in enumerate(POOL_WINDOWS):
                dst = spare[g]
                link(pool.tensor_tensor(dst[:, :, 16:272], src[:, :, 16:272], src[:, :, 16 - w // 2:272 - w // 2], ALU.add))
                half = slice(64 * (g % 2), 64 * (g % 2) + 64)
                link(pool.tensor_copy(pool_s[half, g // 2, :], dst[half, g // 2, 16:272]))
                src = dst
            pool.wait_ge(consts_in, 16)
            link(pool.tensor_tensor(pool_s, pool_s, conc("inv_count").rearrange("p (c t) -> p c t", c=2), ALU.mult))
            pool.tensor_tensor(pool_d, pool_s, pool_a[:, :, 16:272], ALU.subtract).then_inc(pooled, 1)
            for t in range(TT):
                pool.wait_ge(sgu_stat, t + 1)
                link(pool.tensor_scalar(stat(("sgu", t), 1), stat(("sgu", t), 1), EPS, None, ALU.add))
                pool.tensor_tensor(stat(("sgu", t), 1), stat(("sgu", t), 1), conc("neg_half")[:, 0:1],
                                   ALU.pow).then_inc(sgu_rstd, 1)
            load_post_gain(0)
            for name in STATS:
                if name[0] in ("mem2", "cross", "mlp"):
                    continue
                if name[0] not in ("mix", "sgu"):
                    rstd(name, name[0].endswith("_post"))
                if name in (("mem", 1), ("ffn", 1)):
                    load_post_gain(1 if name[0] == "mem" else 2)
            for t in range(TT):
                rstd(("mem2", t), False)
            dw = parc("conv_dw").rearrange("p (c w) -> p c w", c=2)
            pool.wait_ge(*drained(("ug0",)))
            link(pool.tensor_scalar(conv_y[:, 1, :], y_pad[:, 1, 0:SEQ], dw[:, 1, 0:1], parc("dw_b")[:, 1:2], ALU.mult, ALU.add))

            def conv_taps(first, end):
                for w in range(first, end):
                    term = conv_term[w % 2]
                    link(pool.tensor_scalar(term, y_pad[:, 1, w:w + SEQ], dw[:, 1, w:w + 1], None, ALU.mult))
                    ins = pool.tensor_tensor(conv_y[:, 1, :], conv_y[:, 1, :], term, ALU.add)
                    if w == CONV_TAPS - 1:
                        ins.then_inc(conv_out, 1)
                    else:
                        link(ins)

            def causal_index(t):
                pool.wait_ge(idx_sum, t + 1)
                pool.affine_select(out=idx_score[t], in_=idx_score[t], compare_op=ALU.is_ge, fill=FUTURE, base=P * t,
                                   pattern=[[-1, P * (t + 1)]], channel_multiplier=1).then_inc(idx_causal, 1)

            conv_taps(1, 18)
            causal_index(0)
            conv_taps(18, 21)
            causal_index(1)
            conv_taps(21, CONV_TAPS)
            for t in range(TT):
                pool.wait_ge(picked, t + 1)
                link(pool.tensor_scalar(dmask[t], idx_score[t], -3.2e38, 1.0, ALU.is_le, ALU.subtract))
                link(pool.tensor_scalar(dmask[t], dmask[t], -MASKED, None, ALU.mult))
                pool.affine_select(out=dmask[t], in_=dmask[t], compare_op=ALU.is_ge, fill=MASKED, base=P * t,
                                   pattern=[[-1, P * (t + 1)]], channel_multiplier=1).then_inc(dmask_ready, 1)
            for t in range(TT):
                pool.wait_ge(gamma_exp, t + 1)
                for h in range(GDN_HEADS):
                    pool.tensor_tensor(inv[t][:, h, :], Y[t][:, h, :], conc("tri_strict"), ALU.mult)
                for h in range(GDN_HEADS):
                    ins = pool.tensor_tensor(Y[t][:, h, :], Y[t][:, h, :], conc("tri_incl"), ALU.mult)
                ins.then_inc(gamma_ready, 1)
            masks = conc("levels").rearrange("p (l j) -> p l j", l=LEVELS)
            for level in range(LEVELS):
                if level == 1:
                    pool.wait_ge(*full(("do",)))
                elif level == 2:
                    pool.wait_ge(first_invT, TT)
                for t in range(TT):
                    pool.wait_ge(*(full(("y", level - 2, t)) if level >= 2 else drained(("kk", t))))
                    pool.tensor_tensor(AT_level[level % 2][t], AT[t], masks[:, level, :].unsqueeze(1).broadcast_to(
                        [P, GDN_HEADS, P]), ALU.mult).then_inc(level_masked, 1)
            for stage in ("cross", "mlp"):
                for t in range(TT):
                    rstd((stage, t), False)

        @block.scalar
        def _(act):
            chain = [0]

            def link(ins):
                chain[0] += 1
                ins.then_inc(act_chain, 1)
                act.wait_ge(act_chain, chain[0])

            def square(name, views):
                if STATI[name]:
                    act.wait_ge(squares, STATI[name])
                for j, v in enumerate(views):
                    ins = act.activation(junk[:, 0:v.shape[-1]], v, ACT.Square, accum_out=stat(name, j))
                    if j < len(views) - 1:
                        link(ins)
                ins.then_inc(squares, 1)

            def drain(name, dst, src, func=ACT.Copy, **kw):
                act.wait_ge(*full(name))
                return act.activation(dst, src, func, **kw)

            split_done = [0]

            def high_parts(last):
                while split_done[0] < min(last + 1, len(split_units)):
                    i = split_done[0]
                    u = split_units[i]
                    act.wait_ge(*loaded(u))
                    if held_before[u] is not None:
                        act.wait_ge(*LAST_OF_UNIT[held_before[u]])
                    act.activation(slot_of(u)[:, 0, :], weights(u, 2048), ACT.Copy).then_inc(high_ready, 1)
                    split_done[0] += 1

            def high_rows(stage):
                for t in range(TT):
                    for half in range(2):
                        act.wait_ge(*drained(("normT", stage, t, half)))
                        act.activation(act_s[stage][0][:, 4 * half:4 * half + 4, P * t:P * t + P],
                                       hT[:, 4 * half:4 * half + 4, P * t:P * t + P], ACT.Copy).then_inc(acts_high, 1)

            for t in range(TT):
                act.wait_ge(x_in[t], 16)
                square(("mix", t), [x[:, t, :]])
            high_parts(upto("q0"))
            high_rows("mix")
            high_parts(upto("kcvc"))

            def halves(name):
                return bank(name)[:, :].rearrange("p (c t) -> p c t", c=2)

            for i in range(2):
                name = (f"q{i}",)
                drain(name, qT[:, 2 * i:2 * i + 2, :], halves(name), scale=DK ** -0.5).then_inc(reader(name), 1)
                high_parts(upto("kskw") + i)
            drain(("kcvc",), kcvcT, halves(("kcvc",))).then_inc(reader(("kcvc",)), 1)
            act.wait_ge(*full(("normT", "mix", 1, 1)))
            act.dma_start(xn[:, :, :], a["mem"].rearrange("(t p) d -> p t d", p=P)).then_inc(mem_in, 16)
            act.wait_ge(*drained(("kcvc",)))
            for g in range(GROUPS):
                src = kcvcT[DK * g:DK * g + DK]
                act.dma_start(pairs[0:DK, :, g, :], src).then_inc(shifted_in, 16)
                act.dma_start(pairs[DK:P, :, g, 0:SEQ - 1], src[:, :, 1:SEQ]).then_inc(shifted_in, 16)
            high_parts(upto("pool"))
            drain(("kskw",), keysT, halves(("kskw",))).then_inc(reader(("kskw",)), 1)
            high_parts(upto("u"))
            drain(("vsvw",), values.rearrange("p j t d -> p t j d"),
                  bank(("vsvw",))[:, :].rearrange("p (t j d) -> p t j d", t=TT, j=2)).then_inc(reader(("vsvw",)), 1)
            high_parts(upto("v"))
            drain(("gates",), gates.rearrange("p t h b -> p t (h b)"),
                  bank(("gates",))[:, 0:48].rearrange("p (t n) -> p t n", t=TT), ACT.Sigmoid).then_inc(reader(("gates",)), 1)
            drain(("pool",), pool_a[:, :, 16:272], halves(("pool",))).then_inc(reader(("pool",)), 1)
            drain(("u",), uT, halves(("u",)), ACT.Gelu_apprx_tanh).then_inc(reader(("u",)), 1)
            drain(("v",), v_g, halves(("v",)), ACT.Gelu_apprx_tanh).then_inc(reader(("v",)), 1)
            act.wait_ge(*full(("cmp_h",)))
            b1 = parc("cmp_b1")
            for kv in range(2):
                ins = act.activation(cmp_hT[:, kv, 0:30], bank(("cmp_h",))[:, 32 * kv:32 * kv + 30],
                                     ACT.Gelu_apprx_tanh, bias=b1[:, kv:kv + 1])
            ins.then_inc(reader(("cmp_h",)), 1)

            act.wait_ge(mem_in, 16)
            for t in range(TT):
                square(("memkv", t), [xn[:, t, :]])
            high_parts(upto(("mk", 1)))

            n = 0
            for t in range(TT):
                for h in HEAD_ORDER:
                    n += 1
                    act.wait_ge(neg_max, n + t + 1)
                    if h == 0:
                        for hh in range(HEADS):
                            ins = act.activation(cmp_p[:, t, hh, 0:NCMP], cmp_p[:, t, hh, 0:NCMP], ACT.Exp,
                                                 bias=soft[:, t, 0, hh, 0:1], accum_out=soft[:, t, 1, hh, 0:1])
                        ins.then_inc(exped, 1)
                    for j in range(2):
                        ins = act.activation(probs[t][h][:, j, :], probs[t][h][:, j, :], ACT.Exp,
                                             bias=soft[:, t, 0, h, j + 1:j + 2], accum_out=soft[:, t, 1, h, j + 1:j + 2])
                    ins.then_inc(exped, 1)
            high_rows("memkv")
            for c in range(4):
                high_parts(upto(("mk", 2)) + c)
                drain(("mk", c), kmT[:, 2 * c:2 * c + 2, :], halves(("mk", c))).then_inc(reader(("mk", c)), 1)
            high_parts(upto(("mv", 3)))
            for t in range(TT):
                for half in range(2):
                    f = ("mv", 2 * t + half)
                    act.wait_ge(*acc_filled(f))
                    act.activation(vm[:, t, 512 * half:512 * half + 512], acc(f)[:, :], ACT.Copy).then_inc(acc_read, 1)
            def high_mix(product, c, src, ready=None):
                if ready is not None:
                    act.wait_ge(*ready)
                act.activation(act_s[product][0][:, 2 * c:2 * c + 2, :], src, ACT.Copy).then_inc(acts_high, 1)

            high_parts(upto(("out", MIX_ORDER[1])))
            for i in range(2):
                act.wait_ge(*acc_filled(("o", i)))
            act.wait_ge(mix_tail, 1)
            act.wait_ge(*drained(("pool_out",)))
            for c in MIX_ORDER:
                high_mix("out", c, mixT[:, 2 * c:2 * c + 2, :] if c >= 2 else
                         acc(("o", c))[:, :].rearrange("p (c t) -> p c t", c=2))
            high_parts(upto(("mq", 1)))

            def post_squares(product, stage):
                for t in range(TT):
                    act.wait_ge(*acc_filled((product, 2 * t + 1)))
                    square((stage, t), [acc((product, 2 * t + half))[:, :] for half in range(2)])

            def next_squares(stage, n_updates):
                for t in range(TT):
                    act.wait_ge(x_done, n_updates + t + 1)
                    square((stage, t), [x[:, t, :]])

            post_squares("out", "out_post")
            high_parts(upto(("mq", 2)))
            next_squares("mem", 0)
            high_rows("mem")
            for c in range(4):
                drain(("mq", c), qmT[:, 2 * c:2 * c + 2, :], halves(("mq", c)), scale=MEM_DIM ** -0.5).then_inc(reader(("mq", c)), 1)
                if c < 2:
                    high_parts(upto(("mq", 3)) + c)
            m = HEADS * TT + TT
            for t in range(TT):
                for hp in range(2):
                    m += 1
                    act.wait_ge(neg_max, m)
                    for j in range(2):
                        h = 2 * hp + j
                        ins = act.activation(mprobs[t][:, h, :], bank(("ms", t, hp))[:, SEQ * j:SEQ * j + SEQ], ACT.Exp,
                                             bias=msoft[:, t, 0, h:h + 1], accum_out=msoft[:, t, 1, h:h + 1])
                    ins.then_inc(reader(("ms", t, hp)), 1)
            high_parts(upto(("wo", 2)))
            for c in range(4):
                high_mix("wo", c, halves(("mo", c)), full(("mo", c)))
            high_parts(upto(("up", 1)))
            post_squares("wo", "wo_post")
            high_parts(upto(("up", 2)))
            next_squares("ffn", 2)
            high_rows("ffn")
            cw = parc("conv_w").rearrange("p (j g w) -> p j g w", g=2, w=3)
            cb = parc("conv_b").rearrange("p (j g) -> p j g", g=2)

            def last_tap(j):
                name = ("up", j)
                act.wait_ge(*full(name))
                if j >= 3:
                    act.wait_ge(gated, j - 2)
                for g in range(2):
                    ins = act.activation(conv[j % 3][:, g, :], bank(name)[:, SEQ * g:SEQ * g + SEQ], ACT.Identity,
                                         scale=cw[:, j, g, 2:3], bias=cb[:, j, g:g + 1])
                ins.then_inc(tap2, 1)

            def gate_gelu(j):
                act.wait_ge(*drained(("up", j)))
                if j >= 2:
                    act.wait_ge(gated, j - 1)
                act.activation(act_g[j % 2], conv[j % 3][:, 0, :], ACT.Gelu_apprx_tanh).then_inc(gate_act, 1)

            for j in range(FFN_PAIRS + 1):
                if j < FFN_PAIRS:
                    high_parts(min(upto(("up", j)) + ffn_ahead(j), last_down))
                    last_tap(j)
                    high_parts(min(before(("up", j + 1)) + ffn_ahead(j + 1), last_down))
                if j >= 1:
                    gate_gelu(j - 1)
            post_squares("down", "down_post")
            high_parts(upto("ug1"))
            next_squares("mix2", 4)
            high_rows("mix2")

            def across_squares(tag):
                raw, sq = chunk2[tag][:2]
                act.activation(sq, raw, ACT.Square).then_inc(across_sq, 1)

            def across_root(tag):
                raw, sq, scale, bias, _ = chunk2[tag]
                name = ("across", tag)
                act.wait_ge(*full(name))
                src = bank(name)[:, 0:SEQ] if tag == "dk" else halves(name)
                act.activation(sq, src, ACT.Sqrt, scale=scale, bias=eps_col(bias)).then_inc(reader(name), 1)

            act.wait_ge(*full(("normT", "mix2", 1, 1)))
            act.dma_start(xn[:, :, :], a["mem2"].rearrange("(t p) d -> p t d", p=P)).then_inc(mem2_in, 16)
            high_parts(upto("cq"))
            drain(("ug1",), gate_s, halves(("ug1",)), ACT.Sigmoid).then_inc(reader(("ug1",)), 1)
            act.wait_ge(mem2_in, 16)
            for t in range(TT):
                square(("mem2", t), [xn[:, t, :]])
            high_parts(upto("ck"))
            drain(("cq",), cqT, halves(("cq",))).then_inc(reader(("cq",)), 1)
            high_parts(upto(("qkv", 0)))
            drain(("ck",), ckvT, bank(("ck",))[:, 0:SEQ])
            act.activation(kidxT, bank(("ck",))[:, SEQ:512], ACT.Copy).then_inc(reader(("ck",)), 1)
            high_parts(upto(("qkv", 1)))
            name = ("abw",)
            abw = bank(name)[:, 0:24].rearrange("p (t n) -> p t n", t=TT)
            drain(name, ab_cols, abw[:, :, 0:8])
            act.activation(w_idx, abw[:, :, 8:12], ACT.Copy, scale=1.0 / 16).then_inc(reader(name), 1)
            drain(("ab",), row_tmp[0:4, 0, :], bank(("ab",))[0:4, 0:SEQ], ACT.Identity, bias=parc("dt_bias")[0:4, :])
            act.activation(gate_rows[0:4, 0, :], bank(("ab",))[0:4, SEQ:512], ACT.Sigmoid).then_inc(reader(("ab",)), 1)
            act.wait_ge(*drained(("ab",)))
            link(act.activation(row_tmp[0:4, 1, :], row_tmp[0:4, 0, :], ACT.Abs))
            link(act.activation(row_tmp[0:4, 1, :], row_tmp[0:4, 1, :], ACT.Exp, scale=-1.0))
            act.activation(a_rate[0:4, :], parc("a_log")[0:4, :], ACT.Exp)
            act.activation(row_tmp[0:4, 1, :], row_tmp[0:4, 1, :], ACT.Ln, bias=1.0).then_inc(softplus_ln, 1)
            drain(("dq",), dqT, halves(("dq",))).then_inc(reader(("dq",)), 1)
            drain(("dqi",), dqiT, halves(("dqi",))).then_inc(reader(("dqi",)), 1)
            drain(("dk",), dkT, bank(("dk",))[:, 0:SEQ])
            act.activation(dv, bank(("dk",))[:, SEQ:SEQ + P].rearrange("p (t d) -> p t d", t=TT), ACT.Copy
                           ).then_inc(reader(("dk",)), 1)
            act.wait_ge(*drained(("dk",)))
            across_squares("dq")
            across_squares("dk")
            gconv = parc("gdn_conv").rearrange("p (c w) -> p c w", w=4)

            def gdn_last_tap(i):
                name = ("qkv", i)
                act.wait_ge(*full(name))
                for c in range(2):
                    ins = act.activation(qkv[:, 2 * i + c, :], bank(name)[:, SEQ * c:SEQ * c + SEQ], ACT.Copy,
                                         scale=gconv[:, 2 * i + c, 3:4])
                ins.then_inc(tap3, 1)

            def gdn_silu(i):
                act.wait_ge(*drained(("qkv", i)))
                act.activation(qkv[:, 2 * i:2 * i + 2, :], qkv[:, 2 * i:2 * i + 2, :], ACT.Silu).then_inc(silu_done, 1)

            gdn_last_tap(0)
            high_parts(upto(("qkv", 2)))
            across_root("dq")
            across_root("dk")
            for t in range(TT):
                for par in range(2):
                    name = ("il", t, par)
                    n = P * (t + 1)
                    drain(name, relu_l[t][par], bank(name)[:, 0:2 * n].rearrange("p (j s) -> p j s", j=2), ACT.Relu
                          ).then_inc(reader(name), 1)
            act.wait_ge(decay_sum, 1)
            link(act.activation(row_tmp[0:4, 0, :], gate_rows[0:4, 3, :], ACT.Exp))
            act.activation(gate_rows[0:4, 2, :], gate_rows[0:4, 2, :], ACT.Exp).then_inc(decay_exp, 1)
            for i in range(1, 6):
                high_parts(upto(("qkv", i)) + 2)
                gdn_last_tap(i)
                gdn_silu(i - 1)
            gdn_silu(5)
            for t in range(TT):
                act.wait_ge(rstd_ready, STATI[("mem2", t)] + 1)
                act.activation(xn[:, t, :], xn[:, t, :], ACT.Copy, scale=stat(("mem2", t))).then_inc(normed, 1)
            for i in range(2):
                drain(("z", i), zT[:, 2 * i:2 * i + 2, :], halves(("z", i)), ACT.Silu).then_inc(reader(("z", i)), 1)
            act.wait_ge(*drained(("ln_mean",)))
            act.activation(conv_sq, conv_y, ACT.Square).then_inc(conv_sq_ready, 1)

            def row_square(tag):
                raw, sq, n = ROWS[tag][:3]
                for i in range(0, n, 2):
                    ins = act.activation(sq[:, i:i + 2, :], raw[:, i:i + 2, :], ACT.Square)
                ins.then_inc(row_squares, 1)

            def row_root(tag):
                _, _, n, scale, bias, roots = ROWS[tag]
                name = ("row_sum", tag)
                drain(name, roots, bank(name)[0:n, 0:SEQ], ACT.Sqrt, scale=scale, bias=bias).then_inc(reader(name), 1)

            act.wait_ge(silu_done, 6)
            row_square("l")
            drain(("xk", 0), xkT[:, 0:2, :], halves(("xk", 0))).then_inc(reader(("xk", 0)), 1)
            row_root("l")
            n = 0
            for t in range(TT):
                for par in range(2):
                    n += 1
                    act.wait_ge(d_max, n)
                    for j in range(2):
                        h = 2 * j + par
                        ins = act.activation(dprobs[t][:, h, :], dprobs[t][:, h, :], ACT.Exp, bias=dsoft[:, t, 0, h:h + 1],
                                             accum_out=dsoft[:, t, 1, h:h + 1])
                    ins.then_inc(d_exp, 1)
            name = ("ln_var",)
            drain(name, conv_sq[:, 0, :], bank(name)[:, 0:SEQ], ACT.Sqrt, scale=1.0 / SEQ, bias=eps_col(EPS)
                  ).then_inc(reader(name), 1)
            drain(("xk", 1), xkT[:, 2:4, :], halves(("xk", 1))).then_inc(reader(("xk", 1)), 1)
            act.wait_ge(*drained(("xk", 1)))
            row_square("xk")
            for i in range(2):
                act.wait_ge(gamma_diff, i + 1)
                drain(("dr", i), exp_decay[:, 2 * i:2 * i + 2, :], halves(("dr", i)), ACT.Exp
                      ).then_inc(reader(("dr", i)), 1)
            act.wait_ge(gamma_diff, 2)
            for t in range(TT):
                act.activation(Y[t], Y[t], ACT.Exp).then_inc(gamma_exp, 1)
            row_root("xk")
            act.wait_ge(conv_norm, 1)
            for c in range(2):
                ins = act.activation(mixT[:, 6 + c, :], conv_y[:, c, :], ACT.Silu, scale=parc("ln_g")[:, c:c + 1],
                                     bias=parc("ln_b")[:, c:c + 1])
            ins.then_inc(conv_mix, 1)
            drain(("do",), mixT[:, 4:6, :], halves(("do",))).then_inc(reader(("do",)), 1)
            for level in range(1, LEVELS):
                for t in range(TT):
                    name = ("y", level, t)
                    drain(name, Y[t], bank(name)[:, :].rearrange("p (h d) -> p h d", h=GDN_HEADS)).then_inc(reader(name), 1)
            for t in range(TT):
                drain(("gu", t), u_n[t], bank(("gu", t))[:, :].rearrange("p (h d) -> p h d", h=GDN_HEADS)
                      ).then_inc(reader(("gu", t)), 1)
            for t in range(TT):
                drain(("gw", t), wT[t], bank(("gw", t))[:, :].rearrange("p (h d) -> p h d", h=GDN_HEADS)
                      ).then_inc(reader(("gw", t)), 1)
            high_parts(upto(("out2", MIX_ORDER[0])))
            for n in range(NCHUNK):
                name = ("go", n)
                drain(name, oT[:, :, CHUNK * n:CHUNK * n + CHUNK],
                      bank(name)[:, 0:4 * CHUNK].rearrange("p (h i) -> p h i", h=GDN_HEADS)).then_inc(reader(name), 1)
            act.wait_ge(*drained(("go", NCHUNK - 1)))
            row_square("o")
            row_root("o")
            high_parts(upto(("out2", MIX_ORDER[1])))
            for t in range(TT):
                act.wait_ge(*acc_filled(("xv", t)))
                act.activation(xv[:, t, :], acc(("xv", t))[:, :], ACT.Copy).then_inc(acc_read, 1)
            act.wait_ge(conv_mix, 1)
            act.wait_ge(*drained(("do",)))
            for c in MIX_ORDER:
                high_mix("out2", c, mixT[:, 2 * c:2 * c + 2, :], None if c >= 2 else drained(("row_all", "o", c)))
            high_parts(upto(("xq", 1)))

            def squares_of_sum(product, stage):
                for t in range(TT):
                    act.wait_ge(*acc_drained((product, 2 * t + 1)))
                    square((stage, t), [x[:, t, :]])

            squares_of_sum("out2", "cross")
            high_rows("cross")
            high_parts(upto(("xwo", 0)))
            for i in range(2):
                name = ("xq", i)
                drain(name, xq_sq[:, 2 * i:2 * i + 2, :], halves(name), ACT.Square).then_inc(xq_squares, 1)
                act.activation(xqT[:, 2 * i:2 * i + 2, :], halves(name), ACT.Copy, scale=parc("xq_norm")
                               ).then_inc(reader(name), 1)
            drain(("xq_sums",), xq_root, bank(("xq_sums",))[:, 0:8].rearrange("p (t h) -> p t h", t=TT), ACT.Sqrt,
                  bias=eps_col(P * EPS)).then_inc(reader(("xq_sums",)), 1)
            n = 0
            for t in range(TT):
                for hp in range(2):
                    n += 1
                    act.wait_ge(x_max, n)
                    for j in range(2):
                        h = 2 * hp + j
                        ins = act.activation(xprobs[t][:, h, :], bank(("xs", t, hp))[:, SEQ * j:SEQ * j + SEQ], ACT.Exp,
                                             scale=xq_root[:, t, h:h + 1], bias=xsoft[:, t, 0, h:h + 1],
                                             accum_out=xsoft[:, t, 1, h:h + 1])
                    ins.then_inc(reader(("xs", t, hp)), 1)
            high_parts(upto(("m1", 0)))
            for c in range(2):
                high_mix("xwo", c, halves(("xo", c)), full(("xo", c)))
            high_parts(upto(("m1", 1)))
            squares_of_sum("xwo", "mlp")
            high_rows("mlp")
            high_parts(upto(("m1", 2)))
            for j in range(MLP_UNITS):
                high_parts(upto(("m1", j)) + 3)
                if j >= 2:
                    act.wait_ge(relu_sq, j - 1)
                drain(("m1", j), relu_h[j % 2], halves(("m1", j)), ACT.Relu).then_inc(reader(("m1", j)), 1)
                act.wait_ge(*drained(("m1", j)))
                if j >= 3:
                    act.wait_ge(unit_spent, SPENT[("m2", j - 3)])
                act.activation(relu2_s[j % 3][:, 0], relu_h[j % 2], ACT.Square).then_inc(relu_high, 1)
                high_parts(before(("m1", j + 1)) + 3)
            high_parts(len(split_units) - 1)

        @block.vector
        def _(dve):
            chain = [0]

            def link(ins):
                chain[0] += 1
                ins.then_inc(dve_chain, 1)
                dve.wait_ge(dve_chain, chain[0])

            def scale_rows(stage, src, meanwhile=None):
                for t in range(TT):
                    if t == 1 and meanwhile is not None:
                        low_parts(meanwhile)
                    dve.wait_ge(rstd_ready, STATI[(stage, t)] + 1)
                    dve.tensor_scalar(xn[:, t, :], src(t), stat((stage, t)), None, ALU.mult).then_inc(normed, 1)

            def drain_norm(stage):
                free = hT_free[stage]
                if free is not None:
                    dve.wait_ge(*free)
                pieces = [(t, half) for t in range(TT) for half in range(2)]

                def low_rows(t, half):
                    high, low = act_s[stage]
                    at = slice(4 * half, 4 * half + 4), slice(P * t, P * t + P)
                    dve.wait_ge(*high_there(("rows", stage, t, half)))
                    dve.tensor_tensor(low[:, *at], hT[:, *at], high[:, *at], ALU.subtract).then_inc(acts_low, 1)

                for t, half in pieces:
                    name = ("normT", stage, t, half)
                    dve.wait_ge(*full(name))
                    g = gains[:, GAIN[stage], 4 * half:4 * half + 4].unsqueeze(2).broadcast_to([P, 4, P])
                    dve.tensor_tensor(hT[:, 4 * half:4 * half + 4, P * t:P * t + P],
                                      bank(name)[:, :].rearrange("p (k t) -> p k t", k=4), g,
                                      ALU.mult).then_inc(reader(name), 1)
                if stage in SPLIT_STAGES:
                    for t, half in pieces:
                        low_rows(t, half)

            split_done = [0]

            def low_parts(last):
                while split_done[0] < min(last + 1, len(split_units)):
                    i = split_done[0]
                    dve.wait_ge(high_ready, i + 1)
                    slot = slot_of(split_units[i])
                    dve.tensor_tensor(slot[:, 1, :], weights(split_units[i], 2048), slot[:, 0, :], ALU.subtract
                                      ).then_inc(low_ready, 1)
                    split_done[0] += 1

            scale_rows("mix", lambda t: x[:, t, :])
            dve.wait_ge(first_params_in, 16)
            drain_norm("mix")
            low_parts(upto("kcvc"))
            low_parts(upto("kskw"))
            dve.wait_ge(*full(("bias_row",)))
            dve.tensor_copy(bias_rows[0:HEADS, :], bank(("bias_row",))[0:HEADS, 0:384]).then_inc(reader(("bias_row",)), 1)
            low_parts(upto("pool"))
            dve.wait_ge(shifted_in, 64)
            pos = parc("cmp_pos").rearrange("p (v j) -> p v j", v=2)
            for kv in range(2):
                for g in range(GROUPS):
                    v = pairs[:, kv, g, :].rearrange("p (c j e) -> p j c e", j=8, e=2)
                    for hi in range(2):
                        ins = dve.tensor_tensor(blocks[:, kv, 8 * hi:8 * hi + 8, g, :], v[:, :, hi:hi + NCMP, 0],
                                                pos[:, kv, 8 * hi:8 * hi + 8].unsqueeze(2).broadcast_to([P, 8, NCMP]), ALU.add)
            ins.then_inc(blocks_ready, 1)
            low_parts(upto("v"))
            for t in range(TT):
                dve.wait_ge(*drained(("v",)))
                link(dve.bn_stats(soft.rearrange("p t a h b -> p (t a h b)")[:, 6 * t:6 * t + 6], v_g[:, t, :]))
                dve.bn_aggr(stats[:, 2 * STATI[("sgu", t)]:2 * STATI[("sgu", t)] + 2],
                            soft.rearrange("p t a h b -> p (t a h b)")[:, 6 * t:6 * t + 6]).then_inc(sgu_stat, 1)
            for t in range(TT):
                dve.wait_ge(sgu_rstd, t + 1)
                link(dve.tensor_scalar(v_n[:, t, :], v_g[:, t, :], stat(("sgu", t)), stat(("sgu", t), 1),
                                       ALU.subtract, ALU.mult))
                link(dve.tensor_tensor(v_n[:, t, :], v_n[:, t, :], parc("sgu_g"), ALU.mult))
                dve.tensor_tensor(v_n[:, t, :], v_n[:, t, :], parc("sgu_b"), ALU.add).then_inc(sgu_normed, 1)
            name = ("cmp_kv",)
            dve.wait_ge(*full(name))
            dve.tensor_scalar(cmp_kT, bank(name)[:, 0:NCMP], parc("cmp_b2k"), None, ALU.add)
            for j in range(4):
                rows_j = slice(32 * j, 32 * j + NCMP)
                ins = dve.tensor_tensor(cmp_v[rows_j, :], bank(name)[rows_j, 64:64 + P], parc("cmp_b2v")[rows_j, :], ALU.add)
            ins.then_inc(reader(name), 1)

            scale_rows("memkv", lambda t: xn[:, t, :])
            dve.memset(cmp_bias[:, 0, :, :], MASKED).then_inc(cmp_biases, 1)
            dve.wait_ge(bias_tile_in, 16)
            dve.wait_ge(cmp_biases, 1)
            for t in range(TT):
                first = P * t + P - CMP_LEN
                n = first // CMP_STRIDE + 1
                dve.tensor_copy(cmp_bias[:, t, :, 0:n], toeplitz[:, :, 0:first + 1:CMP_STRIDE][:, :, ::-1]
                                ).then_inc(cmp_biases, 1)
            dve.wait_ge(cmp_biases, 3)
            for t in range(TT):
                if t == 0:
                    dve.memset(cmp_p.rearrange("p t h c -> p (t h c)"), 0.0).then_inc(scored, 1)
                    dve.wait_ge(scored, 1)
                for g in range(GROUPS):
                    name = ("cmp_s", t, g)
                    hs = slice(HG * g, HG * g + HG)
                    dve.wait_ge(*full(name))
                    dve.tensor_tensor(cmp_p[:, t, hs, 0:NCMP],
                                      bank(name)[:, 0:HG * NCMP].rearrange("p (h c) -> p h c", h=HG),
                                      cmp_bias[:, t, hs, :], ALU.add).then_inc(reader(name), 1)
                dve.wait_ge(*drained(name))
                link(dve.tensor_reduce(soft[:, t, 0, :, 0], cmp_p[:, t, :, 0:NCMP], AX, ALU.max))
                dve.tensor_scalar(soft[:, t, 0, :, 0], soft[:, t, 0, :, 0], MASKED / 2, -1.0, ALU.max, ALU.mult
                                  ).then_inc(neg_max, 1)
                for h in HEAD_ORDER:
                    name = ("s", t, h)
                    n = P * (t + 1)
                    dve.wait_ge(*full(name))
                    dve.tensor_tensor(probs[t][h], bank(name)[:, 0:2 * n].rearrange("p (j s) -> p j s", j=2),
                                      toeplitz[:, h, 0:n][:, ::-1].unsqueeze(1).broadcast_to([P, 2, n]), ALU.add
                                      ).then_inc(reader(name), 1)
                    dve.wait_ge(*drained(name))
                    dve.tensor_reduce(soft[:, t, 0, h, 1:3], probs[t][h], AX, ALU.max, negate=True).then_inc(neg_max, 1)
                low_parts(upto(("mk", 0)) + t)
            name = ("pool_out",)
            dve.wait_ge(*full(name))
            dve.tensor_tensor(mixT[:, 4:6, :], bank(name)[:, :].rearrange("p (c t) -> p c t", c=2),
                              parc("pool_scale").unsqueeze(2).broadcast_to([P, 2, SEQ]), ALU.mult).then_inc(reader(name), 1)
            name = ("sgu_out",)
            dve.wait_ge(*full(name))
            for c in range(2):
                ins = dve.tensor_tensor(mixT[:, 6 + c, :].rearrange("p (t i) -> p t i", t=TT),
                                        bank(name)[:, SEQ * c:SEQ * c + SEQ].rearrange("p (t i) -> p t i", t=TT),
                                        parc("sgu_bias")[:, P * c:P * c + P].unsqueeze(1).broadcast_to([P, TT, P]), ALU.add)
            ins.then_inc(reader(name), 1)
            dve.wait_ge(*drained(name))
            dve.wait_ge(*drained(("u",)))
            dve.tensor_tensor(mixT[:, 6:8, :], mixT[:, 6:8, :], uT, ALU.mult).then_inc(mix_tail, 1)
            drain_norm("memkv")
            low_parts(upto(("mk", 2)))
            for t in range(TT):
                dve.wait_ge(exped, (HEADS + 1) * (t + 1))
                den = soft[:, t, 1, :, 0:3]
                link(dve.tensor_scalar(den, den, 1.0, None, ALU.max))
                link(dve.reciprocal(den, den))
                link(dve.tensor_tensor(den, den, gates[:, t, :, :], ALU.mult))
                dve.tensor_tensor(cmp_p[:, t, :, 0:NCMP], cmp_p[:, t, :, 0:NCMP],
                                  den[:, :, 0:1].broadcast_to([P, HEADS, NCMP]), ALU.mult).then_inc(weighed, 1)
                for h in range(HEADS):
                    dve.tensor_tensor(probs[t][h], probs[t][h],
                                      den[:, h, 1:3].unsqueeze(2).broadcast_to([P, 2, P * (t + 1)]), ALU.mult
                                      ).then_inc(weighed, 1)
                    if h % 4 == 3:
                        low_parts(upto(("mk", 3)) + 2 * t + h // 4)
            low_parts(upto(("mv", 3)))
            for t in range(TT):
                name = ("cmp_pT", t)
                dve.wait_ge(*full(name))
                dve.tensor_copy(cmp_pT[:, :, P * t:P * t + P], bank(name)[:, 0:SEQ].rearrange("p (g t) -> p g t", g=GROUPS)
                                ).then_inc(reader(name), 1)
            for h in range(HEADS):
                if h in (2, 5):
                    low_parts(upto(("out", MIX_ORDER[int(h == 5)])))
                if h >= 2:
                    k = h - 2
                    dve.wait_ge(*(acc_filled(("o", k // 4)) if k % 4 == 3 else (heads_done, k - k // 4 + 1)))
                for t in range(TT):
                    name = ("pT", t, h)
                    n = t + 1
                    dve.wait_ge(*full(name))
                    dve.tensor_copy(probsT[h % 2][:, :, 0:n, P * t:P * t + P],
                                    bank(name)[:, 0:SEQ * n].rearrange("p (j s t) -> p j s t", j=2, s=n)
                                    ).then_inc(reader(name), 1)

            def post_norm(product, stage, n_gain):
                dve.wait_ge(gain_in, 16 * n_gain)
                for t in range(TT):
                    dve.wait_ge(rstd_ready, STATI[(stage, t)] + 1)
                    for half in range(2):
                        c = slice(512 * half, 512 * half + 512)
                        dve.scalar_tensor_tensor(out=xn[:, t, c], in0=acc((product, 2 * t + half))[:, :],
                                                 scalar=stat((stage, t)), in1=post_gain[:, c], op0=ALU.mult,
                                                 op1=ALU.mult).then_inc(acc_read, 1)
                    dve.wait_ge(*acc_drained((product, 2 * t + 1)))
                    dve.tensor_tensor(x[:, t, :], x[:, t, :], xn[:, t, :], ALU.add).then_inc(x_done, 1)
                    dve.wait_ge(x_done, 2 * (n_gain - 1) + t + 1)

            def low_mix(product, c, src):
                dve.wait_ge(*high_there(("mix", product, c)))
                high, low = act_s[product]
                return dve.tensor_tensor(low[:, 2 * c:2 * c + 2, :], src, high[:, 2 * c:2 * c + 2, :], ALU.subtract)

            for c in MIX_ORDER:
                low_mix("out", c, mixT[:, 2 * c:2 * c + 2, :] if c >= 2 else
                        acc(("o", c))[:, :].rearrange("p (c t) -> p c t", c=2)
                        ).then_inc(acts_low if c >= 2 else acc_read, 1)
            low_parts(upto(("mq", 1)))
            post_norm("out", "out_post", 1)
            scale_rows("mem", lambda t: x[:, t, :], upto(("mq", 2)))
            drain_norm("mem")
            low_parts(upto(("wo", 0)))
            for t in range(TT):
                for hp in range(2):
                    dve.wait_ge(*full(("ms", t, hp)))
                    dve.tensor_reduce(msoft[:, t, 0, 2 * hp:2 * hp + 2],
                                      bank(("ms", t, hp))[:, :].rearrange("p (h s) -> p h s", h=2), AX, ALU.max,
                                      negate=True).then_inc(neg_max, 1)
            for t in range(TT):
                for hp in range(2):
                    dve.wait_ge(*drained(("ms", t, hp)))
                    den = msoft[:, t, 1, 2 * hp:2 * hp + 2]
                    link(dve.reciprocal(den, den))
                    dve.tensor_tensor(mprobs[t][:, 2 * hp:2 * hp + 2, :], mprobs[t][:, 2 * hp:2 * hp + 2, :],
                                      den.unsqueeze(2).broadcast_to([P, 2, SEQ]), ALU.mult).then_inc(weighed, 1)
            for t in range(TT):
                for hp in range(2):
                    name = ("mpT", t, hp)
                    dve.wait_ge(*full(name))
                    dve.tensor_copy(mprobsT[:, 2 * hp:2 * hp + 2, :, P * t:P * t + P],
                                    bank(name)[:, :].rearrange("p (h s t) -> p h s t", h=2, s=TT)
                                    ).then_inc(reader(name), 1)
            low_parts(upto(("wo", 2)))
            for c in range(4):
                low_mix("wo", c, bank(("mo", c))[:, :].rearrange("p (c t) -> p c t", c=2)).then_inc(reader(("mo", c)), 1)
            low_parts(upto(("up", 1)))
            post_norm("wo", "wo_post", 2)
            scale_rows("ffn", lambda t: x[:, t, :], upto(("up", 2)))
            drain_norm("ffn")
            cw = parc("conv_w").rearrange("p (j g w) -> p j g w", g=2, w=3)

            def taps(j):
                name = ("up", j)
                dve.wait_ge(tap2, j + 1)
                for s in (1, 2):
                    for g in range(2):
                        c = conv[j % 3][:, g, s:SEQ]
                        ins = dve.scalar_tensor_tensor(out=c, in0=bank(name)[:, SEQ * g:SEQ * g + SEQ - s],
                                                       scalar=cw[:, j, g, 2 - s:3 - s], in1=c, op0=ALU.mult, op1=ALU.add)
                    if s == 1:
                        link(ins)
                ins.then_inc(reader(name), 1)

            def gate_times_value(j):
                dve.wait_ge(gate_act, j + 1)
                if j >= 4:
                    dve.wait_ge(unit_spent, SPENT[("down", (j - 4) // 2)])
                dve.tensor_tensor(prod_s[j % 4][:, 0, :], act_g[j % 2], conv[j % 3][:, 1, :], ALU.mult)
                link(dve.tensor_tensor(prod[j % 2], act_g[j % 2], conv[j % 3][:, 1, :], ALU.mult))
                dve.tensor_tensor(prod_s[j % 4][:, 1, :], prod[j % 2], prod_s[j % 4][:, 0, :], ALU.subtract
                                  ).then_inc(gated, 1)

            for j in range(FFN_PAIRS + 1):
                if j < FFN_PAIRS:
                    low_parts(min(upto(("up", j)) + ffn_ahead(j), last_down))
                    taps(j)
                    low_parts(min(before(("up", j + 1)) + ffn_ahead(j + 1), last_down))
                if j >= 1:
                    gate_times_value(j - 1)
            post_norm("down", "down_post", 3)
            scale_rows("mix2", lambda t: x[:, t, :], upto("ug0"))
            drain_norm("mix2")
            low_parts(upto("ug1"))
            link(dve.memset(y_pad[:, :, 0:CONV_TAPS - 1], 0.0))
            low_parts(upto("cq"))
            name = ("ug0",)
            dve.wait_ge(*full(name))
            dve.wait_ge(*drained(("ug1",)))
            dve.tensor_tensor(y_pad[:, :, CONV_TAPS - 1:CONV_TAPS - 1 + SEQ], bank(name)[:, :].rearrange("p (c t) -> p c t", c=2),
                              gate_s, ALU.mult).then_inc(reader(name), 1)
            dw = parc("conv_dw").rearrange("p (c w) -> p c w", c=2)
            dve.wait_ge(*drained(("ug0",)))

            def conv_taps(first, end):
                y = conv_y[:, 0, :]
                for w in range(first, min(end, CONV_TAPS)):
                    src = y_pad[:, 0, w:w + SEQ]
                    if w == 0:
                        ins = dve.tensor_scalar(y, src, dw[:, 0, 0:1], parc("dw_b")[:, 0:1], ALU.mult, ALU.add)
                    else:
                        ins = dve.scalar_tensor_tensor(out=y, in0=src, scalar=dw[:, 0, w:w + 1], in1=y, op0=ALU.mult,
                                                       op1=ALU.add)
                    if w == CONV_TAPS - 1:
                        ins.then_inc(conv_out_low, 1)
                    else:
                        link(ins)

            conv_taps(0, 5)
            low_parts(upto("ck"))
            conv_taps(5, 11)
            low_parts(upto(("qkv", 0)))
            conv_taps(11, 18)
            low_parts(upto(("qkv", 1)))
            conv_taps(18, CONV_TAPS)
            gconv = parc("gdn_conv").rearrange("p (c w) -> p c w", w=4)

            def gdn_taps(i):
                name = ("qkv", i)
                dve.wait_ge(tap3, i + 1)
                for s in (1, 2, 3):
                    for c in range(2):
                        o = qkv[:, 2 * i + c, s:SEQ]
                        ins = dve.scalar_tensor_tensor(out=o, in0=bank(name)[:, SEQ * c:SEQ * c + SEQ - s],
                                                       scalar=gconv[:, 2 * i + c, 3 - s:4 - s], in1=o, op0=ALU.mult,
                                                       op1=ALU.add)
                    if s < 3:
                        link(ins)
                ins.then_inc(reader(name), 1)

            def across_norm(tag):
                raw, sq, _, _, gain = chunk2[tag]
                dve.wait_ge(*drained(("across", tag)))
                link(dve.reciprocal(sq, sq))
                if gain is None:
                    ins = dve.tensor_tensor(raw, raw, sq, ALU.mult)
                else:
                    ins = dve.scalar_tensor_tensor(out=raw, in0=raw, scalar=parc(gain), in1=sq, op0=ALU.mult, op1=ALU.mult)
                ins.then_inc(across_done, 1)

            gdn_taps(0)
            low_parts(upto(("qkv", 2)))
            u_row, ln_row = row_tmp[0:4, 0, :], row_tmp[0:4, 1, :]
            dec, last_less = gate_rows[0:4, 3, :], gate_rows[0:4, 2, :]
            dve.wait_ge(softplus_ln, 1)
            link(dve.scalar_tensor_tensor(out=ln_row, in0=u_row, scalar=0.0, in1=ln_row, op0=ALU.max, op1=ALU.add))
            link(dve.tensor_scalar(ln_row, ln_row, a_rate[0:4, :], -1.0, ALU.mult, ALU.mult))
            link(dve.tensor_tensor_scan(dec, conc("chunk_keep")[0:4, :], ln_row, 0.0, ALU.mult, ALU.add))

            def by_chunk(v):
                return v.rearrange("p (n i) -> p n i", n=NCHUNK)

            dve.tensor_tensor(by_chunk(last_less), by_chunk(dec)[:, :, CHUNK - 1:CHUNK].broadcast_to([4, NCHUNK, CHUNK]),
                              by_chunk(dec), ALU.subtract).then_inc(decay_sum, 1)
            across_norm("dq")
            across_norm("dk")
            dve.wait_ge(*drained(("abw",)))
            for t in range(TT):
                for par in range(2):
                    dve.wait_ge(*drained(("il", t, par)))
                s = idx_score[t]
                link(dve.tensor_scalar(s, relu_l[t][0][:, 0, :], w_idx[:, t, 0:1], None, ALU.mult))
                for h in range(1, 4):
                    ins = dve.scalar_tensor_tensor(out=s, in0=relu_l[t][h % 2][:, h // 2, :], scalar=w_idx[:, t, h:h + 1],
                                                   in1=s, op0=ALU.mult, op1=ALU.add)
                    if h < 3:
                        link(ins)
                ins.then_inc(idx_sum, 1)

            low_parts(upto(("qkv", 3)))

            def topk_round(t, last):
                link(dve.max(top8[:, t, :], idx_score[t]))
                ins = dve.match_replace(out=idx_score[t], in_to_replace=top8[:, t, :], in_values=idx_score[t],
                                        imm_value=PICKED)
                if last:
                    ins.then_inc(picked, 1)
                else:
                    link(ins)

            taps_left = list(range(1, 6))

            def next_taps():
                i = taps_left.pop(0)
                low_parts(upto(("qkv", i)) + 2)
                gdn_taps(i)

            for t in range(TT):
                dve.wait_ge(idx_causal, t + 1)
                for r in range(TOPK_ROUNDS):
                    topk_round(t, r == TOPK_ROUNDS - 1)
                    if r % 3 == 2 and taps_left:
                        next_taps()
            while taps_left:
                next_taps()
            name = ("ln_mean",)
            dve.wait_ge(*full(name))
            dve.scalar_tensor_tensor(out=conv_y[:, 0, :], in0=bank(name)[:, 0:SEQ], scalar=-1.0 / SEQ, in1=conv_y[:, 0, :],
                                     op0=ALU.mult, op1=ALU.add)
            dve.scalar_tensor_tensor(out=conv_y[:, 1, :], in0=bank(name)[:, 0:SEQ], scalar=-1.0 / SEQ, in1=conv_y[:, 1, :],
                                     op0=ALU.mult, op1=ALU.add).then_inc(reader(name), 1)
            dve.wait_ge(decay_exp, 1)
            dve.tensor_tensor(gate_rows[0:4, 1, :], gate_rows[0:4, 0, :], u_row, ALU.mult).then_inc(rows_ready, 1)
            drain_norm("mem2")

            def row_inverse(tag):
                roots = ROWS[tag][5]
                dve.wait_ge(*drained(("row_sum", tag)))
                dve.reciprocal(roots, roots).then_inc(row_roots[tag], 1)

            row_inverse("l")
            for t in range(TT):
                dve.wait_ge(dmask_ready, t + 1)
                for par in range(2):
                    name = ("dl", t, par)
                    n = P * (t + 1)
                    v = dprobs[t][:, par::2, :]
                    dve.wait_ge(*full(name))
                    dve.tensor_tensor(v, bank(name)[:, 0:2 * n].rearrange("p (j s) -> p j s", j=2),
                                      dmask[t].unsqueeze(1).broadcast_to([P, 2, n]), ALU.add).then_inc(reader(name), 1)
                    dve.wait_ge(*drained(name))
                    dve.tensor_reduce(dsoft[:, t, 0, par::2], v, AX, ALU.max, negate=True).then_inc(d_max, 1)
            for t in range(TT):
                dve.wait_ge(d_exp, 2 * t + 2)
                den = dsoft[:, t, 1, :]
                link(dve.reciprocal(den, den))
                dve.tensor_tensor(dprobs[t], dprobs[t], den.unsqueeze(2).broadcast_to([P, DSA_HEADS, P * (t + 1)]),
                                  ALU.mult).then_inc(d_weighed, 1)
            for i in range(4):
                name = ("row_all", "l", i)
                dve.wait_ge(*full(name))
                dve.tensor_tensor(qkv[:, 2 * i:2 * i + 2, :], qkv[:, 2 * i:2 * i + 2, :],
                                  bank(name)[:, :].rearrange("p (c t) -> p c t", c=2), ALU.mult).then_inc(reader(name), 1)
            dve.wait_ge(*drained(("ln_var",)))
            link(dve.reciprocal(conv_sq[:, 0, :], conv_sq[:, 0, :]))
            dve.tensor_tensor(conv_y, conv_y, conv_sq[:, 0:1, :].broadcast_to([P, 2, SEQ]), ALU.mult).then_inc(conv_norm, 1)
            dve.wait_ge(*full(("cols",)))
            dve.tensor_copy(gate_cols, bank(("cols",))[:, 0:32].rearrange("p (t k h) -> p t k h", t=TT, k=4)
                            ).then_inc(reader(("cols",)), 1)
            dve.wait_ge(*drained(("cols",)))
            for i in range(2):
                name = ("dr", i)
                dve.wait_ge(*full(name))
                for t in range(TT):
                    for j in range(2):
                        h = 2 * i + j
                        ins = dve.tensor_scalar(Y[t][:, h, :], bank(name)[:, SEQ * j + P * t:SEQ * j + P * t + P],
                                                gate_cols[:, t, 3, h:h + 1], 0.0, ALU.subtract, ALU.min)
                ins.then_inc(gamma_diff, 1)
            qT2, kT2, vT2 = qkv[:, 0:4, :], qkv[:, 4:8, :], qkv[:, 8:12, :]
            dve.wait_ge(*drained(("row_all", "l", 3)))
            dve.wait_ge(*drained(("row_all", "l", 2)))
            for i in range(2):
                name = ("br", i)
                dve.wait_ge(*full(name))
                dve.tensor_tensor(kbT[:, 2 * i:2 * i + 2, :], bank(name)[:, :].rearrange("p (c t) -> p c t", c=2),
                                  kT2[:, 2 * i:2 * i + 2, :], ALU.mult).then_inc(reader(name), 1)
            dve.wait_ge(*drained(("dr", 1)))
            dve.tensor_tensor(qeT, qT2, exp_decay, ALU.mult).then_inc(qe_ready, 1)
            row_inverse("xk")

            def heads(name):
                return bank(name)[:, :].rearrange("p (h d) -> p h d", h=GDN_HEADS)

            def col(t, kind):
                return gate_cols[:, t, kind, :].unsqueeze(2).broadcast_to([P, GDN_HEADS, P])

            for t in range(TT):
                name = ("kA", t)
                dve.wait_ge(*full(name))
                dve.tensor_tensor(bke[t], heads(name), col(t, 1), ALU.mult)
                dve.tensor_tensor(kdec[t], heads(name), col(t, 2), ALU.mult).then_inc(reader(name), 1)
            for t in range(TT):
                name = ("vA", t)
                dve.wait_ge(*full(name))
                dve.tensor_tensor(bv[t], heads(name), col(t, 0), ALU.mult).then_inc(reader(name), 1)
            for kind, dst, decay in (("kk", AT, inv), ("qk", qkT, Y)):
                for t in range(TT):
                    name = (kind, t)
                    dve.wait_ge(*full(name))
                    dve.wait_ge(gamma_ready, t + 1)
                    dve.tensor_tensor(dst[t], heads(name), decay[t], ALU.mult).then_inc(reader(name), 1)

            for t in range(TT):
                dve.wait_ge(*drained(("qk", t)))
            for t in range(TT):
                for par in range(2):
                    name = ("dpT", t, par)
                    n = t + 1
                    dve.wait_ge(*full(name))
                    dve.tensor_copy(dprobsT[par][:, :, 0:n, P * t:P * t + P],
                                    bank(name)[:, 0:SEQ * n].rearrange("p (j s t) -> p j s t", j=2, s=n)
                                    ).then_inc(reader(name), 1)
            for i in range(2):
                name = ("row_all", "xk", i)
                dve.wait_ge(*full(name))
                dve.scalar_tensor_tensor(out=xkT[:, 2 * i:2 * i + 2, :], in0=xkT[:, 2 * i:2 * i + 2, :],
                                         scalar=parc("xk_norm"), in1=bank(name)[:, :].rearrange("p (c t) -> p c t", c=2),
                                         op0=ALU.mult, op1=ALU.mult).then_inc(reader(name), 1)
            eye = ident.unsqueeze(1).broadcast_to([P, GDN_HEADS, P])
            for t in range(TT):
                dve.wait_ge(level_masked, t + 1)
                dve.scalar_tensor_tensor(out=invT[t], in0=AT_level[0][t], scalar=-1.0, in1=eye, op0=ALU.mult,
                                         op1=ALU.add).then_inc(first_invT, 1)
                name = ("y", 0, t)
                dve.wait_ge(*full(name))
                dve.scalar_tensor_tensor(out=inv[t], in0=heads(name), scalar=-1.0, in1=eye, op0=ALU.mult,
                                         op1=ALU.add).then_inc(reader(name), 1)
            for level in range(1, LEVELS):
                for kind, dst in (("d", inv), ("dT", invT)):
                    if (kind, level) == ("d", LEVELS - 1):
                        continue
                    for t in range(TT):
                        name = (kind, level, t)
                        dve.wait_ge(*full(name))
                        dve.scalar_tensor_tensor(out=dst[t], in0=heads(name), scalar=-1.0, in1=dst[t],
                                                 op0=ALU.mult, op1=ALU.add).then_inc(reader(name), 1)
            for n in range(NCHUNK):
                t, r = n // 2, slice(CHUNK * (n % 2), CHUNK * (n % 2) + CHUNK)
                if n == 0:
                    dve.wait_ge(*drained(("gu", 0)))
                    dve.tensor_copy(v_new[r, :, :], u_n[t][r, :, :]).then_inc(v_news, 1)
                else:
                    name = ("ws", n)
                    dve.wait_ge(*full(name))
                    dve.wait_ge(*drained(("gu", t)))
                    dve.scalar_tensor_tensor(out=v_new[r, :, :], in0=heads(name)[r, :, :], scalar=-1.0, in1=u_n[t][r, :, :],
                                             op0=ALU.mult, op1=ALU.add).then_inc(reader(name), 1)
                if n < NCHUNK - 1:
                    name = ("kv", n)
                    dve.wait_ge(*full(name))
                    if n == 0:
                        dve.tensor_copy(state, heads(name)).then_inc(reader(name), 1)
                    else:
                        for h in range(GDN_HEADS):
                            at = CHUNK * n + CHUNK - 1
                            ins = dve.scalar_tensor_tensor(out=state[:, h, :], in0=state[:, h, :],
                                                           scalar=exp_decay[:, h, at:at + 1], in1=heads(name)[:, h, :],
                                                           op0=ALU.mult, op1=ALU.add)
                        ins.then_inc(reader(name), 1)
            low_parts(upto(("out2", MIX_ORDER[0])))
            dve.wait_ge(row_squares, 3)
            dve.wait_ge(*drained(("go", NCHUNK - 1)))
            dve.scalar_tensor_tensor(out=zT, in0=oT, scalar=parc("gdn_norm"), in1=zT, op0=ALU.mult, op1=ALU.mult
                                     ).then_inc(scaled_o, 1)
            row_inverse("o")
            low_parts(upto(("out2", MIX_ORDER[1])))
            for c in MIX_ORDER[:2]:
                low_mix("out2", c, mixT[:, 2 * c:2 * c + 2, :]).then_inc(acts_low, 1)
            dve.wait_ge(scaled_o, 1)
            for i in range(2):
                name = ("row_all", "o", i)
                dve.wait_ge(*full(name))
                dve.tensor_tensor(mixT[:, 2 * i:2 * i + 2, :], zT[:, 2 * i:2 * i + 2, :],
                                  bank(name)[:, :].rearrange("p (c t) -> p c t", c=2), ALU.mult).then_inc(reader(name), 1)
            for c in MIX_ORDER[2:]:
                low_mix("out2", c, mixT[:, 2 * c:2 * c + 2, :]).then_inc(acts_low, 1)
            low_parts(upto(("xq", 1)))

            def add_product(product):
                for t in range(TT):
                    for half in range(2):
                        f = (product, 2 * t + half)
                        c = slice(512 * half, 512 * half + 512)
                        dve.wait_ge(*acc_filled(f))
                        dve.tensor_tensor(x[:, t, c], acc(f)[:, :], x[:, t, c], ALU.add).then_inc(acc_read, 1)

            add_product("out2")
            scale_rows("cross", lambda t: x[:, t, :])
            drain_norm("cross")
            low_parts(upto(("xwo", 0)))
            dve.wait_ge(*drained(("xq_sums",)))
            link(dve.reciprocal(xq_root, xq_root))
            for t in range(TT):
                for hp in range(2):
                    name = ("xs", t, hp)
                    dve.wait_ge(*full(name))
                    high = xsoft[:, t, 0, 2 * hp:2 * hp + 2]
                    link(dve.tensor_reduce(high, bank(name)[:, :].rearrange("p (h s) -> p h s", h=2),
                                           AX, ALU.max, negate=True))
                    dve.tensor_tensor(high, high, xq_root[:, t, 2 * hp:2 * hp + 2], ALU.mult).then_inc(x_max, 1)
            for t in range(TT):
                for hp in range(2):
                    dve.wait_ge(*drained(("xs", t, hp)))
                    den = xsoft[:, t, 1, 2 * hp:2 * hp + 2]
                    link(dve.reciprocal(den, den))
                    dve.tensor_tensor(xprobs[t][:, 2 * hp:2 * hp + 2, :], xprobs[t][:, 2 * hp:2 * hp + 2, :],
                                      den.unsqueeze(2).broadcast_to([P, 2, SEQ]), ALU.mult).then_inc(x_weighed, 1)
            for t in range(TT):
                for hp in range(2):
                    name = ("xpT", t, hp)
                    dve.wait_ge(*full(name))
                    dve.tensor_copy(xprobsT[:, 2 * hp:2 * hp + 2, :, P * t:P * t + P],
                                    bank(name)[:, :].rearrange("p (h s t) -> p h s t", h=2, s=TT)).then_inc(reader(name), 1)
            low_parts(upto(("m1", 0)))
            for c in range(2):
                low_mix("xwo", c, bank(("xo", c))[:, :].rearrange("p (c t) -> p c t", c=2)).then_inc(reader(("xo", c)), 1)
            low_parts(upto(("m1", 1)))
            add_product("xwo")
            scale_rows("mlp", lambda t: x[:, t, :])
            drain_norm("mlp")
            low_parts(upto(("m1", 2)))
            for j in range(MLP_UNITS):
                low_parts(upto(("m1", j)) + 3)
                dve.wait_ge(*drained(("m1", j)))
                link(dve.tensor_tensor(relu2[j % 2], relu_h[j % 2], relu_h[j % 2], ALU.mult))
                dve.wait_ge(relu_high, j + 1)
                dve.tensor_tensor(relu2_s[j % 3][:, 1], relu2[j % 2], relu2_s[j % 3][:, 0], ALU.subtract).then_inc(relu_sq, 1)
                low_parts(before(("m1", j + 1)) + 3)
            low_parts(len(split_units) - 1)
            add_product("m2")

        @block.tensor
        def _(pe):
            def open_tile(name):
                i = TILE[name]
                if i >= NB:
                    pe.wait_ge(tile_read[i % NB], i // NB)
                return banks[i % NB]

            def keep_clock_up(ps, steps):
                for _ in range(steps):
                    pe.matmul(ps[:, :], ident, con[:, 0:512], start=True, stop=True)

            def norm_T(stage, first):
                if stage in WARM_BEFORE:
                    keep_clock_up(open_tile(("normT", stage, 0, 0)), WARM_BEFORE[stage])
                for t in range(TT):
                    pe.wait_ge(normed, first + t + 1)
                    for half in range(2):
                        ps = open_tile(("normT", stage, t, half))
                        for k in range(4):
                            c = P * (4 * half + k)
                            ins = pe.transpose(ps[:, P * k:P * k + P], xn[:, t, c:c + P], ident)
                        ins.then_inc(tile_full, 1)

            def drained_norm(stage):
                for t in range(TT):
                    for half in range(2):
                        pe.wait_ge(*drained(("normT", stage, t, half)))

            def wide(out, w, lo, n=P):
                for k in range(KD):
                    ins = pe.matmul(out, w[:, k, lo:lo + n], hT[:, k, :], start=(k == 0), stop=(k == KD - 1))
                return ins

            def tall(out, w, lo, n, t):
                for k in range(KD):
                    ins = pe.matmul(out, hT[:, k, P * t:P * t + P], w[:, k, lo:lo + n], start=(k == 0), stop=(k == KD - 1))
                return ins

            def pair_of_chunks(name, unit):
                ps = open_tile(name)
                pe.wait_ge(*loaded(unit))
                w = weights(unit, KD, 256)
                wide(ps[:, 0:SEQ], w, 0)
                wide(ps[:, SEQ:512], w, P).then_inc(tile_full, 1)

            def split_matmul(out, lhs, rhs, start, stop):
                for n, (p, q) in enumerate(((0, 0), (0, 1), (1, 0))):
                    ins = pe.matmul(out, lhs(p), rhs(q), start=(start and n == 0), stop=(stop and n == 2))
                return ins

            def split_pair(name, stage, unit=None):
                ps = open_tile(name)
                unit = name if unit is None else unit
                pe.wait_ge(low_ready, SPLIT[unit] + 1)
                w = split_weights(unit, KD, 256)
                for c in range(2):
                    for k in range(KD):
                        ins = split_matmul(ps[:, SEQ * c:SEQ * c + SEQ], lambda p: w[:, p, k, P * c:P * c + P],
                                           lambda p: act_s[stage][p][:, k, :], k == 0, k == KD - 1)
                ins.then_inc(tile_full, 1)

            def split_tall(name, unit, stage):
                ps = open_tile(name)
                pe.wait_ge(low_ready, SPLIT[unit] + 1)
                w = split_weights(unit, KD, 256)
                for t in range(TT):
                    for k in range(KD):
                        ins = split_matmul(ps[:, SEQ * t:SEQ * t + SEQ], lambda p: act_s[stage][p][:, k, P * t:P * t + P],
                                           lambda p: w[:, p, k, :], k == 0, k == KD - 1)
                ins.then_inc(tile_full, 1)

            def split_product_unit(unit, first, last, lhs):
                pe.wait_ge(low_ready, SPLIT[unit] + 1)
                w = split_weights(unit, 2, D)
                for kk in range(2):
                    for t in range(TT):
                        for half in range(2):
                            ins = split_matmul(acc((unit[0], 2 * t + half))[:, :], lambda p: lhs(p, kk, t),
                                               lambda p: w[:, p, kk, 512 * half:512 * half + 512], first and kk == 0,
                                               last and kk == 1)
                            if last and kk == 1:
                                ins.then_inc(acc_full, 1)
                if not last:
                    ins.then_inc(unit_spent, 1)

            def split_product(name, order):
                open_product(name)
                for n, c in enumerate(order):
                    pe.wait_ge(*low_there(("mix", name, c)))
                    split_product_unit((name, c), n == 0, n == len(order) - 1,
                                       lambda p, kk, t: act_s[name][p][:, 2 * c + kk, P * t:P * t + P])

            def rows_split(stage):
                pe.wait_ge(*low_there(("rows", stage, TT - 1, 1)))

            def open_product(product):
                if FILL[(product, 0)]:
                    pe.wait_ge(acc_read, FILL[(product, 0)])

            pe.wait_ge(first_consts_in, 16)
            norm_T("mix", 0)
            drained_norm("mix")
            pair_of_chunks(("q0",), "q0")
            rows_split("mix")
            split_pair(("q1",), "mix", "q1")
            pe.wait_ge(params_in, 16)
            pe.wait_ge(hots_in, 16)
            relb = parc("relb")[0:REL_BUCKETS + 1, :]
            ps = open_tile(("bias_row",))
            pe.matmul(ps[0:HEADS, 0:384], relb, hots[0:REL_BUCKETS + 1, P:DIST_COLS], start=True, stop=True).then_inc(tile_full, 1)
            split_pair(("kcvc",), "mix", "kcvc")
            split_pair(("kskw",), "mix", "kskw")
            split_tall(("vsvw",), "vsvw", "mix")
            ps = open_tile(("gates",))
            pe.wait_ge(*loaded("gates"))
            for t in range(TT):
                ins = tall(ps[:, 24 * t:24 * t + 24], weights("gates", KD, 24), 0, 24, t)
            ins.then_inc(tile_full, 1)
            split_pair(("pool",), "mix", "pool")
            split_pair(("u",), "mix", "u")
            split_tall(("v",), "v", "mix")

            ps = open_tile(("cmp_h",))
            pe.wait_ge(blocks_ready, 1)
            for kv, u in enumerate(("cmp_w1k", "cmp_w1v")):
                pe.wait_ge(*loaded(u))
                w = weights(u, CMP_PAIRS, P)
                for j in range(CMP_PAIRS):
                    ins = pe.matmul(ps[:, 32 * kv:32 * kv + 30], w[:, j, :],
                                    blocks[:, kv, j, :, :].rearrange("p g c -> p (g c)"),
                                    start=(j == 0), stop=(j == CMP_PAIRS - 1))
            ins.then_inc(tile_full, 1)
            ps = open_tile(("cmp_kv",))
            pe.wait_ge(*drained(("cmp_h",)))
            w2 = parc("cmp_w2").rearrange("p (v d) -> p v d", v=2)
            for g in range(GROUPS):
                pe.matmul(ps[DK * g:DK * g + DK, 0:NCMP], w2[:, 0, :], cmp_hT[:, 0, NCMP * g:NCMP * g + NCMP],
                          start=True, stop=True)
            for j in range(4):
                for g in range(GROUPS):
                    ins = pe.matmul(ps[32 * j:32 * j + NCMP, 64 + DK * g:64 + DK * g + DK],
                                    cmp_hT[:, 1, NCMP * g:NCMP * g + NCMP], w2[:, 1, :], start=True, stop=True)
            ins.then_inc(tile_full, 1)

            def head_rows(h):
                return slice(DK * (h // HG), DK * (h // HG) + DK)

            for u in ("q0", "q1", "kskw", "vsvw", "cmp_kv"):
                pe.wait_ge(*drained((u,)))
            for t in range(TT):
                for g in range(GROUPS):
                    ps = open_tile(("cmp_s", t, g))
                    for i in range(HG):
                        ins = pe.matmul(ps[:, NCMP * i:NCMP * i + NCMP], qT[head_rows(HG * g), i, P * t:P * t + P],
                                        cmp_kT[head_rows(HG * g), :], start=True, stop=True)
                    ins.then_inc(tile_full, 1)
                for h in HEAD_ORDER:
                    ps = open_tile(("s", t, h))
                    n = P * (t + 1)
                    pe.matmul(ps[:, 0:2 * n].rearrange("p (j s) -> p j s", j=2), qT[head_rows(h), h % HG, P * t:P * t + P],
                              keysT[head_rows(h), :, 0:n], start=True, stop=True).then_inc(tile_full, 1)
            ps = open_tile(("pool_out",))
            pe.wait_ge(pooled, 1)
            pw = parc("pool_w").rearrange("p (c d) -> p c d", c=2)
            for g in range(4):
                r = slice(64 * (g % 2), 64 * (g % 2) + 64)
                ins = pe.matmul(ps[r, SEQ * (g // 2):SEQ * (g // 2) + SEQ], pw[r, g // 2, :], pool_d[r, g // 2, :],
                                start=True, stop=True)
            ins.then_inc(tile_full, 1)
            ps = open_tile(("sgu_out",))
            pe.wait_ge(sgu_normed, TT)
            pe.wait_ge(masked_ws, 1)
            wsT = parc("sgu_wT").rearrange("p (h t) -> p h t", h=4)
            for h in range(4):
                for t in range(TT):
                    at = SEQ * (h // 2) + P * t
                    ins = pe.matmul(ps[64 * (h % 2):64 * (h % 2) + 64, at:at + P], v_n[:, t, 64 * h:64 * h + 64],
                                    wsT[:, h, :], start=True, stop=True)
            ins.then_inc(tile_full, 1)

            norm_T("memkv", 2)
            drained_norm("memkv")
            pair_of_chunks(("mk", 0), ("mk", 0))
            rows_split("memkv")
            for c in range(1, 4):
                split_pair(("mk", c), "memkv")
            open_product("mv")
            for i in range(4):
                split_product_unit(("mv", i), i == 0, i == 3,
                                   lambda p, kk, t: act_s["memkv"][p][:, 2 * i + kk, P * t:P * t + P])

            for t in range(TT):
                pe.wait_ge(weighed, 1 + t * (HEADS + 1))
                ps = open_tile(("cmp_pT", t))
                for g in range(GROUPS):
                    ins = pe.transpose(ps[:, P * g:P * g + P],
                                       cmp_p[:, t, HG * g:HG * g + HG, :].rearrange("p h c -> p (h c)"), ident)
                ins.then_inc(tile_full, 1)

            def probs_T(h):
                for t in range(TT):
                    pe.wait_ge(weighed, 1 + t * (HEADS + 1) + h + 1)
                    ps = open_tile(("pT", t, h))
                    for j in range(2):
                        for s in range(t + 1):
                            at = P * (j * (t + 1) + s)
                            ins = pe.transpose(ps[:, at:at + P], probs[t][h][:, j, P * s:P * s + P], ident)
                    ins.then_inc(tile_full, 1)

            def attend(h):
                g, c = h // HG, h // 2
                f = ("o", c // 2)
                if h % 4 == 0 and FILL[f] >= 4:
                    pe.wait_ge(acc_read, FILL[f] - 3)
                if h == 0:
                    for t in range(TT):
                        pe.wait_ge(*drained(("cmp_pT", t)))
                for t in range(TT):
                    pe.wait_ge(*drained(("pT", t, h)))
                o = acc(f)[DK * (h % 2):DK * (h % 2) + DK, SEQ * (c % 2):SEQ * (c % 2) + SEQ]
                pT = probsT[h % 2]
                for j in range(2):
                    pe.matmul(o, values[:, j, 0, DK * g:DK * g + DK], pT[:, j, 0, :], start=(j == 0), stop=False)
                    pe.matmul(o[:, P:SEQ], values[:, j, 1, DK * g:DK * g + DK], pT[:, j, 1, P:SEQ], start=False, stop=False)
                r = slice(32 * (h % HG), 32 * (h % HG) + NCMP)
                return pe.matmul(o, cmp_v[r, DK * g:DK * g + DK], cmp_pT[r, g, :], start=False, stop=True)

            for h in range(HEADS + 1):
                if h < HEADS:
                    probs_T(h)
                if h >= 1:
                    attend(h - 1).then_inc(acc_full if (h - 1) % 4 == 3 else heads_done, 1)
            split_product("out", MIX_ORDER)

            norm_T("mem", 4)
            drained_norm("mem")
            pair_of_chunks(("mq", 0), ("mq", 0))
            rows_split("mem")
            for c in range(1, 4):
                split_pair(("mq", c), "mem")
            for c in range(4):
                pe.wait_ge(*drained(("mk", c)))
                pe.wait_ge(*drained(("mq", c)))
            for t in range(TT):
                for hp in range(2):
                    ps = open_tile(("ms", t, hp))
                    for j in range(2):
                        h = 2 * hp + j
                        for dd in range(2):
                            ins = pe.matmul(ps[:, SEQ * j:SEQ * j + SEQ], qmT[:, 2 * h + dd, P * t:P * t + P],
                                            kmT[:, 2 * h + dd, :], start=(dd == 0), stop=(dd == 1))
                    ins.then_inc(tile_full, 1)
            for t in range(TT):
                for hp in range(2):
                    pe.wait_ge(weighed, TT * (HEADS + 1) + 2 * t + hp + 1)
                    ps = open_tile(("mpT", t, hp))
                    for j in range(2):
                        for s in range(TT):
                            at = P * (2 * j + s)
                            ins = pe.transpose(ps[:, at:at + P], mprobs[t][:, 2 * hp + j, P * s:P * s + P], ident)
                    ins.then_inc(tile_full, 1)
            pe.wait_ge(*acc_drained(("mv", 3)))
            for c in range(4):
                if c % 2 == 0:
                    for t in range(TT):
                        pe.wait_ge(*drained(("mpT", t, c // 2)))
                ps = open_tile(("mo", c))
                for dd in range(2):
                    for s in range(TT):
                        ins = pe.matmul(ps[:, SEQ * dd:SEQ * dd + SEQ], vm[:, s, SEQ * c + P * dd:SEQ * c + P * dd + P],
                                        mprobsT[:, c, s, :], start=(s == 0), stop=(s == TT - 1))
                ins.then_inc(tile_full, 1)
            split_product("wo", range(4))

            norm_T("ffn", 6)
            drained_norm("ffn")
            open_product("down")
            for j in range(FFN_PAIRS + DOWN_LAG):
                if j == 0:
                    pair_of_chunks(("up", 0), ("up", 0))
                    rows_split("ffn")
                elif j < FFN_PAIRS:
                    split_pair(("up", j), "ffn")
                if j >= DOWN_LAG and j % 2 == 1:
                    i = (j - DOWN_LAG) // 2
                    pe.wait_ge(gated, 2 * i + 2)
                    split_product_unit(("down", i), i == 0, i == FFN_PAIRS // 2 - 1,
                                       lambda p, kk, t: prod_s[(2 * i + kk) % 4][:, p, P * t:P * t + P])

            def across_sum(tag):
                pe.wait_ge(across_sq, ACROSS[tag] + 1)
                ps = open_tile(("across", tag))
                sq = chunk2[tag][1]
                if tag == "dk":
                    ins = pe.matmul(ps[:, 0:SEQ], conc("block_ones"), sq, start=True, stop=True)
                else:
                    ones = conc("block_ones") if tag == "dq" else conc("ones")
                    ins = pe.matmul(ps[:, :], ones, sq.rearrange("p c t -> p (c t)"), start=True, stop=True)
                ins.then_inc(tile_full, 1)

            norm_T("mix2", 8)
            drained_norm("mix2")
            pair_of_chunks(("ug0",), "ug0")
            rows_split("mix2")
            split_pair(("ug1",), "mix2", "ug1")
            split_pair(("cq",), "mix2", "cq")
            split_pair(("ck",), "mix2", "ck")
            ps = open_tile(("abw",))
            pe.wait_ge(*loaded("ab"))
            for t in range(TT):
                ins = tall(ps[:, 12 * t:12 * t + 12], weights("ab", KD, 12), 0, 12, t)
            ins.then_inc(tile_full, 1)
            ps = open_tile(("ab",))
            pe.wait_ge(*drained(("abw",)))
            for n in range(2):
                for t in range(TT):
                    at = SEQ * n + P * t
                    ins = pe.transpose(ps[0:4, at:at + P], ab_cols[:, t, 4 * n:4 * n + 4], ident)
            ins.then_inc(tile_full, 1)
            w_qb = parc("w_qb").rearrange("p (k c) -> p k c", k=2)
            w_qi = parc("w_qi").rearrange("p (k c) -> p k c", k=2)
            pe.wait_ge(*drained(("cq",)))
            for name, w in ((("dq",), w_qb), (("dqi",), w_qi)):
                ps = open_tile(name)
                for c in range(2):
                    for k in range(2):
                        ins = pe.matmul(ps[:, SEQ * c:SEQ * c + SEQ], w[:, k, P * c:P * c + P], cqT[:, k, :],
                                        start=(k == 0), stop=(k == 1))
                ins.then_inc(tile_full, 1)
            ps = open_tile(("dk",))
            pe.wait_ge(*drained(("ck",)))
            w_kvb = parc("w_kvb")
            pe.matmul(ps[0:DK, 0:SEQ], w_kvb[:, 0:DK], ckvT, start=True, stop=True)
            pe.matmul(ps[DK:P, 0:SEQ], w_kvb[:, 0:DK], ckvT, start=True, stop=True)
            for t in range(TT):
                ins = pe.matmul(ps[:, SEQ + DK * t:SEQ + DK * t + DK], ckvT[:, P * t:P * t + P], w_kvb[:, DK:P],
                                start=True, stop=True)
            ins.then_inc(tile_full, 1)
            split_pair(("qkv", 0), "mix2")
            across_sum("dq")
            across_sum("dk")
            for t in range(TT):
                for par in range(2):
                    ps = open_tile(("il", t, par))
                    pe.wait_ge(*drained(("dqi",)))
                    n = P * (t + 1)
                    r = slice(DK * par, DK * par + DK)
                    for j in range(2):
                        ins = pe.matmul(ps[:, n * j:n * j + n], dqiT[r, j, P * t:P * t + P], kidxT[r, 0:n],
                                        start=True, stop=True)
                    ins.then_inc(tile_full, 1)
            for i in range(1, 6):
                split_pair(("qkv", i), "mix2")
            split_pair(("z", 0), "mix2")
            pe.wait_ge(conv_out_low, 1)
            pe.wait_ge(conv_out, 1)
            ps = open_tile(("ln_mean",))
            for c in range(2):
                ins = pe.matmul(ps[:, 0:SEQ], conc("ones"), conv_y[:, c, :], start=(c == 0), stop=(c == 1))
            ins.then_inc(tile_full, 1)
            split_pair(("z", 1), "mix2")
            def pick_row(n, h):
                return ident[0:n, h:h + 1].broadcast_to([n, P])

            def row_sum(tag):
                sq, n = ROWS[tag][1:3]
                pe.wait_ge(row_squares, ("l", "xk", "o").index(tag) + 1)
                ps = open_tile(("row_sum", tag))
                for h in range(n):
                    lo = 8 - h
                    ins = pe.matmul(ps[0:n, 0:SEQ], conc("pick_col")[:, lo:lo + n], sq[:, h, :], start=(h == 0), stop=(h == n - 1))
                ins.then_inc(tile_full, 1)

            def row_all(tag, i):
                n, roots = ROWS[tag][2], ROWS[tag][5]
                pe.wait_ge(row_roots[tag], 1)
                ps = open_tile(("row_all", tag, i))
                for j in range(2):
                    ins = pe.matmul(ps[:, SEQ * j:SEQ * j + SEQ], pick_row(n, 2 * i + j), roots, start=True, stop=True)
                ins.then_inc(tile_full, 1)

            norm_T("mem2", 10)
            drained_norm("mem2")
            pair_of_chunks(("xk", 0), ("xk", 0))
            row_sum("l")
            pe.wait_ge(across_done, ACROSS["dk"] + 1)
            for t in range(TT):
                for par in range(2):
                    ps = open_tile(("dl", t, par))
                    n = P * (t + 1)
                    r = slice(DK * par, DK * par + DK)
                    for j in range(2):
                        ins = pe.matmul(ps[:, n * j:n * j + n], dqT[r, j, P * t:P * t + P], dkT[r, 0:n],
                                        start=True, stop=True)
                    ins.then_inc(tile_full, 1)
            pe.wait_ge(conv_sq_ready, 1)
            ps = open_tile(("ln_var",))
            for c in range(2):
                ins = pe.matmul(ps[:, 0:SEQ], conc("ones"), conv_sq[:, c, :], start=(c == 0), stop=(c == 1))
            ins.then_inc(tile_full, 1)
            pair_of_chunks(("xk", 1), ("xk", 1))
            for i in range(4):
                row_all("l", i)
            pe.wait_ge(rows_ready, 1)
            ps = open_tile(("cols",))
            for t in range(TT):
                for kind in range(4):
                    at = 16 * t + 4 * kind
                    ins = pe.transpose(ps[:, at:at + 4], gate_rows[0:4, kind, P * t:P * t + P], ident[0:4, 0:4])
            ins.then_inc(tile_full, 1)
            for tag, kind in (("dr", 3), ("br", 0)):
                for i in range(2):
                    ps = open_tile((tag, i))
                    for j in range(2):
                        ins = pe.matmul(ps[:, SEQ * j:SEQ * j + SEQ], pick_row(4, 2 * i + j), gate_rows[0:4, kind, :],
                                        start=True, stop=True)
                    ins.then_inc(tile_full, 1)
            row_sum("xk")
            qT2, kT2, vT2 = qkv[:, 0:4, :], qkv[:, 4:8, :], qkv[:, 8:12, :]
            for i in range(4):
                pe.wait_ge(*drained(("row_all", "l", i)))
            for tag, src in (("kA", kT2), ("vA", vT2)):
                for t in range(TT):
                    ps = open_tile((tag, t))
                    for h in range(GDN_HEADS):
                        ins = pe.transpose(ps[:, P * h:P * h + P], src[:, h, P * t:P * t + P], ident)
                    ins.then_inc(tile_full, 1)
            pe.wait_ge(*drained(("br", 1)))
            for tag, moving in (("kk", kbT), ("qk", qT2)):
                for t in range(TT):
                    ps = open_tile((tag, t))
                    for h in range(GDN_HEADS):
                        ins = pe.matmul(ps[:, P * h:P * h + P], kT2[:, h, P * t:P * t + P], moving[:, h, P * t:P * t + P],
                                        start=True, stop=True)
                    ins.then_inc(tile_full, 1)

            def four(name, lhs, rhs):
                ps = open_tile(name)
                for h in range(GDN_HEADS):
                    ins = pe.matmul(ps[:, P * h:P * h + P], lhs(h), rhs(h), start=True, stop=True)
                ins.then_inc(tile_full, 1)

            for t in range(TT):
                pe.wait_ge(d_weighed, t + 1)
                for par in range(2):
                    ps = open_tile(("dpT", t, par))
                    for j in range(2):
                        for s in range(t + 1):
                            at = P * (j * (t + 1) + s)
                            ins = pe.transpose(ps[:, at:at + P], dprobs[t][:, 2 * j + par, P * s:P * s + P], ident)
                    ins.then_inc(tile_full, 1)
            ps = open_tile(("do",))
            for t in range(TT):
                for par in range(2):
                    pe.wait_ge(*drained(("dpT", t, par)))
            for j in range(2):
                for par in range(2):
                    o = ps[DK * par:DK * par + DK, SEQ * j:SEQ * j + SEQ]
                    pe.matmul(o, dv[:, 0, :], dprobsT[par][:, j, 0, :], start=True, stop=False)
                    ins = pe.matmul(o[:, P:SEQ], dv[:, 1, :], dprobsT[par][:, j, 1, P:SEQ], start=False, stop=True)
            ins.then_inc(tile_full, 1)
            for i in range(2):
                row_all("xk", i)

            pe.wait_ge(acc_read, FILL[("xv", 0)])
            value_steps = [(i, kk, t) for i in range(2) for kk in range(4) for t in range(TT)]

            def cross_values(n):
                for i, kk, t in value_steps[:n]:
                    if kk == 0 and t == 0:
                        pe.wait_ge(*loaded(("xv", i)))
                    ins = pe.matmul(acc(("xv", t))[:, :], hT[:, 4 * i + kk, P * t:P * t + P],
                                    weights(("xv", i), 4, 512)[:, kk, :], start=(i == 0 and kk == 0),
                                    stop=(i == 1 and kk == 3))
                    if i == 1 and kk == 3:
                        ins.then_inc(acc_full, 1)
                    elif kk == 3 and t == 1:
                        ins.then_inc(unit_spent, 1)
                del value_steps[:n]

            for level in range(LEVELS):
                for t in range(TT):
                    pe.wait_ge(level_masked, 2 * level + t + 1)
                    if level:
                        pe.wait_ge(*drained(("d", level - 1, t) if level > 1 else ("y", 0, t)))
                    four(("y", level, t), lambda h: AT_level[level % 2][t][:, h, :],
                         lambda h: inv[t][:, h, :] if level else ident)
                cross_values(1)
                if level == 0:
                    pe.wait_ge(first_invT, 2)
                    continue
                for t in range(TT):
                    pe.wait_ge(*drained(("y", level, t)))
                    if level > 1:
                        pe.wait_ge(*drained(("dT", level - 1, t)))
                if level < LEVELS - 1:
                    for t in range(TT):
                        four(("d", level, t), lambda h: invT[t][:, h, :], lambda h: Y[t][:, h, :])
                for t in range(TT):
                    four(("dT", level, t), lambda h: Y[t][:, h, :], lambda h: invT[t][:, h, :])
            cross_values(1)
            for t in range(TT):
                pe.wait_ge(*drained(("dT", LEVELS - 1, t)))
                four(("gu", t), lambda h: invT[t][:, h, :], lambda h: bv[t][:, h, :])
            for t in range(TT):
                four(("gw", t), lambda h: bke[t][:, h, :], lambda h: invT[t][:, h, :])
            pe.wait_ge(qe_ready, 1)
            for t in range(TT):
                pe.wait_ge(*drained(("gw", t)))
                pe.wait_ge(*drained(("qk", t)))
            for n in range(NCHUNK):
                t, lo = n // 2, CHUNK * (n % 2)
                r = slice(lo, lo + CHUNK)
                if n:
                    cross_values(1)
                    pe.wait_ge(*drained(("kv", n - 1)))
                    ps = open_tile(("ws", n))
                    for h in range(GDN_HEADS):
                        ins = pe.matmul(ps[r, P * h:P * h + P], wT[t][:, h, r], state[:, h, :], start=True, stop=True)
                    ins.then_inc(tile_full, 1)
                    cross_values(1)
                    pe.wait_ge(*drained(("ws", n)))
                else:
                    pe.wait_ge(v_news, 1)
                ps = open_tile(("go", n))
                for h in range(GDN_HEADS):
                    o = ps[:, CHUNK * h:CHUNK * h + CHUNK]
                    if n:
                        pe.matmul(o, state[:, h, :], qeT[:, h, CHUNK * n:CHUNK * n + CHUNK], start=True, stop=False)
                    ins = pe.matmul(o, v_new[r, h, :], qkT[t][r, h, r], start=(n == 0), stop=True)
                ins.then_inc(tile_full, 1)
                if n < NCHUNK - 1:
                    ps = open_tile(("kv", n))
                    for h in range(GDN_HEADS):
                        ins = pe.matmul(ps[:, P * h:P * h + P], kdec[t][r, h, :], v_new[r, h, :], start=True, stop=True)
                    ins.then_inc(tile_full, 1)
            cross_values(1)
            row_sum("o")
            cross_values(2)
            for i in range(2):
                row_all("o", i)
            split_product("out2", MIX_ORDER)

            norm_T("cross", 12)
            drained_norm("cross")
            pair_of_chunks(("xq", 0), ("xq", 0))
            rows_split("cross")
            split_pair(("xq", 1), "cross")
            ps = open_tile(("xq_sums",))
            pe.wait_ge(xq_squares, 2)
            for t in range(TT):
                for h in range(XA_HEADS):
                    at = XA_HEADS * t + h
                    ins = pe.matmul(ps[:, at:at + 1], xq_sq[:, h, P * t:P * t + P], conc("ones")[:, 0:1], start=True, stop=True)
            ins.then_inc(tile_full, 1)
            for i in range(2):
                pe.wait_ge(*drained(("xq", i)))
            for i in range(2):
                pe.wait_ge(*drained(("row_all", "xk", i)))
            for t in range(TT):
                for hp in range(2):
                    ps = open_tile(("xs", t, hp))
                    for j in range(2):
                        h = 2 * hp + j
                        ins = pe.matmul(ps[:, SEQ * j:SEQ * j + SEQ], xqT[:, h, P * t:P * t + P], xkT[:, h, :],
                                        start=True, stop=True)
                    ins.then_inc(tile_full, 1)
            for t in range(TT):
                for hp in range(2):
                    pe.wait_ge(x_weighed, 2 * t + hp + 1)
                    ps = open_tile(("xpT", t, hp))
                    for j in range(2):
                        for s in range(TT):
                            at = P * (2 * j + s)
                            ins = pe.transpose(ps[:, at:at + P], xprobs[t][:, 2 * hp + j, P * s:P * s + P], ident)
                    ins.then_inc(tile_full, 1)
            pe.wait_ge(*acc_drained(("xv", 1)))
            for c in range(2):
                for t in range(TT):
                    pe.wait_ge(*drained(("xpT", t, c)))
                ps = open_tile(("xo", c))
                for j in range(2):
                    h = 2 * c + j
                    for s in range(TT):
                        ins = pe.matmul(ps[:, SEQ * j:SEQ * j + SEQ], xv[:, s, P * h:P * h + P], xprobsT[:, h, s, :],
                                        start=(s == 0), stop=(s == TT - 1))
                ins.then_inc(tile_full, 1)
            split_product("xwo", range(2))

            norm_T("mlp", 14)
            drained_norm("mlp")
            open_product("m2")
            for j in range(MLP_UNITS + MLP_LAG):
                if j == 0:
                    pair_of_chunks(("m1", 0), ("m1", 0))
                    rows_split("mlp")
                elif j < MLP_UNITS:
                    split_pair(("m1", j), "mlp")
                if j >= MLP_LAG:
                    i = j - MLP_LAG
                    pe.wait_ge(relu_sq, i + 1)
                    split_product_unit(("m2", i), i == 0, i == MLP_UNITS - 1,
                                       lambda p, kk, t: relu2_s[i % 3][:, p, kk, P * t:P * t + P])


def pack(n, spec, parts):
    c = np.zeros((P, n), np.float32)
    for name, v in parts.items():
        lo, hi = spec[name]
        v = np.asarray(v)
        c[:v.shape[0], lo:hi] = v.reshape(v.shape[0], hi - lo)
    return c


def by_partition(v, k):
    return np.asarray(v).reshape(k, P).T


def twice(v):
    v = np.asarray(v).reshape(64, -1)
    return np.concatenate([v, v], 0)


def small_parameters(i):
    def a(name):
        return np.asarray(i[name])

    both = {}
    both["gains"] = np.stack([by_partition(a(n), KD) for n in (
        "mix_norm_pre", "mem_norm_kv", "mem_norm_pre", "ffn_norm_pre", "norm_mix_2", "norm_mem_2", "norm_cross_2",
        "norm_mlp_2")], 1)
    both["cmp_pos"] = a("cmp_pos")[0].reshape(2, CMP_PAIRS, P).transpose(2, 0, 1)
    both["cmp_b1"] = a("cmp_b1")[0].T
    both["cmp_w2"] = a("cmp_w2")[0].transpose(1, 0, 2)
    both["cmp_b2k"] = twice(a("cmp_b2")[0, 0])
    both["cmp_b2v"] = np.broadcast_to(np.tile(a("cmp_b2")[0, 1], GROUPS), (P, P))
    both["relb"] = np.concatenate([a("rel_bias"), np.full((1, HEADS), MASKED, np.float32)], 0)
    pw = a("pool_w")[0]
    both["pool_w"] = np.concatenate([pw[0::2].transpose(1, 0, 2), pw[1::2].transpose(1, 0, 2)], 0)
    both["pool_scale"] = by_partition(a("pool_scale")[0], 2)
    both["sgu_g"] = np.broadcast_to(a("sgu_norm_g")[0], (P, 256))
    both["sgu_b"] = np.broadcast_to(a("sgu_norm_b")[0], (P, 256))
    both["sgu_wT"] = a("sgu_w")[0].transpose(2, 0, 1)
    both["sgu_bias"] = np.repeat(a("sgu_b")[0].reshape(2, 2, P).transpose(1, 0, 2), 64, 0)
    both["conv_w"] = a("conv_w")[0].reshape(3, 2, FFN_PAIRS, P).transpose(3, 2, 1, 0)
    both["conv_b"] = a("conv_b")[0].reshape(2, FFN_PAIRS, P).transpose(2, 1, 0)
    both["gdn_conv"] = a("gdn_conv_2")[0].reshape(4, 12, P).transpose(2, 1, 0)
    both["a_log"] = a("gdn_a_log_2")[0].reshape(4, 1)
    both["dt_bias"] = a("gdn_dt_bias_2")[0].reshape(4, 1)
    both["gdn_norm"] = a("gdn_norm_2")[0].reshape(P, 1)
    both["w_qb"] = a("dsa_w_qb_2")[0].reshape(2, P, 256).transpose(1, 0, 2)
    both["w_qi"] = a("dsa_w_qi_2")[0].reshape(2, P, 256).transpose(1, 0, 2)
    both["w_kvb"] = a("dsa_w_kvb_2")[0]
    both["dq_norm"] = twice(a("dsa_q_norm_2")[0])
    both["dk_norm"] = twice(a("dsa_k_norm_2")[0])
    both["conv_dw"] = a("conv_dw_2")[0].reshape(CONV_TAPS, 2, P).transpose(2, 1, 0)
    both["dw_b"] = by_partition(a("conv_dw_b_2")[0], 2)
    both["ln_g"] = by_partition(a("conv_ln_g_2")[0], 2)
    both["ln_b"] = by_partition(a("conv_ln_b_2")[0], 2)
    both["xq_norm"] = a("xa_q_norm_2")[0].reshape(P, 1)
    both["xk_norm"] = a("xa_k_norm_2")[0].reshape(P, 1)
    return pack(NPAR, PAR, both)


def kernel(**inputs):
    import concourse.bacc as bacc
    from concourse.bass_utils import run_bass_kernel_spmd

    i = {n: np.ascontiguousarray(v) for n, v in inputs.items()}
    w_in = i["w_in"][0]
    q = w_in[:, :512].reshape(D, GROUPS, HG, DK).transpose(0, 2, 1, 3).reshape(D, 512)
    kv = w_in[:, 768:1280].reshape(D, 2, 2, GROUPS * DK).transpose(0, 2, 1, 3).reshape(D, 512)
    w_up = i["w_up"][0].reshape(D, 2, FFN_PAIRS, P).transpose(0, 2, 1, 3).reshape(D, 2 * FFN)
    w2 = i["w_in_2"][0]
    w_in2 = np.concatenate([w2[:, :2048], w2[:, 2056:2504], w2[:, 2440:2504], w2[:, 2048:2056], w2[:, 2504:]], 1)
    arrays = {
        "x": i["x"][0], "mem": i["mem"][0], "params": small_parameters(i), "consts": shape_constants(),
        "hots": bucket_one_hots(), "w_in": np.concatenate([q, w_in[:, 512:768], kv, w_in[:, 1280:]], 1), "cmp_w1": i["cmp_w1"][0].reshape(2, CMP_LEN * DK, P),
        "w_out": i["w_out"][0], "w_mk": i["w_mk"][0], "w_mv": i["w_mv"][0], "w_mq": i["w_mq"][0], "w_mo": i["w_mo"][0],
        "w_up": w_up, "w_down": i["w_down"][0], "mix_norm_post": i["mix_norm_post"], "mem_norm_post": i["mem_norm_post"],
        "ffn_norm_post": i["ffn_norm_post"],
        "mem2": i["mem_2"][0], "w_in2": w_in2, "w_out2": i["w_out_2"][0], "xa_wkv": i["xa_wkv_2"][0],
        "xa_wq": i["xa_wq_2"][0], "xa_wo": i["xa_wo_2"][0], "mlp_w1": i["mlp_w1_2"][0], "mlp_w2": i["mlp_w2_2"][0],
    }
    nc = bacc.Bacc("TRN2", target_bir_lowering=False, num_devices=1)
    feed, args = {}, {}
    for n, v in arrays.items():
        v = np.ascontiguousarray(v)
        feed[f"in_{n}"] = v
        args[n] = nc.dram_tensor(f"in_{n}", v.shape, mybir.dt.from_np(v.dtype), kind="ExternalInput").ap()
    out = nc.dram_tensor("out_x", (SEQ, D), F32, kind="ExternalOutput").ap()
    block_kernel(nc, args, out)
    r = run_bass_kernel_spmd(nc, [feed], core_ids=[0])
    return r.results[0]["out_x"].reshape(1, SEQ, D)
```
